# Optimizing a Trainium2 kernel written in Bass

```python
import math
import jax, jax.numpy as jnp
from jax import lax
import numpy as np
import jax
import jax.numpy as jnp

D_MODEL = 1024
BATCH = 1
SEQ = 512
DEPTH = 2

N_MIXERS = 2
N_A = (DEPTH + N_MIXERS - 1) // N_MIXERS
N_B = DEPTH // N_MIXERS

RWKV_HEAD = 64
RWKV_HEADS = D_MODEL // RWKV_HEAD
D_DECAY_LORA = max(32, int(round(1.8 * D_MODEL ** 0.5 / 32)) * 32)
D_AAA_LORA = max(32, int(round(1.8 * D_MODEL ** 0.5 / 32)) * 32)
D_MV_LORA = max(32, int(round(1.3 * D_MODEL ** 0.5 / 32)) * 32)
D_GATE_LORA = max(32, int(round(0.6 * D_MODEL ** 0.8 / 32)) * 32)
GN_EPS = RWKV_HEAD * 1e-5

ATT_HEADS = 16
ATT_HEAD_DIM = D_MODEL // ATT_HEADS
KV_LATENT = 128
IDX_HEADS = 8
IDX_DIM = 64
TOPK_MAX = 256
TOPK_DIV = 4
Q_BLOCK = 128
DSA_PROJ = ATT_HEADS * ATT_HEAD_DIM + KV_LATENT + IDX_HEADS * IDX_DIM + IDX_DIM + IDX_HEADS

REL_BUCKETS = 32
REL_MAX_DIST = 128

FFN_HIDDEN = -(-8 * D_MODEL // (3 * 256)) * 256

DEEPNORM_ALPHA = (2 * DEPTH) ** 0.25
DEEPNORM_BETA = (8 * DEPTH) ** -0.25
LN_EPS = 1e-5


def _layernorm(x, g, b):
    xf = x.astype(jnp.float32)
    mu = xf.mean(-1, keepdims=True)
    var = jnp.square(xf - mu).mean(-1, keepdims=True)
    y = (xf - mu) * lax.rsqrt(var + LN_EPS) * g.astype(jnp.float32) + b.astype(jnp.float32)
    return y.astype(x.dtype)

def _rmsnorm(x, g):
    xf = x.astype(jnp.float32)
    y = xf * lax.rsqrt(jnp.mean(xf * xf, -1, keepdims=True) + 1e-6) * g.astype(jnp.float32)
    return y.astype(x.dtype)

def _t5_bucket(n):
    n = jnp.maximum(n, 0)
    max_exact = REL_BUCKETS // 2
    nf = jnp.maximum(n, 1).astype(jnp.float32)
    large = max_exact + (jnp.log(nf / max_exact) / math.log(REL_MAX_DIST / max_exact)
                         * (REL_BUCKETS - max_exact)).astype(jnp.int32)
    large = jnp.minimum(large, REL_BUCKETS - 1)
    return jnp.where(n < max_exact, n, large)

def _rwkv7_step(S, inp):
    r_t, w_t, k_t, v_t, a_t, b_t = inp
    sa = jnp.einsum('bhij,bhj->bhi', S, a_t)
    S = S * w_t[:, :, None, :] + sa[..., None] * b_t[:, :, None, :] + v_t[..., None] * k_t[:, :, None, :]
    y = jnp.einsum('bhij,bhj->bhi', S, r_t)
    return S, y

def _rwkv7_time_mix(h, v_first, mu, w_rkv, w0, w1, w2, a0, a1, a2, vres,
                    g1, g2, k_k, k_a, r_k, lnx_g, lnx_b, w_out):
    B, T, D = h.shape
    H, N = RWKV_HEADS, RWKV_HEAD
    f32 = jnp.float32
    h_prev = jnp.pad(h, ((0, 0), (1, 0), (0, 0)))[:, :-1]
    xx = h_prev - h
    xs = h[None] + xx[None] * mu[:, None, None, :]
    r, k, v = jnp.einsum('pbtd,pde->pbte', xs[:3], w_rkv)
    xv, xw, xa, xg = xs[2], xs[3], xs[4], xs[5]
    w = -jax.nn.softplus(-(w0 + jnp.tanh(xw @ w1) @ w2)) - 0.5
    if vres is None:
        v_first = v
    else:
        v0, v1, v2 = vres
        v = v + (v_first - v) * jax.nn.sigmoid(v0 + (xv @ v1) @ v2)
    a = jax.nn.sigmoid(a0 + (xa @ a1) @ a2)
    g = jax.nn.sigmoid(xg @ g1) @ g2

    def heads(t):
        return t.reshape(B, T, H, N).astype(f32)

    kk = heads(k * k_k)
    kk = kk / jnp.maximum(jnp.sqrt(jnp.sum(kk * kk, -1, keepdims=True)), 1e-12)
    k = k * (1 + (a - 1) * k_a)
    rh, kh, vh, ah = heads(r), heads(k), heads(v), heads(a)
    decay = jnp.exp(-jnp.exp(heads(w)))

    def tm(t):
        return jnp.swapaxes(t, 0, 1)

    S0 = jnp.zeros((B, H, N, N), f32)
    _, y = lax.scan(_rwkv7_step, S0,
                    (tm(rh), tm(decay), tm(kh), tm(vh), tm(-kk), tm(kk * ah)))
    y = tm(y)
    ym = y.mean(-1, keepdims=True)
    yv = jnp.square(y - ym).mean(-1, keepdims=True)
    yn = ((y - ym) * lax.rsqrt(yv + GN_EPS)).reshape(B, T, D)
    yn = yn * lnx_g.astype(f32) + lnx_b.astype(f32)
    bonus = jnp.sum(rh * kh * r_k.astype(f32), -1, keepdims=True) * vh
    out = (yn + bonus.reshape(B, T, D)).astype(h.dtype) * g
    return out @ w_out, v_first

def _dsa_attention(h, w_in, kv_norm, w_uk, w_uv, w_out, rel_bias):
    B, T, D = h.shape
    H, dh = ATT_HEADS, ATT_HEAD_DIM
    f32 = jnp.float32
    proj = h @ w_in
    c1 = H * dh
    c2 = c1 + KV_LATENT
    c3 = c2 + IDX_HEADS * IDX_DIM
    c4 = c3 + IDX_DIM
    q = proj[..., :c1].reshape(B, T, H, dh)
    ckv = _rmsnorm(proj[..., c1:c2], kv_norm)
    q_idx = proj[..., c2:c3].reshape(B, T, IDX_HEADS, IDX_DIM)
    k_idx = proj[..., c3:c4]
    w_idx = proj[..., c4:] * (IDX_HEADS ** -0.5 * IDX_DIM ** -0.5)

    k_sel = min(TOPK_MAX, T // TOPK_DIV)
    nblk = T // Q_BLOCK

    def to_blocks(t):
        return jnp.swapaxes(t.reshape(B, nblk, Q_BLOCK, *t.shape[2:]), 0, 1)

    pos_blocks = jnp.arange(T, dtype=jnp.int32).reshape(nblk, Q_BLOCK)
    key_pos = jnp.arange(T, dtype=jnp.int32)

    def block(args):
        qb, qib, wib, tpos = args
        s = jnp.einsum('bthd,bsd->bths', qib, k_idx)
        score = jnp.einsum('bth,bths->bts', wib, jax.nn.relu(s))
        causal = key_pos[None, :] <= tpos[:, None]
        score = jnp.where(causal[None], score, -jnp.inf)
        _, idx = lax.top_k(score, k_sel)
        sel = jax.vmap(lambda kv, ix: kv[ix])(ckv, idx)
        q_lat = jnp.einsum('bthd,hdc->bthc', qb, w_uk)
        logits = jnp.einsum('bthc,btkc->bthk', q_lat, sel).astype(f32) * (dh ** -0.5)
        rel = tpos[None, :, None] - idx
        bias = jnp.moveaxis(rel_bias[_t5_bucket(rel)], -1, 2)
        logits = logits + bias.astype(f32)
        logits = jnp.where((rel >= 0)[:, :, None, :], logits, -jnp.inf)
        p = jax.nn.softmax(logits, axis=-1).astype(h.dtype)
        o_lat = jnp.einsum('bthk,btkc->bthc', p, sel)
        o = jnp.einsum('bthc,hcd->bthd', o_lat, w_uv)
        return o.reshape(B, Q_BLOCK, H * dh)

    out = lax.map(block, (to_blocks(q), to_blocks(q_idx), to_blocks(w_idx), pos_blocks))
    out = jnp.swapaxes(out, 0, 1).reshape(B, T, H * dh)
    return out @ w_out

def _swiglu(h, w_in, w_out):
    gate, up = jnp.split(h @ w_in, 2, axis=-1)
    return (jax.nn.silu(gate) * up) @ w_out

def first_inputs(seed: int = 0) -> dict:
    key = jax.random.key(seed)
    ks = iter(jax.random.split(key, 48))
    f32 = jnp.float32
    D = D_MODEL

    def nrm(shape, scale):
        return jax.random.normal(next(ks), shape, f32) * scale

    inp = {}
    inp['x'] = nrm((BATCH, SEQ, D), 1.0)
    inp['c'] = nrm((BATCH, D), 1.0)
    inp['ada_w'] = nrm((DEPTH, D, 6 * D), 0.5 * D ** -0.5)
    inp['ada_b'] = nrm((DEPTH, 6 * D), 0.02)
    inp['ln_g'] = 1.0 + nrm((DEPTH, 2, D), 0.02)
    inp['ln_b'] = nrm((DEPTH, 2, D), 0.02)
    inp['ffn_w_in'] = nrm((DEPTH, D, 2 * FFN_HIDDEN), D ** -0.5)
    inp['ffn_w_out'] = nrm((DEPTH, FFN_HIDDEN, D), FFN_HIDDEN ** -0.5 * DEEPNORM_BETA)
    inp['rwkv_mu'] = jax.random.uniform(next(ks), (N_A, 6, D), f32)
    inp['rwkv_w_rkv'] = nrm((N_A, 3, D, D), D ** -0.5)
    inp['rwkv_w0'] = jax.random.uniform(next(ks), (N_A, D), f32, -4.0, 1.0)
    inp['rwkv_w1'] = nrm((N_A, D, D_DECAY_LORA), D ** -0.5)
    inp['rwkv_w2'] = nrm((N_A, D_DECAY_LORA, D), 0.1 * D_DECAY_LORA ** -0.5)
    inp['rwkv_a0'] = nrm((N_A, D), 0.5)
    inp['rwkv_a1'] = nrm((N_A, D, D_AAA_LORA), D ** -0.5)
    inp['rwkv_a2'] = nrm((N_A, D_AAA_LORA, D), 0.1 * D_AAA_LORA ** -0.5)
    inp['rwkv_v0'] = nrm((N_A - 1, D), 0.5)
    inp['rwkv_v1'] = nrm((N_A - 1, D, D_MV_LORA), D ** -0.5)
    inp['rwkv_v2'] = nrm((N_A - 1, D_MV_LORA, D), 0.1 * D_MV_LORA ** -0.5)
    inp['rwkv_g1'] = nrm((N_A, D, D_GATE_LORA), D ** -0.5)
    inp['rwkv_g2'] = nrm((N_A, D_GATE_LORA, D), D_GATE_LORA ** -0.5)
    inp['rwkv_k_k'] = 0.85 + nrm((N_A, D), 0.02)
    inp['rwkv_k_a'] = 1.0 + nrm((N_A, D), 0.02)
    inp['rwkv_r_k'] = nrm((N_A, RWKV_HEADS, RWKV_HEAD), 0.1)
    inp['rwkv_lnx_g'] = 1.0 + nrm((N_A, D), 0.02)
    inp['rwkv_lnx_b'] = nrm((N_A, D), 0.02)
    inp['rwkv_w_out'] = nrm((N_A, D, D), D ** -0.5 * DEEPNORM_BETA)
    inp['dsa_w_in'] = nrm((N_B, D, DSA_PROJ), D ** -0.5)
    inp['dsa_kv_norm'] = 1.0 + nrm((N_B, KV_LATENT), 0.02)
    inp['dsa_w_uk'] = nrm((N_B, ATT_HEADS, ATT_HEAD_DIM, KV_LATENT), ATT_HEAD_DIM ** -0.5)
    inp['dsa_w_uv'] = nrm((N_B, ATT_HEADS, KV_LATENT, ATT_HEAD_DIM), KV_LATENT ** -0.5)
    inp['dsa_w_out'] = nrm((N_B, ATT_HEADS * ATT_HEAD_DIM, D),
                           (ATT_HEADS * ATT_HEAD_DIM) ** -0.5 * DEEPNORM_BETA)
    inp['rel_bias'] = nrm((REL_BUCKETS, ATT_HEADS), 0.3)
    return inp

def first_block(x, c, ada_w, ada_b, ln_g, ln_b, ffn_w_in, ffn_w_out,
              rwkv_mu, rwkv_w_rkv, rwkv_w0, rwkv_w1, rwkv_w2, rwkv_a0, rwkv_a1, rwkv_a2,
              rwkv_v0, rwkv_v1, rwkv_v2, rwkv_g1, rwkv_g2, rwkv_k_k, rwkv_k_a, rwkv_r_k,
              rwkv_lnx_g, rwkv_lnx_b, rwkv_w_out,
              dsa_w_in, dsa_kv_norm, dsa_w_uk, dsa_w_uv, dsa_w_out, rel_bias):
    cond = jax.nn.silu(c)
    v_first = None
    for i in range(DEPTH):
        mod = cond @ ada_w[i] + ada_b[i]
        sh1, sc1, gt1, sh2, sc2, gt2 = jnp.split(mod[:, None, :], 6, axis=-1)
        hin = x * (1 + sc1) + sh1
        j = i // N_MIXERS
        if i % N_MIXERS == 0:
            vres = None if j == 0 else (rwkv_v0[j - 1], rwkv_v1[j - 1], rwkv_v2[j - 1])
            y, v_first = _rwkv7_time_mix(
                hin, v_first, rwkv_mu[j], rwkv_w_rkv[j], rwkv_w0[j], rwkv_w1[j], rwkv_w2[j],
                rwkv_a0[j], rwkv_a1[j], rwkv_a2[j], vres, rwkv_g1[j], rwkv_g2[j],
                rwkv_k_k[j], rwkv_k_a[j], rwkv_r_k[j], rwkv_lnx_g[j], rwkv_lnx_b[j], rwkv_w_out[j])
        else:
            y = _dsa_attention(hin, dsa_w_in[j], dsa_kv_norm[j], dsa_w_uk[j], dsa_w_uv[j],
                               dsa_w_out[j], rel_bias)
        x = _layernorm(DEEPNORM_ALPHA * x + (1 + gt1) * y, ln_g[i, 0], ln_b[i, 0])
        hin = x * (1 + sc2) + sh2
        y = _swiglu(hin, ffn_w_in[i], ffn_w_out[i])
        x = _layernorm(DEEPNORM_ALPHA * x + (1 + gt2) * y, ln_g[i, 1], ln_b[i, 1])
    return x


DEPTH_2 = 1

HEAD_DIM = 64
N_HEADS_NSA = 8
N_KV_NSA = 2
GROUP_NSA = N_HEADS_NSA // N_KV_NSA
N_HEADS_FOX = 8
MIX_WIDTH = (N_HEADS_NSA + N_HEADS_FOX) * HEAD_DIM
NSA_Q_W = N_HEADS_NSA * HEAD_DIM
NSA_KV_W = N_KV_NSA * HEAD_DIM
FOX_W = N_HEADS_FOX * HEAD_DIM
PROJ_SIZES = (NSA_Q_W, NSA_KV_W, NSA_KV_W, NSA_KV_W, NSA_KV_W, NSA_KV_W, NSA_KV_W,
              3 * N_HEADS_NSA, FOX_W, FOX_W, FOX_W, N_HEADS_FOX)
IN_WIDTH = sum(PROJ_SIZES)
D_FF = 2816
D_PLE = 256
ROPE_THETA = 500000.0
ROT_DIM = HEAD_DIM // 4
CMP_BLOCK = 32
CMP_STRIDE = 16
CMP_HIDDEN = 256
SEL_BLOCK = 64
SEL_TOPK = 16
WINDOW = 512
NSA_Q_BLOCK = 32
FOX_Q_BLOCK = 128
FORCED_SCORE = 1e6
EPS = 1e-6
NEG = -1e30


def rmsnorm(x, g):
    xf = x.astype(jnp.float32)
    y = xf * lax.rsqrt(jnp.mean(xf * xf, axis=-1, keepdims=True) + EPS)
    return (y * g.astype(jnp.float32)).astype(x.dtype)

def swiglu(x, wg, wu, wd):
    return (jax.nn.silu(x @ wg) * (x @ wu)) @ wd

def split_heads(t, n):
    b, s, _ = t.shape
    return t.reshape(b, s, n, HEAD_DIM).transpose(0, 2, 1, 3)

def merge_heads(t):
    b, n, s, d = t.shape
    return t.transpose(0, 2, 1, 3).reshape(b, s, n * d)

def rope_tables(seq):
    pos = jnp.arange(seq, dtype=jnp.float32)
    inv = ROPE_THETA ** (-jnp.arange(0, ROT_DIM, 2, dtype=jnp.float32) / ROT_DIM)
    ang = pos[:, None] * inv[None, :]
    return jnp.cos(ang), jnp.sin(ang)

def partial_rope(x, cos, sin):
    half = ROT_DIM // 2
    xf = x.astype(jnp.float32)
    x1, x2, rest = xf[..., :half], xf[..., half:ROT_DIM], xf[..., ROT_DIM:]
    out = jnp.concatenate([x1 * cos - x2 * sin, x2 * cos + x1 * sin, rest], axis=-1)
    return out.astype(x.dtype)

def masked_softmax(s, mask):
    return jax.nn.softmax(jnp.where(mask, s.astype(jnp.float32), NEG), axis=-1)

def compress_blocks(tok, pos_emb, w1, w2):
    s = tok.shape[2]
    n_cmp = (s - CMP_BLOCK) // CMP_STRIDE + 1
    idx = np.arange(n_cmp)[:, None] * CMP_STRIDE + np.arange(CMP_BLOCK)[None, :]
    blk = tok[:, :, idx, :] + pos_emb
    blk = blk.reshape(blk.shape[0], blk.shape[1], n_cmp, CMP_BLOCK * HEAD_DIM)
    return jax.nn.silu(blk @ w1) @ w2

def nsa_attention(q, k_cmp, v_cmp, k_slc, v_slc, k_win, v_win, gates):
    b, h, s, d = q.shape
    qg = q.reshape(b, N_KV_NSA, GROUP_NSA, s, d)
    gg_all = gates.reshape(b, N_KV_NSA, GROUP_NSA, s, 3)
    n_cmp = k_cmp.shape[2]
    n_sel = s // SEL_BLOCK
    top = min(SEL_TOPK, n_sel)
    cmp_start = np.arange(n_cmp) * CMP_STRIDE
    cmp_end = jnp.asarray(cmp_start + CMP_BLOCK - 1)
    sel_start = np.arange(n_sel) * SEL_BLOCK
    overlap = jnp.asarray(((cmp_start[:, None] <= sel_start[None, :] + SEL_BLOCK - 1)
                           & (cmp_start[:, None] + CMP_BLOCK - 1 >= sel_start[None, :])).astype(np.float32))
    ks_blocks = k_slc.reshape(b, N_KV_NSA, n_sel, SEL_BLOCK, d)
    vs_blocks = v_slc.reshape(b, N_KV_NSA, n_sel, SEL_BLOCK, d)
    pad = ((0, 0), (0, 0), (WINDOW, 0), (0, 0))
    kw_pad = jnp.pad(k_win, pad)
    vw_pad = jnp.pad(v_win, pad)
    bi = np.arange(b)[:, None, None, None]
    hi = np.arange(N_KV_NSA)[None, :, None, None]
    blk_j = jnp.arange(n_sel)
    scale = HEAD_DIM ** -0.5
    qn = NSA_Q_BLOCK

    def block(qb):
        t0 = qb * qn
        tpos = t0 + jnp.arange(qn)
        qq = lax.dynamic_slice_in_dim(qg, t0, qn, axis=3)
        gg = lax.dynamic_slice_in_dim(gg_all, t0, qn, axis=3)
        m_c = cmp_end[None, :] <= tpos[:, None]
        s_c = jnp.einsum('bkgqd,bknd->bkgqn', qq, k_cmp) * scale
        p_c = masked_softmax(s_c, m_c) * m_c
        o_c = jnp.einsum('bkgqn,bknd->bkgqd', p_c.astype(v_cmp.dtype), v_cmp)
        imp = jnp.einsum('bkgqn,nj->bkqj', p_c, overlap)
        cur = tpos // SEL_BLOCK
        valid = blk_j[None, :] <= cur[:, None]
        forced = (blk_j[None, :] == 0) | (blk_j[None, :] == cur[:, None]) | (blk_j[None, :] == cur[:, None] - 1)
        imp = jnp.where(valid, jnp.where(forced, FORCED_SCORE, imp), -1.0)
        vals, sel = lax.top_k(imp, top)
        kg = ks_blocks[bi, hi, sel].reshape(b, N_KV_NSA, qn, top * SEL_BLOCK, d)
        vg = vs_blocks[bi, hi, sel].reshape(b, N_KV_NSA, qn, top * SEL_BLOCK, d)
        kpos = (sel[..., None] * SEL_BLOCK + jnp.arange(SEL_BLOCK)).reshape(b, N_KV_NSA, qn, top * SEL_BLOCK)
        m_s = (kpos <= tpos[:, None]) & jnp.repeat(vals >= 0, SEL_BLOCK, axis=-1)
        s_s = jnp.einsum('bkgqd,bkqnd->bkgqn', qq, kg) * scale
        p_s = masked_softmax(s_s, m_s[:, :, None])
        o_s = jnp.einsum('bkgqn,bkqnd->bkgqd', p_s.astype(vg.dtype), vg)
        kw = lax.dynamic_slice_in_dim(kw_pad, t0, qn + WINDOW, axis=2)
        vw = lax.dynamic_slice_in_dim(vw_pad, t0, qn + WINDOW, axis=2)
        kpos_w = t0 - WINDOW + jnp.arange(qn + WINDOW)
        diff = tpos[:, None] - kpos_w[None, :]
        m_w = (kpos_w[None, :] >= 0) & (diff >= 0) & (diff < WINDOW)
        s_w = jnp.einsum('bkgqd,bknd->bkgqn', qq, kw) * scale
        p_w = masked_softmax(s_w, m_w)
        o_w = jnp.einsum('bkgqn,bknd->bkgqd', p_w.astype(vw.dtype), vw)
        return gg[..., 0:1] * o_c + gg[..., 1:2] * o_s + gg[..., 2:3] * o_w

    out = lax.map(block, jnp.arange(s // qn))
    return jnp.moveaxis(out, 0, 3).reshape(b, h, s, d)

def forgetting_attention(q, k, v, log_f):
    b, h, s, d = q.shape
    c = jnp.cumsum(log_f, axis=-1)
    kpos = jnp.arange(s)
    scale = HEAD_DIM ** -0.5
    qn = FOX_Q_BLOCK

    def block(qb):
        t0 = qb * qn
        tpos = t0 + jnp.arange(qn)
        qq = lax.dynamic_slice_in_dim(q, t0, qn, axis=2)
        cq = lax.dynamic_slice_in_dim(c, t0, qn, axis=2)
        logits = (jnp.einsum('bhqd,bhsd->bhqs', qq, k).astype(jnp.float32) * scale
                  + cq[..., :, None] - c[:, :, None, :])
        p = masked_softmax(logits, kpos[None, :] <= tpos[:, None])
        return jnp.einsum('bhqs,bhsd->bhqd', p.astype(v.dtype), v)

    out = lax.map(block, jnp.arange(s // qn))
    return jnp.moveaxis(out, 0, 2).reshape(b, h, s, d)

def second_inputs(seed: int = 0) -> dict:
    key = jax.random.key(seed)
    ks = iter(jax.random.split(key, 40))
    nrm = lambda shape, sc: jax.random.normal(next(ks), shape, jnp.float32) * sc
    gain = lambda n: 1.0 + nrm((DEPTH_2, n), 0.05)
    L = DEPTH_2
    return {
        'x': nrm((BATCH, SEQ, D_MODEL), 1.0),
        'p': nrm((DEPTH_2, BATCH, SEQ, D_PLE), 1.0),
        'ffn1_norm': gain(D_MODEL),
        'ffn1_wg': nrm((L, D_MODEL, D_FF), D_MODEL ** -0.5),
        'ffn1_wu': nrm((L, D_MODEL, D_FF), D_MODEL ** -0.5),
        'ffn1_wd': nrm((L, D_FF, D_MODEL), D_FF ** -0.5),
        'mix_norm': gain(D_MODEL),
        'w_in': nrm((L, D_MODEL, IN_WIDTH), D_MODEL ** -0.5),
        'b_forget': 4.0 + nrm((L, N_HEADS_FOX), 0.5),
        'q_norm_nsa': gain(HEAD_DIM),
        'k_norm_cmp': gain(HEAD_DIM),
        'k_norm_slc': gain(HEAD_DIM),
        'k_norm_win': gain(HEAD_DIM),
        'cmp_pos_k': nrm((L, CMP_BLOCK, HEAD_DIM), 0.02),
        'cmp_pos_v': nrm((L, CMP_BLOCK, HEAD_DIM), 0.02),
        'cmp_k_w1': nrm((L, CMP_BLOCK * HEAD_DIM, CMP_HIDDEN), (CMP_BLOCK * HEAD_DIM) ** -0.5),
        'cmp_k_w2': nrm((L, CMP_HIDDEN, HEAD_DIM), CMP_HIDDEN ** -0.5),
        'cmp_v_w1': nrm((L, CMP_BLOCK * HEAD_DIM, CMP_HIDDEN), (CMP_BLOCK * HEAD_DIM) ** -0.5),
        'cmp_v_w2': nrm((L, CMP_HIDDEN, HEAD_DIM), CMP_HIDDEN ** -0.5),
        'q_norm_fox': gain(HEAD_DIM),
        'k_norm_fox': gain(HEAD_DIM),
        'out_norm_nsa': gain(NSA_Q_W),
        'out_norm_fox': gain(FOX_W),
        'w_out': nrm((L, MIX_WIDTH, D_MODEL), MIX_WIDTH ** -0.5),
        'ffn2_norm': gain(D_MODEL),
        'ffn2_wg': nrm((L, D_MODEL, D_FF), D_MODEL ** -0.5),
        'ffn2_wu': nrm((L, D_MODEL, D_FF), D_MODEL ** -0.5),
        'ffn2_wd': nrm((L, D_FF, D_MODEL), D_FF ** -0.5),
        'ple_gate_norm': gain(D_MODEL),
        'ple_w_gate': nrm((L, D_MODEL, D_MODEL), D_MODEL ** -0.5),
        'ple_w_proj': nrm((L, D_PLE, D_MODEL), D_PLE ** -0.5),
        'ple_norm': gain(D_MODEL),
    }

def second_block(x, p, ffn1_norm, ffn1_wg, ffn1_wu, ffn1_wd, mix_norm, w_in, b_forget,
              q_norm_nsa, k_norm_cmp, k_norm_slc, k_norm_win, cmp_pos_k, cmp_pos_v,
              cmp_k_w1, cmp_k_w2, cmp_v_w1, cmp_v_w2, q_norm_fox, k_norm_fox,
              out_norm_nsa, out_norm_fox, w_out, ffn2_norm, ffn2_wg, ffn2_wu, ffn2_wd,
              ple_gate_norm, ple_w_gate, ple_w_proj, ple_norm):
    b, s, _ = x.shape
    cos, sin = rope_tables(s)
    split_points = [int(v) for v in np.cumsum(PROJ_SIZES)[:-1]]
    h = x
    for i in range(DEPTH_2):
        h = h + 0.5 * swiglu(rmsnorm(h, ffn1_norm[i]), ffn1_wg[i], ffn1_wu[i], ffn1_wd[i])
        a = rmsnorm(h, mix_norm[i])
        u = a @ w_in[i]
        (qa, kc, vc, ksl, vsl, kwn, vwn, ga, qf, kf, vf, fl) = jnp.split(u, split_points, axis=-1)
        q_a = partial_rope(rmsnorm(split_heads(qa, N_HEADS_NSA), q_norm_nsa[i]), cos, sin)
        kc_tok = partial_rope(split_heads(kc, N_KV_NSA), cos, sin)
        k_cmp = rmsnorm(compress_blocks(kc_tok, cmp_pos_k[i], cmp_k_w1[i], cmp_k_w2[i]), k_norm_cmp[i])
        v_cmp = compress_blocks(split_heads(vc, N_KV_NSA), cmp_pos_v[i], cmp_v_w1[i], cmp_v_w2[i])
        k_slc = partial_rope(rmsnorm(split_heads(ksl, N_KV_NSA), k_norm_slc[i]), cos, sin)
        k_win = partial_rope(rmsnorm(split_heads(kwn, N_KV_NSA), k_norm_win[i]), cos, sin)
        gates = jax.nn.sigmoid(ga).reshape(b, s, N_HEADS_NSA, 3).transpose(0, 2, 1, 3)
        o_a = nsa_attention(q_a, k_cmp, v_cmp, k_slc, split_heads(vsl, N_KV_NSA),
                            k_win, split_heads(vwn, N_KV_NSA), gates)
        q_b = rmsnorm(split_heads(qf, N_HEADS_FOX), q_norm_fox[i])
        k_b = rmsnorm(split_heads(kf, N_HEADS_FOX), k_norm_fox[i])
        log_f = jax.nn.log_sigmoid((fl + b_forget[i]).astype(jnp.float32)).transpose(0, 2, 1)
        o_b = forgetting_attention(q_b, k_b, split_heads(vf, N_HEADS_FOX), log_f)
        mixed = jnp.concatenate([rmsnorm(merge_heads(o_a), out_norm_nsa[i]),
                                 rmsnorm(merge_heads(o_b), out_norm_fox[i])], axis=-1)
        h = h + mixed @ w_out[i]
        h = h + 0.5 * swiglu(rmsnorm(h, ffn2_norm[i]), ffn2_wg[i], ffn2_wu[i], ffn2_wd[i])
        gate = jax.nn.sigmoid(rmsnorm(h, ple_gate_norm[i]) @ ple_w_gate[i])
        e = rmsnorm(p[i] @ ple_w_proj[i], ple_norm[i])
        h = h + gate * e
    return h


def setup_inputs(seed=0):
    out = dict(first_inputs(seed))
    for name, value in second_inputs(seed + 1).items():
        if name != "x":
            out[name + "_2"] = value
    return out


def reference(
    x, c, ada_w, ada_b, ln_g, ln_b, ffn_w_in, ffn_w_out, rwkv_mu, rwkv_w_rkv, rwkv_w0, rwkv_w1,
    rwkv_w2, rwkv_a0, rwkv_a1, rwkv_a2, rwkv_v0, rwkv_v1, rwkv_v2, rwkv_g1, rwkv_g2, rwkv_k_k,
    rwkv_k_a, rwkv_r_k, rwkv_lnx_g, rwkv_lnx_b, rwkv_w_out, dsa_w_in, dsa_kv_norm, dsa_w_uk,
    dsa_w_uv, dsa_w_out, rel_bias, p_2, ffn1_norm_2, ffn1_wg_2, ffn1_wu_2, ffn1_wd_2,
    mix_norm_2, w_in_2, b_forget_2, q_norm_nsa_2, k_norm_cmp_2, k_norm_slc_2, k_norm_win_2,
    cmp_pos_k_2, cmp_pos_v_2, cmp_k_w1_2, cmp_k_w2_2, cmp_v_w1_2, cmp_v_w2_2, q_norm_fox_2,
    k_norm_fox_2, out_norm_nsa_2, out_norm_fox_2, w_out_2, ffn2_norm_2, ffn2_wg_2, ffn2_wu_2,
    ffn2_wd_2, ple_gate_norm_2, ple_w_gate_2, ple_w_proj_2, ple_norm_2,
):
    x = first_block(
        x, c, ada_w, ada_b, ln_g, ln_b, ffn_w_in, ffn_w_out, rwkv_mu, rwkv_w_rkv, rwkv_w0,
        rwkv_w1, rwkv_w2, rwkv_a0, rwkv_a1, rwkv_a2, rwkv_v0, rwkv_v1, rwkv_v2, rwkv_g1,
        rwkv_g2, rwkv_k_k, rwkv_k_a, rwkv_r_k, rwkv_lnx_g, rwkv_lnx_b, rwkv_w_out, dsa_w_in,
        dsa_kv_norm, dsa_w_uk, dsa_w_uv, dsa_w_out, rel_bias,
    )
    return second_block(
        x, p_2, ffn1_norm_2, ffn1_wg_2, ffn1_wu_2, ffn1_wd_2, mix_norm_2, w_in_2, b_forget_2,
        q_norm_nsa_2, k_norm_cmp_2, k_norm_slc_2, k_norm_win_2, cmp_pos_k_2, cmp_pos_v_2,
        cmp_k_w1_2, cmp_k_w2_2, cmp_v_w1_2, cmp_v_w2_2, q_norm_fox_2, k_norm_fox_2,
        out_norm_nsa_2, out_norm_fox_2, w_out_2, ffn2_norm_2, ffn2_wg_2, ffn2_wu_2, ffn2_wd_2,
        ple_gate_norm_2, ple_w_gate_2, ple_w_proj_2, ple_norm_2,
    )


_drawn_inputs = setup_inputs


def setup_inputs(seed=0):
    import zlib

    import numpy as np

    out = dict(_drawn_inputs(seed))
    spreads = {}
    factors = {'rwkv_w1': 8.0,
     'rwkv_w2': 8.0,
     'rwkv_a1': 4.354,
     'rwkv_a2': 4.32,
     'rwkv_k_k': 8.0,
     'rwkv_k_a': 6.0,
     'rwkv_lnx_g': 8.0,
     'rwkv_lnx_b': 5.192,
     'dsa_kv_norm': 6.871,
     'q_norm_nsa_2': 4.349,
     'k_norm_cmp_2': 7.334,
     'k_norm_slc_2': 7.906,
     'k_norm_win_2': 7.759,
     'cmp_pos_k_2': 8.0,
     'cmp_pos_v_2': 5.118,
     'q_norm_fox_2': 3.458,
     'k_norm_fox_2': 3.029,
     'ffn2_norm_2': 4.147,
     'ple_gate_norm_2': 26.316,
     'ple_norm_2': 10.834}
    for name, (base, spread) in spreads.items():
        noise = np.random.default_rng([zlib.crc32(name.encode()), seed]).standard_normal(out[name].shape)
        drawn = base * np.exp(spread * noise) if base else spread * noise
        out[name] = jnp.asarray(drawn.astype(out[name].dtype))
    for name, factor in factors.items():
        out[name] = (out[name] * factor).astype(out[name].dtype)
    return out
```

```python
import math
from contextlib import ExitStack

import numpy as np
import concourse.bass as bass
from concourse import mybir

P = 128
T = 512
D = 1024
KT = D // P
HID = 2816
HT = HID // P
CH = 64
NCH = T // CH
HD = 64
QT = T // P
SLOT = 28 * P
ALPHA = 4.0 ** 0.25
DECAY = math.exp(-0.5)
NEG = -1e30
TAKEN = -3e38
NCMP = 31
CMP_L = 32
CMP_S = 16
BIAS_LEN = T + P
F32 = mybir.dt.float32
ACT = mybir.ActivationFunctionType
ALU = mybir.AluOpType
AX = mybir.AxisListType


def columns(*parts):
    at, out = 0, {}
    for name, width in parts:
        out[name] = (at, width)
        at += width
    out["all"] = (0, at)
    return out


CA = columns(("ident", P), ("blockones", P), ("ones", P), ("ln_eps", 1), ("gn_eps", 1), ("rms_eps", 1))
CR = columns(("strict", P), ("incl", P), *[(f"level{k}", P) for k in range(6)], ("reset", T))
CB = columns(("flip", P), ("causal", T), ("cos", T), ("sin", T), ("rot", P), ("cmp_mask", QT * P),
             ("cmp_valid", QT), ("onehot", BIAS_LEN))
VC = columns(("c", KT), ("ada_b", 96), ("ln_g", 32), ("ln_b", 32), ("mu", 48), ("pair", 56), ("ffn1", KT),
             ("mix", KT), ("ffn2", KT), ("ple_gate", KT), ("ple", KT), ("out_norm", KT), ("kv_norm", 1),
             ("q_nsa", 1), ("k_cmp", 1), ("k_slc", 1), ("k_win", 1), ("q_fox", 1), ("k_fox", 1),
             ("b_forget", 1), ("pos_k", CMP_L), ("pos_v", CMP_L))


class Steps:

    def __init__(self, sem, names):
        self.sem, self.names, self.next = sem, list(names), 0
        self.index = {n: k + 1 for k, n in enumerate(self.names)}
        assert len(self.index) == len(self.names)

    def enter(self, eng):
        eng.sem_inc(self.sem, len(self.names))

    def step(self, name):
        assert self.names[self.next % len(self.names)] == name, (self.names[self.next % len(self.names)], name)
        self.next += 1
        return self.sem, 1

    def __call__(self, name, turn=0, before=0):
        return self.sem, turn * len(self.names) + (len(self.names) * (1 - before) + self.index[name])


def build(nc, d):
    ctx = ExitStack()
    with ctx:
        def sem(name):
            return ctx.enter_context(nc.semaphore(name))

        def keep(name, shape, scope=ctx):
            return scope.enter_context(nc.sbuf_tensor(name, shape, F32))

        def steps(name, names):
            return Steps(sem(name), names)

        waited = sem("waited")

        def reached(who, name, turn=0):
            return who(name, turn)

        def alone(eng):
            eng.sem_inc(waited, 1)

        ca = keep("const_all", [P, CA["all"][1]])
        vec = keep("vectors", [P, VC["all"][1]])
        mods = keep("modulation", [P, 96])
        x = keep("residual", [P, KT, T])
        hin = keep("branch_in", [P, KT, T + 1])
        h = hin[:, :, 1:T + 1]
        slot = [keep(f"weights{s}", [P, SLOT]) for s in range(2)]
        ps = ctx.enter_context(nc.psum_tensor("psum", [P, 8, T], F32))

        def const(name, table=ca, where=CA):
            a, n = where[name]
            return table[:, a:a + n]

        ident, blockones, ones = const("ident"), const("blockones"), const("ones")

        def vcol(name, k=0):
            a = VC[name][0] + k
            return vec[:, a:a + 1]

        def mod(layer, part, j):
            a = layer * 48 + part * 8 + j
            return mods[:, a:a + 1]
        SH1, SC1, GT1, SH2, SC2, GT2 = range(6)

        filled = [sem(f"slot{s}_filled") for s in range(2)]
        planned = [0, 0]
        last_use = [None, None]

        class Loads:

            def __init__(self, s, n, who, name):
                self.s, self.base, self.who, self.name = s, planned[s], who, name
                self.before = last_use[s]
                planned[s] += n
                last_use[s] = (who, name, n - 1)

                self.arrival = filled[s], 16

            def slot(self, src):
                return slot[self.s][:, 0:src.shape[-1]]

            def vacated(self, k=None):
                return reached(*self.before) if k is None else self.who(self.name, k, 1)

            def arrived(self, k=0):
                return filled[self.s], k * 16 + 16 * (self.base + 1)

        def wtile(s, k, rows=P, width=P, at=0):
            return slot[s][0:rows, at + k * width:at + (k + 1) * width]

        def row(name, k):
            return d[name][bass.ds(k, 1), :, :].rearrange("a p n -> (a p) n")

        def mm(out, lhsT, rhs, start=True, stop=True):
            return nc.tensor.matmul(out, lhsT, rhs, start=start, stop=stop)

        def column(t, k):
            return t[:, bass.ds(k, 1)]

        def tile_of(t, k):
            return t[:, bass.ds(k, 1), :].rearrange("p a n -> p (a n)")

        programs = {"sp": [], "pe": [], "act": [], "dve": [], "pool": []}

        def phase(**engines):
            for name, program in engines.items():
                programs[name].append(program)

        tables_in = sem("tables_in")
        x_in = sem("x_in")
        crd_in = sem("recurrence_constants_in")
        att_in = sem("attention_constants_in")

        def modulation():
            pe_done = steps("mod_pe", ["products0", "products1"])
            act_done = steps("mod_act", ["cond"])
            dve_done = steps("mod_dve", ["biased0", "biased1"])
            loads = [Loads(s, 16, pe_done, f"products{s}") for s in range(2)]
            ready = sem("modulation_ready")
            cond = keep("cond", [P, KT])

            def sp(sp):
                sp.dma_start(ca[:, :], d["const_all"][:, :]).then_inc(tables_in, 16)
                sp.dma_start(vec[:, :], d["vectors"][:, :]).then_inc(tables_in, 16)
                with sp.Fori(0, 16) as i:
                    for s in range(2):
                        sp.wait_ge(*loads[s].vacated(i))
                        sp.dma_start(loads[s].slot(row("ada", i * 2 + s)), row("ada", i * 2 + s)).then_inc(*loads[s].arrival)

            def act(act):
                act_done.enter(act)
                act.dma_start(x[:, :, :], d["x"][:, :, :]).then_inc(x_in, 16)
                act.wait_ge(tables_in, 32)
                a, n = VC["c"]
                nc.scalar.activation(cond[:, :], vec[:, a:a + n], ACT.Silu).then_inc(*act_done.step("cond"))

            def pe(pe):
                pe_done.enter(pe)
                pe.wait_ge(*act_done("cond"))
                with pe.Fori(0, 16) as i:
                    for s in range(2):
                        pe.wait_ge(*loads[s].arrived(i))
                        pe.wait_ge(*dve_done(f"biased{s}", i, 1))
                        for m in range(3):
                            for k in range(KT):
                                last = mm(ps[:, s, m:m + 1], wtile(s, m * KT + k), cond[:, k:k + 1], k == 0, k == KT - 1)
                        last.then_inc(*pe_done.step(f"products{s}"))

            def dve(dve):
                dve_done.enter(dve)
                dve.wait_ge(tables_in, 32)
                with dve.Fori(0, 16) as i:
                    for s in range(2):
                        dve.wait_ge(*pe_done(f"products{s}", i))
                        alone(dve)
                        nc.vector.tensor_tensor(
                            mods[:, bass.ds(i * 6 + s * 3, 3)], ps[:, s, 0:3],
                            vec[:, bass.ds(i * 6 + (s * 3 + VC["ada_b"][0]), 3)], ALU.add).then_inc(*dve_done.step(f"biased{s}"))
                dve.wait_ge(*dve_done("biased1", 15))
                for a in (8, 32, 56, 80):
                    nc.vector.tensor_scalar(mods[:, a:a + 16], mods[:, a:a + 16], 1.0, None, ALU.add).then_inc(ready, 1)

            phase(sp=sp, act=act, pe=pe, dve=dve)
            return ready, 4

        MIX = ["r", "k", "v", "w", "a", "g"]

        def time_mix_inputs(scope, mods_ready):
            xs = {m: keep(f"mixed_{m}", [P, KT, T], scope) for m in "rkv"}
            lora = {m: keep(f"lora_{m}", [P, T], scope) for m in ("w", "a", "g0", "g1")}
            pe_done = steps("mix_pe", [f"lora{j}" for j in range(KT)])
            act_done = steps("mix_act", [f"hin{j}" for j in range(KT)] + ["w", "a", "g0", "g1"])
            dve_done = steps("mix_dve", ["zero"] + [f"{n}{j}" for j in range(KT) for n in ["xx"] + MIX])
            zeroed = sem("gate_rows_zeroed")
            loads = Loads(0, 1, pe_done, f"lora{KT - 1}")
            with ExitStack() as own:
                xx = keep("token_shift", [P, 2, T], own)
                tmp = keep("mixed_low_rank", [P, 3, 2, T], own)

            def sp(sp):
                sp.wait_ge(*loads.vacated())
                sp.dma_start(loads.slot(row("lora1", 0)), row("lora1", 0)).then_inc(*loads.arrival)

            def act(act):
                act_done.enter(act)
                act.wait_ge(x_in, 16)
                act.wait_ge(*mods_ready)
                for j in range(KT):
                    nc.scalar.activation(h[:, j, :], x[:, j, :], ACT.Identity, bias=mod(0, SH1, j),
                                                    scale=mod(0, SC1, j)).then_inc(*act_done.step(f"hin{j}"))
                act.wait_ge(*pe_done(f"lora{KT - 1}"))
                nc.scalar.activation(lora["w"][0:64, :], ps[0:64, 0, :], ACT.Tanh).then_inc(*act_done.step("w"))
                nc.scalar.activation(lora["a"][0:64, :], ps[0:64, 1, :], ACT.Copy).then_inc(*act_done.step("a"))
                nc.scalar.activation(lora["g0"][:, :], ps[:, 2, :], ACT.Sigmoid).then_inc(*act_done.step("g0"))
                act.wait_ge(zeroed, 1)
                nc.scalar.activation(lora["g1"][0:32, :], ps[0:32, 3, :], ACT.Sigmoid).then_inc(*act_done.step("g1"))

            def pool(pool):
                nc.gpsimd.memset(lora["g1"][:, :], 0.0).then_inc(zeroed, 1)

            def dve(dve):
                dve_done.enter(dve)
                nc.vector.memset(hin[:, :, 0:1], 0.0).then_inc(*dve_done.step("zero"))
                for j in range(KT):
                    dve.wait_ge(*act_done(f"hin{j}"))
                    if j == 0:
                        dve.wait_ge(*dve_done("zero"))
                    if j >= 2:
                        dve.wait_ge(*dve_done(f"g{j - 2}"))
                    nc.vector.tensor_tensor(xx[:, j % 2, :], hin[:, j, 0:T], h[:, j, :], ALU.subtract).then_inc(*dve_done.step(f"xx{j}"))
                    dve.wait_ge(*dve_done(f"xx{j}"))
                    if j >= 2:
                        dve.wait_ge(*pe_done(f"lora{j - 2}"))
                    for n, m in enumerate(MIX):
                        out = xs[m][:, j, :] if m in xs else tmp[:, n - 3, j % 2, :]
                        nc.vector.scalar_tensor_tensor(out, xx[:, j % 2, :], vcol("mu", n * KT + j),
                                                                  h[:, j, :], ALU.mult, ALU.add).then_inc(*dve_done.step(f"{m}{j}"))

            def pe(pe):
                pe_done.enter(pe)
                pe.wait_ge(*loads.arrived())
                for j in range(KT):
                    w = slot[0][:, j * 288:(j + 1) * 288]
                    for n, (bank, a, b) in enumerate([(0, 0, 64), (1, 64, 128), (2, 128, 256), (3, 256, 288)]):
                        m = min(n, 2)
                        if n < 3:
                            pe.wait_ge(*dve_done(f"{MIX[3 + m]}{j}"))
                        last = mm(ps[0:b - a, bank, :], w[:, a:b], tmp[:, m, j % 2, :], j == 0, j == KT - 1)
                    last.then_inc(*pe_done.step(f"lora{j}"))

            phase(sp=sp, act=act, pe=pe, dve=dve, pool=pool)
            return xs, lora, pe_done, act_done, dve_done

        def recurrence(scope, xs, lora, mix_pe, mix_act, mix_dve):
            cr = keep("const_recurrence", [P, CR["all"][1]], scope)
            N = D // P
            yout = h
            pv = keep("pair_vectors", [P, 7], scope)
            W0, A0, KK, KA, RK, LG, LB = range(7)
            flat = {n: keep(n, [P, T], scope) for n in
                    ("r", "v", "g", "sig", "a", "kk0", "sq", "nrm", "kk", "k", "rkr", "bv", "cum", "Wt", "Winv", "Wprev")}
            pairs = {n: keep(n + "_pairs", [P, NCH, P], scope) for n in ("a", "b", "k", "r", "Nab", "Nak", "XT")}
            for q, n in enumerate(("b_tok", "k_tok", "Nrb", "Nrk")):
                pairs[n] = x[:, 2 * q:2 * q + 2, :].rearrange("p a (c n) -> p (a c) n", n=P)
            pairs["X"], pairs["Y"] = pairs["k"], pairs["b"]
            join = [keep(f"join{n}", [P, NCH, P], scope) for n in range(2)]
            v_tok = keep("v_tok", [P, NCH, CH], scope)
            G = keep("G", [P, 2, CH], scope)
            U = keep("U", [P, 2, CH], scope)
            St = keep("state", [P, 2, CH], scope)

            def by_chunk(t, n=CH):
                return t[:, :].rearrange("p (c n) -> p c n", n=n)
            cump, kka, yg = flat["sq"], flat["nrm"], flat["rkr"]
            yc, ysq, yn = (by_chunk(flat[n]) for n in ("kk0", "cum", "kk"))
            st = keep("group_norm", [P, 4, NCH], scope)
            MEAN, SUM, RSTD, STD = range(4)
            fl = {n: flat[n][:, :] for n in flat}

            PE = (["r", "k", "v", "w", "a", "g", "kk sum", "bonus sum", "v tok", "b tok", "k tok", "Nab", "Nrb", "Nak",
                   "Nrk", "X0"] + [n for k in range(1, 6) for n in ([f"Y{k}", f"X{k}", f"XT{k}"] if k < 5 else [f"Y{k}", f"XT{k}"])]
                  + [f"{n}{c}" for c in range(NCH) for n in (["G", "U", "S", "y"] if c < NCH - 1 else ["G", "U", "y"])] + ["y fm"])
            AC = (["r", "v", "g", "sig", "a", "kk sq", "kk norm", "Wt", "Winv", "Wprev", "v tok", "b tok", "X0"]
                  + [f"Y{k}" for k in range(1, 6)] + [f"G{c}" for c in range(NCH)] + ["y sq", "y std", "y gn"])
            DV = (["pv", "kk0", "cum", "cump", "nrm max", "nrm rec", "kk", "ka", "k", "rkr", "bonus", "kka", "a0", "a1",
                   "b0", "b1", "k tok", "Nab", "Nrb", "Nak", "Nrk"]
                  + [n for k in range(1, 6) for n in ([f"X{k}", f"XT{k}"] if k < 5 else [f"XT{k}"])]
                  + [f"{n}{c}" for c in range(NCH) for n in (["U", "S"] if c < NCH - 1 else ["U"])]
                  + ["y sum", "y mean", "y cen", "y var", "y rstd", "yn"])
            PO = ["k0", "k1", "r0", "r1", "A0", "XT0"] + [f"A{k}" for k in range(1, 6)] + ["y bonus", "y out"]
            pe_done, act_done, dve_done, pool_done = (steps(f"rec_{n}", q) for n, q in
                                          (("pe", PE), ("act", AC), ("dve", DV), ("pool", PO)))
            loads = Loads(0, N, pe_done, "g")
            zeroed = sem("pairs_zeroed")

            def two_banks(b):
                return ps[:, b:b + 2, :].rearrange("p b (c n) -> p (b c) n", n=P)

            def bank(b):
                return ps[:, b, :].rearrange("p (c n) -> p c n", n=CH)

            def spread(mask):
                return mask.unsqueeze(1).to_broadcast([P, NCH, P])

            def cmask(name):
                return const(name, cr, CR)

            def half(t, hh):
                return t[hh * HD:(hh + 1) * HD, :, hh * CH:(hh + 1) * CH]

            def rows(t, hh):
                return by_chunk(t)[hh * HD:(hh + 1) * HD, :, :]

            def sp(sp):
                sp.wait_ge(*loads.vacated())
                sp.dma_start(cr[:, :], d["const_recurrence"][:, :]).then_inc(crd_in, 16)
                with sp.Fori(0, N) as i:
                    sp.wait_ge(*loads.vacated(i))
                    sp.dma_start(loads.slot(row("rwkv", i)), row("rwkv", i)).then_inc(*loads.arrival)

            def pool(pool):
                pool_done.enter(pool)
                pool.wait_ge(*mix_dve(f"g{KT - 1}"))
                pool.wait_ge(*mix_pe(f"lora{KT - 1}"))
                for n in ("a", "b", "k", "r"):
                    nc.gpsimd.memset(pairs[n][:, :, :], 0.0).then_inc(zeroed, 1)
                pool.wait_ge(crd_in, 16)
                pool.wait_ge(tables_in, 32)
                pool.wait_ge(zeroed, 4)
                with pool.Fori(0, N) as i:
                    pool.wait_ge(*dve_done("k", i))
                    pool.wait_ge(*act_done("Winv", i))
                    pool.wait_ge(*pe_done("XT5", i, 1))
                    alone(pool)
                    for hh in range(2):
                        nc.gpsimd.tensor_tensor(half(pairs["k"], hh), rows(flat["k"], hh),
                                                            rows(flat["Winv"], hh), ALU.mult).then_inc(*pool_done.step(f"k{hh}"))
                    pool.wait_ge(*pe_done(f"y{NCH - 1}", i, 1))
                    alone(pool)
                    for hh in range(2):
                        nc.gpsimd.tensor_tensor(half(pairs["r"], hh), rows(flat["r"], hh),
                                                            rows(flat["Wt"], hh), ALU.mult).then_inc(*pool_done.step(f"r{hh}"))
                    pool.wait_ge(*dve_done("Nab", i))
                    alone(pool)
                    nc.gpsimd.tensor_tensor(join[0][:, :, :], pairs["Nab"][:, :, :], spread(cmask("level0")),
                                                        ALU.mult).then_inc(*pool_done.step("A0"))
                    pool.wait_ge(*pool_done("A0", i))
                    alone(pool)
                    nc.gpsimd.tensor_tensor(pairs["XT"][:, :, :], join[0][:, :, :], spread(ident), ALU.add).then_inc(*pool_done.step("XT0"))
                    pool.wait_ge(*pool_done("XT0", i))
                    alone(pool)
                    for k in range(1, 6):
                        if k >= 3:
                            pool.wait_ge(*pe_done(f"Y{k - 2}", i))
                            alone(pool)
                        nc.gpsimd.tensor_tensor(join[k % 2][:, :, :], pairs["Nab"][:, :, :],
                                                            spread(cmask(f"level{k}")), ALU.mult).then_inc(*pool_done.step(f"A{k}"))
                    pool.wait_ge(*act_done("y gn", i))
                    pool.wait_ge(*dve_done("bonus", i))
                    alone(pool)
                    nc.gpsimd.tensor_tensor(fl["sig"], yg[:, :], fl["bv"], ALU.add).then_inc(*pool_done.step("y bonus"))
                    pool.wait_ge(*pool_done("y bonus", i))
                    alone(pool)
                    nc.gpsimd.tensor_tensor(tile_of(yout, i), fl["sig"], fl["g"], ALU.mult).then_inc(*pool_done.step("y out"))

            def act(act):
                act_done.enter(act)
                act.wait_ge(tables_in, 32)
                copy = nc.scalar.activation
                with act.Fori(0, N) as i:
                    act.wait_ge(*pe_done("r", i))
                    act.wait_ge(*dve_done("rkr", i, 1))
                    act.wait_ge(*pool_done("r1", i, 1))
                    copy(fl["r"], ps[:, 0, :], ACT.Copy).then_inc(*act_done.step("r"))
                    act.wait_ge(*pe_done("v", i))
                    act.wait_ge(*dve_done("bonus", i, 1))
                    act.wait_ge(*pe_done("v tok", i, 1))
                    copy(fl["v"], ps[:, 2, :], ACT.Copy).then_inc(*act_done.step("v"))
                    act.wait_ge(*pe_done("g", i))
                    act.wait_ge(*pool_done("y out", i, 1))
                    copy(fl["g"], ps[:, 5, :], ACT.Copy).then_inc(*act_done.step("g"))
                    act.wait_ge(*dve_done("pv", i))
                    copy(fl["sig"], ps[:, 3, :], ACT.Sigmoid, bias=pv[:, W0:W0 + 1]).then_inc(*act_done.step("sig"))
                    act.wait_ge(*dve_done("kka", i, 1))
                    copy(fl["a"], ps[:, 4, :], ACT.Sigmoid, bias=pv[:, A0:A0 + 1]).then_inc(*act_done.step("a"))
                    act.wait_ge(*dve_done("kk0", i))
                    act.wait_ge(*dve_done("yn", i, 1))
                    copy(fl["sq"], fl["kk0"], ACT.Square).then_inc(*act_done.step("kk sq"))
                    act.wait_ge(*pe_done("kk sum", i))
                    copy(fl["nrm"], ps[:, 6, :], ACT.Sqrt).then_inc(*act_done.step("kk norm"))
                    act.wait_ge(*dve_done("cump", i))
                    act.wait_ge(*pool_done("r1", i, 1))
                    copy(fl["Wt"], fl["cum"], ACT.Exp, scale=-DECAY).then_inc(*act_done.step("Wt"))
                    copy(fl["Winv"], fl["cum"], ACT.Exp, scale=DECAY).then_inc(*act_done.step("Winv"))
                    copy(fl["Wprev"], cump[:, :], ACT.Exp, scale=-DECAY).then_inc(*act_done.step("Wprev"))
                    act.wait_ge(*pe_done("v tok", i))
                    act.wait_ge(*pe_done(f"y{NCH - 1}", i, 1))
                    copy(v_tok[:, :, :], bank(0), ACT.Copy).then_inc(*act_done.step("v tok"))
                    act.wait_ge(*pe_done("b tok", i))
                    copy(pairs["b_tok"], two_banks(2), ACT.Copy).then_inc(*act_done.step("b tok"))
                    act.wait_ge(*pe_done("X0", i))
                    copy(pairs["X"][:, :, :], two_banks(6), ACT.Copy).then_inc(*act_done.step("X0"))
                    for k in range(1, 6):
                        act.wait_ge(*pe_done(f"Y{k}", i))
                        copy(pairs["Y"][:, :, :], two_banks(2), ACT.Copy).then_inc(*act_done.step(f"Y{k}"))
                    for c in range(NCH):
                        act.wait_ge(*pe_done(f"G{c}", i))
                        copy(G[:, c % 2, :], bank(0)[:, c, :], ACT.Copy).then_inc(*act_done.step(f"G{c}"))
                    act.wait_ge(*dve_done("y cen", i))
                    copy(ysq, yc, ACT.Square).then_inc(*act_done.step("y sq"))
                    act.wait_ge(*dve_done("y var", i))
                    copy(st[:, STD, :], st[:, SUM, :], ACT.Sqrt, bias=const("gn_eps"), scale=1.0 / HD).then_inc(*act_done.step("y std"))
                    act.wait_ge(*pe_done("y fm", i))
                    copy(yg[:, :], ps[:, 4, :], ACT.Identity, bias=pv[:, LB:LB + 1], scale=pv[:, LG:LG + 1]).then_inc(*act_done.step("y gn"))

            def dve(dve):
                dve_done.enter(dve)
                dve.wait_ge(crd_in, 16)
                dve.wait_ge(tables_in, 32)
                dve.wait_ge(zeroed, 4)
                tt, ts, stt = nc.vector.tensor_tensor, nc.vector.tensor_scalar, nc.vector.scalar_tensor_tensor
                with dve.Fori(0, N) as i:
                    dve.wait_ge(*act_done("y gn", i, 1))
                    alone(dve)
                    nc.vector.tensor_copy(pv[:, :], vec[:, bass.ds(i * 7 + VC["pair"][0], 7)]).then_inc(*dve_done.step("pv"))
                    dve.wait_ge(*pe_done("k", i))
                    dve.wait_ge(*dve_done("pv", i))
                    ts(fl["kk0"], ps[:, 1, :], pv[:, KK:KK + 1], None, ALU.mult).then_inc(*dve_done.step("kk0"))
                    dve.wait_ge(*act_done("sig", i))
                    dve.wait_ge(*act_done("y sq", i, 1))
                    nc.vector.tensor_tensor_scan(fl["cum"], cmask("reset"), fl["sig"], 0.0, ALU.mult, ALU.add).then_inc(*dve_done.step("cum"))
                    dve.wait_ge(*dve_done("cum", i))
                    dve.wait_ge(*pe_done("kk sum", i))
                    tt(cump[:, :], fl["cum"], fl["sig"], ALU.subtract).then_inc(*dve_done.step("cump"))
                    dve.wait_ge(*act_done("kk norm", i))
                    ts(fl["nrm"], fl["nrm"], 1e-12, None, ALU.max).then_inc(*dve_done.step("nrm max"))
                    dve.wait_ge(*dve_done("nrm max", i))
                    nc.vector.reciprocal(fl["nrm"], fl["nrm"]).then_inc(*dve_done.step("nrm rec"))
                    dve.wait_ge(*dve_done("nrm rec", i))
                    dve.wait_ge(*pe_done("y fm", i, 1))
                    tt(fl["kk"], fl["kk0"], fl["nrm"], ALU.mult).then_inc(*dve_done.step("kk"))
                    dve.wait_ge(*act_done("a", i))
                    dve.wait_ge(*pool_done("y bonus", i, 1))
                    ts(fl["rkr"], fl["a"], 1.0, pv[:, KA:KA + 1], ALU.subtract, ALU.mult).then_inc(*dve_done.step("ka"))
                    dve.wait_ge(*dve_done("ka", i))
                    dve.wait_ge(*pool_done("k1", i, 1))
                    stt(fl["k"], fl["rkr"], 1.0, ps[:, 1, :], ALU.add, ALU.mult).then_inc(*dve_done.step("k"))
                    dve.wait_ge(*dve_done("k", i))
                    dve.wait_ge(*act_done("r", i))
                    stt(fl["rkr"], fl["r"], pv[:, RK:RK + 1], fl["k"], ALU.mult, ALU.mult).then_inc(*dve_done.step("rkr"))
                    dve.wait_ge(*pe_done("bonus sum", i))
                    dve.wait_ge(*act_done("v", i))
                    dve.wait_ge(*pool_done("y bonus", i, 1))
                    tt(fl["bv"], ps[:, 7, :], fl["v"], ALU.mult).then_inc(*dve_done.step("bonus"))
                    dve.wait_ge(*dve_done("kk", i))
                    tt(kka[:, :], fl["kk"], fl["a"], ALU.mult).then_inc(*dve_done.step("kka"))
                    dve.wait_ge(*act_done("Wprev", i))
                    dve.wait_ge(*pe_done(f"G{NCH - 1}", i, 1))
                    for hh in range(2):
                        stt(half(pairs["a"], hh), rows(flat["kk"], hh), -1.0, rows(flat["Wprev"], hh),
                                       ALU.mult, ALU.mult).then_inc(*dve_done.step(f"a{hh}"))
                    dve.wait_ge(*dve_done("kka", i))
                    dve.wait_ge(*pe_done("XT5", i, 1))
                    for hh in range(2):
                        tt(half(pairs["b"], hh), rows(kka, hh), rows(flat["Winv"], hh), ALU.mult).then_inc(*dve_done.step(f"b{hh}"))
                    dve.wait_ge(*pe_done("k tok", i))
                    nc.vector.tensor_copy(pairs["k_tok"], two_banks(4)).then_inc(*dve_done.step("k tok"))
                    for n, b, mask in (("Nab", 6, "strict"), ("Nrb", 2, "incl"), ("Nak", 4, "strict"), ("Nrk", 0, "incl")):
                        dve.wait_ge(*pe_done(n, i))
                        tt(pairs[n][:, :, :], two_banks(b), spread(cmask(mask)), ALU.mult).then_inc(*dve_done.step(n))
                    for k in range(1, 6):
                        if k < 5:
                            dve.wait_ge(*pe_done(f"X{k}", i))
                            if k == 1:
                                dve.wait_ge(*act_done("X0", i))
                            tt(pairs["X"][:, :, :], pairs["X"][:, :, :], two_banks(4), ALU.add).then_inc(*dve_done.step(f"X{k}"))
                        dve.wait_ge(*pe_done(f"XT{k}", i))
                        tt(pairs["XT"][:, :, :], pairs["XT"][:, :, :], two_banks(6), ALU.add).then_inc(*dve_done.step(f"XT{k}"))
                    for c in range(NCH):
                        dve.wait_ge(*pe_done(f"U{c}", i))
                        if c >= 2:
                            dve.wait_ge(*pe_done(f"y{c - 2}", i))
                        nc.vector.tensor_copy(U[:, c % 2, :], bank(1)[:, c, :]).then_inc(*dve_done.step(f"U{c}"))
                        if c < NCH - 1:
                            dve.wait_ge(*pe_done(f"S{c}", i))
                            if c >= 2:
                                dve.wait_ge(*pe_done(f"y{c - 1}", i))
                            end = c * CH + CH - 1
                            ts(St[:, c % 2, :], bank(2)[:, c, :], flat["Wt"][:, end:end + 1], None, ALU.mult).then_inc(*dve_done.step(f"S{c}"))
                    dve.wait_ge(*pe_done(f"y{NCH - 1}", i))
                    yps = bank(3)
                    nc.vector.tensor_reduce(st[:, MEAN, :], yps, AX.X, ALU.add).then_inc(*dve_done.step("y sum"))
                    dve.wait_ge(*dve_done("y sum", i))
                    ts(st[:, MEAN, :], st[:, MEAN, :], 1.0 / HD, None, ALU.mult).then_inc(*dve_done.step("y mean"))
                    dve.wait_ge(*dve_done("y mean", i))
                    tt(yc, yps, st[:, MEAN, :].unsqueeze(2).to_broadcast([P, NCH, CH]), ALU.subtract).then_inc(*dve_done.step("y cen"))
                    dve.wait_ge(*act_done("y sq", i))
                    nc.vector.tensor_reduce(st[:, SUM, :], ysq, AX.X, ALU.add).then_inc(*dve_done.step("y var"))
                    dve.wait_ge(*act_done("y std", i))
                    nc.vector.reciprocal(st[:, RSTD, :], st[:, STD, :]).then_inc(*dve_done.step("y rstd"))
                    dve.wait_ge(*dve_done("y rstd", i))
                    tt(yn, yc, st[:, RSTD, :].unsqueeze(2).to_broadcast([P, NCH, CH]), ALU.mult).then_inc(*dve_done.step("yn"))

            def pe(pe):
                pe_done.enter(pe)
                pe.wait_ge(*mix_act("g1"))
                pe.wait_ge(*mix_dve(f"g{KT - 1}"))
                with pe.Fori(0, N) as i:
                    pe.wait_ge(*loads.arrived(i))
                    for n, (m, w0) in enumerate((("r", 0), ("k", KT), ("v", 2 * KT))):
                        if n == 0:
                            pe.wait_ge(*dve_done("yn", i, 1))
                            pe.wait_ge(*act_done("y gn", i, 1))
                        for k in range(KT):
                            last = mm(ps[:, n, :], wtile(0, w0 + k), xs[m][:, k, :], k == 0, k == KT - 1)
                        last.then_inc(*pe_done.step(m))
                    mm(ps[:, 3, :], wtile(0, 24, HD), lora["w"][0:HD, :]).then_inc(*pe_done.step("w"))
                    mm(ps[:, 4, :], wtile(0, 25, HD), lora["a"][0:HD, :]).then_inc(*pe_done.step("a"))
                    mm(ps[:, 5, :], wtile(0, 26), lora["g0"][:, :], True, False)
                    mm(ps[:, 5, :], wtile(0, 27), lora["g1"][:, :], False, True).then_inc(*pe_done.step("g"))
                    pe.wait_ge(*act_done("kk sq", i))
                    mm(ps[:, 6, :], blockones, fl["sq"]).then_inc(*pe_done.step("kk sum"))
                    pe.wait_ge(*dve_done("rkr", i))
                    mm(ps[:, 7, :], blockones, fl["rkr"]).then_inc(*pe_done.step("bonus sum"))
                    pe.wait_ge(*act_done("v", i))
                    for c in range(NCH):
                        for hh in range(2):
                            last = mm(bank(0)[hh * CH:(hh + 1) * CH, c, :], flat["v"][:, c * CH:(c + 1) * CH],
                                      ident[:, hh * HD:(hh + 1) * HD])
                    last.then_inc(*pe_done.step("v tok"))
                    pe.wait_ge(*dve_done("b1", i))
                    pe.wait_ge(*act_done("sig", i))
                    for c in range(NCH):
                        last = nc.tensor.transpose(two_banks(2)[:, c, :], pairs["b"][:, c, :], ident)
                    last.then_inc(*pe_done.step("b tok"))
                    pe.wait_ge(*pool_done("k1", i))
                    pe.wait_ge(*act_done("g", i))
                    pe.wait_ge(*act_done("a", i))
                    for c in range(NCH):
                        last = nc.tensor.transpose(two_banks(4)[:, c, :], pairs["k"][:, c, :], ident)
                    last.then_inc(*pe_done.step("k tok"))
                    pe.wait_ge(*pool_done("r1", i))
                    pe.wait_ge(*dve_done("bonus", i))
                    for n, b, left, right in (("Nab", 6, "b", "a"), ("Nrb", 2, "b", "r"), ("Nak", 4, "k", "a"), ("Nrk", 0, "k", "r")):
                        if n == "Nrb":
                            pe.wait_ge(*act_done("b tok", i))
                        elif n == "Nak":
                            pe.wait_ge(*dve_done("k tok", i))
                        elif n == "Nrk":
                            pe.wait_ge(*act_done("v tok", i))
                        for c in range(NCH):
                            last = mm(two_banks(b)[:, c, :], pairs[left][:, c, :], pairs[right][:, c, :])
                        last.then_inc(*pe_done.step(n))
                    pe.wait_ge(*pool_done("XT0", i))
                    for c in range(NCH):
                        last = nc.tensor.transpose(two_banks(6)[:, c, :], pairs["XT"][:, c, :], ident)
                    last.then_inc(*pe_done.step("X0"))
                    for k in range(1, 6):
                        pe.wait_ge(*pool_done(f"A{k}", i))
                        if k == 1:
                            pe.wait_ge(*act_done("X0", i))
                            pe.wait_ge(*dve_done("Nrk", i))
                        else:
                            pe.wait_ge(*dve_done(f"XT{k - 1}", i))
                        for c in range(NCH):
                            last = mm(two_banks(2)[:, c, :], join[k % 2][:, c, :], pairs["X"][:, c, :])
                        last.then_inc(*pe_done.step(f"Y{k}"))
                        pe.wait_ge(*act_done(f"Y{k}", i))
                        for out, b, left, right in (("X", 4, "XT", "Y"), ("XT", 6, "Y", "XT")):
                            if k == 5 and out == "X":
                                continue
                            for c in range(NCH):
                                last = mm(two_banks(b)[:, c, :], pairs[left][:, c, :], pairs[right][:, c, :])
                            last.then_inc(*pe_done.step(f"{out}{k}"))
                    pe.wait_ge(*dve_done("XT5", i))
                    for c in range(NCH):
                        S0 = St[:, (c - 1) % 2, :]
                        last = mm(bank(0)[:, c, :], pairs["Nak"][:, c, :], v_tok[:, c, :], True, c == 0)
                        if c:
                            pe.wait_ge(*dve_done(f"S{c - 1}", i))
                            last = mm(bank(0)[:, c, :], pairs["a"][:, c, :], S0, False, True)
                        last.then_inc(*pe_done.step(f"G{c}"))
                        pe.wait_ge(*act_done(f"G{c}", i))
                        mm(bank(1)[:, c, :], pairs["XT"][:, c, :], G[:, c % 2, :]).then_inc(*pe_done.step(f"U{c}"))
                        pe.wait_ge(*dve_done(f"U{c}", i))
                        if c < NCH - 1:
                            mm(bank(2)[:, c, :], pairs["b_tok"][:, c, :], U[:, c % 2, :], True, False)
                            if c:
                                mm(bank(2)[:, c, :], ident, S0, False, False)
                            mm(bank(2)[:, c, :], pairs["k_tok"][:, c, :], v_tok[:, c, :], False, True).then_inc(*pe_done.step(f"S{c}"))
                        mm(bank(3)[:, c, :], pairs["Nrb"][:, c, :], U[:, c % 2, :], True, False)
                        if c:
                            mm(bank(3)[:, c, :], pairs["r"][:, c, :], S0, False, False)
                        mm(bank(3)[:, c, :], pairs["Nrk"][:, c, :], v_tok[:, c, :], False, True).then_inc(*pe_done.step(f"y{c}"))
                    pe.wait_ge(*dve_done("yn", i))
                    for c in range(NCH):
                        for hh in range(2):
                            last = mm(ps[hh * HD:(hh + 1) * HD, 4, c * CH:(c + 1) * CH], yn[:, c, :],
                                      ident[:, hh * CH:(hh + 1) * CH])
                    last.then_inc(*pe_done.step("y fm"))

            phase(sp=sp, act=act, pe=pe, dve=dve, pool=pool)
            return yout, pool_done, "y out", N - 1

        def project(name, stream, sources, ready, factor, x_ready=()):
            n = KT // 2
            pe_done = steps(f"{name}_pe", ["product0", "product1"])
            dve_done = steps(f"{name}_dve", ["sum0", "sum1"])
            loads = [Loads(s, n, pe_done, f"product{s}") for s in range(2)]

            def sp(sp):
                for s in range(2):
                    sp.wait_ge(*loads[s].vacated())
                with sp.Fori(0, n) as i:
                    for s in range(2):
                        sp.wait_ge(*loads[s].vacated(i))
                        sp.dma_start(loads[s].slot(row(stream, i * 2 + s)), row(stream, i * 2 + s)).then_inc(*loads[s].arrival)

            def pe(pe):
                pe_done.enter(pe)
                for r in ready:
                    pe.wait_ge(*reached(*r))
                with pe.Fori(0, n) as i:
                    for s in range(2):
                        pe.wait_ge(*loads[s].arrived(i))
                        pe.wait_ge(*dve_done(f"sum{s}", i, 1))
                        for k, src in enumerate(sources):
                            last = mm(ps[:, s, :], wtile(s, k), src, k == 0, k == len(sources) - 1)
                        last.then_inc(*pe_done.step(f"product{s}"))

            def dve(dve):
                dve_done.enter(dve)
                for r in x_ready:
                    dve.wait_ge(*reached(*r))
                with dve.Fori(0, n) as i:
                    for s in range(2):
                        dve.wait_ge(*pe_done(f"product{s}", i))
                        f = factor if isinstance(factor, float) else mods[:, bass.ds(i * 2 + (s + factor[0] * 48 + factor[1] * 8), 1)]
                        nc.vector.scalar_tensor_tensor(tile_of(x, i * 2 + s), ps[:, s, :], f,
                                                                  tile_of(x, i * 2 + s), ALU.mult, ALU.add).then_inc(*dve_done.step(f"sum{s}"))

            phase(sp=sp, pe=pe, dve=dve)
            return [(dve_done, f"sum{j % 2}", j // 2) for j in range(KT)]

        def residual_again(ready):
            again = sem("residual_again")
            act_done = steps("again_act", ["scaled"])

            def sp(sp):
                for r in ready:
                    sp.wait_ge(*reached(*r))
                sp.dma_start(x[:, :, :], d["x"][:, :, :]).then_inc(again, 16)

            def act(act):
                act_done.enter(act)
                act.wait_ge(again, 16)
                nc.scalar.activation(x[:, :, :], x[:, :, :], ACT.Copy, scale=ALPHA).then_inc(*act_done.step("scaled"))

            phase(sp=sp, act=act)
            return act_done, "scaled"

        def layer_norm(name, scope, layer, half_layer, ready, following):
            mean, std, rstd = (keep(f"{name}_{n}", [P, T], scope) for n in ("mean", "std", "rstd"))
            sq = keep(f"{name}_sq", [P, 2, T], scope)
            col = (layer * 2 + half_layer) * KT
            pe_done = steps(f"{name}_pe", ["sum"] + [f"sq{j}" for j in range(KT)])
            act_done = steps(f"{name}_act", ["mean"] + [f"sq{j}" for j in range(KT)] + ["std"]
                          + [f"{n}{j}" for j in range(KT) for n in (["shift", "in"] if following else ["shift"])])
            dve_done = steps(f"{name}_dve", [f"centred{j}" for j in range(KT)] + ["rstd"] + [f"scaled{j}" for j in range(KT)])
            pool_done = steps(f"{name}_pool", [f"alpha{j}" for j in range(KT)])

            def pe(pe):
                pe_done.enter(pe)
                for j in range(KT):
                    pe.wait_ge(*reached(*ready[j]))
                    last = mm(ps[:, 4, :], ones, x[:, j, :], j == 0, j == KT - 1)
                last.then_inc(*pe_done.step("sum"))
                for j in range(KT):
                    pe.wait_ge(*act_done(f"sq{j}"))
                    mm(ps[:, 5, :], ones, sq[:, j % 2, :], j == 0, j == KT - 1).then_inc(*pe_done.step(f"sq{j}"))

            def act(act):
                act_done.enter(act)
                act.wait_ge(*pe_done("sum"))
                nc.scalar.activation(mean[:, :], ps[:, 4, :], ACT.Copy, scale=1.0 / D).then_inc(*act_done.step("mean"))
                for j in range(KT):
                    act.wait_ge(*dve_done(f"centred{j}"))
                    if j >= 2:
                        act.wait_ge(*pe_done(f"sq{j - 2}"))
                    nc.scalar.activation(sq[:, j % 2, :], x[:, j, :], ACT.Square).then_inc(*act_done.step(f"sq{j}"))
                act.wait_ge(*pe_done(f"sq{KT - 1}"))
                nc.scalar.activation(std[:, :], ps[:, 5, :], ACT.Sqrt, bias=const("ln_eps"), scale=1.0 / D).then_inc(*act_done.step("std"))
                for j in range(KT):
                    act.wait_ge(*dve_done(f"scaled{j}"))
                    nc.scalar.activation(x[:, j, :], x[:, j, :], ACT.Identity, bias=vcol("ln_b", col + j)).then_inc(*act_done.step(f"shift{j}"))
                    if following:
                        l, sh, sc = following
                        act.wait_ge(*act_done(f"shift{j}"))
                        nc.scalar.activation(h[:, j, :], x[:, j, :], ACT.Identity, bias=mod(l, sh, j),
                                                        scale=mod(l, sc, j)).then_inc(*act_done.step(f"in{j}"))

            def dve(dve):
                dve_done.enter(dve)
                dve.wait_ge(*act_done("mean"))
                for j in range(KT):
                    nc.vector.tensor_tensor(x[:, j, :], x[:, j, :], mean[:, :], ALU.subtract).then_inc(*dve_done.step(f"centred{j}"))
                dve.wait_ge(*act_done("std"))
                nc.vector.reciprocal(rstd[:, :], std[:, :]).then_inc(*dve_done.step("rstd"))
                dve.wait_ge(*dve_done("rstd"))
                for j in range(KT):
                    nc.vector.scalar_tensor_tensor(x[:, j, :], x[:, j, :], vcol("ln_g", col + j), rstd[:, :],
                                                              ALU.mult, ALU.mult).then_inc(*dve_done.step(f"scaled{j}"))

            def pool(pool):
                pool_done.enter(pool)
                for j in range(KT):
                    pool.wait_ge(*act_done(f"in{j}"))
                    nc.gpsimd.tensor_scalar(x[:, j, :], x[:, j, :], ALPHA, None, ALU.mult).then_inc(*pool_done.step(f"alpha{j}"))

            if following:
                phase(pe=pe, act=act, dve=dve, pool=pool)
                return [(act_done, f"in{j}") for j in range(KT)], [(pool_done, f"alpha{KT - 1}")]
            phase(pe=pe, act=act, dve=dve)
            return [(act_done, f"shift{j}") for j in range(KT)], []

        def rms_norm(name, scope, source, ready, gains, out):
            n = len(source)
            std, rstd = (keep(f"{name}_{m}", [P, T], scope) for m in ("std", "rstd"))
            sq = keep(f"{name}_sq", [P, 2, T], scope)
            pe_done = steps(f"{name}_pe", [f"sq{j}" for j in range(n)])
            act_done = steps(f"{name}_act", [f"sq{j}" for j in range(n)] + ["std"])
            dve_done = steps(f"{name}_dve", ["rstd"] + [f"out{j}" for j in range(n)])

            def act(act):
                act_done.enter(act)
                act.wait_ge(*reached(*ready[n - 1]))
                for j in range(n):
                    if j >= 2:
                        act.wait_ge(*pe_done(f"sq{j - 2}"))
                    nc.scalar.activation(sq[:, j % 2, :], source[j], ACT.Square).then_inc(*act_done.step(f"sq{j}"))
                act.wait_ge(*pe_done(f"sq{n - 1}"))
                nc.scalar.activation(std[:, :], ps[:, 5, :], ACT.Sqrt, bias=const("rms_eps"), scale=1.0 / (n * P)).then_inc(*act_done.step("std"))

            def pe(pe):
                pe_done.enter(pe)
                for j in range(n):
                    pe.wait_ge(*act_done(f"sq{j}"))
                    mm(ps[:, 5, :], ones, sq[:, j % 2, :], j == 0, j == n - 1).then_inc(*pe_done.step(f"sq{j}"))

            def dve(dve):
                dve_done.enter(dve)
                dve.wait_ge(*act_done("std"))
                nc.vector.reciprocal(rstd[:, :], std[:, :]).then_inc(*dve_done.step("rstd"))
                dve.wait_ge(*dve_done("rstd"))
                for j in range(n):
                    nc.vector.scalar_tensor_tensor(out[j], source[j], gains[j], rstd[:, :], ALU.mult, ALU.mult).then_inc(*dve_done.step(f"out{j}"))

            phase(pe=pe, act=act, dve=dve)
            return [(dve_done, f"out{j}") for j in range(n)]

        def gated(name, hid, sg, ready):
            n = HT // 2
            pe_done = steps(f"{name}_pe", ["gate0", "up0", "gate1", "up1"])
            act_done = steps(f"{name}_act", ["silu0", "silu1"])
            dve_done = steps(f"{name}_dve", ["hidden0", "hidden1"])
            loads = [Loads(s, n, pe_done, f"up{s}") for s in range(2)]

            def sp(sp):
                for s in range(2):
                    sp.wait_ge(*loads[s].vacated())
                with sp.Fori(0, n) as i:
                    for s in range(2):
                        sp.wait_ge(*loads[s].vacated(i))
                        sp.dma_start(loads[s].slot(row(f"{name}_in", i * 2 + s)), row(f"{name}_in", i * 2 + s)).then_inc(*loads[s].arrival)

            def pe(pe):
                pe_done.enter(pe)
                for r in ready:
                    pe.wait_ge(*reached(*r))
                with pe.Fori(0, n) as i:
                    for s in range(2):
                        pe.wait_ge(*loads[s].arrived(i))
                        pe.wait_ge(*dve_done(f"hidden{s}", i, 1))
                        for u, part in enumerate(("gate", "up")):
                            for k in range(KT):
                                last = mm(ps[:, 2 * s + u, :], wtile(s, u * KT + k), h[:, k, :], k == 0, k == KT - 1)
                            last.then_inc(*pe_done.step(f"{part}{s}"))

            def act(act):
                act_done.enter(act)
                with act.Fori(0, n) as i:
                    for s in range(2):
                        act.wait_ge(*pe_done(f"gate{s}", i))
                        act.wait_ge(*dve_done(f"hidden{s}", i, 1))
                        nc.scalar.activation(sg[:, s, :], ps[:, 2 * s, :], ACT.Silu).then_inc(*act_done.step(f"silu{s}"))

            def dve(dve):
                dve_done.enter(dve)
                with dve.Fori(0, n) as i:
                    for s in range(2):
                        dve.wait_ge(*act_done(f"silu{s}", i))
                        dve.wait_ge(*pe_done(f"up{s}", i))
                        nc.vector.tensor_tensor(tile_of(hid, i * 2 + s), sg[:, s, :], ps[:, 2 * s + 1, :], ALU.mult).then_inc(*dve_done.step(f"hidden{s}"))

            phase(sp=sp, pe=pe, act=act, dve=dve)
            return [(dve_done, "hidden1", n - 1)]

        def feed_forward(name, scope, ready, factor, x_ready=()):
            hid = keep(f"{name}_hidden", [P, HT, T], scope)
            sg = keep(f"{name}_silu", [P, 2, T], scope)
            done = gated(name, hid, sg, ready)
            return project(f"{name}_down", f"{name}_out", [hid[:, k, :] for k in range(HT)], done, factor, x_ready)

        def attend(name, scope, turns, work, out, ready, before, zero_first=()):
            N = len(work)
            sx = keep(f"{name}_masked", [P, 3, T], scope)
            probs = keep(f"{name}_probs", [P, 3, T], scope)
            probsT = keep(f"{name}_probsT", [P, 2, T], scope)
            diag = keep(f"{name}_diag", [P, 3, P], scope)
            stat = keep(f"{name}_stat", [P, 3, 4], scope)
            MAX, SUM, INV = range(3)
            L, TR, O = 0, 3, 5
            order = []
            for t in range(N + 3):
                order += [("L", t)] * (t < N) + [("T", t - 2)] * (2 <= t < N + 2) + [("O", t - 3)] * (t >= 3)
            a_order = []
            for t in range(N + 2):
                a_order += [("exp", t)] * (t < N) + [("PT", t - 2)] * (t >= 2)
            d_order = []
            for t in range(N + 1):
                d_order += [("max", t), ("neg", t)] * (t < N) + [("inv", t - 1), ("diag", t - 1)] * (t >= 1)

            def names(eng, seq):
                return before[eng][0] + [f"{a}{n}" for a, n in seq]
            S = {"pe": steps(f"{name}_pe", names("pe", order)), "act": steps(f"{name}_act", names("act", a_order) + ["out"]),
                 "dve": steps(f"{name}_dve", names("dve", d_order))}

            def earlier(what, n, back, turn):
                who = S[{"max": "dve", "T": "pe", "PT": "act", "O": "pe"}[what]]
                return who(f"{what}{n - back}", turn) if n >= back else who(f"{what}{N + n - back}", turn, 1)

            def pe(pe):
                S["pe"].enter(pe)
                for r in ready:
                    pe.wait_ge(*reached(*r))
                with pe.Fori(0, turns) as i:
                    before["pe"][1](pe, i, S)
                    for what, n in order:
                        w = work[n]
                        if what == "L":
                            pe.wait_ge(*earlier("max", n, 3, i))
                            out_l = ps[:, L + n % 3, 0:w["w"]]
                            extra = w.get("extra")
                            ins = mm(out_l, w["query"], w["keys"], True, not extra)
                            if extra:
                                ins = mm(out_l, *extra, False, True)
                        elif what == "T":
                            pe.wait_ge(*S["dve"](f"diag{n}", i))
                            pe.wait_ge(*earlier("PT", n, 2, i))
                            for b in range(w["w"] // P):
                                ins = mm(ps[:, TR + n % 2, b * P:(b + 1) * P], probs[:, n % 3, b * P:(b + 1) * P], diag[:, n % 3, :])
                        else:
                            pe.wait_ge(*S["act"](f"PT{n}", i))
                            if n == 0:
                                pe.wait_ge(*S["act"]("out", i, 1))
                            hh, q = w["head"], w["tile"]
                            nb = w["w"] // P
                            for b in range(nb):
                                ins = mm(ps[hh * HD:(hh + 1) * HD, O, q * P:(q + 1) * P], w["values"][b],
                                         probsT[:, n % 2, b * P:(b + 1) * P], w["first"] and b == 0, w["last"] and b == nb - 1)
                        ins.then_inc(*S["pe"].step(f"{what}{n}"))

            def act(act):
                S["act"].enter(act)
                with act.Fori(0, turns) as i:
                    before["act"][1](act, i, S)
                    for what, n in a_order:
                        w = work[n]["w"]
                        if what == "exp":
                            act.wait_ge(*S["dve"](f"neg{n}", i))
                            act.wait_ge(*earlier("T", n, 3, i))
                            ins = nc.scalar.activation(probs[:, n % 3, 0:w], sx[:, n % 3, 0:w], ACT.Exp,
                                                       bias=stat[:, MAX, n % 4:n % 4 + 1], accum_out=stat[:, SUM, n % 4:n % 4 + 1])
                        else:
                            act.wait_ge(*S["pe"](f"T{n}", i))
                            act.wait_ge(*earlier("O", n, 2, i))
                            ins = nc.scalar.activation(probsT[:, n % 2, 0:w], ps[:, TR + n % 2, 0:w], ACT.Copy)
                        ins.then_inc(*S["act"].step(f"{what}{n}"))
                    act.wait_ge(*S["pe"](f"O{N - 1}", i))
                    alone(act)
                    nc.scalar.activation(tile_of(out, i), ps[:, O, :], ACT.Copy).then_inc(*S["act"].step("out"))

            def dve(dve):
                S["dve"].enter(dve)
                with dve.Fori(0, turns) as i:
                    before["dve"][1](dve, i, S)
                    for what, n in d_order:
                        w = work[n]
                        m = n % 4
                        if what == "max":
                            dve.wait_ge(*S["pe"](f"L{n}", i))
                            alone(dve)
                            ins = nc.vector.tensor_tensor_reduce(
                                out=sx[:, n % 3, 0:w["w"]], in0=ps[:, L + n % 3, 0:w["w"]], in1=w["mask"], scale=1.0,
                                scalar=-3e38, op0=ALU.add, op1=ALU.max, accum_out=stat[:, MAX, m:m + 1])
                        elif what == "neg":
                            dve.wait_ge(*S["dve"](f"max{n}", i))
                            ins = nc.vector.tensor_scalar(stat[:, MAX, m:m + 1], stat[:, MAX, m:m + 1], -1.0, None, ALU.mult)
                        elif what == "inv":
                            dve.wait_ge(*S["act"](f"exp{n}", i))
                            ins = nc.vector.reciprocal(stat[:, INV, m:m + 1], stat[:, SUM, m:m + 1])
                        else:
                            dve.wait_ge(*S["dve"](f"inv{n}", i))
                            dve.wait_ge(*earlier("T", n, 3, i))
                            gate = w.get("gate")
                            ins = nc.vector.tensor_scalar(diag[:, n % 3, :], ident, stat[:, INV, m:m + 1], gate, ALU.mult,
                                                          ALU.mult if gate is not None else ALU.bypass)
                        ins.then_inc(*S["dve"].step(f"{what}{n}"))

            phase(pe=pe, act=act, dve=dve)
            return S

        IH = 8
        TOPK = 128

        def load_attention_constants(cb, before, done):
            def sp(sp):
                for r in before:
                    sp.wait_ge(*reached(*r))
                sp.dma_start(cb[:, :], d["const_attention"][:, :]).then_inc(att_in, 16)
            phase(sp=sp)

        def sparse_attention(scope, branch, out):
            cb = keep("const_attention_1", [P, CB["all"][1]], scope)

            def cc(name):
                return const(name, cb, CB)
            ckv = keep("latent", [P, T], scope)
            kidx = keep("index_keys", [P, T], scope)
            tmp = keep("latent_norm", [P, 2, T], scope)
            qi = keep("index_queries", [P, 2, 2, T], scope)
            wts = keep("index_weights", [P, QT, IH], scope)
            rel = keep("index_relu", [P, 2, T], scope)
            score = keep("index_scores", [P, QT, T], scope)
            best = keep("best", [P, QT, 8], scope)
            relb = keep("rel_bias", [32, 16], scope)
            brow = keep("bias_rows", [16, BIAS_LEN], scope)
            small_in, zeroed, rows_out = sem("rel_bias_in"), sem("index_queries_zeroed"), sem("bias_rows_out")
            scratch = d["bias_scratch"]
            todo = [(m, hh, q) for m in range(IH // 2) for hh in range(2) for q in range(1, QT)]
            NI = len(todo)
            pe_done = steps("idx_pe", ["ckv", "kidx", "widx", "qi0", "qi1", "ckv sq", "bias"]
                         + [n for t, (m, hh, q) in enumerate(todo)
                            for n in (([f"qi{m + 1}"] if hh == 0 and q == 1 and m >= 1 and m < 3 else []) + [f"score{t}"])])
            act_done = steps("idx_act", ["ckv sq", "kidx", "qi0a", "qi0b", "ckv std", "bias"]
                          + [n for t, (m, hh, q) in enumerate(todo)
                             for n in ([f"relu{t}"] + ([f"qi{m + 1}a", f"qi{m + 1}b"] if hh == 0 and q == 3 and m < 3 else []))])
            dve_done = steps("idx_dve", ["widx", "ckv rstd", "ckv"] + [f"add{t}" for t in range(NI)] + [f"causal{q}" for q in range(1, QT)])
            topk_done = steps("top_dve", [f"max{q}" for q in range(1, QT)] + [f"take{q}" for q in range(1, QT)])
            selected = steps("sel_dve", [f"select{q}" for q in range(1, QT)])
            load_a, load_b = Loads(0, 1, pe_done, "widx"), Loads(1, 1, pe_done, "qi1")
            load_c = Loads(0, 1, pe_done, "qi3")

            def sp(sp):
                sp.wait_ge(*load_a.vacated())
                sp.dma_start(load_a.slot(row("dsa_first", 0)), row("dsa_first", 0)).then_inc(*load_a.arrival)
                sp.wait_ge(*load_b.vacated())
                sp.dma_start(load_b.slot(row("dsa_index", 0)), row("dsa_index", 0)).then_inc(*load_b.arrival)
                sp.wait_ge(*reached(*branch[0]))
                sp.dma_start(relb[:, :], d["rel_bias"][:, :]).then_inc(small_in, 16)
                sp.dma_start(cb[:, :], d["const_attention"][:, :]).then_inc(att_in, 16)
                sp.wait_ge(*load_c.vacated())
                sp.dma_start(load_c.slot(row("dsa_index", 1)), row("dsa_index", 1)).then_inc(*load_c.arrival)
                sp.wait_ge(*act_done("bias"))
                sp.dma_start(scratch[:, :], brow[:, :]).then_inc(rows_out, 16)

            def pool(pool):
                pool.wait_ge(*reached(*branch[0]))
                nc.gpsimd.memset(qi[:, :, :, :], 0.0).then_inc(zeroed, 1)

            def pe(pe):
                pe_done.enter(pe)
                pe.wait_ge(*load_a.arrived())
                for n, (name, bank) in enumerate((("ckv", 0), ("kidx", 1))):
                    for k in range(KT):
                        if n == 0:
                            pe.wait_ge(*reached(*branch[k]))
                        last = mm(ps[:, bank, :], wtile(0, n * KT + k), h[:, k, :], k == 0, k == KT - 1)
                    last.then_inc(*pe_done.step(name))
                for q in range(QT):
                    for k in range(KT):
                        last = mm(ps[:, 2, q * IH:(q + 1) * IH], h[:, k, q * P:(q + 1) * P], wtile(0, k, P, IH, 2 * KT * P),
                                  k == 0, k == KT - 1)
                last.then_inc(*pe_done.step("widx"))

                def index_queries(m):
                    load = load_b if m < 2 else load_c
                    if m % 2 == 0:
                        pe.wait_ge(*load.arrived())
                    if m >= 2:
                        pe.wait_ge(*act_done(f"qi{m - 2}b"))
                    for k in range(KT):
                        last = mm(ps[:, 4 + m % 2, :], wtile(load.s, (m % 2) * KT + k), h[:, k, :], k == 0, k == KT - 1)
                    last.then_inc(*pe_done.step(f"qi{m}"))
                index_queries(0)
                index_queries(1)
                pe.wait_ge(*act_done("ckv sq"))
                mm(ps[:, 3, :], ones, tmp[:, 0, :]).then_inc(*pe_done.step("ckv sq"))
                pe.wait_ge(small_in, 16)
                pe.wait_ge(att_in, 16)
                pe.wait_ge(*dve_done("ckv"))
                pe.wait_ge(*act_done("kidx"))
                mm(ps[0:16, 0, :], relb[:, :], cc("onehot")[0:32, 0:T])
                mm(ps[0:16, 1, 0:P], relb[:, :], cc("onehot")[0:32, T:BIAS_LEN]).then_inc(*pe_done.step("bias"))
                for t, (m, hh, q) in enumerate(todo):
                    if hh == 0 and q == 1:
                        if m >= 1 and m < 3:
                            index_queries(m + 1)
                        pe.wait_ge(*act_done(f"qi{m}b"))
                    if t >= 2:
                        pe.wait_ge(*act_done(f"relu{t - 2}"))
                    w = (q + 1) * P
                    mm(ps[:, 6 + t % 2, 0:w], qi[:, m % 2, hh, q * P:(q + 1) * P], kidx[:, 0:w]).then_inc(*pe_done.step(f"score{t}"))

            def act(act):
                act_done.enter(act)
                act.wait_ge(*pe_done("ckv"))
                nc.scalar.activation(tmp[:, 0, :], ps[:, 0, :], ACT.Square).then_inc(*act_done.step("ckv sq"))
                act.wait_ge(*pe_done("kidx"))
                nc.scalar.activation(kidx[:, :], ps[:, 1, :], ACT.Copy).then_inc(*act_done.step("kidx"))
                act.wait_ge(zeroed, 1)

                def index_queries(m):
                    if m >= 2:
                        t = todo.index((m - 2, 1, QT - 1))
                        act.wait_ge(*pe_done(f"score{t}"))
                    act.wait_ge(*pe_done(f"qi{m}"))
                    for hh, ab in ((0, "a"), (1, "b")):
                        r = slice(hh * HD, (hh + 1) * HD)
                        nc.scalar.activation(qi[r, m % 2, hh, :], ps[r, 4 + m % 2, :], ACT.Copy).then_inc(*act_done.step(f"qi{m}{ab}"))
                index_queries(0)
                act.wait_ge(*pe_done("ckv sq"))
                nc.scalar.activation(tmp[:, 1, :], ps[:, 3, :], ACT.Sqrt, bias=const("rms_eps"), scale=1.0 / P).then_inc(*act_done.step("ckv std"))
                act.wait_ge(*pe_done("bias"))
                nc.scalar.activation(brow[:, T:BIAS_LEN], ps[0:16, 1, 0:P], ACT.Copy)
                nc.scalar.activation(brow[:, 0:T], ps[0:16, 0, :], ACT.Copy).then_inc(*act_done.step("bias"))
                for t, (m, hh, q) in enumerate(todo):
                    w = (q + 1) * P
                    act.wait_ge(*pe_done(f"score{t}"))
                    if t >= 2:
                        act.wait_ge(*dve_done(f"add{t - 2}"))
                    nc.scalar.activation(rel[:, t % 2, 0:w], ps[:, 6 + t % 2, 0:w], ACT.Relu).then_inc(*act_done.step(f"relu{t}"))
                    if hh == 0 and q == 3 and m < 3:
                        index_queries(m + 1)

            def dve(dve):
                dve_done.enter(dve)
                topk_done.enter(dve)
                selected.enter(dve)
                dve.wait_ge(*pe_done("widx"))
                nc.vector.tensor_scalar(wts[:, :, :], ps[:, 2, 0:QT * IH].rearrange("p (q h) -> p q h", h=IH),
                                                   IH ** -0.5 * HD ** -0.5, None, ALU.mult).then_inc(*dve_done.step("widx"))
                dve.wait_ge(*act_done("ckv std"))
                nc.vector.reciprocal(tmp[:, 1, :], tmp[:, 1, :]).then_inc(*dve_done.step("ckv rstd"))
                dve.wait_ge(*dve_done("ckv rstd"))
                nc.vector.scalar_tensor_tensor(ckv[:, :], ps[:, 0, :], vcol("kv_norm"), tmp[:, 1, :], ALU.mult, ALU.mult).then_inc(*dve_done.step("ckv"))
                for t, (m, hh, q) in enumerate(todo):
                    w, head = (q + 1) * P, 2 * m + hh
                    dve.wait_ge(*act_done(f"relu{t}"))
                    weight = wts[:, q, head:head + 1]
                    if head == 0:
                        ins = nc.vector.tensor_scalar(score[:, q, 0:w], rel[:, t % 2, 0:w], weight, None, ALU.mult)
                    else:
                        dve.wait_ge(*dve_done(f"add{t - QT + 1}"))
                        ins = nc.vector.scalar_tensor_tensor(score[:, q, 0:w], rel[:, t % 2, 0:w], weight, score[:, q, 0:w],
                                                             ALU.mult, ALU.add)
                    ins.then_inc(*dve_done.step(f"add{t}"))
                dve.wait_ge(att_in, 16)
                dve.wait_ge(*dve_done(f"add{NI - 1}"))
                for q in range(1, QT):
                    own = score[:, q, q * P:(q + 1) * P]
                    nc.vector.tensor_tensor(own, own, cc("causal")[:, T - P:T], ALU.add).then_inc(*dve_done.step(f"causal{q}"))
                dve.wait_ge(*dve_done(f"causal{QT - 1}"))
                with dve.Fori(0, TOPK // 8) as i:
                    for q in range(1, QT):
                        dve.wait_ge(*topk_done(f"take{q}", i, 1))
                        alone(dve)
                        nc.vector.max(best[:, q, :], score[:, q, 0:(q + 1) * P]).then_inc(*topk_done.step(f"max{q}"))
                    for q in range(1, QT):
                        w = (q + 1) * P
                        dve.wait_ge(*topk_done(f"max{q}", i))
                        alone(dve)
                        nc.vector.match_replace(score[:, q, 0:w], best[:, q, :], score[:, q, 0:w], TAKEN).then_inc(*topk_done.step(f"take{q}"))
                dve.wait_ge(*topk_done(f"take{QT - 1}", TOPK // 8 - 1))
                for q in range(1, QT):
                    w = (q + 1) * P
                    nc.vector.tensor_scalar(score[:, q, 0:w], score[:, q, 0:w], TAKEN / 2, NEG, ALU.is_ge, ALU.mult).then_inc(*selected.step(f"select{q}"))

            phase(sp=sp, pool=pool, pe=pe, act=act, dve=dve)

            qs = keep("scaled_queries", [P, T], scope)
            qz = keep("latent_queries", [P, 2, T], scope)
            vals = keep("dsa_values", [P, QT, P], scope)
            hank = keep("bias_hankel", [P, 2, T], scope)
            hank_in = sem("bias_hankel_in")
            N = KT
            work = []
            for hh in range(2):
                for q in range(QT):
                    w = (q + 1) * P
                    off = T - P - q * P
                    work.append({"head": hh, "tile": q, "w": w, "query": qz[:, hh, q * P:(q + 1) * P], "keys": ckv[:, 0:w],
                                 "mask": cc("causal")[:, T - P:T] if q == 0 else score[:, q, 0:w],
                                 "extra": (cc("flip"), hank[:, hh, off:off + w]),
                                 "values": [vals[:, b, hh * HD:(hh + 1) * HD] for b in range(q + 1)], "first": True, "last": True})
            W = len(work)

            def before_pe(pe, i, S):
                pe.wait_ge(*load.arrived(i))
                pe.wait_ge(*S["act"]("lat0", i, 1))
                for k in range(KT):
                    last = mm(ps[:, 6, :], wtile(0, k), h[:, k, :], k == 0, k == KT - 1)
                last.then_inc(*S["pe"].step("q"))
                pe.wait_ge(*S["act"]("lat1", i, 1))
                for b in range(QT):
                    last = mm(ps[:, 7, b * P:(b + 1) * P], ckv[:, b * P:(b + 1) * P], wtile(0, KT + 2))
                last.then_inc(*S["pe"].step("v"))
                pe.wait_ge(*S["act"]("q", i))
                mm(ps[:, 6, :], wtile(0, KT), qs[:, :]).then_inc(*S["pe"].step("lat0"))
                pe.wait_ge(*S["dve"]("v", i))
                mm(ps[:, 7, :], wtile(0, KT + 1), qs[:, :]).then_inc(*S["pe"].step("lat1"))
                pe.wait_ge(*S["act"]("lat1", i))
                pe.wait_ge(hank_in, i * 16 + 16)

            def before_act(act, i, S):
                act.wait_ge(*S["pe"]("q", i))
                nc.scalar.activation(qs[:, :], ps[:, 6, :], ACT.Copy, scale=HD ** -0.5).then_inc(*S["act"].step("q"))
                for hh in range(2):
                    act.wait_ge(*S["pe"](f"lat{hh}", i))
                    nc.scalar.activation(qz[:, hh, :], ps[:, 6 + hh, :], ACT.Copy).then_inc(*S["act"].step(f"lat{hh}"))

            def before_dve(dve, i, S):
                dve.wait_ge(*S["pe"]("v", i))
                nc.vector.tensor_copy(vals[:, :, :], ps[:, 7, :].rearrange("p (b n) -> p b n", n=P)).then_inc(*S["dve"].step("v"))

            S = attend("dsa", scope, N, work, out,
                       [(selected, f"select{QT - 1}"), (act_done, f"relu{NI - 1}"), (dve_done, "ckv")],
                       {"pe": (["q", "v", "lat0", "lat1"], before_pe), "act": (["q", "lat0", "lat1"], before_act),
                        "dve": (["v"], before_dve)})
            load = Loads(0, N, S["pe"], "lat1")

            def sp2(sp):
                sp.wait_ge(*load.vacated())
                sp.wait_ge(rows_out, 16)
                with sp.Fori(0, N) as i:
                    sp.wait_ge(*load.vacated(i))
                    sp.dma_start(load.slot(row("dsa_heads", i)), row("dsa_heads", i)).then_inc(*load.arrival)
                    sp.wait_ge(*S["pe"](f"L{W - 1}", i, 1))
                    sp.dma_start(hank[:, :, :], bass.AP(tensor=scratch.tensor, offset=i * (2 * BIAS_LEN),
                                                              ap=[[1, P], [BIAS_LEN, 2], [1, T]])).then_inc(hank_in, 16)

            phase(sp=sp2)
            return [(S["act"], "out", N - 1)]

        def mixer_inputs(scope, branch):
            t = {}

            def have(name, shape):
                t[name] = keep(name, shape, scope)
                return t[name]
            cb = have("const_attention_2", [P, CB["all"][1]])

            def cc(name):
                return const(name, cb, CB)
            kz = {n: have(f"tokens_{n}", [P, 2, T]) for n in "kv"}
            keys = {n: have(f"keys_{n}", [P, T]) for n in ("slc", "win")}
            vals = have("values", [P, QT, 2 * P])
            gates = have("gates", [P, QT, 24])
            kcmp, vcmp = have("keys_cmp", [P, P]), have("values_cmp", [P, P])
            with ExitStack() as own:
                raw = keep("keys_raw", [P, 3, T], own)
                sq = keep("keys_sq", [P, 2, T], own)
                rstd = keep("keys_rstd", [P, 2, T], own)
                cos = keep("keys_cos", [P, T], own)
                sin = keep("keys_sin", [P, 3, T], own)
                z = keep("forget", [8, 5, T], own)
                c2 = keep("forget_sums", [8, 2, T], own)
                hidden = keep("cmp_hidden", [P, 2, 2, 2 * NCMP], own)
                posb = keep("cmp_pos", [P, 4], own)
                w2 = keep("cmp_w2", [P, 4 * HD], own)
                csq = keep("cmp_sq", [P, 3, NCMP], own)
            zeroed, const_in, w2_in, sums_out = sem("mixer_zeroed"), sem("mixer_constants_in"), sem("cmp_w2_in"), sem("forget_sums_out")
            loads_n = 8
            PE = (["kc", "vc", "slc", "gates", "fl", "win", "vals", "slc sum", "win sum", "kc rot", "slc rot", "win rot"]
                  + [f"cmp{n}" for n in range(loads_n)] + ["k2", "v2", "k2 sum"])
            AC = ["slc sq", "kc", "v0", "v1", "gates", "win sq", "slc std", "win std", "abs", "exp", "ln",
                  "hid k0", "hid k1", "hid v0", "hid v1", "k2 sq", "v2", "k2 std"]
            DV = (["z", "vals0", "vals1"] + [f"{n} {m}" for n in ("slc", "win") for m in ("rstd", "n")]
                  + ["kc cos", "kc sin", "kc0", "kc1"] + [f"{n} {m}" for n in ("slc", "win") for m in ("cos", "sin", "add")]
                  + ["1+e", "min", "logf", "cum", "-cum", "pos k", "pos v", "k2 rstd", "k2"])
            pe_done, act_done, dve_done = (steps(f"in2_{n}", q) for n, q in (("pe", PE), ("act", AC), ("dve", DV)))
            load_a, load_b = Loads(0, 1, pe_done, "fl"), Loads(1, 1, pe_done, "vals")
            cmp_loads = [Loads(n % 2, 1, pe_done, f"cmp{n}") for n in range(loads_n)]

            def sp(sp):
                for n, l in enumerate((load_a, load_b)):
                    sp.wait_ge(*l.vacated())
                    sp.dma_start(l.slot(row(f"mix_{n}", 0)), row(f"mix_{n}", 0)).then_inc(*l.arrival)
                sp.wait_ge(*reached(*branch[0]))
                sp.dma_start(cb[:, :], d["const_attention"][:, :]).then_inc(const_in, 16)
                sp.dma_start(w2[:, :], d["cmp_w2"][:, :]).then_inc(w2_in, 16)
                for n, l in enumerate(cmp_loads):
                    sp.wait_ge(*l.vacated())
                    sp.dma_start(l.slot(row("cmp_w1", n)), row("cmp_w1", n)).then_inc(*l.arrival)
                sp.wait_ge(*dve_done("-cum"))
                sp.dma_start(d["forget_scratch"].rearrange("s h t -> h s t"), c2[:, :, :]).then_inc(sums_out, 16)

            def pool(pool):
                pool.wait_ge(*reached(*branch[0]))
                for n in (kz["k"], kz["v"]):
                    nc.gpsimd.memset(n[:, :, :], 0.0).then_inc(zeroed, 1)
                for n in (kcmp, vcmp):
                    nc.gpsimd.memset(n[:, :], 0.0).then_inc(zeroed, 1)
                nc.gpsimd.memset(z[:, 4, :], 1.0).then_inc(zeroed, 1)

            def pe(pe):
                pe_done.enter(pe)
                pe.wait_ge(*load_a.arrived())
                for n, (name, bank) in enumerate((("kc", 0), ("vc", 1), ("slc", 2))):
                    for k in range(KT):
                        if n == 0:
                            pe.wait_ge(*reached(*branch[k]))
                        last = mm(ps[:, bank, :], wtile(0, n * KT + k), h[:, k, :], k == 0, k == KT - 1)
                    last.then_inc(*pe_done.step(name))
                at = 3 * KT * P
                for q in range(QT):
                    for k in range(KT):
                        last = mm(ps[:, 3, q * 24:(q + 1) * 24], h[:, k, q * P:(q + 1) * P], wtile(0, k, P, 24, at), k == 0, k == KT - 1)
                last.then_inc(*pe_done.step("gates"))
                for k in range(KT):
                    last = mm(ps[0:8, 4, :], wtile(0, k, P, 8, at + 24 * KT), h[:, k, :], k == 0, k == KT - 1)
                last.then_inc(*pe_done.step("fl"))
                pe.wait_ge(*load_b.arrived())
                for k in range(KT):
                    last = mm(ps[:, 5, :], wtile(1, k), h[:, k, :], k == 0, k == KT - 1)
                last.then_inc(*pe_done.step("win"))
                for q in range(QT):
                    for k in range(KT):
                        last = mm(ps[:, 6 + q // 2, (q % 2) * 256:(q % 2) * 256 + 256], h[:, k, q * P:(q + 1) * P],
                                  wtile(1, k, P, 2 * P, KT * P), k == 0, k == KT - 1)
                last.then_inc(*pe_done.step("vals"))
                pe.wait_ge(const_in, 16)
                for n, (name, bank, free) in enumerate((("slc", 3, (act_done, "gates")), ("win", 4, (dve_done, "z")))):
                    pe.wait_ge(*act_done(f"{name} sq"))
                    pe.wait_ge(*reached(*free))
                    mm(ps[:, bank, :], blockones, sq[:, n, :]).then_inc(*pe_done.step(f"{name} sum"))
                pe.wait_ge(*act_done("kc"))
                mm(ps[:, 0, :], cc("rot"), raw[:, 2, :]).then_inc(*pe_done.step("kc rot"))
                for n, (name, bank) in enumerate((("slc", 2), ("win", 5))):
                    pe.wait_ge(*dve_done(f"{name} n"))
                    mm(ps[:, bank, :], cc("rot"), raw[:, n, :]).then_inc(*pe_done.step(f"{name} rot"))
                pe.wait_ge(*dve_done("kc1"))
                pe.wait_ge(*act_done("v1"))
                pe.wait_ge(*dve_done("win sin"))
                pe.wait_ge(*dve_done("vals1"))
                for n, l in enumerate(cmp_loads):
                    pe.wait_ge(*l.arrived())
                    u, part = n // 4, n % 4
                    for e in range(CMP_L // 4):
                        tok = part * (CMP_L // 4) + e
                        first, final = tok == 0, tok == CMP_L - 1
                        for m in range(2):
                            w = wtile(n % 2, e * 2 + m)
                            toks = kz["kv"[u]][:, :, tok:tok + CMP_S * (NCMP - 1) + 1:CMP_S]
                            mm(ps[:, 2 * u + m, 0:2 * NCMP].rearrange("p (g n) -> p g n", g=2), w, toks, first, final)
                            last = mm(ps[:, 4 + 2 * u + m, 0:1], w, vcol("pos_" + "kv"[u], tok), first, final)
                    last.then_inc(*pe_done.step(f"cmp{n}"))
                pe.wait_ge(w2_in, 16)
                pe.wait_ge(*act_done("hid k1"))
                for g in range(2):
                    for m in range(2):
                        last = mm(ps[g * HD:(g + 1) * HD, 0, 0:NCMP], w2[:, m * HD:(m + 1) * HD],
                                  hidden[:, 0, m, g * NCMP:(g + 1) * NCMP], m == 0, m == 1)
                last.then_inc(*pe_done.step("k2"))
                pe.wait_ge(*act_done("hid v1"))
                for g in range(2):
                    for m in range(2):
                        last = mm(ps[0:NCMP, 2, g * HD:(g + 1) * HD], hidden[:, 1, m, g * NCMP:(g + 1) * NCMP],
                                  w2[:, (2 + m) * HD:(3 + m) * HD], m == 0, m == 1)
                last.then_inc(*pe_done.step("v2"))
                pe.wait_ge(*act_done("k2 sq"))
                mm(ps[:, 1, 0:NCMP], blockones, csq[:, 0, :]).then_inc(*pe_done.step("k2 sum"))

            def act(act):
                act_done.enter(act)
                a = nc.scalar.activation
                act.wait_ge(*pe_done("slc"))
                a(sq[:, 0, :], ps[:, 2, :], ACT.Square).then_inc(*act_done.step("slc sq"))
                a(raw[:, 2, :], ps[:, 0, :], ACT.Copy).then_inc(*act_done.step("kc"))
                act.wait_ge(zeroed, 5)
                for g in range(2):
                    r = slice(g * HD, (g + 1) * HD)
                    a(kz["v"][r, g, :], ps[r, 1, :], ACT.Copy).then_inc(*act_done.step(f"v{g}"))
                act.wait_ge(*pe_done("gates"))
                a(gates[:, :, :], ps[:, 3, 0:QT * 24].rearrange("p (q n) -> p q n", n=24), ACT.Sigmoid).then_inc(*act_done.step("gates"))
                act.wait_ge(*pe_done("win"))
                a(sq[:, 1, :], ps[:, 5, :], ACT.Square).then_inc(*act_done.step("win sq"))
                for n, (name, bank) in enumerate((("slc", 3), ("win", 4))):
                    act.wait_ge(*pe_done(f"{name} sum"))
                    a(rstd[:, n, :], ps[:, bank, :], ACT.Sqrt, bias=const("rms_eps"), scale=1.0 / HD).then_inc(*act_done.step(f"{name} std"))
                act.wait_ge(*dve_done("z"))
                a(z[:, 1, :], z[:, 0, :], ACT.Abs).then_inc(*act_done.step("abs"))
                act.wait_ge(*act_done("abs"))
                a(z[:, 2, :], z[:, 1, :], ACT.Exp, scale=-1.0).then_inc(*act_done.step("exp"))
                act.wait_ge(*dve_done("1+e"))
                a(z[:, 3, :], z[:, 2, :], ACT.Ln).then_inc(*act_done.step("ln"))
                for u in range(2):
                    act.wait_ge(*dve_done("pos " + "kv"[u]))
                    for m in range(2):
                        a(hidden[:, u, m, :], ps[:, 2 * u + m, 0:2 * NCMP], ACT.Silu, bias=posb[:, 2 * u + m:2 * u + m + 1]).then_inc(*act_done.step(f"hid {'kv'[u]}{m}"))
                act.wait_ge(*pe_done("k2"))
                a(csq[:, 0, :], ps[:, 0, 0:NCMP], ACT.Square).then_inc(*act_done.step("k2 sq"))
                act.wait_ge(*pe_done("v2"))
                a(vcmp[0:NCMP, :], ps[0:NCMP, 2, 0:P], ACT.Copy).then_inc(*act_done.step("v2"))
                act.wait_ge(*pe_done("k2 sum"))
                a(csq[:, 1, :], ps[:, 1, 0:NCMP], ACT.Sqrt, bias=const("rms_eps"), scale=1.0 / HD).then_inc(*act_done.step("k2 std"))

            def dve(dve):
                dve_done.enter(dve)
                tt, ts, stt = nc.vector.tensor_tensor, nc.vector.tensor_scalar, nc.vector.scalar_tensor_tensor
                dve.wait_ge(*pe_done("fl"))
                ts(z[:, 0, :], ps[0:8, 4, :], vcol("b_forget")[0:8, :], None, ALU.add).then_inc(*dve_done.step("z"))
                dve.wait_ge(*pe_done("vals"))
                for b in range(2):
                    nc.vector.tensor_copy(vals[:, 2 * b:2 * b + 2, :], ps[:, 6 + b, :].rearrange("p (q n) -> p q n", q=2)).then_inc(*dve_done.step(f"vals{b}"))
                for n, (name, bank) in enumerate((("slc", 2), ("win", 5))):
                    dve.wait_ge(*act_done(f"{name} std"))
                    nc.vector.reciprocal(rstd[:, n, :], rstd[:, n, :]).then_inc(*dve_done.step(f"{name} rstd"))
                    dve.wait_ge(*dve_done(f"{name} rstd"))
                    stt(raw[:, n, :], ps[:, bank, :], vcol(f"k_{name}"), rstd[:, n, :], ALU.mult, ALU.mult).then_inc(*dve_done.step(f"{name} n"))
                dve.wait_ge(const_in, 16)
                dve.wait_ge(*act_done("kc"))
                tt(cos[:, :], raw[:, 2, :], cc("cos"), ALU.mult).then_inc(*dve_done.step("kc cos"))
                dve.wait_ge(*pe_done("kc rot"))
                tt(sin[:, 2, :], ps[:, 0, :], cc("sin"), ALU.mult).then_inc(*dve_done.step("kc sin"))
                dve.wait_ge(zeroed, 5)
                dve.wait_ge(*dve_done("kc sin"))
                for g in range(2):
                    r = slice(g * HD, (g + 1) * HD)
                    tt(kz["k"][r, g, :], cos[r, :], sin[r, 2, :], ALU.add).then_inc(*dve_done.step(f"kc{g}"))
                for n, (name, bank) in enumerate((("slc", 2), ("win", 5))):
                    dve.wait_ge(*dve_done(f"{name} n"))
                    tt(keys[name][:, :], raw[:, n, :], cc("cos"), ALU.mult).then_inc(*dve_done.step(f"{name} cos"))
                    dve.wait_ge(*pe_done(f"{name} rot"))
                    tt(sin[:, n, :], ps[:, bank, :], cc("sin"), ALU.mult).then_inc(*dve_done.step(f"{name} sin"))
                    dve.wait_ge(*dve_done(f"{name} sin"))
                    tt(keys[name][:, :], keys[name][:, :], sin[:, n, :], ALU.add).then_inc(*dve_done.step(f"{name} add"))
                dve.wait_ge(*act_done("exp"))
                ts(z[:, 2, :], z[:, 2, :], 1.0, None, ALU.add).then_inc(*dve_done.step("1+e"))
                ts(z[:, 1, :], z[:, 0, :], 0.0, None, ALU.min).then_inc(*dve_done.step("min"))
                dve.wait_ge(*dve_done("min"))
                dve.wait_ge(*act_done("ln"))
                tt(z[:, 0, :], z[:, 1, :], z[:, 3, :], ALU.subtract).then_inc(*dve_done.step("logf"))
                dve.wait_ge(*dve_done("logf"))
                nc.vector.tensor_tensor_scan(c2[:, 0, :], z[:, 4, :], z[:, 0, :], 0.0, ALU.mult, ALU.add).then_inc(*dve_done.step("cum"))
                dve.wait_ge(*dve_done("cum"))
                ts(c2[:, 1, :], c2[:, 0, :], -1.0, None, ALU.mult).then_inc(*dve_done.step("-cum"))
                for u in range(2):
                    dve.wait_ge(*pe_done(f"cmp{4 * u + 3}"))
                    nc.vector.tensor_copy(posb[:, 2 * u:2 * u + 2], ps[:, 4 + 2 * u:6 + 2 * u, 0]).then_inc(*dve_done.step("pos " + "kv"[u]))
                dve.wait_ge(*act_done("k2 std"))
                nc.vector.reciprocal(csq[:, 2, :], csq[:, 1, :]).then_inc(*dve_done.step("k2 rstd"))
                dve.wait_ge(*dve_done("k2 rstd"))
                stt(kcmp[:, 0:NCMP], ps[:, 0, 0:NCMP], vcol("k_cmp"), csq[:, 2, :], ALU.mult, ALU.mult).then_inc(*dve_done.step("k2"))

            phase(sp=sp, pool=pool, pe=pe, act=act, dve=dve)
            return t, cc, [(dve_done, "k2"), (act_done, "v2")], sums_out

        def grouped_attention(scope, t, cc, ready, out):
            qz = keep("nsa_queries", [P, 2, T], scope)
            sq, std, qn, qc, qsin = (keep(f"nsa_q_{n}", [P, T], scope) for n in ("sq", "std", "n", "cos", "sin"))
            gst = keep("pair_gates", [P, QT, 6], scope)
            zeroed = sem("nsa_queries_zeroed")
            N = 4
            work = []
            for hh in range(2):
                for q in range(QT):
                    for b, (keys, v0) in enumerate(((t["keys_cmp"], None), (t["keys_slc"], 0), (t["keys_win"], P))):
                        w = P if b == 0 else (q + 1) * P
                        mask = cc("cmp_mask")[:, q * P:(q + 1) * P] if b == 0 else cc("causal")[:, T - w:T]
                        values = ([t["values_cmp"][:, hh * HD:(hh + 1) * HD]] if b == 0 else
                                  [t["values"][:, s, v0 + hh * HD:v0 + (hh + 1) * HD] for s in range(q + 1)])
                        work.append({"head": hh, "tile": q, "w": w, "query": qz[:, hh, q * P:(q + 1) * P], "keys": keys[:, 0:w],
                                     "mask": mask, "values": values, "gate": gst[:, q, hh * 3 + b:hh * 3 + b + 1],
                                     "first": b == 0, "last": b == 2})
            W = len(work)

            def before_pe(pe, i, S):
                pe.wait_ge(*load.arrived(i))
                pe.wait_ge(*S["dve"]("qn", i, 1))
                for k in range(KT):
                    last = mm(ps[:, 6, :], wtile(0, k), h[:, k, :], k == 0, k == KT - 1)
                last.then_inc(*S["pe"].step("q"))
                pe.wait_ge(*S["act"]("q sq", i))
                pe.wait_ge(*S["dve"]("q sin", i, 1))
                mm(ps[:, 7, :], blockones, sq[:, :]).then_inc(*S["pe"].step("q sum"))
                pe.wait_ge(*S["dve"]("qn", i))
                mm(ps[:, 7, :], cc("rot"), qn[:, :]).then_inc(*S["pe"].step("q rot"))
                pe.wait_ge(*S["act"]("q1", i))

            def before_act(act, i, S):
                act.wait_ge(*S["pe"]("q", i))
                nc.scalar.activation(sq[:, :], ps[:, 6, :], ACT.Square).then_inc(*S["act"].step("q sq"))
                act.wait_ge(*S["pe"]("q sum", i))
                nc.scalar.activation(std[:, :], ps[:, 7, :], ACT.Sqrt, bias=const("rms_eps"), scale=1.0 / HD).then_inc(*S["act"].step("q std"))
                act.wait_ge(*S["dve"]("q add", i))
                act.wait_ge(zeroed, 1)
                for hh in range(2):
                    r = slice(hh * HD, (hh + 1) * HD)
                    nc.scalar.activation(qz[r, hh, :], qc[r, :], ACT.Copy, scale=HD ** -0.5).then_inc(*S["act"].step(f"q{hh}"))

            def before_dve(dve, i, S):
                dve.wait_ge(*S["dve"](f"diag{W - 1}", i, 1))
                alone(dve)
                nc.vector.tensor_copy(gst[:, :, :], t["gates"][:, :, bass.ds(i * 6, 6)]).then_inc(*S["dve"].step("gates"))
                dve.wait_ge(*S["dve"]("gates", i))
                if_valid = cc("cmp_valid")[:, 0:1]
                for hh in range(2):
                    nc.vector.tensor_scalar(gst[:, 0, hh * 3:hh * 3 + 1], gst[:, 0, hh * 3:hh * 3 + 1], if_valid, None,
                                                          ALU.mult).then_inc(*S["dve"].step(f"valid{hh}"))
                dve.wait_ge(*S["act"]("q std", i))
                nc.vector.reciprocal(std[:, :], std[:, :]).then_inc(*S["dve"].step("q rstd"))
                dve.wait_ge(*S["dve"]("q rstd", i))
                nc.vector.scalar_tensor_tensor(qn[:, :], ps[:, 6, :], vcol("q_nsa"), std[:, :], ALU.mult, ALU.mult).then_inc(*S["dve"].step("qn"))
                dve.wait_ge(*S["dve"]("qn", i))
                nc.vector.tensor_tensor(qc[:, :], qn[:, :], cc("cos"), ALU.mult).then_inc(*S["dve"].step("q cos"))
                dve.wait_ge(*S["pe"]("q rot", i))
                nc.vector.tensor_tensor(qsin[:, :], ps[:, 7, :], cc("sin"), ALU.mult).then_inc(*S["dve"].step("q sin"))
                dve.wait_ge(*S["dve"]("q sin", i))
                nc.vector.tensor_tensor(qc[:, :], qc[:, :], qsin[:, :], ALU.add).then_inc(*S["dve"].step("q add"))

            def pool(pool):
                for r in ready:
                    pool.wait_ge(*reached(*r))
                nc.gpsimd.memset(qz[:, :, :], 0.0).then_inc(zeroed, 1)

            S = attend("nsa", scope, N, work, out, ready,
                       {"pe": (["q", "q sum", "q rot"], before_pe), "act": (["q sq", "q std", "q0", "q1"], before_act),
                        "dve": (["gates", "valid0", "valid1", "q rstd", "qn", "q cos", "q sin", "q add"], before_dve)})
            load = Loads(0, N, S["pe"], "q")

            def sp(sp):
                sp.wait_ge(*load.vacated())
                with sp.Fori(0, N) as i:
                    sp.wait_ge(*load.vacated(i))
                    sp.dma_start(load.slot(row("nsa_q", i)), row("nsa_q", i)).then_inc(*load.arrival)

            phase(sp=sp, pool=pool)
            return [(S["act"], "out", N - 1)], [(S["pe"], f"O{W - 1}", N - 1)]

        def forgetting_attention(scope, cc, ready, sums_out, out):
            qz = keep("fox_queries", [P, 2, T], scope)
            kn = keep("fox_keys", [P, T], scope)
            vals = keep("fox_values", [P, QT, P], scope)
            sq, std = (keep(f"fox_{n}", [P, T], scope) for n in ("sq", "std"))
            left, right = (keep(f"forget_{n}", [P, 2, T], scope) for n in ("left", "right"))
            zeroed, sums_in = sem("fox_zeroed"), sem("forget_sums_in")
            N = 4
            work = []
            for hh in range(2):
                for q in range(QT):
                    w = (q + 1) * P
                    tok = slice(q * P, (q + 1) * P)
                    work.append({"head": hh, "tile": q, "w": w, "query": qz[:, hh, tok], "keys": kn[:, 0:w],
                                 "mask": cc("causal")[:, T - w:T], "extra": (left[:, hh, tok], right[:, hh, 0:w]),
                                 "values": [vals[:, s, hh * HD:(hh + 1) * HD] for s in range(q + 1)], "first": True, "last": True})
            W = len(work)

            def before_pe(pe, i, S):
                pe.wait_ge(*load.arrived(i))
                for n, name in enumerate("qk"):
                    pe.wait_ge(*S["dve"](*(("kn", i, 1) if n == 0 else ("q1", i))))
                    for k in range(KT):
                        last = mm(ps[:, 6, :], wtile(1, n * KT + k), h[:, k, :], k == 0, k == KT - 1)
                    last.then_inc(*S["pe"].step(name))
                    pe.wait_ge(*S["act"](f"{name} sq", i))
                    if n == 0:
                        pe.wait_ge(*S["act"]("v", i, 1))
                    else:
                        pe.wait_ge(*S["act"]("q std", i))
                    mm(ps[:, 7, :], blockones, sq[:, :]).then_inc(*S["pe"].step(f"{name} sum"))
                pe.wait_ge(*S["act"]("k std", i))
                for b in range(QT):
                    for k in range(KT):
                        last = mm(ps[:, 7, b * P:(b + 1) * P], h[:, k, b * P:(b + 1) * P], wtile(1, 2 * KT + k), k == 0, k == KT - 1)
                last.then_inc(*S["pe"].step("v"))
                pe.wait_ge(*S["dve"]("kn", i))
                pe.wait_ge(*S["act"]("v", i))
                pe.wait_ge(sums_in, i * 32 + 32)

            def before_act(act, i, S):
                for name in "qk":
                    act.wait_ge(*S["pe"](name, i))
                    if name == "k":
                        act.wait_ge(*S["pe"]("q sum", i))
                    nc.scalar.activation(sq[:, :], ps[:, 6, :], ACT.Square).then_inc(*S["act"].step(f"{name} sq"))
                    act.wait_ge(*S["pe"](f"{name} sum", i))
                    if name == "k":
                        act.wait_ge(*S["dve"]("q1", i))
                    nc.scalar.activation(std[:, :], ps[:, 7, :], ACT.Sqrt, bias=const("rms_eps"), scale=1.0 / HD).then_inc(*S["act"].step(f"{name} std"))
                act.wait_ge(*S["pe"]("v", i))
                nc.scalar.activation(vals[:, :, :], ps[:, 7, :].rearrange("p (b n) -> p b n", n=P), ACT.Copy).then_inc(*S["act"].step("v"))

            def before_dve(dve, i, S):
                dve.wait_ge(*S["act"]("q std", i))
                nc.vector.reciprocal(std[:, :], std[:, :]).then_inc(*S["dve"].step("q rstd"))
                dve.wait_ge(*S["dve"]("q rstd", i))
                dve.wait_ge(zeroed, 5)
                for hh in range(2):
                    r = slice(hh * HD, (hh + 1) * HD)
                    nc.vector.scalar_tensor_tensor(qz[r, hh, :], ps[r, 6, :], qg[r, :], std[r, :], ALU.mult, ALU.mult).then_inc(*S["dve"].step(f"q{hh}"))
                dve.wait_ge(*S["act"]("k std", i))
                nc.vector.reciprocal(std[:, :], std[:, :]).then_inc(*S["dve"].step("k rstd"))
                dve.wait_ge(*S["dve"]("k rstd", i))
                nc.vector.scalar_tensor_tensor(kn[:, :], ps[:, 6, :], vcol("k_fox"), std[:, :], ALU.mult, ALU.mult).then_inc(*S["dve"].step("kn"))

            qg = keep("fox_query_gain", [P, 1], scope)

            def pool(pool):
                for r in ready:
                    pool.wait_ge(*reached(*r))
                for n in (qz, left, right):
                    nc.gpsimd.memset(n[:, :, :], 0.0).then_inc(zeroed, 1)
                nc.gpsimd.tensor_scalar(qg[:, :], vcol("q_fox"), HD ** -0.5, None, ALU.mult).then_inc(zeroed, 1)
                pool.wait_ge(zeroed, 4)
                nc.gpsimd.memset(left[32:33, :, :], 1.0)
                nc.gpsimd.memset(right[0:1, :, :], 1.0).then_inc(zeroed, 1)

            S = attend("fox", scope, N, work, out, ready,
                       {"pe": (["q", "q sum", "k", "k sum", "v"], before_pe),
                        "act": (["q sq", "q std", "k sq", "k std", "v"], before_act),
                        "dve": (["q rstd", "q0", "q1", "k rstd", "kn"], before_dve)})
            load = Loads(1, N, S["pe"], "v")

            def sp(sp):
                sp.wait_ge(*load.vacated())
                sp.wait_ge(sums_out, 16)
                sp.wait_ge(zeroed, 5)
                with sp.Fori(0, N) as i:
                    sp.wait_ge(*load.vacated(i))
                    sp.dma_start(load.slot(row("fox_qkv", i)), row("fox_qkv", i)).then_inc(*load.arrival)
                    sp.wait_ge(*S["pe"](f"L{W - 1}", i, 1))
                    sums = d["forget_scratch"]
                    sp.dma_start(left[0:1, :, :], sums[0:1, bass.ds(i * 2, 2), :]).then_inc(sums_in, 16)
                    sp.dma_start(right[32:33, :, :], sums[1:2, bass.ds(i * 2, 2), :]).then_inc(sums_in, 16)

            phase(sp=sp, pool=pool)
            return [(S["act"], "out", N - 1)]

        def gated_embedding(scope, branch):
            emb = keep("embedding", [P, 2, T], scope)
            e = keep("projected", [P, KT, T], scope)
            g = keep("embedding_gate", [P, KT, T], scope)
            n = KT // 2
            emb_in, written = sem("embedding_in"), sem("result_written")
            pe_done = steps("ple_pe", ["gate0", "e0", "gate1", "e1"])
            act_done = steps("ple_act", ["gate0", "gate1"])
            dve_done = steps("ple_dve", ["e0", "e1"])
            loads = [Loads(s, n, pe_done, f"e{s}") for s in range(2)]

            def sp(sp):
                sp.wait_ge(*reached(*branch[0]))
                sp.dma_start(emb[:, :, :], d["embedding"][:, :, :]).then_inc(emb_in, 16)
                for s in range(2):
                    sp.wait_ge(*loads[s].vacated())
                with sp.Fori(0, n) as i:
                    for s in range(2):
                        sp.wait_ge(*loads[s].vacated(i))
                        sp.dma_start(loads[s].slot(row("ple", i * 2 + s)), row("ple", i * 2 + s)).then_inc(*loads[s].arrival)

            def pe(pe):
                pe_done.enter(pe)
                for r in branch:
                    pe.wait_ge(*reached(*r))
                pe.wait_ge(emb_in, 16)
                with pe.Fori(0, n) as i:
                    for s in range(2):
                        pe.wait_ge(*loads[s].arrived(i))
                        pe.wait_ge(*act_done(f"gate{s}", i, 1))
                        for k in range(KT):
                            last = mm(ps[:, 2 * s, :], wtile(s, k), h[:, k, :], k == 0, k == KT - 1)
                        last.then_inc(*pe_done.step(f"gate{s}"))
                        pe.wait_ge(*dve_done(f"e{s}", i, 1))
                        for k in range(2):
                            last = mm(ps[:, 2 * s + 1, :], wtile(s, KT + k), emb[:, k, :], k == 0, k == 1)
                        last.then_inc(*pe_done.step(f"e{s}"))

            def act(act):
                act_done.enter(act)
                with act.Fori(0, n) as i:
                    for s in range(2):
                        act.wait_ge(*pe_done(f"gate{s}", i))
                        alone(act)
                        nc.scalar.activation(tile_of(g, i * 2 + s), ps[:, 2 * s, :], ACT.Sigmoid).then_inc(*act_done.step(f"gate{s}"))

            def dve(dve):
                dve_done.enter(dve)
                with dve.Fori(0, n) as i:
                    for s in range(2):
                        dve.wait_ge(*pe_done(f"e{s}", i))
                        alone(dve)
                        nc.vector.tensor_copy(tile_of(e, i * 2 + s), ps[:, 2 * s + 1, :]).then_inc(*dve_done.step(f"e{s}"))

            phase(sp=sp, pe=pe, act=act, dve=dve)
            tiles = [e[:, j, :] for j in range(KT)]
            normed = rms_norm("ple_norm", scope, tiles, [(dve_done, f"e{j % 2}", j // 2) for j in range(KT)],
                              [vcol("ple", j) for j in range(KT)], tiles)
            pool_done = steps("ple_pool", [f"gated{j}" for j in range(KT)])
            sum_done = steps("ple_sum", [f"sum{j}" for j in range(KT)])

            def gate(pool):
                pool_done.enter(pool)
                pool.wait_ge(*act_done("gate1", n - 1))
                for j in range(KT):
                    pool.wait_ge(*reached(*normed[j]))
                    nc.gpsimd.tensor_tensor(e[:, j, :], e[:, j, :], g[:, j, :], ALU.mult).then_inc(*pool_done.step(f"gated{j}"))

            def add(dve):
                sum_done.enter(dve)
                for j in range(KT):
                    dve.wait_ge(*pool_done(f"gated{j}"))
                    nc.vector.tensor_tensor(x[:, j, :], x[:, j, :], e[:, j, :], ALU.add).then_inc(*sum_done.step(f"sum{j}"))

            def store(sp):
                for j in range(KT):
                    sp.wait_ge(*sum_done(f"sum{j}"))
                    sp.dma_start(d["out"][:, j, :], x[:, j, :]).then_inc(written, 16)
                sp.wait_ge(written, 16 * KT)

            phase(pool=gate, dve=add, sp=store)

        ready = modulation()
        with ExitStack() as scope:
            xs, lora, mix_pe, mix_act, mix_dve = time_mix_inputs(scope, ready)
            yout, rec_done, name, turn = recurrence(scope, xs, lora, mix_pe, mix_act, mix_dve)
        recurred = (rec_done, name, turn)
        scaled = residual_again([recurred])
        summed = project("rwkv_out", "rwkv_out", [yout[:, k, :] for k in range(KT)], [recurred], (0, GT1), [scaled])
        with ExitStack() as scope:
            branch, x_ready = layer_norm("ln00", scope, 0, 0, summed, (0, SH2, SC2))
            summed = feed_forward("ff0", scope, branch, (0, GT2), x_ready)
        with ExitStack() as scope:
            branch, x_ready = layer_norm("ln01", scope, 0, 1, summed, (1, SH1, SC1))
            mixed = keep("attended", [P, KT, T], scope)
            done = sparse_attention(scope, branch, mixed)
            summed = project("dsa_out", "dsa_out", [mixed[:, k, :] for k in range(KT)], done, (1, GT1), x_ready)
        with ExitStack() as scope:
            branch, x_ready = layer_norm("ln10", scope, 1, 0, summed, (1, SH2, SC2))
            summed = feed_forward("ff1", scope, branch, (1, GT2), x_ready)
        tiles_of_x, tiles_of_h = [x[:, j, :] for j in range(KT)], [h[:, j, :] for j in range(KT)]

        def gains(name):
            return [vcol(name, j) for j in range(KT)]
        with ExitStack() as scope:
            normed, _ = layer_norm("ln11", scope, 1, 1, summed, None)
        with ExitStack() as scope:
            branch = rms_norm("rms1", scope, tiles_of_x, normed, gains("ffn1"), tiles_of_h)
            summed = feed_forward("ffn1", scope, branch, 0.5)
        with ExitStack() as scope:
            branch = rms_norm("rms2", scope, tiles_of_x, summed, gains("mix"), tiles_of_h)
        with ExitStack() as scope:
            mixed = keep("mixed", [P, KT, T], scope)
            t, cc, ready, sums_out = mixer_inputs(scope, branch)
            with ExitStack() as own:
                nsa_done, nsa_pe = grouped_attention(own, t, cc, ready, mixed[:, 0:4, :])
            with ExitStack() as own:
                fox_done = forgetting_attention(own, cc, nsa_done + nsa_pe, sums_out, mixed[:, 4:8, :])
            with ExitStack() as own:
                outs = []
                for n, (part, done) in enumerate((("nsa", nsa_done), ("fox", fox_done))):
                    part_tiles = [mixed[:, 4 * n + j, :] for j in range(4)]
                    outs += rms_norm(f"rms_{part}", own, part_tiles, [fox_done[0]] * 4,
                                     [vcol("out_norm", 4 * n + j) for j in range(4)], part_tiles)
                summed = project("mix_out", "mix_out", [mixed[:, k, :] for k in range(KT)], outs, 1.0)
        with ExitStack() as scope:
            branch = rms_norm("rms3", scope, tiles_of_x, summed, gains("ffn2"), tiles_of_h)
            summed = feed_forward("ffn2", scope, branch, 0.5)
        with ExitStack() as scope:
            branch = rms_norm("rms4", scope, tiles_of_x, summed, gains("ple_gate"), tiles_of_h)
            gated_embedding(scope, branch)

        block = ctx.enter_context(nc.Block())

        @block.sync
        def _(eng):
            for program in programs["sp"]:
                program(eng)

        @block.tensor
        def _(eng):
            for program in programs["pe"]:
                program(eng)

        @block.scalar
        def _(eng):
            for program in programs["act"]:
                program(eng)

        @block.vector
        def _(eng):
            for program in programs["dve"]:
                program(eng)

        @block.gpsimd
        def _(eng):
            for program in programs["pool"]:
                program(eng)


def constant_tables():
    s, t = np.arange(P)[:, None], np.arange(P)[None, :]
    same = (s // CH) == (t // CH)
    ca = np.zeros((P, CA["all"][1]), np.float32)
    cr = np.zeros((P, CR["all"][1]), np.float32)
    cb = np.zeros((P, CB["all"][1]), np.float32)

    def put(table, where, name, values):
        a, n = where[name]
        table[:np.shape(values)[0], a:a + n] = np.reshape(values, (np.shape(values)[0], n))

    put(ca, CA, "ident", s == t)
    put(ca, CA, "blockones", same)
    put(ca, CA, "ones", np.ones((P, P)))
    for name, eps in (("ln_eps", 1e-5), ("gn_eps", HD * 1e-5), ("rms_eps", 1e-6)):
        put(ca, CA, name, np.full((P, 1), eps))
    put(cr, CR, "strict", same & (s < t))
    put(cr, CR, "incl", same & (s <= t))
    for k in range(6):
        put(cr, CR, f"level{k}", ((s >> (k + 1)) == (t >> (k + 1))) & ((s >> k) % 2 == 0) & ((t >> k) % 2 == 1))
    put(cr, CR, "reset", np.tile(np.arange(T) % CH != 0, (P, 1)))
    put(cb, CB, "flip", s + t == P - 1)
    u = np.arange(T)[None, :]
    put(cb, CB, "causal", np.where(u - (T - P) > s, NEG, 0.0))
    half = HD // 8
    inv = np.float32(500000.0) ** (-np.arange(0, 2 * half, 2, dtype=np.float32) / np.float32(2 * half))
    angle = np.arange(T, dtype=np.float32)[None, :] * inv[:, None]
    cos, sin, rot = np.ones((HD, T)), np.zeros((HD, T)), np.zeros((P, P))
    for part in range(2):
        cos[part * half:(part + 1) * half] = np.cos(angle)
        sin[part * half:(part + 1) * half] = np.sin(angle)
    put(cb, CB, "cos", np.tile(cos, (2, 1)))
    put(cb, CB, "sin", np.tile(sin, (2, 1)))
    for g in range(2):
        for e in range(half):
            rot[g * HD + e + half, g * HD + e] = -1.0
            rot[g * HD + e, g * HD + e + half] = 1.0
    put(cb, CB, "rot", rot)
    token = np.arange(P)[:, None, None] + P * np.arange(QT)[None, :, None]
    ends = np.arange(P)[None, None, :] * CMP_S + CMP_L - 1
    put(cb, CB, "cmp_mask", np.where((ends <= token) & (np.arange(P) < NCMP), 0.0, NEG))
    put(cb, CB, "cmp_valid", token[:, :, 0] >= CMP_L - 1)
    n = np.maximum(T - 1 - np.arange(BIAS_LEN), 0)
    large = 16 + (np.log(np.maximum(n, 1).astype(np.float32) / np.float32(16)) / np.float32(math.log(128 / 16))
                  * np.float32(16)).astype(np.int32)
    bucket = np.where(n < 16, n, np.minimum(large, 31))
    put(cb, CB, "onehot", bucket[None, :] == np.arange(32)[:, None])
    return ca, cr, cb


def kernel(**inputs):
    import concourse.bacc as bacc
    from concourse.bass_utils import run_bass_kernel_spmd

    a = {k: np.asarray(v) for k, v in inputs.items()}

    def tiles(w):
        k, m = w.shape
        return w.reshape(k // P, P, m // P, P).transpose(2, 1, 0, 3).reshape(m // P, P, (k // P) * P)

    def rows(w):
        return w.reshape(-1, P, w.shape[1]).transpose(1, 0, 2).reshape(P, -1)

    def col(v):
        return v.reshape(-1, P).T

    def pad(w, n):
        return np.concatenate([w, np.zeros((n - w.shape[0],) + w.shape[1:], np.float32)], 0)

    def feature_major(v):
        return np.ascontiguousarray(v.reshape(T, -1, P).transpose(2, 1, 0))

    ca, cr, cb = constant_tables()
    d = {"const_all": ca, "const_recurrence": cr, "const_attention": cb, "x": feature_major(a["x"][0])}
    pair = np.stack([col(a[n].reshape(-1)) for n in ("rwkv_w0", "rwkv_a0", "rwkv_k_k", "rwkv_k_a", "rwkv_r_k", "rwkv_lnx_g",
                                                     "rwkv_lnx_b")], 2).reshape(P, -1)
    order = np.concatenate([np.arange(g * 256 + j * HD, g * 256 + j * HD + HD) for j in range(4) for g in range(2)])

    def twice(v):
        return np.concatenate([v.reshape(-1)] * 2)[:, None]

    vectors = [col(a["c"]), col(a["ada_b"]), col(a["ln_g"]), col(a["ln_b"]), col(a["rwkv_mu"]), pair, col(a["ffn1_norm_2"]),
               col(a["mix_norm_2"]), col(a["ffn2_norm_2"]), col(a["ple_gate_norm_2"]), col(a["ple_norm_2"]),
               col(np.concatenate([a["out_norm_nsa_2"][0][order], a["out_norm_fox_2"][0]])), col(a["dsa_kv_norm"]),
               twice(a["q_norm_nsa_2"]), twice(a["k_norm_cmp_2"]), twice(a["k_norm_slc_2"]), twice(a["k_norm_win_2"]),
               twice(a["q_norm_fox_2"]), twice(a["k_norm_fox_2"]), pad(a["b_forget_2"].reshape(-1, 1), P),
               pad(a["cmp_pos_k_2"][0].T, P), pad(a["cmp_pos_v_2"][0].T, P)]
    d["vectors"] = np.concatenate(vectors, 1)
    d["ada"] = np.concatenate([tiles(a["ada_w"][i]).reshape(16, 3, P, D).transpose(0, 2, 1, 3).reshape(16, P, 3 * D)
                               for i in range(2)])
    d["lora1"] = rows(np.concatenate([a["rwkv_w1"][0], a["rwkv_a1"][0], a["rwkv_g1"][0]], 1))[None]
    second = [tiles(pad(w, P)) for w in (a["rwkv_w2"][0], a["rwkv_a2"][0], a["rwkv_g2"][0][:P], a["rwkv_g2"][0][P:])]
    d["rwkv"] = np.concatenate([tiles(a["rwkv_w_rkv"][0, m]) for m in range(3)] + second, 2)
    d["rwkv_out"] = tiles(a["rwkv_w_out"][0])

    def feed_forward(name, gate, up, down):
        d[f"{name}_in"] = np.concatenate([tiles(gate), tiles(up)], 2)
        d[f"{name}_out"] = tiles(down)

    for i in range(2):
        feed_forward(f"ff{i}", a["ffn_w_in"][i][:, :HID], a["ffn_w_in"][i][:, HID:], a["ffn_w_out"][i])
    for i in (1, 2):
        feed_forward(f"ffn{i}", a[f"ffn{i}_wg_2"][0], a[f"ffn{i}_wu_2"][0], a[f"ffn{i}_wd_2"][0])
    w = a["dsa_w_in"][0]
    cut = [D, D + P, D + P + 512, D + P + 576]
    wq, wc, wqi, wki, wwi = np.split(w, cut, 1)
    d["dsa_first"] = np.concatenate([tiles(wc)[0], tiles(np.concatenate([wki, wki], 1))[0], rows(wwi)], 1)[None]
    d["dsa_index"] = tiles(wqi).reshape(2, 2, P, D).transpose(0, 2, 1, 3).reshape(2, P, 2 * D)
    uk, uv = a["dsa_w_uk"][0], a["dsa_w_uv"][0]
    none = np.zeros((8, HD, P), np.float32)
    d["dsa_heads"] = np.concatenate([tiles(wq), np.concatenate([uk[0::2], none], 1), np.concatenate([none, uk[1::2]], 1),
                                     np.concatenate([uv[0::2], uv[1::2]], 2)], 2)
    d["dsa_out"] = tiles(a["dsa_w_out"][0])
    d["rel_bias"] = a["rel_bias"]
    sizes = (512, P, P, P, P, P, P, 24, 512, 512, 512, 8)
    qa, kc, vc, ks, vs, kw, vw, ga, qf, kf, vf, fl = np.split(a["w_in_2"][0], np.cumsum(sizes)[:-1], 1)
    ga = ga.reshape(D, 2, 4, 3).transpose(0, 2, 1, 3).reshape(D, 24)
    d["mix_0"] = np.concatenate([tiles(kc)[0], tiles(vc)[0], tiles(ks)[0], rows(ga), rows(fl)], 1)[None]
    d["mix_1"] = np.concatenate([tiles(kw)[0], rows(np.concatenate([vs, vw], 1))], 1)[None]
    d["nsa_q"] = tiles(qa[:, order])
    d["fox_qkv"] = np.concatenate([tiles(qf), tiles(kf), tiles(vf)], 2)

    def first_map(w):
        w = w.reshape(4, 8, HD, 256).transpose(0, 2, 1, 3).reshape(4, HD, 8 * 256)
        return np.concatenate([w, w], 1)

    d["cmp_w1"] = np.concatenate([first_map(a["cmp_k_w1_2"][0]), first_map(a["cmp_v_w1_2"][0])])
    d["cmp_w2"] = np.concatenate([rows(a["cmp_k_w2_2"][0]), rows(a["cmp_v_w2_2"][0])], 1)
    w = a["w_out_2"][0]
    d["mix_out"] = tiles(np.concatenate([w[:512][order], w[512:]]))
    d["ple"] = np.concatenate([tiles(a["ple_w_gate_2"][0]), tiles(a["ple_w_proj_2"][0])], 2)
    d["embedding"] = feature_major(a["p_2"][0, 0])
    d = {k: np.ascontiguousarray(v) for k, v in d.items()}

    nc = bacc.Bacc("TRN2", target_bir_lowering=False, num_devices=1)
    d = {"in_" + k: v for k, v in d.items()}
    t = {k[3:]: nc.dram_tensor(k, v.shape, F32, kind="ExternalInput").ap() for k, v in d.items()}
    t["out"] = nc.dram_tensor("out_features", (P, KT, T), F32, kind="ExternalOutput").ap()
    scratch = nc.dram_tensor("bias_scratch", (16, BIAS_LEN), F32, kind="Internal")
    t["bias_scratch"] = scratch.ap()
    t["forget_scratch"] = nc.dram_tensor("forget_scratch", (2, 8, T), F32, kind="Internal").ap()
    build(nc, t)
    got = run_bass_kernel_spmd(nc, [d], core_ids=[0]).results[0]["out_features"]
    return np.ascontiguousarray(got.transpose(2, 1, 0)).reshape(1, T, D)
```

```python
import math
from contextlib import ExitStack

import numpy as np
import concourse.bass as bass
from concourse import mybir

P = 128
T = 512
D = 1024
KT = D // P
HID = 2816
HT = HID // P
CH = 64
NCH = T // CH
HD = 64
QT = T // P
SLOTS = (28 * P, 24 * P)
ALPHA = 4.0 ** 0.25
DECAY = math.exp(-0.5)
NEG = -1e30
TAKEN = -3e38
NCMP = 31
CMP_L = 32
CMP_S = 16
BIAS_LEN = T + P
F32 = mybir.dt.float32
F32R = mybir.dt.float32r
ACT = mybir.ActivationFunctionType
ALU = mybir.AluOpType
AX = mybir.AxisListType


def columns(*parts):
    at, out = 0, {}
    for name, width in parts:
        out[name] = (at, width)
        at += width
    out["all"] = (0, at)
    return out


CA = columns(("ident", P), ("blockones", P), ("ones", P), ("ln_eps", 1), ("gn_eps", 1), ("rms_eps", 1))
CR = columns(("strict", P), ("incl", P), *[(f"level{k}", P) for k in range(6)], ("reset", T))
CB = columns(("flip", P), ("causal", T), ("cos", T), ("sin", T), ("rot", P), ("twice0", P), ("twice1", P), ("cmp_mask", QT * P),
             ("cmp_valid", QT), ("onehot", BIAS_LEN))
VC = columns(("ada_b", 96), ("ln_g", 32), ("ln_b", 32), ("mu", 48), ("pair", 56), ("ffn1", KT),
             ("mix", KT), ("ffn2", KT), ("ple_gate", KT), ("ple", KT), ("out_norm", KT), ("kv_norm", 1),
             ("q_nsa", 1), ("k_cmp", 1), ("k_slc", 1), ("k_win", 1), ("q_fox", 1), ("k_fox", 1),
             ("b_forget", 1), ("pos_k", CMP_L // 2), ("pos_v", CMP_L // 2))


class Steps:

    def __init__(self, sem, names):
        self.sem, self.names, self.next = sem, list(names), 0
        self.index = {n: k + 1 for k, n in enumerate(self.names)}
        assert len(self.index) == len(self.names)

    def enter(self, eng):
        eng.sem_inc(self.sem, len(self.names))

    def step(self, name):
        assert self.names[self.next % len(self.names)] == name, (self.names[self.next % len(self.names)], name)
        self.next += 1
        return self.sem, 1

    def __call__(self, name, turn=0, before=0):
        return self.sem, turn * len(self.names) + (len(self.names) * (1 - before) + self.index[name])


class Units:

    def __init__(self, sem):
        self.sem = sem

    def step(self):
        return self.sem, 1

    def unit(self, turn, s, u):
        return self.sem, turn * 4 + (2 * s + u + 1)

    def __call__(self, s, turn, before=0):
        return self.sem, turn * 4 + (2 * s + 2 - 4 * before)


def build(nc, d):
    ctx = ExitStack()
    with ctx:
        def sem(name):
            return ctx.enter_context(nc.semaphore(name))

        def keep(name, shape, scope=ctx, dtype=F32):
            return scope.enter_context(nc.sbuf_tensor(name, shape, dtype))

        def steps(name, names):
            return Steps(sem(name), names)

        waited = sem("waited")

        def reached(who, name, turn=0):
            return who(name, turn)

        def alone(eng):
            eng.sem_inc(waited, 1)

        ca = keep("const_all", [P, CA["all"][1]])
        vec = keep("vectors", [P, VC["all"][1]])
        mods = keep("modulation", [P, 96])
        x = keep("residual", [P, KT, T])
        slot = [keep(f"weights{s}", [P, SLOTS[s]]) for s in range(2)]
        ps = ctx.enter_context(nc.psum_tensor("psum", [P, 8, T], F32))

        def const(name, table=ca, where=CA):
            a, n = where[name]
            return table[:, a:a + n]

        ident, blockones, ones = const("ident"), const("blockones"), const("ones")

        def vcol(name, k=0):
            a = VC[name][0] + k
            return vec[:, a:a + 1]

        def mod(layer, part, j):
            a = layer * 48 + part * 8 + j
            return mods[:, a:a + 1]
        SH1, SC1, GT1, SH2, SC2, GT2 = range(6)

        filled = [sem(f"slot{s}_filled") for s in range(2)]
        planned = [0, 0]
        last_use = [None, None]

        class Loads:

            def __init__(self, s, n, who, name):
                self.s, self.base, self.who, self.name = s, planned[s], who, name
                self.before = last_use[s]
                planned[s] += n
                last_use[s] = (who, name, n - 1)

                self.arrival = filled[s], 16

            def slot(self, src):
                return slot[self.s][:, 0:src.shape[-1]]

            def vacated(self, k=None):
                return reached(*self.before) if k is None else self.who(self.name, k, 1)

            def arrived(self, k=0):
                return filled[self.s], k * 16 + 16 * (self.base + 1)

        def wtile(s, k, rows=P, width=P, at=0):
            return slot[s][0:rows, at + k * width:at + (k + 1) * width]

        def row(name, k):
            return d[name][bass.ds(k, 1), :, :].rearrange("a p n -> (a p) n")

        def mm(out, lhsT, rhs, start=True, stop=True):
            return nc.tensor.matmul(out, lhsT, rhs, start=start, stop=stop)

        def column(t, k):
            return t[:, bass.ds(k, 1)]

        def tile_of(t, k):
            return t[:, bass.ds(k, 1), :].rearrange("p a n -> p (a n)")

        programs = {"sp": [], "pe": [], "act": [], "dve": [], "pool": []}

        def phase(**engines):
            for name, program in engines.items():
                programs[name].append(program)

        tables_in = sem("tables_in")
        x_in = sem("x_in")
        crd_in = sem("recurrence_constants_in")
        att_in = sem("attention_constants_in")

        ADA_FIRST, ADA_TURN = 2 * KT, (12 - 2) * KT // (D // P)
        ada_at = [(0, 0), (0, D), (1, 0), (1, D)]
        cond = slot[1][:, 2 * D:3 * D]
        inner = keep("modulation_inner", [P, ADA_FIRST])

        def ada_tile(n):
            s, at = ada_at[n]
            return slot[s][:, at:at + D]

        def inner_product(n, j):
            return nc.vector.tensor_tensor_reduce(ada_tile(n), ada_tile(n), cond, scale=1.0, scalar=0.0, op0=ALU.mult,
                                                  op1=ALU.add, accum_out=inner[:, j:j + 1])

        def modulation():
            n = len(ada_at)
            act_done = steps("mod_act", ["cond"])
            dve_done = steps("mod_dve", [f"inner{j}" for j in range(ADA_FIRST)] + ["biased"])
            ready = sem("modulation_ready")
            cond_in = sem("cond_in")
            arrived = [sem(f"ada{j}_in") for j in range(n)]
            last_use[0], last_use[1] = [(dve_done, f"inner{ADA_FIRST - j}", 0) for j in (3, 1)]

            def sp(sp):
                sp.dma_start(cond, d["c_rows"][:, :]).then_inc(cond_in, 16)
                for j in range(ADA_FIRST):
                    if j >= n:
                        sp.wait_ge(*dve_done(f"inner{j - n}"))
                    sp.dma_start(ada_tile(j % n), d["ada"][j, :, :]).then_inc(arrived[j % n], 16)

            def act(act):
                act_done.enter(act)
                act.dma_start(vec[:, :], d["vectors"][:, :]).then_inc(tables_in, 16)
                act.dma_start(ca[:, :], d["const_all"][:, :]).then_inc(tables_in, 16)
                act.dma_start(x[:, :, :], d["x"][:, :, :]).then_inc(x_in, 16)
                act.wait_ge(cond_in, 16)
                nc.scalar.activation(cond, cond, ACT.Silu).then_inc(*act_done.step("cond"))

            def dve(dve):
                dve_done.enter(dve)
                dve.wait_ge(*act_done("cond"))
                for j in range(ADA_FIRST):
                    dve.wait_ge(arrived[j % n], j // n * 16 + 16)
                    inner_product(j % n, j).then_inc(*dve_done.step(f"inner{j}"))
                dve.wait_ge(*dve_done(f"inner{ADA_FIRST - 1}"))
                dve.wait_ge(tables_in, 32)
                a = VC["ada_b"][0]
                nc.vector.tensor_tensor(mods[:, 0:ADA_FIRST], inner[:, :], vec[:, a:a + ADA_FIRST], ALU.add).then_inc(
                    *dve_done.step("biased"))
                dve.wait_ge(*dve_done("biased"))
                nc.vector.tensor_scalar(mods[:, KT:2 * KT], mods[:, KT:2 * KT], 1.0, None, ALU.add).then_inc(ready, 1)

            phase(sp=sp, act=act, dve=dve)
            return ready, 1

        MIX = ["r", "k", "v", "w", "a", "g"]

        def time_mix_inputs(scope, hin, mods_ready):
            h = hin[:, :, 1:T + 1]
            xs = {m: keep(f"mixed_{m}", [P, KT, T], scope) for m in "rkv"}
            lora = {m: keep(f"lora_{m}", [P, T], scope) for m in ("w", "a", "g0", "g1")}
            pe_done = steps("mix_pe", [f"lora{j}" for j in range(KT)])
            act_done = steps("mix_act", [f"hin{j}" for j in range(KT)] + ["w", "a", "g0", "g1"])
            dve_done = steps("mix_dve", ["zero"] + [f"{n}{j}" for j in range(KT) for n in ["xx"] + MIX])
            zeroed = sem("gate_rows_zeroed")
            loads = Loads(0, 1, pe_done, f"lora{KT - 1}")
            with ExitStack() as own:
                xx = keep("token_shift", [P, 2, T], own)
                tmp = keep("mixed_low_rank", [P, 3, 2, T], own)

            def sp(sp):
                sp.wait_ge(*loads.vacated())
                sp.dma_start(loads.slot(row("lora1", 0)), row("lora1", 0)).then_inc(*loads.arrival)

            def act(act):
                act_done.enter(act)
                act.wait_ge(x_in, 16)
                act.wait_ge(*mods_ready)
                for j in range(KT):
                    nc.scalar.activation(h[:, j, :], x[:, j, :], ACT.Identity, bias=mod(0, SH1, j),
                                                    scale=mod(0, SC1, j)).then_inc(*act_done.step(f"hin{j}"))
                act.wait_ge(*pe_done(f"lora{KT - 1}"))
                nc.scalar.activation(lora["w"][0:64, :], ps[0:64, 0, :], ACT.Tanh).then_inc(*act_done.step("w"))
                nc.scalar.activation(lora["a"][0:64, :], ps[0:64, 1, :], ACT.Copy).then_inc(*act_done.step("a"))
                nc.scalar.activation(lora["g0"][:, :], ps[:, 2, :], ACT.Sigmoid).then_inc(*act_done.step("g0"))
                act.wait_ge(zeroed, 1)
                nc.scalar.activation(lora["g1"][0:32, :], ps[0:32, 3, :], ACT.Sigmoid).then_inc(*act_done.step("g1"))

            def pool(pool):
                nc.gpsimd.memset(lora["g1"][:, :], 0.0).then_inc(zeroed, 1)

            def dve(dve):
                dve_done.enter(dve)
                nc.vector.memset(hin[:, :, 0:1], 0.0).then_inc(*dve_done.step("zero"))
                for j in range(KT):
                    dve.wait_ge(*act_done(f"hin{j}"))
                    if j == 0:
                        dve.wait_ge(*dve_done("zero"))
                    if j >= 2:
                        dve.wait_ge(*dve_done(f"g{j - 2}"))
                    nc.vector.tensor_tensor(xx[:, j % 2, :], hin[:, j, 0:T], h[:, j, :], ALU.subtract).then_inc(*dve_done.step(f"xx{j}"))
                    dve.wait_ge(*dve_done(f"xx{j}"))
                    if j >= 2:
                        dve.wait_ge(*pe_done(f"lora{j - 2}"))
                    for n, m in enumerate(MIX):
                        out = xs[m][:, j, :] if m in xs else tmp[:, n - 3, j % 2, :]
                        nc.vector.scalar_tensor_tensor(out, xx[:, j % 2, :], vcol("mu", n * KT + j),
                                                                  h[:, j, :], ALU.mult, ALU.add).then_inc(*dve_done.step(f"{m}{j}"))

            def pe(pe):
                pe_done.enter(pe)
                pe.wait_ge(*loads.arrived())
                for j in range(KT):
                    w = slot[0][:, j * 288:(j + 1) * 288]
                    for n, (bank, a, b) in enumerate([(0, 0, 64), (1, 64, 128), (2, 128, 256), (3, 256, 288)]):
                        m = min(n, 2)
                        if n < 3:
                            pe.wait_ge(*dve_done(f"{MIX[3 + m]}{j}"))
                        last = mm(ps[0:b - a, bank, :], w[:, a:b], tmp[:, m, j % 2, :], j == 0, j == KT - 1)
                    last.then_inc(*pe_done.step(f"lora{j}"))

            phase(sp=sp, act=act, pe=pe, dve=dve, pool=pool)
            return xs, lora, pe_done, act_done, dve_done

        def recurrence(scope, h, xs, lora, mix_pe, mix_act, mix_dve):
            cr = keep("const_recurrence", [P, CR["all"][1]], scope)
            N = D // P
            yout = h
            pv = keep("pair_vectors", [P, 7], scope)
            W0, A0, KK, KA, RK, LG, LB = range(7)
            flat = {n: keep(n, [P, T], scope) for n in
                    ("r", "v", "g", "sig", "a", "kk0", "sq", "nrm", "kk", "k", "rkr", "bv", "cum", "Wt", "Winv", "Wprev")}
            pairs = {n: keep(n + "_pairs", [P, NCH, P], scope) for n in ("a", "b", "k", "r", "Nab", "Nak", "XT")}
            both = x[:, 0:4, :].rearrange("p a (c n) -> p (a c) n", n=2 * P)
            pairs["b_tok"], pairs["Nrb"] = both[:, :, 0:P], both[:, :, P:2 * P]
            for q, n in ((4, "k_tok"), (6, "Nrk")):
                pairs[n] = x[:, q:q + 2, :].rearrange("p a (c n) -> p (a c) n", n=P)
            before_X = keep("before_X", [P, NCH, P + CH], scope)
            after_X = keep("after_X", [P, NCH, P + CH], scope)
            M, R = pairs["Nab"], pairs["r"]
            pairs["X"], pairs["Y"] = pairs["k"], pairs["b"]
            join = [keep(f"join{n}", [P, NCH, P], scope) for n in range(2)]
            v_tok = keep("v_tok", [P, NCH, CH], scope)
            St = keep("state", [P, 2, CH], scope)

            def by_chunk(t, n=CH):
                return t[:, :].rearrange("p (c n) -> p c n", n=n)
            cump, kka, yg, ysum = flat["sq"], flat["nrm"], flat["sig"], flat["kk0"]
            yc, ysq, yn = (by_chunk(flat[n]) for n in ("kk0", "sig", "a"))
            st = keep("group_norm", [P, 4, NCH], scope)
            MEAN, SUM, RSTD, STD = range(4)
            fl = {n: flat[n][:, :] for n in flat}

            in_pe = steps("inputs_pe", ["r", "k", "w", "a", "kk sum", "v", "b tok", "k tok", "bonus sum", "g"])
            in_act = steps("inputs_act", ["r", "k", "kk sq", "sig", "a", "kk norm", "Winv", "Wprev", "v", "Wt", "b tok"])
            in_dve = steps("inputs_dve", ["pv", "kk0", "cum", "cump", "ka", "nrm max", "nrm rec", "kk", "kka", "k", "rkr", "k tok"])
            in_pool = steps("inputs_pool", ["a0", "a1", "b0", "b1", "k0", "k1", "r0", "r1"])
            PE = (["v tok", "Nab", "Nrb", "Nak", "Nrk", "X0"]
                  + [n for k in range(1, 6) for n in ([f"Y{k}", f"X{k}", f"XT{k}"] if k < 5 else [f"Y{k}", f"XT{k}"])]
                  + ["F0", "F1", "MR0", "S0", "y0", "MR1"] + [f"{n}{c}" for c in range(1, NCH) for n in ["S"] * (c < NCH - 1) + ["y"]]
                  + ["y fm"])
            PE.insert(PE.index("Y1") + 1, "a tok")
            PE.insert(PE.index("Y2") + 1, "Nak v")
            AC = ["v tok", "g", "X0", "Y1", "a tok", "Y2", "Nak v", "Y3", "Y4", "Y5", "F0", "F1", "y sq", "y std", "y gn"]
            DV = (["pv", "bonus", "Nab", "Nrb", "Nak", "Nrk"]
                  + [n for k in range(1, 6) for n in ([f"X{k}", f"XT{k}"] if k < 5 else [f"XT{k}"])]
                  + ["M0", "S0", "R0", "S1", "M1", "S2", "R1"] + [f"S{c}" for c in range(3, NCH - 1)]
                  + ["y sum", "y mean", "y cen", "y var", "y rstd", "yn"])
            PO = ["A0", "XT0"] + [f"A{k}" for k in range(1, 6)] + ["y bonus", "y out"]
            pe_done, act_done, dve_done, pool_done = (steps(f"rec_{n}", q) for n, q in
                                          (("pe", PE), ("act", AC), ("dve", DV), ("pool", PO)))
            ada_done = steps("rec_ada", [f"ada{j}" for j in range(ADA_TURN)] + ["ada bias"])
            loads = Loads(0, N, in_pe, "g")
            zeroed = sem("pairs_zeroed")
            ada_in = [sem(f"ada_pair{n}_in") for n in range(2)]
            mods_ready = sem("modulations_ready")
            last_use[1] = (ada_done, f"ada{ADA_TURN - 1}", N - 1)

            def two_banks(b):
                return ps[:, b:b + 2, :].rearrange("p b (c n) -> p (b c) n", n=P)

            def two_a_bank(b, n):
                return ps[:, b:b + 4, 0:2 * n].rearrange("p b (c n) -> p b c n", n=n)

            def by_bank(t):
                return t[:, :, :].rearrange("p (b c) n -> p b c n", c=2)

            def bank(b):
                return ps[:, b, :].rearrange("p (c n) -> p c n", n=CH)

            def spread(mask):
                return mask.unsqueeze(1).to_broadcast([P, NCH, P])

            def cmask(name):
                return const(name, cr, CR)

            def half(t, hh):
                return t[hh * HD:(hh + 1) * HD, :, hh * CH:(hh + 1) * CH]

            def rows(t, hh):
                return by_chunk(t)[hh * HD:(hh + 1) * HD, :, :]

            def sp(sp):
                sp.wait_ge(*loads.vacated())
                sp.dma_start(cr[:, :], d["const_recurrence"][:, :]).then_inc(crd_in, 16)
                sp.dma_start(loads.slot(row("rwkv", 0)), row("rwkv", 0)).then_inc(*loads.arrival)

                def modulations(i):
                    for j in range(ADA_TURN):
                        if j < 2:
                            sp.wait_ge(*ada_done(f"ada{ADA_TURN - 2 + j}", i, 1))
                        else:
                            sp.wait_ge(*ada_done(f"ada{j - 2}", i))
                        sp.dma_start(ada_tile(2 + j % 2), row("ada", i * ADA_TURN + (ADA_FIRST + j))).then_inc(ada_in[j % 2], 16)
                with sp.Fori(0, N - 1) as i:
                    sp.wait_ge(*loads.vacated(i + 1))
                    sp.dma_start(loads.slot(row("rwkv", i + 1)), row("rwkv", i + 1)).then_inc(*loads.arrival)
                    modulations(i)
                modulations(N - 1)

            def pool(pool):
                in_pool.enter(pool)
                pool_done.enter(pool)
                pool.wait_ge(*mix_dve(f"g{KT - 1}"))
                pool.wait_ge(*mix_pe(f"lora{KT - 1}"))
                for n in ("a", "b", "k", "r"):
                    nc.gpsimd.memset(pairs[n][:, :, :], 0.0).then_inc(zeroed, 1)
                pool.wait_ge(crd_in, 16)
                pool.wait_ge(tables_in, 32)
                pool.wait_ge(zeroed, 4)

                def inputs(p):
                    if not isinstance(p, int):
                        pool.wait_ge(*pool_done("A5", p - 1))
                    pool.wait_ge(*in_dve("kk", p))
                    pool.wait_ge(*in_act("Wprev", p))
                    alone(pool)
                    for hh in range(2):
                        nc.gpsimd.tensor_tensor(half(pairs["a"], hh), rows(flat["kk"], hh), rows(flat["Wprev"], hh),
                                                ALU.mult).then_inc(*in_pool.step(f"a{hh}"))
                    pool.wait_ge(*in_dve("kka", p))
                    pool.wait_ge(*pe_done("XT5", p, 1))
                    alone(pool)
                    for hh in range(2):
                        nc.gpsimd.tensor_tensor(half(pairs["b"], hh), rows(kka, hh), rows(flat["Winv"], hh),
                                                ALU.mult).then_inc(*in_pool.step(f"b{hh}"))
                    pool.wait_ge(*in_dve("k", p))
                    alone(pool)
                    for hh in range(2):
                        nc.gpsimd.tensor_tensor(half(pairs["k"], hh), rows(flat["k"], hh), rows(flat["Winv"], hh),
                                                ALU.mult).then_inc(*in_pool.step(f"k{hh}"))
                    pool.wait_ge(*in_act("Wt", p))
                    pool.wait_ge(*in_act("r", p))
                    pool.wait_ge(*pe_done(f"y{NCH - 1}", p, 1))
                    alone(pool)
                    for hh in range(2):
                        nc.gpsimd.tensor_tensor(half(pairs["r"], hh), rows(flat["r"], hh), rows(flat["Wt"], hh),
                                                ALU.mult).then_inc(*in_pool.step(f"r{hh}"))

                def turn(i, more):
                    pool.wait_ge(*dve_done("Nab", i))
                    pool.wait_ge(*in_pool("r1", i))
                    alone(pool)
                    nc.gpsimd.tensor_tensor(join[0][:, :, :], pairs["Nab"][:, :, :], spread(cmask("level0")),
                                                        ALU.mult).then_inc(*pool_done.step("A0"))
                    pool.wait_ge(*pool_done("A0", i))
                    alone(pool)
                    nc.gpsimd.tensor_tensor(pairs["XT"][:, :, :], join[0][:, :, :], spread(ident), ALU.add).then_inc(*pool_done.step("XT0"))
                    pool.wait_ge(*pool_done("XT0", i))
                    alone(pool)
                    for k in range(1, 6):
                        if k >= 3:
                            pool.wait_ge(*pe_done(f"Y{k - 2}", i))
                            alone(pool)
                        nc.gpsimd.tensor_tensor(join[k % 2][:, :, :], pairs["Nab"][:, :, :],
                                                            spread(cmask(f"level{k}")), ALU.mult).then_inc(*pool_done.step(f"A{k}"))
                    if more:
                        inputs(i + 1)
                        pool.wait_ge(*in_pool("r1", i + 1))
                    pool.wait_ge(*act_done("y gn", i))
                    pool.wait_ge(*dve_done("bonus", i))
                    alone(pool)
                    nc.gpsimd.tensor_tensor(ysum[:, :], yg[:, :], fl["bv"], ALU.add).then_inc(*pool_done.step("y bonus"))
                    pool.wait_ge(*pool_done("y bonus", i))
                    alone(pool)
                    nc.gpsimd.tensor_tensor(tile_of(yout, i), ysum[:, :], fl["g"], ALU.mult).then_inc(*pool_done.step("y out"))
                inputs(0)
                with pool.Fori(0, N - 1) as i:
                    turn(i, True)
                turn(N - 1, False)

            def act(act):
                in_act.enter(act)
                act_done.enter(act)
                act.wait_ge(tables_in, 32)
                copy = nc.scalar.activation

                def r_input(p):
                    act.wait_ge(*in_pe("r", p))
                    act.wait_ge(*in_dve("rkr", p, 1))
                    act.wait_ge(*in_pool("r1", p, 1))
                    copy(fl["r"], ps[:, 1, :], ACT.Copy).then_inc(*in_act.step("r"))

                def k_input(p):
                    act.wait_ge(*in_pe("k", p))
                    act.wait_ge(*in_pool("k1", p, 1))
                    copy(fl["k"], ps[:, 0, :], ACT.Copy).then_inc(*in_act.step("k"))
                    act.wait_ge(*in_dve("kk0", p))
                    copy(fl["sq"], fl["kk0"], ACT.Square).then_inc(*in_act.step("kk sq"))

                def decay_and_rate(p):
                    act.wait_ge(*in_pe("w", p))
                    if not isinstance(p, int):
                        act.wait_ge(*pool_done("y bonus", p - 1, 1))
                    copy(fl["sig"], ps[:, 1, :], ACT.Sigmoid, bias=pv[:, W0:W0 + 1]).then_inc(*in_act.step("sig"))
                    act.wait_ge(*in_pe("a", p))
                    copy(fl["a"], ps[:, 0, :], ACT.Sigmoid, bias=pv[:, A0:A0 + 1]).then_inc(*in_act.step("a"))

                def kk_norm(p):
                    act.wait_ge(*in_pe("kk sum", p))
                    act.wait_ge(*in_pool("b1", p, 1))
                    copy(fl["nrm"], ps[:, 1, :], ACT.Sqrt).then_inc(*in_act.step("kk norm"))

                def decays(p):
                    act.wait_ge(*in_dve("cump", p))
                    act.wait_ge(*in_pool("k1", p, 1))
                    copy(fl["Winv"], fl["cum"], ACT.Exp, scale=DECAY).then_inc(*in_act.step("Winv"))
                    copy(fl["Wprev"], cump[:, :], ACT.Exp, scale=-DECAY).then_inc(*in_act.step("Wprev"))

                def v_input(p):
                    act.wait_ge(*in_pe("v", p))
                    copy(fl["v"], ps[:, 4, :], ACT.Copy).then_inc(*in_act.step("v"))

                def chunk_decay(p):
                    act.wait_ge(*dve_done(f"S{NCH - 2}", p, 1))
                    copy(fl["Wt"], fl["cum"], ACT.Exp, scale=-DECAY).then_inc(*in_act.step("Wt"))

                def b_by_tokens(p):
                    act.wait_ge(*in_pe("b tok", p))
                    copy(pairs["b_tok"], two_banks(2), ACT.Copy).then_inc(*in_act.step("b tok"))

                def turn(i, more):
                    act.wait_ge(*pe_done("v tok", i))
                    copy(v_tok[:, :, :], bank(1), ACT.Copy).then_inc(*act_done.step("v tok"))
                    act.wait_ge(*in_pe("g", i))
                    act.wait_ge(*pool_done("y out", i, 1))
                    copy(fl["g"], ps[:, 5, :], ACT.Copy).then_inc(*act_done.step("g"))
                    act.wait_ge(*pe_done("X0", i))
                    copy(pairs["X"][:, :, :], two_banks(6), ACT.Copy).then_inc(*act_done.step("X0"))
                    for k in range(1, 6):
                        act.wait_ge(*pe_done(f"Y{k}", i))
                        copy(pairs["Y"][:, :, :], two_banks(2), ACT.Copy).then_inc(*act_done.step(f"Y{k}"))
                        if k == 1:
                            act.wait_ge(*pe_done("a tok", i))
                            copy(before_X[:, :, 0:P], two_banks(0), ACT.Copy).then_inc(*act_done.step("a tok"))
                        if k == 2:
                            act.wait_ge(*pe_done("Nak v", i))
                            copy(before_X[:, :, P:P + CH], bank(0), ACT.Copy).then_inc(*act_done.step("Nak v"))
                        if more and k == 2:
                            r_input(i + 1)
                        if more and k == 3:
                            k_input(i + 1)
                        if more and k == 4:
                            decay_and_rate(i + 1)
                            kk_norm(i + 1)
                        if more and k == 5:
                            decays(i + 1)
                            v_input(i + 1)
                    for h in range(2):
                        act.wait_ge(*pe_done(f"F{h}", i))
                        b = slice(2 * h, 2 * h + 2)
                        copy(by_bank(after_X)[:, b], two_a_bank(0, P + CH)[:, b], ACT.Copy).then_inc(*act_done.step(f"F{h}"))
                    if more:
                        chunk_decay(i + 1)
                    act.wait_ge(*dve_done("y cen", i))
                    copy(ysq, yc, ACT.Square).then_inc(*act_done.step("y sq"))
                    act.wait_ge(*dve_done("y var", i))
                    copy(st[:, STD, :], st[:, SUM, :], ACT.Sqrt, bias=const("gn_eps"), scale=1.0 / HD).then_inc(*act_done.step("y std"))
                    if more:
                        b_by_tokens(i + 1)
                    act.wait_ge(*pe_done("y fm", i))
                    copy(yg[:, :], ps[:, 4, :], ACT.Identity, bias=pv[:, LB:LB + 1], scale=pv[:, LG:LG + 1]).then_inc(*act_done.step("y gn"))
                for inputs in (r_input, k_input, decay_and_rate, kk_norm, decays, v_input, chunk_decay, b_by_tokens):
                    inputs(0)
                with act.Fori(0, N - 1) as i:
                    turn(i, True)
                turn(N - 1, False)

            def dve(dve):
                in_dve.enter(dve)
                dve_done.enter(dve)
                ada_done.enter(dve)
                dve.wait_ge(crd_in, 16)
                dve.wait_ge(tables_in, 32)
                dve.wait_ge(zeroed, 4)
                tt, ts, stt = nc.vector.tensor_tensor, nc.vector.tensor_scalar, nc.vector.scalar_tensor_tensor

                def modulations(i, tiles):
                    for j in tiles:
                        dve.wait_ge(ada_in[j % 2], i * (ADA_TURN // 2 * 16) + (j // 2 * 16 + 16))
                        if j == 0:
                            dve.wait_ge(*ada_done("ada bias", i, 1))
                        alone(dve)
                        inner_product(2 + j % 2, j).then_inc(*ada_done.step(f"ada{j}"))
                    if j == ADA_TURN - 1:
                        dve.wait_ge(*ada_done(f"ada{ADA_TURN - 1}", i))
                        alone(dve)
                        tt(mods[:, bass.ds(i * ADA_TURN + ADA_FIRST, ADA_TURN)], inner[:, 0:ADA_TURN],
                           vec[:, bass.ds(i * ADA_TURN + (ADA_FIRST + VC["ada_b"][0]), ADA_TURN)], ALU.add).then_inc(
                            *ada_done.step("ada bias"))

                def vectors_input(p):
                    dve.wait_ge(*in_act("a", p, 1))
                    dve.wait_ge(*in_dve("rkr", p, 1))
                    alone(dve)
                    nc.vector.tensor_copy(pv[:, 0:LG], vec[:, bass.ds(p * 7 + VC["pair"][0], LG)]).then_inc(*in_dve.step("pv"))

                def kk_input(p):
                    dve.wait_ge(*in_act("k", p))
                    dve.wait_ge(*in_dve("pv", p))
                    if not isinstance(p, int):
                        dve.wait_ge(*pool_done("y out", p - 1, 1))
                    ts(fl["kk0"], fl["k"], pv[:, KK:KK + 1], None, ALU.mult).then_inc(*in_dve.step("kk0"))

                def decay_input(p):
                    dve.wait_ge(*in_act("sig", p))
                    dve.wait_ge(*in_act("Wt", p, 1))
                    nc.vector.tensor_tensor_scan(fl["cum"], cmask("reset"), fl["sig"], 0.0, ALU.mult, ALU.add).then_inc(*in_dve.step("cum"))
                    dve.wait_ge(*in_dve("cum", p))
                    dve.wait_ge(*in_pe("kk sum", p))
                    tt(cump[:, :], fl["cum"], fl["sig"], ALU.subtract).then_inc(*in_dve.step("cump"))
                    dve.wait_ge(*in_act("a", p))
                    dve.wait_ge(*in_pe("bonus sum", p, 1))
                    ts(fl["rkr"], fl["a"], 1.0, pv[:, KA:KA + 1], ALU.subtract, ALU.mult).then_inc(*in_dve.step("ka"))

                def norm_input(p):
                    dve.wait_ge(*in_act("kk norm", p))
                    ts(fl["nrm"], fl["nrm"], 1e-12, None, ALU.max).then_inc(*in_dve.step("nrm max"))
                    dve.wait_ge(*in_dve("nrm max", p))
                    nc.vector.reciprocal(fl["nrm"], fl["nrm"]).then_inc(*in_dve.step("nrm rec"))

                def kk_and_rate_input(p):
                    dve.wait_ge(*in_dve("nrm rec", p))
                    dve.wait_ge(*in_pool("a1", p, 1))
                    stt(fl["kk"], fl["kk0"], -1.0, fl["nrm"], ALU.mult, ALU.mult).then_inc(*in_dve.step("kk"))
                    dve.wait_ge(*in_dve("kk", p))
                    stt(kka[:, :], fl["kk"], -1.0, fl["a"], ALU.mult, ALU.mult).then_inc(*in_dve.step("kka"))

                def key_input(p):
                    dve.wait_ge(*in_dve("ka", p))
                    stt(fl["k"], fl["rkr"], 1.0, fl["k"], ALU.add, ALU.mult).then_inc(*in_dve.step("k"))

                def k_by_tokens(p):
                    dve.wait_ge(*in_pe("k tok", p))
                    nc.vector.tensor_copy(pairs["k_tok"], two_banks(6)).then_inc(*in_dve.step("k tok"))

                def bonus_input(p):
                    dve.wait_ge(*in_dve("k", p))
                    dve.wait_ge(*in_act("r", p))
                    stt(fl["rkr"], fl["r"], pv[:, RK:RK + 1], fl["k"], ALU.mult, ALU.mult).then_inc(*in_dve.step("rkr"))

                def turn(i, more):
                    dve.wait_ge(*act_done("y gn", i, 1))
                    alone(dve)
                    nc.vector.tensor_copy(pv[:, LG:LB + 1], vec[:, bass.ds(i * 7 + (VC["pair"][0] + LG), 2)]).then_inc(*dve_done.step("pv"))
                    if more:
                        vectors_input(i + 1)
                    dve.wait_ge(*in_pe("bonus sum", i))
                    dve.wait_ge(*in_act("v", i))
                    dve.wait_ge(*pool_done("y bonus", i, 1))
                    tt(fl["bv"], ps[:, 0, :], fl["v"], ALU.mult).then_inc(*dve_done.step("bonus"))
                    for n, b, mask in (("Nab", 6, "strict"), ("Nrb", 2, "incl"), ("Nak", 4, "strict"), ("Nrk", 0, "incl")):
                        dve.wait_ge(*pe_done(n, i))
                        tt(pairs[n][:, :, :], two_banks(b), spread(cmask(mask)), ALU.mult).then_inc(*dve_done.step(n))
                    for k in range(1, 6):
                        if k < 5:
                            dve.wait_ge(*pe_done(f"X{k}", i))
                            if k == 1:
                                dve.wait_ge(*act_done("X0", i))
                            tt(pairs["X"][:, :, :], pairs["X"][:, :, :], two_banks(4), ALU.add).then_inc(*dve_done.step(f"X{k}"))
                        dve.wait_ge(*pe_done(f"XT{k}", i))
                        tt(pairs["XT"][:, :, :], pairs["XT"][:, :, :], two_banks(6), ALU.add).then_inc(*dve_done.step(f"XT{k}"))
                        if k == 1:
                            modulations(i, range(0, 2))
                        if k == 2:
                            modulations(i, range(2, 4))
                        if k == 3:
                            if more:
                                kk_input(i + 1)
                            modulations(i, range(4, 6))
                        if k == 4:
                            modulations(i, range(6, 8))
                            if more:
                                decay_input(i + 1)
                    if more:
                        norm_input(i + 1)

                    def maps(h, which):
                        c = slice(max(1, 4 * h), 4 * h + 4)
                        made = ps[:, 4:8, :].rearrange("p b (c n) -> p (b c) n", n=2 * P)[:, c, :]
                        dve.wait_ge(*pe_done(f"MR{h}", i))
                        if which == "M":
                            tt(M[:, c, :], made[:, :, 0:P], ident.unsqueeze(1).to_broadcast([P, c.stop - c.start, P]),
                               ALU.add).then_inc(*dve_done.step(f"M{h}"))
                        else:
                            tt(R[:, c, :], made[:, :, P:2 * P], R[:, c, :], ALU.add).then_inc(*dve_done.step(f"R{h}"))

                    def state(c):
                        dve.wait_ge(*pe_done(f"S{c}", i))
                        end = c * CH + CH - 1
                        ts(St[:, c % 2, :], bank(2 * (c % 2))[:, c, :], flat["Wt"][:, end:end + 1], None, ALU.mult).then_inc(
                            *dve_done.step(f"S{c}"))
                    maps(0, "M")
                    state(0)
                    maps(0, "R")
                    if more:
                        kk_and_rate_input(i + 1)
                    state(1)
                    maps(1, "M")
                    state(2)
                    maps(1, "R")
                    for c in range(3, NCH - 1):
                        state(c)
                        if more and c == 3:
                            key_input(i + 1)
                        if more and c == 4:
                            bonus_input(i + 1)
                    dve.wait_ge(*pe_done(f"y{NCH - 1}", i))
                    yps = bank(1)
                    nc.vector.tensor_reduce(st[:, MEAN, :], yps, AX.X, ALU.add).then_inc(*dve_done.step("y sum"))
                    dve.wait_ge(*dve_done("y sum", i))
                    ts(st[:, MEAN, :], st[:, MEAN, :], 1.0 / HD, None, ALU.mult).then_inc(*dve_done.step("y mean"))
                    dve.wait_ge(*dve_done("y mean", i))
                    tt(yc, yps, st[:, MEAN, :].unsqueeze(2).to_broadcast([P, NCH, CH]), ALU.subtract).then_inc(*dve_done.step("y cen"))
                    dve.wait_ge(*act_done("y sq", i))
                    nc.vector.tensor_reduce(st[:, SUM, :], ysq, AX.X, ALU.add).then_inc(*dve_done.step("y var"))
                    dve.wait_ge(*act_done("y std", i))
                    nc.vector.reciprocal(st[:, RSTD, :], st[:, STD, :]).then_inc(*dve_done.step("y rstd"))
                    dve.wait_ge(*dve_done("y rstd", i))
                    tt(yn, yc, st[:, RSTD, :].unsqueeze(2).to_broadcast([P, NCH, CH]), ALU.mult).then_inc(*dve_done.step("yn"))
                    if more:
                        k_by_tokens(i + 1)
                    modulations(i, range(8, ADA_TURN))
                for inputs in (vectors_input, kk_input, decay_input, norm_input, kk_and_rate_input, key_input, bonus_input, k_by_tokens):
                    inputs(0)
                with dve.Fori(0, N - 1) as i:
                    turn(i, True)
                turn(N - 1, False)
                dve.wait_ge(*ada_done("ada bias", N - 1))
                for a, b in ((2, 3), (4, 6), (7, 9), (10, 12)):
                    ts(mods[:, a * KT:b * KT], mods[:, a * KT:b * KT], 1.0, None, ALU.add).then_inc(mods_ready, 1)
                dve.wait_ge(mods_ready, 4)

            def pe(pe):
                in_pe.enter(pe)
                pe_done.enter(pe)
                pe.wait_ge(*mix_act("g1"))
                pe.wait_ge(*mix_dve(f"g{KT - 1}"))

                def projection(m, b, tiles):
                    at = "rkv".index(m) * KT
                    for k in tiles:
                        last = mm(ps[:, b, :], wtile(0, at + k), xs[m][:, k, :], k == 0, k == KT - 1)
                    if k == KT - 1:
                        last.then_inc(*in_pe.step(m))

                def decay_and_rate(p):
                    pe.wait_ge(*in_act("r", p))
                    mm(ps[:, 1, :], wtile(0, 24, HD), lora["w"][0:HD, :]).then_inc(*in_pe.step("w"))
                    pe.wait_ge(*in_act("k", p))
                    mm(ps[:, 0, :], wtile(0, 25, HD), lora["a"][0:HD, :]).then_inc(*in_pe.step("a"))

                def kk_sum(p):
                    pe.wait_ge(*in_act("kk sq", p))
                    pe.wait_ge(*in_act("sig", p))
                    mm(ps[:, 1, :], blockones, fl["sq"]).then_inc(*in_pe.step("kk sum"))

                def by_tokens(p):
                    pe.wait_ge(*in_pool("b1", p))
                    pe.wait_ge(*dve_done(f"S{NCH - 2}", p, 1))
                    for c in range(NCH):
                        last = nc.tensor.transpose(two_banks(2)[:, c, :], pairs["b"][:, c, :], ident)
                    last.then_inc(*in_pe.step("b tok"))
                    pe.wait_ge(*in_pool("k1", p))
                    for c in range(NCH):
                        last = nc.tensor.transpose(two_banks(6)[:, c, :], pairs["k"][:, c, :], ident)
                    last.then_inc(*in_pe.step("k tok"))
                    pe.wait_ge(*in_dve("rkr", p))
                    mm(ps[:, 0, :], blockones, fl["rkr"]).then_inc(*in_pe.step("bonus sum"))
                    mm(ps[:, 5, :], wtile(0, 26), lora["g0"][:, :], True, False)
                    mm(ps[:, 5, :], wtile(0, 27), lora["g1"][:, :], False, True).then_inc(*in_pe.step("g"))

                def turn(i, more):
                    pe.wait_ge(*in_act("v", i))
                    pe.wait_ge(*dve_done("yn", i, 1))
                    for c in range(NCH):
                        for hh in range(2):
                            last = mm(bank(1)[hh * CH:(hh + 1) * CH, c, :], flat["v"][:, c * CH:(c + 1) * CH],
                                      ident[:, hh * HD:(hh + 1) * HD])
                    last.then_inc(*pe_done.step("v tok"))
                    for n, b, left, right in (("Nab", 6, "b", "a"), ("Nrb", 2, "b", "r"), ("Nak", 4, "k", "a"), ("Nrk", 0, "k", "r")):
                        if n == "Nab":
                            pe.wait_ge(*in_dve("k tok", i))
                        elif n == "Nrb":
                            pe.wait_ge(*in_pool("r1", i))
                            pe.wait_ge(*in_act("b tok", i))
                        elif n == "Nak":
                            pe.wait_ge(*act_done("y gn", i, 1))
                            pe.wait_ge(*act_done("g", i))
                        elif n == "Nrk":
                            pe.wait_ge(*act_done("v tok", i))
                            pe.wait_ge(*dve_done("bonus", i))
                        for c in range(NCH):
                            last = mm(two_banks(b)[:, c, :], pairs[left][:, c, :], pairs[right][:, c, :])
                        last.then_inc(*pe_done.step(n))
                    pe.wait_ge(*pool_done("XT0", i))
                    for c in range(NCH):
                        last = nc.tensor.transpose(two_banks(6)[:, c, :], pairs["XT"][:, c, :], ident)
                    last.then_inc(*pe_done.step("X0"))
                    for k in range(1, 6):
                        pe.wait_ge(*pool_done(f"A{k}", i))
                        if k == 1:
                            pe.wait_ge(*act_done("X0", i))
                            pe.wait_ge(*dve_done("Nrk", i))
                        else:
                            pe.wait_ge(*dve_done(f"XT{k - 1}", i))
                        for c in range(NCH):
                            last = mm(two_banks(2)[:, c, :], join[k % 2][:, c, :], pairs["X"][:, c, :])
                        last.then_inc(*pe_done.step(f"Y{k}"))
                        if k == 1:
                            for c in range(NCH):
                                last = nc.tensor.transpose(two_banks(0)[:, c, :], pairs["a"][:, c, :], ident)
                            last.then_inc(*pe_done.step("a tok"))
                        if k == 2:
                            pe.wait_ge(*act_done("a tok", i))
                            for c in range(NCH):
                                last = mm(bank(0)[:, c, :], pairs["Nak"][:, c, :], v_tok[:, c, :])
                            last.then_inc(*pe_done.step("Nak v"))
                        if more and k == 3:
                            pe.wait_ge(*act_done("Nak v", i))
                            projection("k", 0, range(0, 4))
                        if more and k == 4:
                            decay_and_rate(i + 1)
                        if more and k == 5:
                            projection("v", 4, range(0, 4))
                        pe.wait_ge(*act_done(f"Y{k}", i))
                        for out, b, left, right in (("X", 4, "XT", "Y"), ("XT", 6, "Y", "XT")):
                            if k == 5 and out == "X":
                                continue
                            for c in range(NCH):
                                last = mm(two_banks(b)[:, c, :], pairs[left][:, c, :], pairs[right][:, c, :])
                            last.then_inc(*pe_done.step(f"{out}{k}"))
                        if more and k == 1:
                            pe.wait_ge(*act_done("a tok", i))
                            pe.wait_ge(*loads.arrived(i + 1))
                            projection("r", 1, range(0, 4))
                        if more and k == 2:
                            projection("r", 1, range(4, KT))
                        if more and k == 3:
                            projection("k", 0, range(4, KT))
                        if more and k == 4:
                            kk_sum(i + 1)
                        if more and k == 5:
                            projection("v", 4, range(4, KT))
                    pe.wait_ge(*dve_done("XT5", i))
                    pe.wait_ge(*act_done("Nak v", i))
                    if more:
                        pe.wait_ge(*in_act("kk norm", i + 1))
                    for c in range(NCH):
                        last = mm(two_a_bank(0, P + CH)[:, c // 2, c % 2, :], pairs["XT"][:, c, :], before_X[:, c, :])
                        if c % 4 == 3:
                            last.then_inc(*pe_done.step(f"F{c // 4}"))

                    def maps(h):
                        for c in range(max(1, 4 * h), 4 * h + 4):
                            last = mm(two_a_bank(4, 2 * P)[:, c // 2, c % 2, :], after_X[:, c, 0:P], both[:, c, :])
                        last.then_inc(*pe_done.step(f"MR{h}"))

                    def chunk(c):
                        S0, Sp, yp, q = St[:, (c - 1) % 2, :], bank(2 * (c % 2))[:, c, :], bank(1)[:, c, :], after_X[:, c, P:P + CH]
                        if c < NCH - 1:
                            mm(Sp, pairs["b_tok"][:, c, :], q, True, False)
                            Send = mm(Sp, pairs["k_tok"][:, c, :], v_tok[:, c, :], False, c == 0)
                        mm(yp, pairs["Nrb"][:, c, :], q, True, False)
                        yend = mm(yp, pairs["Nrk"][:, c, :], v_tok[:, c, :], False, c == 0)
                        if c:
                            pe.wait_ge(*dve_done(f"S{c - 1}", i))
                            if c == 4:
                                pe.wait_ge(*dve_done("M1", i))
                            if c < NCH - 1:
                                Send = mm(Sp, M[:, c, :], S0, False, True)
                            if c in (1, 4):
                                pe.wait_ge(*dve_done(f"R{c // 4}", i))
                            yend = mm(yp, R[:, c, :], S0, False, True)
                        if c < NCH - 1:
                            Send.then_inc(*pe_done.step(f"S{c}"))
                        yend.then_inc(*pe_done.step(f"y{c}"))
                    pe.wait_ge(*act_done("F0", i))
                    maps(0)
                    chunk(0)
                    pe.wait_ge(*act_done("F1", i))
                    maps(1)
                    for c in range(1, NCH):
                        chunk(c)
                    if more:
                        by_tokens(i + 1)
                    pe.wait_ge(*dve_done("yn", i))
                    for c in range(NCH):
                        for hh in range(2):
                            last = mm(ps[hh * HD:(hh + 1) * HD, 4, c * CH:(c + 1) * CH], yn[:, c, :],
                                      ident[:, hh * CH:(hh + 1) * CH])
                    last.then_inc(*pe_done.step("y fm"))
                pe.wait_ge(*loads.arrived(0))
                projection("r", 1, range(KT))
                projection("k", 0, range(KT))
                decay_and_rate(0)
                kk_sum(0)
                projection("v", 4, range(KT))
                by_tokens(0)
                with pe.Fori(0, N - 1) as i:
                    turn(i, True)
                turn(N - 1, False)

            phase(sp=sp, act=act, pe=pe, dve=dve, pool=pool)
            return yout, pool_done, "y out", N - 1

        def project(name, stream, sources, ready, factor, x_ready=()):
            n = KT // 2
            pe_done = steps(f"{name}_pe", ["product0", "product1"])
            dve_done = steps(f"{name}_dve", ["sum0", "sum1"])
            loads = [Loads(s, n, pe_done, f"product{s}") for s in range(2)]

            def sp(sp):
                for s in range(2):
                    sp.wait_ge(*loads[s].vacated())
                with sp.Fori(0, n) as i:
                    for s in range(2):
                        sp.wait_ge(*loads[s].vacated(i))
                        sp.dma_start(loads[s].slot(row(stream, i * 2 + s)), row(stream, i * 2 + s)).then_inc(*loads[s].arrival)

            def pe(pe):
                pe_done.enter(pe)
                for r in ready:
                    pe.wait_ge(*reached(*r))
                with pe.Fori(0, n) as i:
                    for s in range(2):
                        pe.wait_ge(*loads[s].arrived(i))
                        pe.wait_ge(*dve_done(f"sum{s}", i, 1))
                        for k, src in enumerate(sources):
                            last = mm(ps[:, s, :], wtile(s, k), src, k == 0, k == len(sources) - 1)
                        last.then_inc(*pe_done.step(f"product{s}"))

            def dve(dve):
                dve_done.enter(dve)
                for r in x_ready:
                    dve.wait_ge(*reached(*r))
                with dve.Fori(0, n) as i:
                    for s in range(2):
                        dve.wait_ge(*pe_done(f"product{s}", i))
                        f = factor if isinstance(factor, float) else mods[:, bass.ds(i * 2 + (s + factor[0] * 48 + factor[1] * 8), 1)]
                        nc.vector.scalar_tensor_tensor(tile_of(x, i * 2 + s), ps[:, s, :], f,
                                                                  tile_of(x, i * 2 + s), ALU.mult, ALU.add).then_inc(*dve_done.step(f"sum{s}"))

            phase(sp=sp, pe=pe, dve=dve)
            return [(dve_done, f"sum{j % 2}", j // 2) for j in range(KT)]

        def residual_again(ready):
            again = sem("residual_again")
            act_done = steps("again_act", ["scaled"])

            def sp(sp):
                for r in ready:
                    sp.wait_ge(*reached(*r))
                sp.dma_start(x[:, :, :], d["x"][:, :, :]).then_inc(again, 16)

            def act(act):
                act_done.enter(act)
                act.wait_ge(again, 16)
                nc.scalar.activation(x[:, :, :], x[:, :, :], ACT.Copy, scale=ALPHA).then_inc(*act_done.step("scaled"))

            phase(sp=sp, act=act)
            return act_done, "scaled"

        def layer_norm(name, scope, layer, half_layer, ready, following):
            parts = following and isinstance(following[3], tuple)
            full = keep(f"{name}_in", [P, 2, T], scope) if parts else None
            mean, std, rstd = (keep(f"{name}_{n}", [P, T], scope) for n in ("mean", "std", "rstd"))
            sq = keep(f"{name}_sq", [P, 2, T], scope)
            col = (layer * 2 + half_layer) * KT
            pe_done = steps(f"{name}_pe", ["sum"] + [f"sq{j}" for j in range(KT)])
            act_done = steps(f"{name}_act", ["mean"] + [f"sq{j}" for j in range(KT)] + ["std"]
                          + [f"{n}{j}" for j in range(KT) for n in (["shift", "in", "hi"] if parts else ["shift", "in"] if following else ["shift"])])
            dve_done = steps(f"{name}_dve", [f"centred{j}" for j in range(KT)] + ["rstd"] + [f"scaled{j}" for j in range(KT)]
                             + [f"lo{j}" for j in range(KT) if parts])
            pool_done = steps(f"{name}_pool", [f"alpha{j}" for j in range(KT)])

            def pe(pe):
                pe_done.enter(pe)
                for j in range(KT):
                    pe.wait_ge(*reached(*ready[j]))
                    last = mm(ps[:, 4, :], ones, x[:, j, :], j == 0, j == KT - 1)
                last.then_inc(*pe_done.step("sum"))
                for j in range(KT):
                    pe.wait_ge(*act_done(f"sq{j}"))
                    mm(ps[:, 5, :], ones, sq[:, j % 2, :], j == 0, j == KT - 1).then_inc(*pe_done.step(f"sq{j}"))

            def act(act):
                act_done.enter(act)
                act.wait_ge(*pe_done("sum"))
                nc.scalar.activation(mean[:, :], ps[:, 4, :], ACT.Copy, scale=1.0 / D).then_inc(*act_done.step("mean"))
                for j in range(KT):
                    act.wait_ge(*dve_done(f"centred{j}"))
                    if j >= 2:
                        act.wait_ge(*pe_done(f"sq{j - 2}"))
                    nc.scalar.activation(sq[:, j % 2, :], x[:, j, :], ACT.Square).then_inc(*act_done.step(f"sq{j}"))
                act.wait_ge(*pe_done(f"sq{KT - 1}"))
                nc.scalar.activation(std[:, :], ps[:, 5, :], ACT.Sqrt, bias=const("ln_eps"), scale=1.0 / D).then_inc(*act_done.step("std"))
                for j in range(KT):
                    act.wait_ge(*dve_done(f"scaled{j}"))
                    nc.scalar.activation(x[:, j, :], x[:, j, :], ACT.Identity, bias=vcol("ln_b", col + j)).then_inc(*act_done.step(f"shift{j}"))
                    if following:
                        l, sh, sc, to = following
                        act.wait_ge(*act_done(f"shift{j}"))
                        if parts and j >= 2:
                            act.wait_ge(*dve_done(f"lo{j - 2}"))
                        nc.scalar.activation(full[:, j % 2, :] if parts else to[:, j, :], x[:, j, :], ACT.Identity,
                                             bias=mod(l, sh, j), scale=mod(l, sc, j)).then_inc(*act_done.step(f"in{j}"))
                        if parts:
                            act.wait_ge(*act_done(f"in{j}"))
                            nc.scalar.activation(to[0][:, j, :], full[:, j % 2, :], ACT.Copy).then_inc(*act_done.step(f"hi{j}"))

            def dve(dve):
                dve_done.enter(dve)
                dve.wait_ge(*act_done("mean"))
                for j in range(KT):
                    nc.vector.tensor_tensor(x[:, j, :], x[:, j, :], mean[:, :], ALU.subtract).then_inc(*dve_done.step(f"centred{j}"))
                dve.wait_ge(*act_done("std"))
                nc.vector.reciprocal(rstd[:, :], std[:, :]).then_inc(*dve_done.step("rstd"))
                dve.wait_ge(*dve_done("rstd"))
                for j in range(KT):
                    nc.vector.scalar_tensor_tensor(x[:, j, :], x[:, j, :], vcol("ln_g", col + j), rstd[:, :],
                                                              ALU.mult, ALU.mult).then_inc(*dve_done.step(f"scaled{j}"))
                if parts:
                    for j in range(KT):
                        dve.wait_ge(*act_done(f"hi{j}"))
                        hi = following[3][0][:, j, :].bitcast(F32)
                        nc.vector.tensor_tensor(following[3][1][:, j, :], full[:, j % 2, :], hi, ALU.subtract).then_inc(
                            *dve_done.step(f"lo{j}"))

            def pool(pool):
                pool_done.enter(pool)
                for j in range(KT):
                    pool.wait_ge(*act_done(f"in{j}"))
                    nc.gpsimd.tensor_scalar(x[:, j, :], x[:, j, :], ALPHA, None, ALU.mult).then_inc(*pool_done.step(f"alpha{j}"))

            if following:
                phase(pe=pe, act=act, dve=dve, pool=pool)
                inputs = [(dve_done, f"lo{j}") if parts else (act_done, f"in{j}") for j in range(KT)]
                return inputs, [(pool_done, f"alpha{KT - 1}")]
            phase(pe=pe, act=act, dve=dve)
            return [(act_done, f"shift{j}") for j in range(KT)], []

        def rms_norm(name, scope, source, ready, gains, out):
            n = len(source)
            parts = isinstance(out, tuple)
            full = keep(f"{name}_in", [P, 2, T], scope) if parts else None
            std, rstd = (keep(f"{name}_{m}", [P, T], scope) for m in ("std", "rstd"))
            sq = keep(f"{name}_sq", [P, 2, T], scope)
            pe_done = steps(f"{name}_pe", [f"sq{j}" for j in range(n)])
            act_done = steps(f"{name}_act", [f"sq{j}" for j in range(n)] + ["std"] + [f"hi{j}" for j in range(n) if parts])
            dve_done = steps(f"{name}_dve", ["rstd"] + [m for j in range(n + 1) for m in
                                                        [f"out{j}"] * (j < n) + [f"lo{j - 1}"] * (parts and j >= 1)])

            def act(act):
                act_done.enter(act)
                act.wait_ge(*reached(*ready[n - 1]))
                for j in range(n):
                    if j >= 2:
                        act.wait_ge(*pe_done(f"sq{j - 2}"))
                    nc.scalar.activation(sq[:, j % 2, :], source[j], ACT.Square).then_inc(*act_done.step(f"sq{j}"))
                act.wait_ge(*pe_done(f"sq{n - 1}"))
                nc.scalar.activation(std[:, :], ps[:, 5, :], ACT.Sqrt, bias=const("rms_eps"), scale=1.0 / (n * P)).then_inc(*act_done.step("std"))

                if parts:
                    for j in range(n):
                        act.wait_ge(*dve_done(f"out{j}"))
                        nc.scalar.activation(out[0][j], full[:, j % 2, :], ACT.Copy).then_inc(*act_done.step(f"hi{j}"))

            def pe(pe):
                pe_done.enter(pe)
                for j in range(n):
                    pe.wait_ge(*act_done(f"sq{j}"))
                    mm(ps[:, 5, :], ones, sq[:, j % 2, :], j == 0, j == n - 1).then_inc(*pe_done.step(f"sq{j}"))

            def dve(dve):
                dve_done.enter(dve)
                dve.wait_ge(*act_done("std"))
                nc.vector.reciprocal(rstd[:, :], std[:, :]).then_inc(*dve_done.step("rstd"))
                dve.wait_ge(*dve_done("rstd"))
                for j in range(n + 1):
                    if j < n:
                        nc.vector.scalar_tensor_tensor(full[:, j % 2, :] if parts else out[j], source[j], gains[j], rstd[:, :],
                                                       ALU.mult, ALU.mult).then_inc(*dve_done.step(f"out{j}"))
                    if parts and j >= 1:
                        dve.wait_ge(*act_done(f"hi{j - 1}"))
                        nc.vector.tensor_tensor(out[1][j - 1], full[:, (j - 1) % 2, :], out[0][j - 1].bitcast(F32),
                                                ALU.subtract).then_inc(*dve_done.step(f"lo{j - 1}"))
                        dve.wait_ge(*dve_done(f"lo{j - 1}"))

            phase(pe=pe, act=act, dve=dve)
            return [(dve_done, f"{'lo' if parts else 'out'}{j}") for j in range(n)]

        class Split:
            def __init__(self, name, scope):
                self.hi = [keep(f"{name}_hi{u}", [P, HT // 2 * P], scope, F32R) for u in range(2)]
                self.lo = [keep(f"{name}_lo{u}", [P, HT // 2 * P], scope, F32R) for u in range(2)]

        def split_hi(sp_, s, u, width):
            return nc.scalar.activation(sp_.hi[u][:, 0:width], slot[s][:, u * width:(u + 1) * width], ACT.Copy)

        def split_lo(sp_, s, u, width):
            return nc.vector.tensor_tensor(sp_.lo[u][:, 0:width], slot[s][:, u * width:(u + 1) * width],
                                           sp_.hi[u][:, 0:width].bitcast(F32), ALU.subtract)

        def three_passes(out, sp_, u, k, source, first, final):
            hi, lo = sp_.hi[u][:, k * P:(k + 1) * P], sp_.lo[u][:, k * P:(k + 1) * P]
            mm(out, hi, source[0], first, False)
            mm(out, hi, source[1], False, False)
            return mm(out, lo, source[0], False, final)

        def gated(name, split, scope, source, hid, ready):
            n = HT // 2
            width = KT * P
            sg = keep(f"{name}_silu", [P, 2, T], scope)
            full = keep(f"{name}_full", [P, 2, T], scope)
            pe_done = steps(f"{name}_pe", ["gate0", "up0", "gate1", "up1"])
            act_done = steps(f"{name}_act", ["silu0", "hi0", "silu1", "hi1"])
            dve_done = steps(f"{name}_dve", ["hidden0", "lo0", "hidden1", "lo1"])
            hi_split, lo_split = Units(sem(f"{name}_hi_split")), Units(sem(f"{name}_lo_split"))
            loads = [Loads(s, n, lo_split, s) for s in range(2)]
            PART = ("gate", "up")

            def sp(sp):
                for s in range(2):
                    sp.wait_ge(*loads[s].vacated())
                    sp.dma_start(loads[s].slot(row(f"{name}_in", s)), row(f"{name}_in", s)).then_inc(*loads[s].arrival)
                with sp.Fori(1, n) as i:
                    for s in range(2):
                        sp.wait_ge(*loads[s].vacated(i))
                        sp.dma_start(loads[s].slot(row(f"{name}_in", i * 2 + s)), row(f"{name}_in", i * 2 + s)).then_inc(*loads[s].arrival)

            def pe(pe):
                pe_done.enter(pe)
                for r in ready:
                    pe.wait_ge(*reached(*r))
                with pe.Fori(0, n) as i:
                    for s in range(2):
                        pe.wait_ge(*dve_done(f"hidden{s}", i, 1))
                        for u, part in enumerate(PART):
                            pe.wait_ge(*lo_split.unit(i, s, u))
                            for k in range(KT):
                                last = three_passes(ps[:, 2 * s + u, :], split, u, k, (source[0][:, k, :], source[1][:, k, :]),
                                                    k == 0, k == KT - 1)
                            last.then_inc(*pe_done.step(f"{part}{s}"))

            def act(act):
                act_done.enter(act)

                def hidden(i, s):
                    act.wait_ge(*dve_done(f"hidden{s}", i))
                    act.wait_ge(*pe_done(f"up{s}", i))
                    alone(act)
                    nc.scalar.activation(tile_of(hid[0], i * 2 + s), full[:, s, :], ACT.Copy).then_inc(*act_done.step(f"hi{s}"))

                def turn(i, more):
                    for s in range(2):
                        for u, part in enumerate(PART):
                            if s == 0 or more:
                                if u == 0:
                                    act.wait_ge(*loads[1 - s].arrived(i + s))
                                act.wait_ge(*pe_done(f"{part}{s}", i))
                                split_hi(split, 1 - s, u, width).then_inc(*hi_split.step())
                            if u == 0:
                                act.wait_ge(*pe_done(f"gate{s}", i))
                                act.wait_ge(*dve_done(f"hidden{s}", i, 1))
                                nc.scalar.activation(sg[:, s, :], ps[:, 2 * s, :], ACT.Silu).then_inc(*act_done.step(f"silu{s}"))
                            else:
                                hidden(i, s)
                for r in ready:
                    act.wait_ge(*reached(*r))
                act.wait_ge(*loads[0].arrived(0))
                for u in range(2):
                    split_hi(split, 0, u, width).then_inc(*hi_split.step())
                with act.Fori(0, n - 1) as i:
                    turn(i, True)
                turn(n - 1, False)

            def dve(dve):
                dve_done.enter(dve)

                def turn(i, more):
                    for s in range(2):
                        for u in range(2):
                            if s == 0 or more:
                                dve.wait_ge(*hi_split.unit(i + s, 1 - s, u))
                                split_lo(split, 1 - s, u, width).then_inc(*lo_split.step())
                            if u == 0:
                                dve.wait_ge(*act_done(f"silu{s}", i))
                                dve.wait_ge(*pe_done(f"up{s}", i))
                                dve.wait_ge(*act_done(f"hi{s}", i, 1))
                                dve.wait_ge(*dve_done(f"lo{s}", i, 1))
                                nc.vector.tensor_tensor(full[:, s, :], sg[:, s, :], ps[:, 2 * s + 1, :], ALU.mult).then_inc(
                                    *dve_done.step(f"hidden{s}"))
                            else:
                                dve.wait_ge(*act_done(f"hi{s}", i))
                                nc.vector.tensor_tensor(tile_of(hid[1], i * 2 + s), full[:, s, :],
                                                        tile_of(hid[0], i * 2 + s).bitcast(F32), ALU.subtract).then_inc(
                                    *dve_done.step(f"lo{s}"))
                for u in range(2):
                    dve.wait_ge(*hi_split.unit(0, 0, u))
                    split_lo(split, 0, u, width).then_inc(*lo_split.step())
                with dve.Fori(0, n - 1) as i:
                    turn(i, True)
                turn(n - 1, False)

            phase(sp=sp, pe=pe, act=act, dve=dve)
            return [(dve_done, "lo1", n - 1)], [(pe_done, f"{part}1", n - 1) for part in PART]

        def split_project(name, stream, split, source, ready, units_free, factor, x_ready):
            n = KT // 2
            half = len(source) // 2
            width = half * P
            pe_done = steps(f"{name}_pe", ["half0", "product0", "half1", "product1"])
            dve_done = steps(f"{name}_dve", ["sum0", "sum1"])
            hi_split, lo_split = Units(sem(f"{name}_hi_split")), Units(sem(f"{name}_lo_split"))
            loads = [Loads(s, n, lo_split, s) for s in range(2)]
            PART = ("half", "product")

            def sp(sp):
                for s in range(2):
                    sp.wait_ge(*loads[s].vacated())
                    sp.dma_start(loads[s].slot(row(stream, s)), row(stream, s)).then_inc(*loads[s].arrival)
                with sp.Fori(1, n) as i:
                    for s in range(2):
                        sp.wait_ge(*loads[s].vacated(i))
                        sp.dma_start(loads[s].slot(row(stream, i * 2 + s)), row(stream, i * 2 + s)).then_inc(*loads[s].arrival)

            def pe(pe):
                pe_done.enter(pe)
                for r in ready:
                    pe.wait_ge(*reached(*r))
                with pe.Fori(0, n) as i:
                    for s in range(2):
                        pe.wait_ge(*dve_done(f"sum{s}", i, 1))
                        for u, part in enumerate(PART):
                            pe.wait_ge(*lo_split.unit(i, s, u))
                            for k in range(half):
                                last = three_passes(ps[:, s, :], split, u, k, source[u * half + k], u == 0 and k == 0,
                                                    u == 1 and k == half - 1)
                            last.then_inc(*pe_done.step(f"{part}{s}"))

            def act(act):
                def turn(i, more):
                    for s in range(2):
                        for u, part in enumerate(PART):
                            if s == 0 or more:
                                if u == 0:
                                    act.wait_ge(*loads[1 - s].arrived(i + s))
                                act.wait_ge(*pe_done(f"{part}{s}", i))
                                split_hi(split, 1 - s, u, width).then_inc(*hi_split.step())
                act.wait_ge(*loads[0].arrived(0))
                for u in range(2):
                    act.wait_ge(*reached(*units_free[u]))
                    split_hi(split, 0, u, width).then_inc(*hi_split.step())
                with act.Fori(0, n - 1) as i:
                    turn(i, True)
                turn(n - 1, False)

            def dve(dve):
                dve_done.enter(dve)

                def turn(i, more):
                    for s in range(2):
                        for u in range(2):
                            if s == 0 or more:
                                dve.wait_ge(*hi_split.unit(i + s, 1 - s, u))
                                split_lo(split, 1 - s, u, width).then_inc(*lo_split.step())
                        dve.wait_ge(*pe_done(f"product{s}", i))
                        if isinstance(factor, float):
                            f = factor
                        else:
                            f = mods[:, bass.ds(i * 2 + (s + factor[0] * 48 + factor[1] * 8), 1)]
                        nc.vector.scalar_tensor_tensor(tile_of(x, i * 2 + s), ps[:, s, :], f, tile_of(x, i * 2 + s),
                                                       ALU.mult, ALU.add).then_inc(*dve_done.step(f"sum{s}"))
                for u in range(2):
                    dve.wait_ge(*hi_split.unit(0, 0, u))
                    split_lo(split, 0, u, width).then_inc(*lo_split.step())
                for r in x_ready:
                    dve.wait_ge(*reached(*r))
                with dve.Fori(0, n - 1) as i:
                    turn(i, True)
                turn(n - 1, False)

            phase(sp=sp, pe=pe, act=act, dve=dve)
            return [(dve_done, f"sum{j % 2}", j // 2) for j in range(KT)]

        def parts_of(name, scope, n=KT):
            return tuple(keep(f"{name}_{p}", [P, n, T], scope, F32R) for p in ("hi", "lo"))

        def feed_forward(name, scope, source, ready, factor, x_ready=()):
            split = Split(f"{name}_weights", scope)
            hid = parts_of(f"{name}_hidden", scope, HT)
            done, free = gated(name, split, scope, source, hid, ready)
            return split_project(f"{name}_down", f"{name}_out", split, [(hid[0][:, k, :], hid[1][:, k, :]) for k in range(HT)], done,
                                 free, factor, x_ready)

        def attend(name, scope, turns, work, out, ready, before, zero_first=()):
            N = len(work)
            sx = keep(f"{name}_masked", [P, 3, T], scope)
            probs = keep(f"{name}_probs", [P, 3, T], scope)
            probsT = keep(f"{name}_probsT", [P, 2, T], scope)
            diag = keep(f"{name}_diag", [P, 3, P], scope)
            stat = keep(f"{name}_stat", [P, 3, 4], scope)
            MAX, SUM, INV = range(3)
            L, TR, O = 0, 3, 5
            order = []
            for t in range(N + 3):
                order += [("L", t)] * (t < N) + [("T", t - 2)] * (2 <= t < N + 2) + [("O", t - 3)] * (t >= 3)
            a_order = []
            for t in range(N + 2):
                a_order += [("exp", t)] * (t < N) + [("PT", t - 2)] * (t >= 2)
            d_order = []
            for t in range(N + 1):
                d_order += [("max", t), ("neg", t)] * (t < N) + [("inv", t - 1), ("diag", t - 1)] * (t >= 1)

            def names(eng, seq):
                return before[eng][0] + [f"{a}{n}" for a, n in seq]
            S = {"pe": steps(f"{name}_pe", names("pe", order)), "act": steps(f"{name}_act", names("act", a_order) + ["out"]),
                 "dve": steps(f"{name}_dve", names("dve", d_order))}

            def earlier(what, n, back, turn):
                who = S[{"max": "dve", "T": "pe", "PT": "act", "O": "pe"}[what]]
                return who(f"{what}{n - back}", turn) if n >= back else who(f"{what}{N + n - back}", turn, 1)

            def pe(pe):
                S["pe"].enter(pe)
                for r in ready:
                    pe.wait_ge(*reached(*r))
                with pe.Fori(0, turns) as i:
                    before["pe"][1](pe, i, S)
                    for what, n in order:
                        w = work[n]
                        if what == "L":
                            pe.wait_ge(*earlier("max", n, 3, i))
                            out_l = ps[:, L + n % 3, 0:w["w"]]
                            extra = w.get("extra")
                            keys = tile_of(w["keys_of_turn"], i)[:, 0:w["w"]] if "keys_of_turn" in w else w["keys"]
                            ins = mm(out_l, w["query"], keys, True, not extra)
                            if extra:
                                ins = mm(out_l, *extra, False, True)
                        elif what == "T":
                            pe.wait_ge(*S["dve"](f"diag{n}", i))
                            pe.wait_ge(*earlier("PT", n, 2, i))
                            for b in range(w["w"] // P):
                                ins = mm(ps[:, TR + n % 2, b * P:(b + 1) * P], probs[:, n % 3, b * P:(b + 1) * P], diag[:, n % 3, :])
                        else:
                            pe.wait_ge(*S["act"](f"PT{n}", i))
                            if n == 0:
                                pe.wait_ge(*S["act"]("out", i, 1))
                            hh, q = w["head"], w["tile"]
                            nb = w["w"] // P
                            for b in range(nb):
                                ins = mm(ps[hh * HD:(hh + 1) * HD, O, q * P:(q + 1) * P], w["values"][b],
                                         probsT[:, n % 2, b * P:(b + 1) * P], w["first"] and b == 0, w["last"] and b == nb - 1)
                        ins.then_inc(*S["pe"].step(f"{what}{n}"))

            def act(act):
                S["act"].enter(act)
                with act.Fori(0, turns) as i:
                    before["act"][1](act, i, S)
                    for what, n in a_order:
                        w = work[n]["w"]
                        if what == "exp":
                            act.wait_ge(*S["dve"](f"neg{n}", i))
                            act.wait_ge(*earlier("T", n, 3, i))
                            ins = nc.scalar.activation(probs[:, n % 3, 0:w], sx[:, n % 3, 0:w], ACT.Exp,
                                                       bias=stat[:, MAX, n % 4:n % 4 + 1], accum_out=stat[:, SUM, n % 4:n % 4 + 1])
                        else:
                            act.wait_ge(*S["pe"](f"T{n}", i))
                            act.wait_ge(*earlier("O", n, 2, i))
                            ins = nc.scalar.activation(probsT[:, n % 2, 0:w], ps[:, TR + n % 2, 0:w], ACT.Copy)
                        ins.then_inc(*S["act"].step(f"{what}{n}"))
                    act.wait_ge(*S["pe"](f"O{N - 1}", i))
                    alone(act)
                    nc.scalar.activation(tile_of(out, i), ps[:, O, :], ACT.Copy).then_inc(*S["act"].step("out"))

            def dve(dve):
                S["dve"].enter(dve)
                with dve.Fori(0, turns) as i:
                    before["dve"][1](dve, i, S)
                    for what, n in d_order:
                        w = work[n]
                        m = n % 4
                        if what == "max":
                            dve.wait_ge(*S["pe"](f"L{n}", i))
                            alone(dve)
                            ins = nc.vector.tensor_tensor_reduce(
                                out=sx[:, n % 3, 0:w["w"]], in0=ps[:, L + n % 3, 0:w["w"]], in1=w["mask"], scale=1.0,
                                scalar=-3e38, op0=ALU.add, op1=ALU.max, accum_out=stat[:, MAX, m:m + 1])
                        elif what == "neg":
                            dve.wait_ge(*S["dve"](f"max{n}", i))
                            ins = nc.vector.tensor_scalar(stat[:, MAX, m:m + 1], stat[:, MAX, m:m + 1], -1.0, None, ALU.mult)
                        elif what == "inv":
                            dve.wait_ge(*S["act"](f"exp{n}", i))
                            ins = nc.vector.reciprocal(stat[:, INV, m:m + 1], stat[:, SUM, m:m + 1])
                        else:
                            dve.wait_ge(*S["dve"](f"inv{n}", i))
                            dve.wait_ge(*earlier("T", n, 3, i))
                            gate = w.get("gate")
                            ins = nc.vector.tensor_scalar(diag[:, n % 3, :], ident, stat[:, INV, m:m + 1], gate, ALU.mult,
                                                          ALU.mult if gate is not None else ALU.bypass)
                        ins.then_inc(*S["dve"].step(f"{what}{n}"))

            phase(pe=pe, act=act, dve=dve)
            return S

        IH = 8
        TOPK = 128

        def sparse_attention(scope, h, branch, out):
            cb = keep("const_attention_1", [P, CB["all"][1]], scope)

            def cc(name):
                return const(name, cb, CB)
            ckv = keep("latent", [P, T], scope)
            kidx = keep("index_keys", [P, T], scope)
            tmp = keep("latent_norm", [P, 2, T], scope)
            qi = keep("index_queries", [P, 2, 2, T], scope)
            wts = keep("index_weights", [P, QT, IH], scope)
            rel = keep("index_relu", [P, 2, T], scope)
            score = keep("index_scores", [P, QT, T], scope)
            best = keep("best", [P, QT, 8], scope)
            relb = keep("rel_bias", [32, 16], scope)
            brow = keep("bias_rows", [16, BIAS_LEN], scope)
            small_in, zeroed, rows_out = sem("rel_bias_in"), sem("index_queries_zeroed"), sem("bias_rows_out")
            scratch = d["bias_scratch"]
            todo = [(m, hh, q) for m in range(IH // 2) for hh in range(2) for q in range(1, QT)]
            NI = len(todo)
            pe_done = steps("idx_pe", ["ckv", "kidx", "widx", "qi0", "qi1", "ckv sq", "bias"]
                         + [n for t, (m, hh, q) in enumerate(todo)
                            for n in (([f"qi{m + 1}"] if hh == 0 and q == 1 and m >= 1 and m < 3 else []) + [f"score{t}"])])
            act_done = steps("idx_act", ["ckv sq", "kidx", "qi0a", "qi0b", "ckv std", "bias"]
                          + [n for t, (m, hh, q) in enumerate(todo)
                             for n in ([f"relu{t}"] + ([f"qi{m + 1}a", f"qi{m + 1}b"] if hh == 0 and q == 3 and m < 3 else []))])
            dve_done = steps("idx_dve", ["widx", "ckv rstd", "ckv"] + [f"add{t}" for t in range(NI)] + [f"causal{q}" for q in range(1, QT)])
            topk_done = steps("top_dve", [f"max{q}" for q in range(1, QT)] + [f"take{q}" for q in range(1, QT)])
            selected = steps("sel_dve", [f"select{q}" for q in range(1, QT)])
            load_a, load_b = Loads(0, 1, pe_done, "widx"), Loads(1, 1, pe_done, "qi1")
            load_c = Loads(0, 1, pe_done, "qi3")

            def sp(sp):
                sp.wait_ge(*load_a.vacated())
                sp.dma_start(load_a.slot(row("dsa_first", 0)), row("dsa_first", 0)).then_inc(*load_a.arrival)
                sp.wait_ge(*load_b.vacated())
                sp.dma_start(load_b.slot(row("dsa_index", 0)), row("dsa_index", 0)).then_inc(*load_b.arrival)
                sp.wait_ge(*reached(*branch[0]))
                sp.dma_start(relb[:, :], d["rel_bias"][:, :]).then_inc(small_in, 16)
                sp.dma_start(cb[:, :], d["const_attention"][:, :]).then_inc(att_in, 16)
                sp.wait_ge(*load_c.vacated())
                sp.dma_start(load_c.slot(row("dsa_index", 1)), row("dsa_index", 1)).then_inc(*load_c.arrival)
                sp.wait_ge(*act_done("bias"))
                sp.dma_start(scratch[:, :], brow[:, :]).then_inc(rows_out, 16)

            def pool(pool):
                pool.wait_ge(*reached(*branch[0]))
                nc.gpsimd.memset(qi[:, :, :, :], 0.0).then_inc(zeroed, 1)

            def pe(pe):
                pe_done.enter(pe)
                pe.wait_ge(*load_a.arrived())
                for n, (name, bank) in enumerate((("ckv", 0), ("kidx", 1))):
                    for k in range(KT):
                        if n == 0:
                            pe.wait_ge(*reached(*branch[k]))
                        last = mm(ps[:, bank, :], wtile(0, n * KT + k), h[:, k, :], k == 0, k == KT - 1)
                    last.then_inc(*pe_done.step(name))
                for q in range(QT):
                    for k in range(KT):
                        last = mm(ps[:, 2, q * IH:(q + 1) * IH], h[:, k, q * P:(q + 1) * P], wtile(0, k, P, IH, 2 * KT * P),
                                  k == 0, k == KT - 1)
                last.then_inc(*pe_done.step("widx"))

                def index_queries(m):
                    load = load_b if m < 2 else load_c
                    if m % 2 == 0:
                        pe.wait_ge(*load.arrived())
                    if m >= 2:
                        pe.wait_ge(*act_done(f"qi{m - 2}b"))
                    for k in range(KT):
                        last = mm(ps[:, 4 + m % 2, :], wtile(load.s, (m % 2) * KT + k), h[:, k, :], k == 0, k == KT - 1)
                    last.then_inc(*pe_done.step(f"qi{m}"))
                index_queries(0)
                index_queries(1)
                pe.wait_ge(*act_done("ckv sq"))
                mm(ps[:, 3, :], ones, tmp[:, 0, :]).then_inc(*pe_done.step("ckv sq"))
                pe.wait_ge(small_in, 16)
                pe.wait_ge(att_in, 16)
                pe.wait_ge(*dve_done("ckv"))
                pe.wait_ge(*act_done("kidx"))
                mm(ps[0:16, 0, :], relb[:, :], cc("onehot")[0:32, 0:T])
                mm(ps[0:16, 1, 0:P], relb[:, :], cc("onehot")[0:32, T:BIAS_LEN]).then_inc(*pe_done.step("bias"))
                for t, (m, hh, q) in enumerate(todo):
                    if hh == 0 and q == 1:
                        if m >= 1 and m < 3:
                            index_queries(m + 1)
                        pe.wait_ge(*act_done(f"qi{m}b"))
                    if t >= 2:
                        pe.wait_ge(*act_done(f"relu{t - 2}"))
                    w = (q + 1) * P
                    mm(ps[:, 6 + t % 2, 0:w], qi[:, m % 2, hh, q * P:(q + 1) * P], kidx[:, 0:w]).then_inc(*pe_done.step(f"score{t}"))

            def act(act):
                act_done.enter(act)
                act.wait_ge(*pe_done("ckv"))
                nc.scalar.activation(tmp[:, 0, :], ps[:, 0, :], ACT.Square).then_inc(*act_done.step("ckv sq"))
                act.wait_ge(*pe_done("kidx"))
                nc.scalar.activation(kidx[:, :], ps[:, 1, :], ACT.Copy).then_inc(*act_done.step("kidx"))
                act.wait_ge(zeroed, 1)

                def index_queries(m):
                    if m >= 2:
                        t = todo.index((m - 2, 1, QT - 1))
                        act.wait_ge(*pe_done(f"score{t}"))
                    act.wait_ge(*pe_done(f"qi{m}"))
                    for hh, ab in ((0, "a"), (1, "b")):
                        r = slice(hh * HD, (hh + 1) * HD)
                        nc.scalar.activation(qi[r, m % 2, hh, :], ps[r, 4 + m % 2, :], ACT.Copy).then_inc(*act_done.step(f"qi{m}{ab}"))
                index_queries(0)
                act.wait_ge(*pe_done("ckv sq"))
                nc.scalar.activation(tmp[:, 1, :], ps[:, 3, :], ACT.Sqrt, bias=const("rms_eps"), scale=1.0 / P).then_inc(*act_done.step("ckv std"))
                act.wait_ge(*pe_done("bias"))
                nc.scalar.activation(brow[:, T:BIAS_LEN], ps[0:16, 1, 0:P], ACT.Copy)
                nc.scalar.activation(brow[:, 0:T], ps[0:16, 0, :], ACT.Copy).then_inc(*act_done.step("bias"))
                for t, (m, hh, q) in enumerate(todo):
                    w = (q + 1) * P
                    act.wait_ge(*pe_done(f"score{t}"))
                    if t >= 2:
                        act.wait_ge(*dve_done(f"add{t - 2}"))
                    nc.scalar.activation(rel[:, t % 2, 0:w], ps[:, 6 + t % 2, 0:w], ACT.Relu).then_inc(*act_done.step(f"relu{t}"))
                    if hh == 0 and q == 3 and m < 3:
                        index_queries(m + 1)

            def dve(dve):
                dve_done.enter(dve)
                topk_done.enter(dve)
                selected.enter(dve)
                dve.wait_ge(*pe_done("widx"))
                nc.vector.tensor_scalar(wts[:, :, :], ps[:, 2, 0:QT * IH].rearrange("p (q h) -> p q h", h=IH),
                                                   IH ** -0.5 * HD ** -0.5, None, ALU.mult).then_inc(*dve_done.step("widx"))
                dve.wait_ge(*act_done("ckv std"))
                nc.vector.reciprocal(tmp[:, 1, :], tmp[:, 1, :]).then_inc(*dve_done.step("ckv rstd"))
                dve.wait_ge(*dve_done("ckv rstd"))
                nc.vector.scalar_tensor_tensor(ckv[:, :], ps[:, 0, :], vcol("kv_norm"), tmp[:, 1, :], ALU.mult, ALU.mult).then_inc(*dve_done.step("ckv"))
                for t, (m, hh, q) in enumerate(todo):
                    w, head = (q + 1) * P, 2 * m + hh
                    dve.wait_ge(*act_done(f"relu{t}"))
                    weight = wts[:, q, head:head + 1]
                    if head == 0:
                        ins = nc.vector.tensor_scalar(score[:, q, 0:w], rel[:, t % 2, 0:w], weight, None, ALU.mult)
                    else:
                        dve.wait_ge(*dve_done(f"add{t - QT + 1}"))
                        ins = nc.vector.scalar_tensor_tensor(score[:, q, 0:w], rel[:, t % 2, 0:w], weight, score[:, q, 0:w],
                                                             ALU.mult, ALU.add)
                    ins.then_inc(*dve_done.step(f"add{t}"))
                dve.wait_ge(att_in, 16)
                dve.wait_ge(*dve_done(f"add{NI - 1}"))
                for q in range(1, QT):
                    own = score[:, q, q * P:(q + 1) * P]
                    nc.vector.tensor_tensor(own, own, cc("causal")[:, T - P:T], ALU.add).then_inc(*dve_done.step(f"causal{q}"))
                dve.wait_ge(*dve_done(f"causal{QT - 1}"))
                with dve.Fori(0, TOPK // 8) as i:
                    for q in range(1, QT):
                        dve.wait_ge(*topk_done(f"take{q}", i, 1))
                        alone(dve)
                        nc.vector.max(best[:, q, :], score[:, q, 0:(q + 1) * P]).then_inc(*topk_done.step(f"max{q}"))
                    for q in range(1, QT):
                        w = (q + 1) * P
                        dve.wait_ge(*topk_done(f"max{q}", i))
                        alone(dve)
                        nc.vector.match_replace(score[:, q, 0:w], best[:, q, :], score[:, q, 0:w], TAKEN).then_inc(*topk_done.step(f"take{q}"))
                dve.wait_ge(*topk_done(f"take{QT - 1}", TOPK // 8 - 1))
                for q in range(1, QT):
                    w = (q + 1) * P
                    nc.vector.tensor_scalar(score[:, q, 0:w], score[:, q, 0:w], TAKEN / 2, NEG, ALU.is_ge, ALU.mult).then_inc(*selected.step(f"select{q}"))

            phase(sp=sp, pool=pool, pe=pe, act=act, dve=dve)

            qs = keep("scaled_queries", [P, KT, T], scope)
            q_pe = steps("dsa_queries_pe", ["query0", "query1"])
            q_act = steps("dsa_queries_act", ["query0", "query1"])
            q_loads = [Loads(s, KT // 2, q_pe, f"query{s}") for s in range(2)]

            def sp_queries(sp):
                for s in range(2):
                    sp.wait_ge(*q_loads[s].vacated())
                with sp.Fori(0, KT // 2) as i:
                    for s in range(2):
                        sp.wait_ge(*q_loads[s].vacated(i))
                        sp.dma_start(q_loads[s].slot(row("dsa_q", i * 2 + s)), row("dsa_q", i * 2 + s)).then_inc(*q_loads[s].arrival)

            def pe_queries(pe):
                q_pe.enter(pe)
                pe.wait_ge(*act_done("bias"))
                with pe.Fori(0, KT // 2) as i:
                    for s in range(2):
                        pe.wait_ge(*q_loads[s].arrived(i))
                        pe.wait_ge(*q_act(f"query{s}", i, 1))
                        for k in range(KT):
                            last = mm(ps[:, s, :], wtile(s, k), h[:, k, :], k == 0, k == KT - 1)
                        last.then_inc(*q_pe.step(f"query{s}"))

            def act_queries(act):
                q_act.enter(act)
                with act.Fori(0, KT // 2) as i:
                    for s in range(2):
                        act.wait_ge(*q_pe(f"query{s}", i))
                        alone(act)
                        nc.scalar.activation(tile_of(qs, i * 2 + s), ps[:, s, :], ACT.Copy, scale=HD ** -0.5).then_inc(
                            *q_act.step(f"query{s}"))

            phase(sp=sp_queries, pe=pe_queries, act=act_queries)
            qz = keep("latent_queries", [P, 2, T], scope)
            vals = keep("dsa_values", [P, QT, P], scope)
            hank = keep("bias_hankel", [P, 2, T], scope)
            hank_in = sem("bias_hankel_in")
            N = KT
            work = []
            for hh in range(2):
                for q in range(QT):
                    w = (q + 1) * P
                    off = T - P - q * P
                    work.append({"head": hh, "tile": q, "w": w, "query": qz[:, hh, q * P:(q + 1) * P], "keys": ckv[:, 0:w],
                                 "mask": cc("causal")[:, T - P:T] if q == 0 else score[:, q, 0:w],
                                 "extra": (cc("flip"), hank[:, hh, off:off + w]),
                                 "values": [vals[:, b, hh * HD:(hh + 1) * HD] for b in range(q + 1)], "first": True, "last": True})
            W = len(work)

            def before_pe(pe, i, S):
                pe.wait_ge(*load.arrived(i))
                pe.wait_ge(*S["act"]("lat1", i, 1))
                mm(ps[:, 6, :], wtile(0, 0), tile_of(qs, i)).then_inc(*S["pe"].step("lat0"))
                mm(ps[:, 7, :], wtile(0, 1), tile_of(qs, i)).then_inc(*S["pe"].step("lat1"))
                pe.wait_ge(*S["act"]("lat0", i))
                for b in range(QT):
                    last = mm(ps[:, 6, b * P:(b + 1) * P], ckv[:, b * P:(b + 1) * P], wtile(0, 2))
                last.then_inc(*S["pe"].step("v"))
                pe.wait_ge(*S["act"]("lat1", i))
                pe.wait_ge(hank_in, i * 16 + 16)

            def before_act(act, i, S):
                for hh in range(2):
                    act.wait_ge(*S["pe"](f"lat{hh}", i))
                    nc.scalar.activation(qz[:, hh, :], ps[:, 6 + hh, :], ACT.Copy).then_inc(*S["act"].step(f"lat{hh}"))

            def before_dve(dve, i, S):
                dve.wait_ge(*S["pe"]("v", i))
                nc.vector.tensor_copy(vals[:, :, :], ps[:, 6, :].rearrange("p (b n) -> p b n", n=P)).then_inc(*S["dve"].step("v"))

            S = attend("dsa", scope, N, work, out,
                       [(selected, f"select{QT - 1}"), (act_done, f"relu{NI - 1}"), (dve_done, "ckv"),
                        (q_act, f"query{1}", KT // 2 - 1)],
                       {"pe": (["lat0", "lat1", "v"], before_pe), "act": (["lat0", "lat1"], before_act),
                        "dve": (["v"], before_dve)})
            load = Loads(0, N, S["pe"], "v")

            def sp2(sp):
                sp.wait_ge(*load.vacated())
                sp.wait_ge(rows_out, 16)
                with sp.Fori(0, N) as i:
                    sp.wait_ge(*load.vacated(i))
                    sp.dma_start(load.slot(row("dsa_heads", i)), row("dsa_heads", i)).then_inc(*load.arrival)
                    sp.wait_ge(*S["pe"](f"L{W - 1}", i, 1))
                    sp.dma_start(hank[:, :, :], bass.AP(tensor=scratch.tensor, offset=i * (2 * BIAS_LEN),
                                                              ap=[[1, P], [BIAS_LEN, 2], [1, T]])).then_inc(hank_in, 16)

            phase(sp=sp2)
            return [(S["act"], "out", N - 1)]

        def mixer_inputs(scope, h, branch):
            t = {}

            def have(name, shape):
                t[name] = keep(name, shape, scope)
                return t[name]
            cb = have("const_attention_2", [P, CB["all"][1]])

            def cc(name):
                return const(name, cb, CB)
            keys = {n: have(f"keys_{n}", [P, T]) for n in ("slc", "win")}
            vals = have("values", [P, QT, 2 * P])
            gates = have("gates", [P, QT, 24])
            kcmp, vcmp = have("keys_cmp", [P, P]), have("values_cmp", [P, P])
            with ExitStack() as own:
                raw = keep("keys_raw", [P, 3, T], own)
                sq = keep("keys_sq", [P, 2, T], own)
                rstd = keep("keys_rstd", [P, 2, T], own)
                cos = keep("keys_cos", [P, T], own)
                sin = keep("keys_sin", [P, 3, T], own)
                z = keep("forget", [8, 5, T], own)
                c2 = keep("forget_sums", [8, 2, T], own)
                hidden = keep("cmp_hidden", [P, 2, 2, 2 * NCMP], own)
                toks = keep("cmp_tokens", [P, 2, T], own)
                blocks = keep("cmp_blocks", [P, 2, CMP_L // 2, 2 * NCMP], own)
                w2 = keep("cmp_w2", [P, 4 * HD], own)
                csq = keep("cmp_sq", [P, 3, NCMP], own)
            zeroed, const_in, w2_in, sums_out = sem("mixer_zeroed"), sem("mixer_constants_in"), sem("cmp_w2_in"), sem("forget_sums_out")
            loads_n = 4
            PE = (["kc", "vc", "slc", "gates", "fl", "win", "vals", "kc rot", "slc sum", "win sum", "v twice", "k twice", "slc rot",
                   "win rot"] + [f"cmp{n}" for n in range(loads_n)] + ["k2", "v2", "k2 sum"])
            AC = ["slc sq", "kc", "vc", "gates", "win sq", "slc std", "win std", "abs", "exp", "ln",
                  "hid k0", "hid k1", "hid v0", "hid v1", "k2 sq", "v2", "k2 std"]
            DV = (["z", "vals0", "vals1", "kc cos", "kc sin", "kc"] + [f"{n} {m}" for n in ("slc", "win") for m in ("rstd", "n")]
                  + [f"blocks {u}{g}{r}{n}" for u in "vk" for g in range(2) for r in range(2) for n in range(2)] + [f"{n} {m}" for n in ("slc", "win") for m in ("cos", "sin", "add")]
                  + ["1+e", "min", "logf", "cum", "-cum", "k2 rstd", "k2"])
            pe_done, act_done, dve_done = (steps(f"in2_{n}", q) for n, q in (("pe", PE), ("act", AC), ("dve", DV)))
            load_a, load_b = Loads(0, 1, pe_done, "fl"), Loads(1, 1, pe_done, "vals")
            CMP_BANKS = ((3, 4), (2, 5))
            cmp_loads = [Loads(n % 2, 1, pe_done, f"cmp{n}") for n in range(loads_n)]

            def sp(sp):
                for n, l in enumerate((load_a, load_b)):
                    sp.wait_ge(*l.vacated())
                    sp.dma_start(l.slot(row(f"mix_{n}", 0)), row(f"mix_{n}", 0)).then_inc(*l.arrival)
                sp.wait_ge(*reached(*branch[0]))
                sp.dma_start(cb[:, :], d["const_attention"][:, :]).then_inc(const_in, 16)
                sp.dma_start(w2[:, :], d["cmp_w2"][:, :]).then_inc(w2_in, 16)
                for n, l in enumerate(cmp_loads):
                    sp.wait_ge(*l.vacated())
                    sp.dma_start(l.slot(row("cmp_w1", n)), row("cmp_w1", n)).then_inc(*l.arrival)
                sp.wait_ge(*dve_done("-cum"))
                sp.dma_start(d["forget_scratch"].rearrange("s h t -> h s t"), c2[:, :, :]).then_inc(sums_out, 16)

            def pool(pool):
                pool.wait_ge(*reached(*branch[0]))
                for n in (kcmp, vcmp):
                    nc.gpsimd.memset(n[:, :], 0.0).then_inc(zeroed, 1)
                nc.gpsimd.memset(z[:, 4, :], 1.0).then_inc(zeroed, 1)

            def pe(pe):
                pe_done.enter(pe)
                pe.wait_ge(*load_a.arrived())
                for n, (name, bank) in enumerate((("kc", 0), ("vc", 1), ("slc", 2))):
                    for k in range(KT):
                        if n == 0:
                            pe.wait_ge(*reached(*branch[k]))
                        last = mm(ps[:, bank, :], wtile(0, n * KT + k), h[:, k, :], k == 0, k == KT - 1)
                    last.then_inc(*pe_done.step(name))
                at = 3 * KT * P
                for q in range(QT):
                    for k in range(KT):
                        last = mm(ps[:, 3, q * 24:(q + 1) * 24], h[:, k, q * P:(q + 1) * P], wtile(0, k, P, 24, at), k == 0, k == KT - 1)
                last.then_inc(*pe_done.step("gates"))
                for k in range(KT):
                    last = mm(ps[0:8, 4, :], wtile(0, k, P, 8, at + 24 * KT), h[:, k, :], k == 0, k == KT - 1)
                last.then_inc(*pe_done.step("fl"))
                pe.wait_ge(*load_b.arrived())
                for k in range(KT):
                    last = mm(ps[:, 5, :], wtile(1, k), h[:, k, :], k == 0, k == KT - 1)
                last.then_inc(*pe_done.step("win"))
                for q in range(QT):
                    for k in range(KT):
                        last = mm(ps[:, 6 + q // 2, (q % 2) * 256:(q % 2) * 256 + 256], h[:, k, q * P:(q + 1) * P],
                                  wtile(1, k, P, 2 * P, KT * P), k == 0, k == KT - 1)
                last.then_inc(*pe_done.step("vals"))
                pe.wait_ge(const_in, 16)
                pe.wait_ge(*act_done("kc"))
                mm(ps[:, 0, :], cc("rot"), raw[:, 2, :]).then_inc(*pe_done.step("kc rot"))
                for n, (name, bank, free) in enumerate((("slc", 3, (act_done, "gates")), ("win", 4, (dve_done, "z")))):
                    pe.wait_ge(*act_done(f"{name} sq"))
                    pe.wait_ge(*reached(*free))
                    mm(ps[:, bank, :], blockones, sq[:, n, :]).then_inc(*pe_done.step(f"{name} sum"))
                for u, ready, banks in (("v", (act_done, "vc"), (6, 7)), ("k", (dve_done, "kc"), (0, 1))):
                    pe.wait_ge(*reached(*ready))
                    if u == "v":
                        pe.wait_ge(*dve_done("vals1"))
                    for g in range(2):
                        last = mm(ps[:, banks[g], :], cc(f"twice{g}"), toks[:, "kv".index(u), :])
                    last.then_inc(*pe_done.step(f"{u} twice"))
                for n, (name, bank) in enumerate((("slc", 2), ("win", 5))):
                    pe.wait_ge(*dve_done(f"{name} n"))
                    mm(ps[:, bank, :], cc("rot"), raw[:, n, :]).then_inc(*pe_done.step(f"{name} rot"))
                pe.wait_ge(*act_done("win std"))
                for n, l in enumerate(cmp_loads):
                    u, part = n // 2, n % 2
                    pe.wait_ge(*dve_done(f"blocks {'kv'[u]}111"))
                    pe.wait_ge(*dve_done("win sin"))
                    pe.wait_ge(*l.arrived())
                    for e in range(CMP_L // 4):
                        pair = part * (CMP_L // 4) + e
                        for m in range(2):
                            last = mm(ps[:, CMP_BANKS[u][m], 0:2 * NCMP], wtile(n % 2, e * 2 + m), blocks[:, u, pair, :],
                                      pair == 0, pair == CMP_L // 2 - 1)
                    last.then_inc(*pe_done.step(f"cmp{n}"))
                pe.wait_ge(w2_in, 16)
                pe.wait_ge(*act_done("hid k1"))
                for g in range(2):
                    for m in range(2):
                        last = mm(ps[g * HD:(g + 1) * HD, 0, 0:NCMP], w2[:, m * HD:(m + 1) * HD],
                                  hidden[:, 0, m, g * NCMP:(g + 1) * NCMP], m == 0, m == 1)
                last.then_inc(*pe_done.step("k2"))
                pe.wait_ge(*act_done("hid v1"))
                for g in range(2):
                    for m in range(2):
                        last = mm(ps[0:NCMP, 6, g * HD:(g + 1) * HD], hidden[:, 1, m, g * NCMP:(g + 1) * NCMP],
                                  w2[:, (2 + m) * HD:(3 + m) * HD], m == 0, m == 1)
                last.then_inc(*pe_done.step("v2"))
                pe.wait_ge(*act_done("k2 sq"))
                mm(ps[:, 1, 0:NCMP], blockones, csq[:, 0, :]).then_inc(*pe_done.step("k2 sum"))

            def act(act):
                act_done.enter(act)
                a = nc.scalar.activation
                act.wait_ge(*pe_done("slc"))
                a(sq[:, 0, :], ps[:, 2, :], ACT.Square).then_inc(*act_done.step("slc sq"))
                a(raw[:, 2, :], ps[:, 0, :], ACT.Copy).then_inc(*act_done.step("kc"))
                a(toks[:, 1, :], ps[:, 1, :], ACT.Copy).then_inc(*act_done.step("vc"))
                act.wait_ge(*pe_done("gates"))
                a(gates[:, :, :], ps[:, 3, 0:QT * 24].rearrange("p (q n) -> p q n", n=24), ACT.Sigmoid).then_inc(*act_done.step("gates"))
                act.wait_ge(*pe_done("win"))
                a(sq[:, 1, :], ps[:, 5, :], ACT.Square).then_inc(*act_done.step("win sq"))
                for n, (name, bank) in enumerate((("slc", 3), ("win", 4))):
                    act.wait_ge(*pe_done(f"{name} sum"))
                    a(rstd[:, n, :], ps[:, bank, :], ACT.Sqrt, bias=const("rms_eps"), scale=1.0 / HD).then_inc(*act_done.step(f"{name} std"))
                act.wait_ge(*dve_done("z"))
                a(z[:, 1, :], z[:, 0, :], ACT.Abs).then_inc(*act_done.step("abs"))
                act.wait_ge(*act_done("abs"))
                a(z[:, 2, :], z[:, 1, :], ACT.Exp, scale=-1.0).then_inc(*act_done.step("exp"))
                act.wait_ge(*dve_done("1+e"))
                a(z[:, 3, :], z[:, 2, :], ACT.Ln).then_inc(*act_done.step("ln"))
                for u in range(2):
                    act.wait_ge(*pe_done(f"cmp{2 * u + 1}"))
                    for m in range(2):
                        a(hidden[:, u, m, :], ps[:, CMP_BANKS[u][m], 0:2 * NCMP], ACT.Silu).then_inc(*act_done.step(f"hid {'kv'[u]}{m}"))
                act.wait_ge(*pe_done("k2"))
                a(csq[:, 0, :], ps[:, 0, 0:NCMP], ACT.Square).then_inc(*act_done.step("k2 sq"))
                act.wait_ge(*pe_done("v2"))
                act.wait_ge(zeroed, 3)
                a(vcmp[0:NCMP, :], ps[0:NCMP, 6, 0:P], ACT.Copy).then_inc(*act_done.step("v2"))
                act.wait_ge(*pe_done("k2 sum"))
                a(csq[:, 1, :], ps[:, 1, 0:NCMP], ACT.Sqrt, bias=const("rms_eps"), scale=1.0 / HD).then_inc(*act_done.step("k2 std"))

            def dve(dve):
                dve_done.enter(dve)
                tt, ts, stt = nc.vector.tensor_tensor, nc.vector.tensor_scalar, nc.vector.scalar_tensor_tensor
                dve.wait_ge(*pe_done("fl"))
                ts(z[:, 0, :], ps[0:8, 4, :], vcol("b_forget")[0:8, :], None, ALU.add).then_inc(*dve_done.step("z"))
                dve.wait_ge(*pe_done("vals"))
                for b in range(2):
                    nc.vector.tensor_copy(vals[:, 2 * b:2 * b + 2, :], ps[:, 6 + b, :].rearrange("p (q n) -> p q n", q=2)).then_inc(*dve_done.step(f"vals{b}"))
                dve.wait_ge(const_in, 16)
                dve.wait_ge(*act_done("kc"))
                tt(cos[:, :], raw[:, 2, :], cc("cos"), ALU.mult).then_inc(*dve_done.step("kc cos"))
                dve.wait_ge(*pe_done("kc rot"))
                tt(sin[:, 2, :], ps[:, 0, :], cc("sin"), ALU.mult).then_inc(*dve_done.step("kc sin"))
                dve.wait_ge(*dve_done("kc sin"))
                tt(toks[:, 0, :], cos[:, :], sin[:, 2, :], ALU.add).then_inc(*dve_done.step("kc"))
                for n, (name, bank) in enumerate((("slc", 2), ("win", 5))):
                    dve.wait_ge(*act_done(f"{name} std"))
                    nc.vector.reciprocal(rstd[:, n, :], rstd[:, n, :]).then_inc(*dve_done.step(f"{name} rstd"))
                    dve.wait_ge(*dve_done(f"{name} rstd"))
                    stt(raw[:, n, :], ps[:, bank, :], vcol(f"k_{name}"), rstd[:, n, :], ALU.mult, ALU.mult).then_inc(*dve_done.step(f"{name} n"))
                for u, banks in (("v", (6, 7)), ("k", (0, 1))):
                    dve.wait_ge(*pe_done(f"{u} twice"))
                    for g in range(2):
                        for r in range(2):
                            for later in range(2):
                                rows, pairs = slice(r * HD, (r + 1) * HD), slice(8 * later, 8 * later + 8)
                                tokens = ps[rows, banks[g], CMP_S * later:CMP_S * (later + NCMP)].rearrange(
                                    "p (n e r) -> p e n r", e=8, r=2)[:, :, :, r]
                                a, _ = VC[f"pos_{u}"]
                                position = vec[rows, a + 8 * later:a + 8 * later + 8].unsqueeze(2).to_broadcast([HD, 8, NCMP])
                                tt(blocks[rows, "kv".index(u), pairs, g * NCMP:(g + 1) * NCMP], tokens, position,
                                   ALU.add).then_inc(*dve_done.step(f"blocks {u}{g}{r}{later}"))
                for n, (name, bank) in enumerate((("slc", 2), ("win", 5))):
                    dve.wait_ge(*dve_done(f"{name} n"))
                    tt(keys[name][:, :], raw[:, n, :], cc("cos"), ALU.mult).then_inc(*dve_done.step(f"{name} cos"))
                    dve.wait_ge(*pe_done(f"{name} rot"))
                    tt(sin[:, n, :], ps[:, bank, :], cc("sin"), ALU.mult).then_inc(*dve_done.step(f"{name} sin"))
                    dve.wait_ge(*dve_done(f"{name} sin"))
                    tt(keys[name][:, :], keys[name][:, :], sin[:, n, :], ALU.add).then_inc(*dve_done.step(f"{name} add"))
                dve.wait_ge(*act_done("exp"))
                ts(z[:, 2, :], z[:, 2, :], 1.0, None, ALU.add).then_inc(*dve_done.step("1+e"))
                ts(z[:, 1, :], z[:, 0, :], 0.0, None, ALU.min).then_inc(*dve_done.step("min"))
                dve.wait_ge(*dve_done("min"))
                dve.wait_ge(*act_done("ln"))
                tt(z[:, 0, :], z[:, 1, :], z[:, 3, :], ALU.subtract).then_inc(*dve_done.step("logf"))
                dve.wait_ge(*dve_done("logf"))
                dve.wait_ge(zeroed, 3)
                nc.vector.tensor_tensor_scan(c2[:, 0, :], z[:, 4, :], z[:, 0, :], 0.0, ALU.mult, ALU.add).then_inc(*dve_done.step("cum"))
                dve.wait_ge(*dve_done("cum"))
                ts(c2[:, 1, :], c2[:, 0, :], -1.0, None, ALU.mult).then_inc(*dve_done.step("-cum"))
                dve.wait_ge(*act_done("k2 std"))
                nc.vector.reciprocal(csq[:, 2, :], csq[:, 1, :]).then_inc(*dve_done.step("k2 rstd"))
                dve.wait_ge(*dve_done("k2 rstd"))
                stt(kcmp[:, 0:NCMP], ps[:, 0, 0:NCMP], vcol("k_cmp"), csq[:, 2, :], ALU.mult, ALU.mult).then_inc(*dve_done.step("k2"))

            phase(sp=sp, pool=pool, pe=pe, act=act, dve=dve)
            return t, cc, [(dve_done, "k2"), (act_done, "v2")], sums_out

        def head_inputs(scope, h, cc, ready):
            N = 4
            out = {n: keep(f"heads_{n}", [P, N, T], scope) for n in ("nsa_q", "fox_q", "fox_k", "fox_v")}
            NQ, FQ, FK, V, NSUM, QSUM, KSUM, ROT = 7, 1, 2, 3, 4, 5, 6, 0
            pe_done = steps("heads_pe", ["nq", "fq", "nq sum", "fk", "fq sum", "v", "rot", "fk sum"])
            act_done = steps("heads_act", ["nq sq", "fq sq", "nq std", "fk sq", "fq std", "v", "fk std"])
            scaled = sem("heads_gains_scaled")
            dve_done = steps("heads_dve", ["nq rstd", "nq n", "nq cos", "fq rstd", "fq", "nq sin", "nq", "fk rstd", "fk"])
            n_load, f_load = Loads(0, N, pe_done, "nq"), Loads(1, N, pe_done, "v")
            with ExitStack() as own:
                sq, std = ({n: keep(f"heads_{n}_{m}", [P, T], own) for n in ("nq", "fq", "fk")} for m in ("sq", "std"))
                qn, qc, qsin = (keep(f"heads_nq_{m}", [P, T], own) for m in ("n", "cos", "sin"))
                gains = keep("heads_query_gains", [P, 2], own)

            def sp(sp):
                sp.wait_ge(*n_load.vacated())
                sp.wait_ge(*f_load.vacated())
                with sp.Fori(0, N) as i:
                    for load, stream in ((n_load, "nsa_q"), (f_load, "fox_qkv")):
                        sp.wait_ge(*load.vacated(i))
                        sp.dma_start(load.slot(row(stream, i)), row(stream, i)).then_inc(*load.arrival)

            def pe(pe):
                pe_done.enter(pe)

                def product(bank, s, at, name):
                    for k in range(KT):
                        last = mm(ps[:, bank, :], wtile(s, at + k), h[:, k, :], k == 0, k == KT - 1)
                    last.then_inc(*pe_done.step(name))

                def turn(i, first):
                    pe.wait_ge(*n_load.arrived(i))
                    pe.wait_ge(*dve_done("nq n", i, 1))
                    product(NQ, 0, 0, "nq")
                    if first:
                        for r in ready:
                            pe.wait_ge(*reached(*r))
                    pe.wait_ge(*f_load.arrived(i))
                    pe.wait_ge(*dve_done("fq", i, 1))
                    product(FQ, 1, 0, "fq")
                    pe.wait_ge(*act_done("nq sq", i))
                    mm(ps[:, NSUM, :], blockones, sq["nq"][:, :]).then_inc(*pe_done.step("nq sum"))
                    pe.wait_ge(*dve_done("fk", i, 1))
                    product(FK, 1, KT, "fk")
                    pe.wait_ge(*act_done("fq sq", i))
                    mm(ps[:, QSUM, :], blockones, sq["fq"][:, :]).then_inc(*pe_done.step("fq sum"))
                    pe.wait_ge(*act_done("v", i, 1))
                    for b in range(QT):
                        for k in range(KT):
                            last = mm(ps[:, V, b * P:(b + 1) * P], h[:, k, b * P:(b + 1) * P], wtile(1, 2 * KT + k), k == 0, k == KT - 1)
                    last.then_inc(*pe_done.step("v"))
                    pe.wait_ge(*dve_done("nq n", i))
                    mm(ps[:, ROT, :], cc("rot"), qn[:, :]).then_inc(*pe_done.step("rot"))
                    pe.wait_ge(*act_done("fk sq", i))
                    mm(ps[:, KSUM, :], blockones, sq["fk"][:, :]).then_inc(*pe_done.step("fk sum"))
                turn(0, True)
                with pe.Fori(1, N) as i:
                    turn(i, False)

            def act(act):
                act_done.enter(act)

                def square(name, bank, i):
                    act.wait_ge(*pe_done(name, i))
                    nc.scalar.activation(sq[name][:, :], ps[:, bank, :], ACT.Square).then_inc(*act_done.step(f"{name} sq"))

                def root(name, bank, read_by, i):
                    act.wait_ge(*pe_done(f"{name} sum", i))
                    act.wait_ge(*dve_done(read_by, i, 1))
                    nc.scalar.activation(std[name][:, :], ps[:, bank, :], ACT.Sqrt, bias=const("rms_eps"), scale=1.0 / HD).then_inc(
                        *act_done.step(f"{name} std"))
                for r in ready:
                    act.wait_ge(*reached(*r))
                with act.Fori(0, N) as i:
                    square("nq", NQ, i)
                    square("fq", FQ, i)
                    root("nq", NSUM, "nq n", i)
                    square("fk", FK, i)
                    root("fq", QSUM, "fq", i)
                    act.wait_ge(*pe_done("v", i))
                    alone(act)
                    nc.scalar.activation(tile_of(out["fox_v"], i), ps[:, V, :], ACT.Copy).then_inc(*act_done.step("v"))
                    root("fk", KSUM, "fk", i)

            def dve(dve):
                dve_done.enter(dve)
                tt, stt = nc.vector.tensor_tensor, nc.vector.scalar_tensor_tensor

                def normed(name, bank, gain, to, step, i):
                    dve.wait_ge(*act_done(f"{name} std", i))
                    nc.vector.reciprocal(std[name][:, :], std[name][:, :]).then_inc(*dve_done.step(f"{name} rstd"))
                    dve.wait_ge(*dve_done(f"{name} rstd", i))
                    alone(dve)
                    stt(to, ps[:, bank, :], gain, std[name][:, :], ALU.mult, ALU.mult).then_inc(*dve_done.step(step))
                for r in ready:
                    dve.wait_ge(*reached(*r))
                for n, name in enumerate(("q_nsa", "q_fox")):
                    nc.vector.tensor_scalar(gains[:, n:n + 1], vcol(name), HD ** -0.5, None, ALU.mult).then_inc(scaled, 1)
                dve.wait_ge(scaled, 2)
                with dve.Fori(0, N) as i:
                    dve.wait_ge(*pe_done("rot", i, 1))
                    normed("nq", NQ, gains[:, 0:1], qn[:, :], "nq n", i)
                    dve.wait_ge(*dve_done("nq n", i))
                    dve.wait_ge(*dve_done("nq", i, 1))
                    tt(qc[:, :], qn[:, :], cc("cos"), ALU.mult).then_inc(*dve_done.step("nq cos"))
                    normed("fq", FQ, gains[:, 1:2], tile_of(out["fox_q"], i), "fq", i)
                    dve.wait_ge(*pe_done("rot", i))
                    tt(qsin[:, :], ps[:, ROT, :], cc("sin"), ALU.mult).then_inc(*dve_done.step("nq sin"))
                    dve.wait_ge(*dve_done("nq sin", i))
                    alone(dve)
                    tt(tile_of(out["nsa_q"], i), qc[:, :], qsin[:, :], ALU.add).then_inc(*dve_done.step("nq"))
                    normed("fk", FK, vcol("k_fox"), tile_of(out["fox_k"], i), "fk", i)

            phase(sp=sp, pe=pe, act=act, dve=dve)
            return out, [(dve_done, "fk", N - 1), (act_done, "fk std", N - 1)]

        def pair_queries(name, scope, source, ready):
            qz = keep(f"{name}_queries", [P, 2, T], scope)
            zeroed = sem(f"{name}_queries_zeroed")

            def pool(pool):
                for r in ready:
                    pool.wait_ge(*reached(*r))
                nc.gpsimd.memset(qz[:, :, :], 0.0).then_inc(zeroed, 1)

            def copies(dve, i, S, last):
                dve.wait_ge(zeroed, 1)
                dve.wait_ge(*S["pe"](last, i, 1))
                alone(dve)
                for hh in range(2):
                    r = slice(hh * HD, (hh + 1) * HD)
                    nc.vector.tensor_copy(qz[r, hh, :], tile_of(source, i)[r, :]).then_inc(*S["dve"].step(f"q{hh}"))
            return qz, pool, copies

        def grouped_attention(scope, queries, t, cc, ready, out):
            gst = keep("pair_gates", [P, QT, 6], scope)
            N = 4
            qz, pool, copy_queries = pair_queries("nsa", scope, queries, ready)
            work = []
            for hh in range(2):
                for q in range(QT):
                    for b, (keys, v0) in enumerate(((t["keys_cmp"], None), (t["keys_slc"], 0), (t["keys_win"], P))):
                        w = P if b == 0 else (q + 1) * P
                        mask = cc("cmp_mask")[:, q * P:(q + 1) * P] if b == 0 else cc("causal")[:, T - w:T]
                        values = ([t["values_cmp"][:, hh * HD:(hh + 1) * HD]] if b == 0 else
                                  [t["values"][:, s, v0 + hh * HD:v0 + (hh + 1) * HD] for s in range(q + 1)])
                        work.append({"head": hh, "tile": q, "w": w, "query": qz[:, hh, q * P:(q + 1) * P], "keys": keys[:, 0:w],
                                     "mask": mask, "values": values, "gate": gst[:, q, hh * 3 + b:hh * 3 + b + 1],
                                     "first": b == 0, "last": b == 2})

            def before_pe(pe, i, S):
                pe.wait_ge(*S["dve"]("q1", i))

            def before_act(act, i, S):
                pass

            def before_dve(dve, i, S):
                copy_queries(dve, i, S, f"L{W - 1}")
                dve.wait_ge(*S["dve"](f"diag{W - 1}", i, 1))
                alone(dve)
                nc.vector.tensor_copy(gst[:, :, :], t["gates"][:, :, bass.ds(i * 6, 6)]).then_inc(*S["dve"].step("gates"))
                dve.wait_ge(*S["dve"]("gates", i))
                if_valid = cc("cmp_valid")[:, 0:1]
                for hh in range(2):
                    nc.vector.tensor_scalar(gst[:, 0, hh * 3:hh * 3 + 1], gst[:, 0, hh * 3:hh * 3 + 1], if_valid, None,
                                                          ALU.mult).then_inc(*S["dve"].step(f"valid{hh}"))

            W = len(work)
            S = attend("nsa", scope, N, work, out, ready,
                       {"pe": ([], before_pe), "act": ([], before_act),
                        "dve": (["q0", "q1", "gates", "valid0", "valid1"], before_dve)})
            phase(pool=pool)
            return [(S["act"], "out", N - 1)], [(S["pe"], f"O{W - 1}", N - 1)]

        def forgetting_attention(scope, heads, cc, ready, sums_out, out):
            N = 4
            W = 2 * QT
            qz, pool_queries, copy_queries = pair_queries("fox", scope, heads["fox_q"], ready)
            vals = keep("fox_values", [P, QT, P], scope)
            left, right = (keep(f"forget_{n}", [P, 2, T], scope) for n in ("left", "right"))
            zeroed, sums_in = sem("fox_zeroed"), sem("forget_sums_in")
            work = []
            for hh in range(2):
                for q in range(QT):
                    w = (q + 1) * P
                    tok = slice(q * P, (q + 1) * P)
                    work.append({"head": hh, "tile": q, "w": w, "query": qz[:, hh, tok], "keys_of_turn": heads["fox_k"],
                                 "mask": cc("causal")[:, T - w:T], "extra": (left[:, hh, tok], right[:, hh, 0:w]),
                                 "values": [vals[:, s, hh * HD:(hh + 1) * HD] for s in range(q + 1)], "first": True, "last": True})

            def before_pe(pe, i, S):
                pe.wait_ge(sums_in, i * 32 + 32)
                pe.wait_ge(*S["dve"]("values", i))

            def before_act(act, i, S):
                pass

            def before_dve(dve, i, S):
                copy_queries(dve, i, S, f"L{W - 1}")
                dve.wait_ge(*S["pe"](f"O{W - 1}", i, 1))
                alone(dve)
                nc.vector.tensor_copy(vals[:, :, :], tile_of(heads["fox_v"], i).rearrange("p (b n) -> p b n", n=P)).then_inc(
                    *S["dve"].step("values"))

            def pool(pool):
                for r in ready:
                    pool.wait_ge(*reached(*r))
                for n in (left, right):
                    nc.gpsimd.memset(n[:, :, :], 0.0).then_inc(zeroed, 1)
                pool.wait_ge(zeroed, 2)
                nc.gpsimd.memset(left[32:33, :, :], 1.0)
                nc.gpsimd.memset(right[0:1, :, :], 1.0).then_inc(zeroed, 1)
            phase(pool=pool_queries)
            phase(pool=pool)
            S = attend("fox", scope, N, work, out, ready,
                       {"pe": ([], before_pe), "act": ([], before_act), "dve": (["q0", "q1", "values"], before_dve)})

            def sp(sp):
                sp.wait_ge(sums_out, 16)
                sp.wait_ge(zeroed, 3)
                with sp.Fori(0, N) as i:
                    sp.wait_ge(*S["pe"](f"L{W - 1}", i, 1))
                    sums = d["forget_scratch"]
                    sp.dma_start(left[0:1, :, :], sums[0:1, bass.ds(i * 2, 2), :]).then_inc(sums_in, 16)
                    sp.dma_start(right[32:33, :, :], sums[1:2, bass.ds(i * 2, 2), :]).then_inc(sums_in, 16)

            phase(sp=sp)
            return [(S["act"], "out", N - 1)]

        def gated_embedding(scope, h, branch):
            emb = keep("embedding", [P, 2, T], scope)
            e = keep("projected", [P, KT, T], scope)
            g = keep("embedding_gate", [P, KT, T], scope)
            n = KT // 2
            emb_in, written = sem("embedding_in"), sem("result_written")
            pe_done = steps("ple_pe", ["gate0", "e0", "gate1", "e1"])
            act_done = steps("ple_act", ["gate0", "gate1"])
            dve_done = steps("ple_dve", ["e0", "e1"])
            loads = [Loads(s, n, pe_done, f"e{s}") for s in range(2)]

            def sp(sp):
                sp.wait_ge(*reached(*branch[0]))
                sp.dma_start(emb[:, :, :], d["embedding"][:, :, :]).then_inc(emb_in, 16)
                for s in range(2):
                    sp.wait_ge(*loads[s].vacated())
                with sp.Fori(0, n) as i:
                    for s in range(2):
                        sp.wait_ge(*loads[s].vacated(i))
                        sp.dma_start(loads[s].slot(row("ple", i * 2 + s)), row("ple", i * 2 + s)).then_inc(*loads[s].arrival)

            def pe(pe):
                pe_done.enter(pe)
                for r in branch:
                    pe.wait_ge(*reached(*r))
                pe.wait_ge(emb_in, 16)
                with pe.Fori(0, n) as i:
                    for s in range(2):
                        pe.wait_ge(*loads[s].arrived(i))
                        pe.wait_ge(*act_done(f"gate{s}", i, 1))
                        for k in range(KT):
                            last = mm(ps[:, 2 * s, :], wtile(s, k), h[:, k, :], k == 0, k == KT - 1)
                        last.then_inc(*pe_done.step(f"gate{s}"))
                        pe.wait_ge(*dve_done(f"e{s}", i, 1))
                        for k in range(2):
                            last = mm(ps[:, 2 * s + 1, :], wtile(s, KT + k), emb[:, k, :], k == 0, k == 1)
                        last.then_inc(*pe_done.step(f"e{s}"))

            def act(act):
                act_done.enter(act)
                with act.Fori(0, n) as i:
                    for s in range(2):
                        act.wait_ge(*pe_done(f"gate{s}", i))
                        alone(act)
                        nc.scalar.activation(tile_of(g, i * 2 + s), ps[:, 2 * s, :], ACT.Sigmoid).then_inc(*act_done.step(f"gate{s}"))

            def dve(dve):
                dve_done.enter(dve)
                with dve.Fori(0, n) as i:
                    for s in range(2):
                        dve.wait_ge(*pe_done(f"e{s}", i))
                        alone(dve)
                        nc.vector.tensor_copy(tile_of(e, i * 2 + s), ps[:, 2 * s + 1, :]).then_inc(*dve_done.step(f"e{s}"))

            phase(sp=sp, pe=pe, act=act, dve=dve)
            tiles = [e[:, j, :] for j in range(KT)]
            normed = rms_norm("ple_norm", scope, tiles, [(dve_done, f"e{j % 2}", j // 2) for j in range(KT)],
                              [vcol("ple", j) for j in range(KT)], tiles)
            pool_done = steps("ple_pool", [f"gated{j}" for j in range(KT)])
            sum_done = steps("ple_sum", [f"sum{j}" for j in range(KT)])

            def gate(pool):
                pool_done.enter(pool)
                pool.wait_ge(*act_done("gate1", n - 1))
                for j in range(KT):
                    pool.wait_ge(*reached(*normed[j]))
                    nc.gpsimd.tensor_tensor(e[:, j, :], e[:, j, :], g[:, j, :], ALU.mult).then_inc(*pool_done.step(f"gated{j}"))

            def add(dve):
                sum_done.enter(dve)
                for j in range(KT):
                    dve.wait_ge(*pool_done(f"gated{j}"))
                    nc.vector.tensor_tensor(x[:, j, :], x[:, j, :], e[:, j, :], ALU.add).then_inc(*sum_done.step(f"sum{j}"))

            def store(sp):
                for j in range(KT):
                    sp.wait_ge(*sum_done(f"sum{j}"))
                    sp.dma_start(d["out"][:, j, :], x[:, j, :]).then_inc(written, 16)
                sp.wait_ge(written, 16 * KT)

            phase(pool=gate, dve=add, sp=store)

        ready = modulation()
        with ExitStack() as outer:
            hin = keep("branch_in", [P, KT, T + 1], outer)
            with ExitStack() as scope:
                xs, lora, mix_pe, mix_act, mix_dve = time_mix_inputs(scope, hin, ready)
                yout, rec_done, name, turn = recurrence(scope, hin[:, :, 1:T + 1], xs, lora, mix_pe, mix_act, mix_dve)
            recurred = (rec_done, name, turn)
            scaled = residual_again([recurred])
            summed = project("rwkv_out", "rwkv_out", [yout[:, k, :] for k in range(KT)], [recurred], (0, GT1), [scaled])
        with ExitStack() as outer:
            source = parts_of("ff0_in", outer)
            with ExitStack() as scope:
                branch, x_ready = layer_norm("ln00", scope, 0, 0, summed, (0, SH2, SC2, source))

            with ExitStack() as scope:
                summed = feed_forward("ff0", scope, source, branch, (0, GT2), x_ready)
        with ExitStack() as outer:
            h = keep("attention_in", [P, KT, T], outer)
            with ExitStack() as scope:
                branch, x_ready = layer_norm("ln01", scope, 0, 1, summed, (1, SH1, SC1, h))

            with ExitStack() as scope:
                mixed = keep("attended", [P, KT, T], scope)
                done = sparse_attention(scope, h, branch, mixed)
                summed = project("dsa_out", "dsa_out", [mixed[:, k, :] for k in range(KT)], done, (1, GT1), x_ready)
        with ExitStack() as outer:
            source = parts_of("ff1_in", outer)
            with ExitStack() as scope:
                branch, x_ready = layer_norm("ln10", scope, 1, 0, summed, (1, SH2, SC2, source))

            with ExitStack() as scope:
                summed = feed_forward("ff1", scope, source, branch, (1, GT2), x_ready)
        tiles_of_x = [x[:, j, :] for j in range(KT)]

        def tiles_of(t):
            return [t[:, j, :] for j in range(KT)]

        def gains(name):
            return [vcol(name, j) for j in range(KT)]
        with ExitStack() as scope:
            normed, _ = layer_norm("ln11", scope, 1, 1, summed, None)
        with ExitStack() as outer:
            source = parts_of("ffn1_in", outer)
            with ExitStack() as scope:
                branch = rms_norm("rms1", scope, tiles_of_x, normed, gains("ffn1"), (tiles_of(source[0]), tiles_of(source[1])))
            with ExitStack() as scope:
                summed = feed_forward("ffn1", scope, source, branch, 0.5)

        with ExitStack() as outer:
            h = keep("mixer_in", [P, KT, T], outer)
            with ExitStack() as scope:
                branch = rms_norm("rms2", scope, tiles_of_x, summed, gains("mix"), tiles_of(h))
            with ExitStack() as scope:
                mixed = keep("mixed", [P, KT, T], scope)
                t, cc, ready, sums_out = mixer_inputs(scope, h, branch)
                heads, ready = head_inputs(scope, h, cc, ready)
                with ExitStack() as own:
                    nsa_done, nsa_pe = grouped_attention(own, heads["nsa_q"], t, cc, ready, mixed[:, 0:4, :])
                with ExitStack() as own:
                    fox_done = forgetting_attention(own, heads, cc, nsa_done + nsa_pe, sums_out, mixed[:, 4:8, :])
                with ExitStack() as own:
                    outs = []
                    for n, part in enumerate(("nsa", "fox")):
                        part_tiles = [mixed[:, 4 * n + j, :] for j in range(4)]
                        outs += rms_norm(f"rms_{part}", own, part_tiles, [fox_done[0]] * 4,
                                         [vcol("out_norm", 4 * n + j) for j in range(4)], part_tiles)
                    summed = project("mix_out", "mix_out", [mixed[:, k, :] for k in range(KT)], outs, 1.0)

        with ExitStack() as outer:
            source = parts_of("ffn2_in", outer)
            with ExitStack() as scope:
                branch = rms_norm("rms3", scope, tiles_of_x, summed, gains("ffn2"), (tiles_of(source[0]), tiles_of(source[1])))
            with ExitStack() as scope:
                summed = feed_forward("ffn2", scope, source, branch, 0.5)
        with ExitStack() as scope:
            h = keep("embedding_in", [P, KT, T], scope)
            branch = rms_norm("rms4", scope, tiles_of_x, summed, gains("ple_gate"), tiles_of(h))
            gated_embedding(scope, h, branch)

        block = ctx.enter_context(nc.Block())

        @block.sync
        def _(eng):
            for program in programs["sp"]:
                program(eng)

        @block.tensor
        def _(eng):
            for program in programs["pe"]:
                program(eng)

        @block.scalar
        def _(eng):
            for program in programs["act"]:
                program(eng)

        @block.vector
        def _(eng):
            for program in programs["dve"]:
                program(eng)

        @block.gpsimd
        def _(eng):
            for program in programs["pool"]:
                program(eng)


def constant_tables():
    s, t = np.arange(P)[:, None], np.arange(P)[None, :]
    same = (s // CH) == (t // CH)
    ca = np.zeros((P, CA["all"][1]), np.float32)
    cr = np.zeros((P, CR["all"][1]), np.float32)
    cb = np.zeros((P, CB["all"][1]), np.float32)

    def put(table, where, name, values):
        a, n = where[name]
        table[:np.shape(values)[0], a:a + n] = np.reshape(values, (np.shape(values)[0], n))

    put(ca, CA, "ident", s == t)
    put(ca, CA, "blockones", same)
    put(ca, CA, "ones", np.ones((P, P)))
    for name, eps in (("ln_eps", 1e-5), ("gn_eps", HD * 1e-5), ("rms_eps", 1e-6)):
        put(ca, CA, name, np.full((P, 1), eps))
    put(cr, CR, "strict", same & (s < t))
    put(cr, CR, "incl", same & (s <= t))
    for k in range(6):
        put(cr, CR, f"level{k}", ((s >> (k + 1)) == (t >> (k + 1))) & ((s >> k) % 2 == 0) & ((t >> k) % 2 == 1))
    put(cr, CR, "reset", np.tile(np.arange(T) % CH != 0, (P, 1)))
    put(cb, CB, "flip", s + t == P - 1)
    u = np.arange(T)[None, :]
    put(cb, CB, "causal", np.where(u - (T - P) > s, NEG, 0.0))
    half = HD // 8
    inv = np.float32(500000.0) ** (-np.arange(0, 2 * half, 2, dtype=np.float32) / np.float32(2 * half))
    angle = np.arange(T, dtype=np.float32)[None, :] * inv[:, None]
    cos, sin, rot = np.ones((HD, T)), np.zeros((HD, T)), np.zeros((P, P))
    for part in range(2):
        cos[part * half:(part + 1) * half] = np.cos(angle)
        sin[part * half:(part + 1) * half] = np.sin(angle)
    put(cb, CB, "cos", np.tile(cos, (2, 1)))
    put(cb, CB, "sin", np.tile(sin, (2, 1)))
    for g in range(2):
        for e in range(half):
            rot[g * HD + e + half, g * HD + e] = -1.0
            rot[g * HD + e, g * HD + e + half] = 1.0
    put(cb, CB, "rot", rot)
    for g in range(2):
        put(cb, CB, f"twice{g}", s == g * HD + t % HD)
    token = np.arange(P)[:, None, None] + P * np.arange(QT)[None, :, None]
    ends = np.arange(P)[None, None, :] * CMP_S + CMP_L - 1
    put(cb, CB, "cmp_mask", np.where((ends <= token) & (np.arange(P) < NCMP), 0.0, NEG))
    put(cb, CB, "cmp_valid", token[:, :, 0] >= CMP_L - 1)
    n = np.maximum(T - 1 - np.arange(BIAS_LEN), 0)
    large = 16 + (np.log(np.maximum(n, 1).astype(np.float32) / np.float32(16)) / np.float32(math.log(128 / 16))
                  * np.float32(16)).astype(np.int32)
    bucket = np.where(n < 16, n, np.minimum(large, 31))
    put(cb, CB, "onehot", bucket[None, :] == np.arange(32)[:, None])
    return ca, cr, cb


def kernel(**inputs):
    import concourse.bacc as bacc
    from concourse.bass_utils import run_bass_kernel_spmd

    a = {k: np.asarray(v) for k, v in inputs.items()}

    def tiles(w):
        k, m = w.shape
        return w.reshape(k // P, P, m // P, P).transpose(2, 1, 0, 3).reshape(m // P, P, (k // P) * P)

    def rows(w):
        return w.reshape(-1, P, w.shape[1]).transpose(1, 0, 2).reshape(P, -1)

    def col(v):
        return v.reshape(-1, P).T

    def pad(w, n):
        return np.concatenate([w, np.zeros((n - w.shape[0],) + w.shape[1:], np.float32)], 0)

    def feature_major(v):
        return np.ascontiguousarray(v.reshape(T, -1, P).transpose(2, 1, 0))

    ca, cr, cb = constant_tables()
    d = {"const_all": ca, "const_recurrence": cr, "const_attention": cb, "x": feature_major(a["x"][0])}
    pair = np.stack([col(a[n].reshape(-1)) for n in ("rwkv_w0", "rwkv_a0", "rwkv_k_k", "rwkv_k_a", "rwkv_r_k", "rwkv_lnx_g",
                                                     "rwkv_lnx_b")], 2).reshape(P, -1)
    order = np.concatenate([np.arange(g * 256 + j * HD, g * 256 + j * HD + HD) for j in range(4) for g in range(2)])

    def twice(v):
        return np.concatenate([v.reshape(-1)] * 2)[:, None]

    def two_by_two(v):
        return v.reshape(-1, P).T

    vectors = [col(a["ada_b"]), col(a["ln_g"]), col(a["ln_b"]), col(a["rwkv_mu"]), pair, col(a["ffn1_norm_2"]),
               col(a["mix_norm_2"]), col(a["ffn2_norm_2"]), col(a["ple_gate_norm_2"]), col(a["ple_norm_2"]),
               col(np.concatenate([a["out_norm_nsa_2"][0][order], a["out_norm_fox_2"][0]])), col(a["dsa_kv_norm"]),
               twice(a["q_norm_nsa_2"]), twice(a["k_norm_cmp_2"]), twice(a["k_norm_slc_2"]), twice(a["k_norm_win_2"]),
               twice(a["q_norm_fox_2"]), twice(a["k_norm_fox_2"]), pad(a["b_forget_2"].reshape(-1, 1), P),
               two_by_two(a["cmp_pos_k_2"][0]), two_by_two(a["cmp_pos_v_2"][0])]
    d["vectors"] = np.concatenate(vectors, 1)
    d["ada"] = np.concatenate([a["ada_w"][i].T.reshape(6 * KT, P, D) for i in range(2)])
    d["c_rows"] = np.broadcast_to(a["c"].reshape(1, D), (P, D))
    d["lora1"] = rows(np.concatenate([a["rwkv_w1"][0], a["rwkv_a1"][0], a["rwkv_g1"][0]], 1))[None]
    second = [tiles(pad(w, P)) for w in (a["rwkv_w2"][0], a["rwkv_a2"][0], a["rwkv_g2"][0][:P], a["rwkv_g2"][0][P:])]
    d["rwkv"] = np.concatenate([tiles(a["rwkv_w_rkv"][0, m]) for m in range(3)] + second, 2)
    d["rwkv_out"] = tiles(a["rwkv_w_out"][0])

    def feed_forward(name, gate, up, down):
        d[f"{name}_in"] = np.concatenate([tiles(gate), tiles(up)], 2)
        d[f"{name}_out"] = tiles(down)

    for i in range(2):
        feed_forward(f"ff{i}", a["ffn_w_in"][i][:, :HID], a["ffn_w_in"][i][:, HID:], a["ffn_w_out"][i])
    for i in (1, 2):
        feed_forward(f"ffn{i}", a[f"ffn{i}_wg_2"][0], a[f"ffn{i}_wu_2"][0], a[f"ffn{i}_wd_2"][0])
    w = a["dsa_w_in"][0]
    cut = [D, D + P, D + P + 512, D + P + 576]
    wq, wc, wqi, wki, wwi = np.split(w, cut, 1)
    d["dsa_first"] = np.concatenate([tiles(wc)[0], tiles(np.concatenate([wki, wki], 1))[0], rows(wwi)], 1)[None]
    d["dsa_index"] = tiles(wqi).reshape(2, 2, P, D).transpose(0, 2, 1, 3).reshape(2, P, 2 * D)
    uk, uv = a["dsa_w_uk"][0], a["dsa_w_uv"][0]
    none = np.zeros((8, HD, P), np.float32)
    d["dsa_q"] = tiles(wq)
    d["dsa_heads"] = np.concatenate([np.concatenate([uk[0::2], none], 1), np.concatenate([none, uk[1::2]], 1),
                                     np.concatenate([uv[0::2], uv[1::2]], 2)], 2)
    d["dsa_out"] = tiles(a["dsa_w_out"][0])
    d["rel_bias"] = a["rel_bias"]
    sizes = (512, P, P, P, P, P, P, 24, 512, 512, 512, 8)
    qa, kc, vc, ks, vs, kw, vw, ga, qf, kf, vf, fl = np.split(a["w_in_2"][0], np.cumsum(sizes)[:-1], 1)
    ga = ga.reshape(D, 2, 4, 3).transpose(0, 2, 1, 3).reshape(D, 24)
    d["mix_0"] = np.concatenate([tiles(kc)[0], tiles(vc)[0], tiles(ks)[0], rows(ga), rows(fl)], 1)[None]
    d["mix_1"] = np.concatenate([tiles(kw)[0], rows(np.concatenate([vs, vw], 1))], 1)[None]
    d["nsa_q"] = tiles(qa[:, order])
    d["fox_qkv"] = np.concatenate([tiles(qf), tiles(kf), tiles(vf)], 2)

    def first_map(w):
        return w.reshape(2, 8, P, 256).transpose(0, 2, 1, 3).reshape(2, P, 8 * 256)

    d["cmp_w1"] = np.concatenate([first_map(a["cmp_k_w1_2"][0]), first_map(a["cmp_v_w1_2"][0])])
    d["cmp_w2"] = np.concatenate([rows(a["cmp_k_w2_2"][0]), rows(a["cmp_v_w2_2"][0])], 1)
    w = a["w_out_2"][0]
    d["mix_out"] = tiles(np.concatenate([w[:512][order], w[512:]]))
    d["ple"] = np.concatenate([tiles(a["ple_w_gate_2"][0]), tiles(a["ple_w_proj_2"][0])], 2)
    d["embedding"] = feature_major(a["p_2"][0, 0])
    d = {k: np.ascontiguousarray(v) for k, v in d.items()}

    nc = bacc.Bacc("TRN2", target_bir_lowering=False, num_devices=1)
    d = {"in_" + k: v for k, v in d.items()}
    t = {k[3:]: nc.dram_tensor(k, v.shape, F32, kind="ExternalInput").ap() for k, v in d.items()}
    t["out"] = nc.dram_tensor("out_features", (P, KT, T), F32, kind="ExternalOutput").ap()
    scratch = nc.dram_tensor("bias_scratch", (16, BIAS_LEN), F32, kind="Internal")
    t["bias_scratch"] = scratch.ap()
    t["forget_scratch"] = nc.dram_tensor("forget_scratch", (2, 8, T), F32, kind="Internal").ap()
    build(nc, t)
    got = run_bass_kernel_spmd(nc, [d], core_ids=[0]).results[0]["out_features"]
    return np.ascontiguousarray(got.transpose(2, 1, 0)).reshape(1, T, D)
```

```python
import math
from contextlib import ExitStack

import numpy as np
import concourse.bass as bass
from concourse import mybir

P = 128
T = 512
D = 1024
KT = D // P
HID = 2816
HT = HID // P
CH = 64
NCH = T // CH
HD = 64
QT = T // P
SLOTS = (28 * P, 24 * P)
ALPHA = 4.0 ** 0.25
DECAY = math.exp(-0.5)
NEG = -1e30
TAKEN = -3e38
NCMP = 31
CMP_L = 32
CMP_S = 16
BIAS_LEN = T + P
F32 = mybir.dt.float32
F32R = mybir.dt.float32r
ACT = mybir.ActivationFunctionType
ALU = mybir.AluOpType
AX = mybir.AxisListType


def columns(*parts):
    at, out = 0, {}
    for name, width in parts:
        out[name] = (at, width)
        at += width
    out["all"] = (0, at)
    return out


CA = columns(("ident", P), ("blockones", P), ("ones", P), ("ln_eps", 1), ("gn_eps", 1), ("rms_eps", 1))
CR = columns(("strict", P), ("incl", P), *[(f"level{k}", P) for k in range(6)], ("reset", T))
CB = columns(("flip", P), ("causal", T), ("cos", T), ("sin", T), ("rot", P), ("twice0", P), ("twice1", P), ("cmp_mask", QT * P),
             ("cmp_valid", QT), ("onehot", BIAS_LEN))
VC = columns(("ada_b", 96), ("ln_g", 32), ("ln_b", 32), ("mu", 48), ("pair", 56), ("ffn1", KT),
             ("mix", KT), ("ffn2", KT), ("ple_gate", KT), ("ple", KT), ("out_norm", KT), ("kv_norm", 1),
             ("q_nsa", 1), ("k_cmp", 1), ("k_slc", 1), ("k_win", 1), ("q_fox", 1), ("k_fox", 1),
             ("b_forget", 1), ("pos_k", CMP_L // 2), ("pos_v", CMP_L // 2))


class Steps:

    def __init__(self, sem, names):
        self.sem, self.names, self.next = sem, list(names), 0
        self.index = {n: k + 1 for k, n in enumerate(self.names)}
        assert len(self.index) == len(self.names)

    def enter(self, eng, less=0):
        eng.sem_inc(self.sem, len(self.names) - less)

    def step(self, name):
        assert self.names[self.next % len(self.names)] == name, (self.names[self.next % len(self.names)], name)
        self.next += 1
        return self.sem, 1

    def __call__(self, name, turn=0, before=0):
        return self.sem, turn * len(self.names) + (len(self.names) * (1 - before) + self.index[name])


class Units:

    def __init__(self, sem):
        self.sem = sem

    def step(self):
        return self.sem, 1

    def unit(self, turn, s, u):
        return self.sem, turn * 4 + (2 * s + u + 1)

    def __call__(self, s, turn, before=0):
        return self.sem, turn * 4 + (2 * s + 2 - 4 * before)


def build(nc, d):
    ctx = ExitStack()
    with ctx:
        def sem(name):
            return ctx.enter_context(nc.semaphore(name))

        def keep(name, shape, scope=ctx, dtype=F32):
            return scope.enter_context(nc.sbuf_tensor(name, shape, dtype))

        def steps(name, names):
            return Steps(sem(name), names)

        waited = sem("waited")

        def reached(who, name, turn=0):
            return who(name, turn)

        def alone(eng):
            eng.sem_inc(waited, 1)

        ca = keep("const_all", [P, CA["all"][1]])
        vec = keep("vectors", [P, VC["all"][1]])
        mods = keep("modulation", [P, 96])
        x = keep("residual", [P, KT, T])
        slot = [keep(f"weights{s}", [P, SLOTS[s]]) for s in range(2)]
        ps = ctx.enter_context(nc.psum_tensor("psum", [P, 8, T], F32))

        def const(name, table=ca, where=CA):
            a, n = where[name]
            return table[:, a:a + n]

        ident, blockones, ones = const("ident"), const("blockones"), const("ones")

        def vcol(name, k=0):
            a = VC[name][0] + k
            return vec[:, a:a + 1]

        def mod(layer, part, j):
            a = layer * 48 + part * 8 + j
            return mods[:, a:a + 1]
        SH1, SC1, GT1, SH2, SC2, GT2 = range(6)

        filled = [sem(f"slot{s}_filled") for s in range(2)]
        planned = [0, 0]
        last_use = [None, None]

        class Loads:

            def __init__(self, s, n, who, name):
                self.s, self.base, self.who, self.name = s, planned[s], who, name
                self.before = last_use[s]
                planned[s] += n
                last_use[s] = (who, name, n - 1)

                self.arrival = filled[s], 16

            def slot(self, src):
                return slot[self.s][:, 0:src.shape[-1]]

            def vacated(self, k=None):
                return reached(*self.before) if k is None else self.who(self.name, k, 1)

            def arrived(self, k=0):
                return filled[self.s], k * 16 + 16 * (self.base + 1)

        def wtile(s, k, rows=P, width=P, at=0):
            return slot[s][0:rows, at + k * width:at + (k + 1) * width]

        def row(name, k):
            return d[name][bass.ds(k, 1), :, :].rearrange("a p n -> (a p) n")

        def mm(out, lhsT, rhs, start=True, stop=True):
            return nc.tensor.matmul(out, lhsT, rhs, start=start, stop=stop)

        def column(t, k):
            return t[:, bass.ds(k, 1)]

        def tile_of(t, k):
            return t[:, bass.ds(k, 1), :].rearrange("p a n -> p (a n)")

        programs = {"sp": [], "pe": [], "act": [], "dve": [], "pool": []}

        def phase(**engines):
            for name, program in engines.items():
                programs[name].append(program)

        tables_in = sem("tables_in")
        x_in = sem("x_in")
        modulated = sem("modulated")
        once_in = sem("loaded_once")
        att_in = sem("attention_constants_in")

        ADA_FIRST, ADA_TURN = 2 * KT, (12 - 2) * KT // (D // P)
        ada_at = [(0, 0), (0, D), (1, 0), (1, D)]
        cond = slot[1][:, 2 * D:3 * D]
        inner = keep("modulation_inner", [P, ADA_FIRST])

        def ada_tile(n):
            s, at = ada_at[n]
            return slot[s][:, at:at + D]

        def inner_product(n, j):
            return nc.vector.tensor_tensor_reduce(ada_tile(n), ada_tile(n), cond, scale=1.0, scalar=0.0, op0=ALU.mult,
                                                  op1=ALU.add, accum_out=inner[:, j:j + 1])

        def modulation():
            n = len(ada_at)
            act_done = steps("mod_act", ["cond"])
            dve_done = steps("mod_dve", [f"inner{j}" for j in range(ADA_FIRST)] + ["biased"])
            cond_in = sem("cond_in")
            arrived = [sem(f"ada{j}_in") for j in range(n)]
            last_use[0], last_use[1] = [(dve_done, f"inner{ADA_FIRST - j}", 0) for j in (3, 1)]

            def sp(sp):
                sp.dma_start(cond, d["c_rows"][:, :]).then_inc(cond_in, 16)
                for j in range(ADA_FIRST):
                    if j >= n:
                        sp.wait_ge(*dve_done(f"inner{j - n}"))
                    sp.dma_start(ada_tile(j % n), d["ada"][j, :, :]).then_inc(arrived[j % n], 16)

            def act(act):
                act_done.enter(act)
                act.dma_start(vec[:, :], d["vectors"][:, :]).then_inc(tables_in, 16)
                act.dma_start(ca[:, :], d["const_all"][:, :]).then_inc(tables_in, 16)
                act.dma_start(x[:, :, :], d["x"][:, :, :]).then_inc(x_in, 16)
                act.wait_ge(cond_in, 16)
                nc.scalar.activation(cond, cond, ACT.Silu).then_inc(*act_done.step("cond"))

            def dve(dve):
                dve_done.enter(dve)
                dve.wait_ge(*act_done("cond"))
                for j in range(ADA_FIRST):
                    dve.wait_ge(arrived[j % n], j // n * 16 + 16)
                    inner_product(j % n, j).then_inc(*dve_done.step(f"inner{j}"))
                dve.wait_ge(*dve_done(f"inner{ADA_FIRST - 1}"))
                dve.wait_ge(tables_in, 32)
                a = VC["ada_b"][0]
                nc.vector.tensor_tensor(mods[:, 0:ADA_FIRST], inner[:, :], vec[:, a:a + ADA_FIRST], ALU.add).then_inc(
                    *dve_done.step("biased"))
                dve.wait_ge(*dve_done("biased"))
                nc.vector.tensor_scalar(mods[:, KT:2 * KT], mods[:, KT:2 * KT], 1.0, None, ALU.add).then_inc(modulated, 1)

            phase(sp=sp, act=act, dve=dve)
            return modulated, 1

        MIX = ["r", "k", "v", "w", "a", "g"]

        def time_mix_inputs(scope, hin, mods_ready):
            h = hin[:, :, 1:T + 1]
            xs = {m: keep(f"mixed_{m}", [P, KT, T], scope) for m in "rkv"}
            lora = {m: keep(f"lora_{m}", [P, T], scope) for m in ("w", "a", "g0", "g1")}
            pe_done = steps("mix_pe", [f"lora{j}" for j in range(KT)])
            act_done = steps("mix_act", [f"hin{j}" for j in range(KT)] + ["w", "a", "g0", "g1"])
            dve_done = steps("mix_dve", [f"{m}{j}" for j in range(KT) for m in "wag"] + [f"{m}{j}" for m in "rkv" for j in range(KT)])
            pool_done = steps("mix_pool", ["zero"] + [f"xx{j}" for j in range(KT)])
            zeroed = sem("gate_rows_zeroed")
            with ExitStack() as own:
                xx = keep("token_shift", [P, KT, T], own)
                tmp = keep("mixed_low_rank", [P, 3, 2, T], own)
                first = keep("lora_first", [P, KT * 288], own)

            def sp(sp):
                sp.dma_start(first[:, :], d["lora1"][0, :, :]).then_inc(once_in, 16)

            def act(act):
                act_done.enter(act)
                act.wait_ge(x_in, 16)
                act.wait_ge(*mods_ready)
                for j in range(KT):
                    nc.scalar.activation(h[:, j, :], x[:, j, :], ACT.Identity, bias=mod(0, SH1, j),
                                                    scale=mod(0, SC1, j)).then_inc(*act_done.step(f"hin{j}"))
                act.wait_ge(*pe_done(f"lora{KT - 1}"))
                nc.scalar.activation(lora["w"][0:64, :], ps[0:64, 0, :], ACT.Tanh).then_inc(*act_done.step("w"))
                nc.scalar.activation(lora["a"][0:64, :], ps[0:64, 1, :], ACT.Copy).then_inc(*act_done.step("a"))
                nc.scalar.activation(lora["g0"][:, :], ps[:, 2, :], ACT.Sigmoid).then_inc(*act_done.step("g0"))
                act.wait_ge(zeroed, 1)
                nc.scalar.activation(lora["g1"][0:32, :], ps[0:32, 3, :], ACT.Sigmoid).then_inc(*act_done.step("g1"))

            def pool(pool):
                pool_done.enter(pool)
                nc.gpsimd.memset(lora["g1"][:, :], 0.0).then_inc(zeroed, 1)
                nc.gpsimd.memset(hin[:, :, 0:1], 0.0).then_inc(*pool_done.step("zero"))
                pool.wait_ge(*pool_done("zero"))
                for j in range(KT):
                    pool.wait_ge(*act_done(f"hin{j}"))
                    nc.gpsimd.tensor_tensor(xx[:, j, :], hin[:, j, 0:T], h[:, j, :], ALU.subtract).then_inc(*pool_done.step(f"xx{j}"))

            def mix(m, j, out):
                nc.vector.scalar_tensor_tensor(out, xx[:, j, :], vcol("mu", MIX.index(m) * KT + j), h[:, j, :],
                                               ALU.mult, ALU.add).then_inc(*dve_done.step(f"{m}{j}"))

            def dve(dve):
                dve_done.enter(dve)
                for j in range(KT):
                    dve.wait_ge(*act_done(f"hin{j}"))
                    dve.wait_ge(*pool_done(f"xx{j}"))
                    if j >= 2:
                        dve.wait_ge(*pe_done(f"lora{j - 2}"))
                    for n, m in enumerate("wag"):
                        mix(m, j, tmp[:, n, j % 2, :])
                for m in "rkv":
                    for j in range(KT):
                        mix(m, j, xs[m][:, j, :])

            def pe(pe):
                pe_done.enter(pe)
                pe.wait_ge(once_in, 16)
                for j in range(KT):
                    w = first[:, j * 288:(j + 1) * 288]
                    for n, (bank, a, b) in enumerate([(0, 0, 64), (1, 64, 128), (2, 128, 256), (3, 256, 288)]):
                        m = min(n, 2)
                        if n < 3:
                            pe.wait_ge(*dve_done(f"{MIX[3 + m]}{j}"))
                        last = mm(ps[0:b - a, bank, :], w[:, a:b], tmp[:, m, j % 2, :], j == 0, j == KT - 1)
                    last.then_inc(*pe_done.step(f"lora{j}"))

            phase(sp=sp, act=act, pe=pe, dve=dve, pool=pool)
            return xs, lora, pe_done, act_done, dve_done

        def recurrence(scope, h, xs, lora, mix_pe, mix_act, mix_dve):
            pairs = {n: keep(n + "_pairs", [P, NCH, P], scope) for n in ("a", "b", "k", "r", "Nab", "Nak", "XT")}
            cr = keep("const_recurrence", [P, CR["all"][1]], scope)
            N = D // P
            yout = h
            pv = keep("pair_vectors", [P, 7], scope)
            W0, A0, KK, KA, RK, LG, LB = range(7)
            flat = {n: keep(n, [P, T], scope) for n in
                    ("r", "v", "g", "sig", "a", "kk0", "sq", "nrm", "kk", "k", "rkr", "bv", "cum", "Wt", "Winv", "Wprev")}
            both = x[:, 0:4, :].rearrange("p a (c n) -> p (a c) n", n=2 * P)
            pairs["b_tok"], pairs["Nrb"] = both[:, :, 0:P], both[:, :, P:2 * P]
            for q, n in ((4, "k_tok"), (6, "Nrk")):
                pairs[n] = x[:, q:q + 2, :].rearrange("p a (c n) -> p (a c) n", n=P)
            before_X = keep("before_X", [P, NCH, P + CH], scope)
            after_X = keep("after_X", [P, NCH, P + CH], scope)
            M, R = pairs["Nab"], pairs["r"]
            pairs["X"], pairs["Y"] = pairs["k"], pairs["b"]
            join = [keep(f"join{n}", [P, NCH, P], scope) for n in range(2)]
            v_tok = keep("v_tok", [P, NCH, CH], scope)
            St = keep("state", [P, 2, CH], scope)

            def by_chunk(t, n=CH):
                return t[:, :].rearrange("p (c n) -> p c n", n=n)
            cump, kka, yg, ysum = flat["sq"], flat["nrm"], flat["sig"], flat["kk0"]
            yc, ysq, yn = (by_chunk(flat[n]) for n in ("kk0", "sig", "a"))
            st = keep("group_norm", [P, 4, NCH], scope)
            MEAN, SUM, RSTD, STD = range(4)
            fl = {n: flat[n][:, :] for n in flat}

            in_pe = steps("inputs_pe", ["r", "k", "w", "a", "kk sum", "v", "b tok", "k tok", "bonus sum", "g"])
            in_act = steps("inputs_act", ["r", "k", "kk sq", "sig", "a", "kk norm", "Winv", "Wprev", "v", "Wt", "b tok"])
            in_dve = steps("inputs_dve", ["pv", "kk0", "cum", "cump", "ka", "nrm max", "nrm rec", "kk", "kka", "k", "rkr", "k tok"])
            in_pool = steps("inputs_pool", ["a0", "a1", "b0", "b1", "k0", "k1", "r0", "r1"])
            PE = (["v tok", "Nab", "Nrb", "Nak", "Nrk", "X0"]
                  + [n for k in range(1, 6) for n in ([f"Y{k}", f"X{k}", f"XT{k}"] if k < 5 else [f"Y{k}", f"XT{k}"])]
                  + ["F0", "F1", "MR0", "S0", "y0", "MR1"] + [f"{n}{c}" for c in range(1, NCH) for n in ["S"] * (c < NCH - 1) + ["y"]]
                  + ["y fm"])
            PE.insert(PE.index("Y1") + 1, "a tok")
            PE.insert(PE.index("Y2") + 1, "Nak v")
            AC = ["v tok", "g", "X0", "Y1", "a tok", "Y2", "Nak v", "Y3", "Y4", "Y5", "F0", "F1", "y sq", "y std", "y gn"]
            DV = (["pv", "bonus", "Nab", "Nrb", "Nak", "Nrk"]
                  + [n for k in range(1, 6) for n in ([f"X{k}", f"XT{k}"] if k < 5 else [f"XT{k}"])]
                  + ["M0", "S0", "R0", "S1", "M1", "S2", "R1"] + [f"S{c}" for c in range(3, NCH - 1)]
                  + ["y sum", "y mean", "y cen", "y var", "y rstd", "yn"])
            PO = ["A0", "XT0"] + [f"A{k}" for k in range(1, 6)] + ["y bonus", "y out"]
            pe_done, act_done, dve_done, pool_done = (steps(f"rec_{n}", q) for n, q in
                                          (("pe", PE), ("act", AC), ("dve", DV), ("pool", PO)))
            ada_done = steps("rec_ada", [f"ada{j}" for j in range(ADA_TURN)] + ["ada bias"])
            loads = Loads(0, N, in_pe, "g")
            zeroed = sem("pairs_zeroed")
            ada_in = [sem(f"ada_pair{n}_in") for n in range(2)]
            last_use[1] = (ada_done, f"ada{ADA_TURN - 1}", N - 1)

            def two_banks(b):
                return ps[:, b:b + 2, :].rearrange("p b (c n) -> p (b c) n", n=P)

            def two_a_bank(b, n):
                return ps[:, b:b + 4, 0:2 * n].rearrange("p b (c n) -> p b c n", n=n)

            def by_bank(t):
                return t[:, :, :].rearrange("p (b c) n -> p b c n", c=2)

            def bank(b):
                return ps[:, b, :].rearrange("p (c n) -> p c n", n=CH)

            def spread(mask):
                return mask.unsqueeze(1).to_broadcast([P, NCH, P])

            def cmask(name):
                return const(name, cr, CR)

            def half(t, hh):
                return t[hh * HD:(hh + 1) * HD, :, hh * CH:(hh + 1) * CH]

            def rows(t, hh):
                return by_chunk(t)[hh * HD:(hh + 1) * HD, :, :]

            def sp(sp):
                sp.wait_ge(*loads.vacated())
                sp.dma_start(loads.slot(row("rwkv", 0)), row("rwkv", 0)).then_inc(*loads.arrival)
                sp.wait_ge(*mix_pe(f"lora{KT - 1}"))
                sp.dma_start(cr[:, :], d["const_recurrence"][:, :]).then_inc(once_in, 16)

                def modulations(i):
                    for j in range(ADA_TURN):
                        if j < 2:
                            sp.wait_ge(*ada_done(f"ada{ADA_TURN - 2 + j}", i, 1))
                        else:
                            sp.wait_ge(*ada_done(f"ada{j - 2}", i))
                        sp.dma_start(ada_tile(2 + j % 2), row("ada", i * ADA_TURN + (ADA_FIRST + j))).then_inc(ada_in[j % 2], 16)
                with sp.Fori(0, N - 1) as i:
                    sp.wait_ge(*loads.vacated(i + 1))
                    sp.dma_start(loads.slot(row("rwkv", i + 1)), row("rwkv", i + 1)).then_inc(*loads.arrival)
                    modulations(i)
                modulations(N - 1)

            def pool(pool):
                in_pool.enter(pool)
                pool_done.enter(pool)
                pool.wait_ge(*mix_dve(f"v{KT - 1}"))
                pool.wait_ge(*mix_pe(f"lora{KT - 1}"))
                for n in ("a", "b", "k", "r"):
                    nc.gpsimd.memset(pairs[n][:, :, :], 0.0).then_inc(zeroed, 1)
                pool.wait_ge(once_in, 32)
                pool.wait_ge(tables_in, 32)
                pool.wait_ge(zeroed, 4)

                def inputs(p):
                    if not isinstance(p, int):
                        pool.wait_ge(*pool_done("A5", p - 1))
                    pool.wait_ge(*in_dve("kk", p))
                    pool.wait_ge(*in_act("Wprev", p))
                    alone(pool)
                    for hh in range(2):
                        nc.gpsimd.tensor_tensor(half(pairs["a"], hh), rows(flat["kk"], hh), rows(flat["Wprev"], hh),
                                                ALU.mult).then_inc(*in_pool.step(f"a{hh}"))
                    pool.wait_ge(*in_dve("kka", p))
                    pool.wait_ge(*pe_done("XT5", p, 1))
                    alone(pool)
                    for hh in range(2):
                        nc.gpsimd.tensor_tensor(half(pairs["b"], hh), rows(kka, hh), rows(flat["Winv"], hh),
                                                ALU.mult).then_inc(*in_pool.step(f"b{hh}"))
                    pool.wait_ge(*in_dve("k", p))
                    alone(pool)
                    for hh in range(2):
                        nc.gpsimd.tensor_tensor(half(pairs["k"], hh), rows(flat["k"], hh), rows(flat["Winv"], hh),
                                                ALU.mult).then_inc(*in_pool.step(f"k{hh}"))
                    pool.wait_ge(*in_act("Wt", p))
                    pool.wait_ge(*in_act("r", p))
                    pool.wait_ge(*pe_done(f"y{NCH - 1}", p, 1))
                    alone(pool)
                    for hh in range(2):
                        nc.gpsimd.tensor_tensor(half(pairs["r"], hh), rows(flat["r"], hh), rows(flat["Wt"], hh),
                                                ALU.mult).then_inc(*in_pool.step(f"r{hh}"))

                def turn(i, more):
                    pool.wait_ge(*dve_done("Nab", i))
                    pool.wait_ge(*in_pool("r1", i))
                    alone(pool)
                    nc.gpsimd.tensor_tensor(join[0][:, :, :], pairs["Nab"][:, :, :], spread(cmask("level0")),
                                                        ALU.mult).then_inc(*pool_done.step("A0"))
                    pool.wait_ge(*pool_done("A0", i))
                    alone(pool)
                    nc.gpsimd.tensor_tensor(pairs["XT"][:, :, :], join[0][:, :, :], spread(ident), ALU.add).then_inc(*pool_done.step("XT0"))
                    pool.wait_ge(*pool_done("XT0", i))
                    alone(pool)
                    for k in range(1, 6):
                        if k >= 3:
                            pool.wait_ge(*pe_done(f"Y{k - 2}", i))
                            alone(pool)
                        nc.gpsimd.tensor_tensor(join[k % 2][:, :, :], pairs["Nab"][:, :, :],
                                                            spread(cmask(f"level{k}")), ALU.mult).then_inc(*pool_done.step(f"A{k}"))
                    if more:
                        inputs(i + 1)
                        pool.wait_ge(*in_pool("r1", i + 1))
                    pool.wait_ge(*act_done("y gn", i))
                    pool.wait_ge(*dve_done("bonus", i))
                    alone(pool)
                    nc.gpsimd.tensor_tensor(ysum[:, :], yg[:, :], fl["bv"], ALU.add).then_inc(*pool_done.step("y bonus"))
                    pool.wait_ge(*pool_done("y bonus", i))
                    alone(pool)
                    nc.gpsimd.tensor_tensor(tile_of(yout, i), ysum[:, :], fl["g"], ALU.mult).then_inc(*pool_done.step("y out"))
                inputs(0)
                with pool.Fori(0, N - 1) as i:
                    turn(i, True)
                turn(N - 1, False)

            def act(act):
                in_act.enter(act)
                act_done.enter(act)
                act.wait_ge(tables_in, 32)
                copy = nc.scalar.activation

                def r_input(p):
                    act.wait_ge(*in_pe("r", p))
                    act.wait_ge(*in_dve("rkr", p, 1))
                    act.wait_ge(*in_pool("r1", p, 1))
                    copy(fl["r"], ps[:, 1, :], ACT.Copy).then_inc(*in_act.step("r"))

                def k_input(p):
                    act.wait_ge(*in_pe("k", p))
                    act.wait_ge(*in_pool("k1", p, 1))
                    copy(fl["k"], ps[:, 0, :], ACT.Copy).then_inc(*in_act.step("k"))
                    act.wait_ge(*in_dve("kk0", p))
                    copy(fl["sq"], fl["kk0"], ACT.Square).then_inc(*in_act.step("kk sq"))

                def decay_and_rate(p):
                    act.wait_ge(*in_pe("w", p))
                    if not isinstance(p, int):
                        act.wait_ge(*pool_done("y bonus", p - 1, 1))
                    copy(fl["sig"], ps[:, 1, :], ACT.Sigmoid, bias=pv[:, W0:W0 + 1]).then_inc(*in_act.step("sig"))
                    act.wait_ge(*in_pe("a", p))
                    copy(fl["a"], ps[:, 0, :], ACT.Sigmoid, bias=pv[:, A0:A0 + 1]).then_inc(*in_act.step("a"))

                def kk_norm(p):
                    act.wait_ge(*in_pe("kk sum", p))
                    act.wait_ge(*in_pool("b1", p, 1))
                    copy(fl["nrm"], ps[:, 1, :], ACT.Sqrt).then_inc(*in_act.step("kk norm"))

                def decays(p):
                    act.wait_ge(*in_dve("cump", p))
                    act.wait_ge(*in_pool("k1", p, 1))
                    copy(fl["Winv"], fl["cum"], ACT.Exp, scale=DECAY).then_inc(*in_act.step("Winv"))
                    copy(fl["Wprev"], cump[:, :], ACT.Exp, scale=-DECAY).then_inc(*in_act.step("Wprev"))

                def v_input(p):
                    act.wait_ge(*in_pe("v", p))
                    copy(fl["v"], ps[:, 4, :], ACT.Copy).then_inc(*in_act.step("v"))

                def chunk_decay(p):
                    act.wait_ge(*dve_done(f"S{NCH - 2}", p, 1))
                    copy(fl["Wt"], fl["cum"], ACT.Exp, scale=-DECAY).then_inc(*in_act.step("Wt"))

                def b_by_tokens(p):
                    act.wait_ge(*in_pe("b tok", p))
                    copy(pairs["b_tok"], two_banks(2), ACT.Copy).then_inc(*in_act.step("b tok"))

                def turn(i, more):
                    act.wait_ge(*pe_done("v tok", i))
                    copy(v_tok[:, :, :], bank(1), ACT.Copy).then_inc(*act_done.step("v tok"))
                    act.wait_ge(*in_pe("g", i))
                    act.wait_ge(*pool_done("y out", i, 1))
                    copy(fl["g"], ps[:, 5, :], ACT.Copy).then_inc(*act_done.step("g"))
                    act.wait_ge(*pe_done("X0", i))
                    copy(pairs["X"][:, :, :], two_banks(6), ACT.Copy).then_inc(*act_done.step("X0"))
                    for k in range(1, 6):
                        act.wait_ge(*pe_done(f"Y{k}", i))
                        copy(pairs["Y"][:, :, :], two_banks(2), ACT.Copy).then_inc(*act_done.step(f"Y{k}"))
                        if k == 1:
                            act.wait_ge(*pe_done("a tok", i))
                            copy(before_X[:, :, 0:P], two_banks(0), ACT.Copy).then_inc(*act_done.step("a tok"))
                        if k == 2:
                            act.wait_ge(*pe_done("Nak v", i))
                            copy(before_X[:, :, P:P + CH], bank(0), ACT.Copy).then_inc(*act_done.step("Nak v"))
                        if more and k == 2:
                            r_input(i + 1)
                        if more and k == 3:
                            k_input(i + 1)
                        if more and k == 4:
                            decay_and_rate(i + 1)
                            kk_norm(i + 1)
                        if more and k == 5:
                            decays(i + 1)
                            v_input(i + 1)
                    for h in range(2):
                        act.wait_ge(*pe_done(f"F{h}", i))
                        b = slice(2 * h, 2 * h + 2)
                        copy(by_bank(after_X)[:, b], two_a_bank(0, P + CH)[:, b], ACT.Copy).then_inc(*act_done.step(f"F{h}"))
                    if more:
                        chunk_decay(i + 1)
                    act.wait_ge(*dve_done("y cen", i))
                    copy(ysq, yc, ACT.Square).then_inc(*act_done.step("y sq"))
                    act.wait_ge(*dve_done("y var", i))
                    copy(st[:, STD, :], st[:, SUM, :], ACT.Sqrt, bias=const("gn_eps"), scale=1.0 / HD).then_inc(*act_done.step("y std"))
                    if more:
                        b_by_tokens(i + 1)
                    act.wait_ge(*pe_done("y fm", i))
                    copy(yg[:, :], ps[:, 4, :], ACT.Identity, bias=pv[:, LB:LB + 1], scale=pv[:, LG:LG + 1]).then_inc(*act_done.step("y gn"))
                for inputs in (r_input, k_input, decay_and_rate, kk_norm, decays, v_input, chunk_decay, b_by_tokens):
                    inputs(0)
                with act.Fori(0, N - 1) as i:
                    turn(i, True)
                turn(N - 1, False)

            def dve(dve):
                in_dve.enter(dve)
                dve_done.enter(dve)
                ada_done.enter(dve)
                dve.wait_ge(once_in, 32)
                dve.wait_ge(tables_in, 32)
                dve.wait_ge(zeroed, 4)
                tt, ts, stt = nc.vector.tensor_tensor, nc.vector.tensor_scalar, nc.vector.scalar_tensor_tensor

                def modulations(i, tiles):
                    for j in tiles:
                        dve.wait_ge(ada_in[j % 2], i * (ADA_TURN // 2 * 16) + (j // 2 * 16 + 16))
                        if j == 0:
                            dve.wait_ge(*ada_done("ada bias", i, 1))
                        alone(dve)
                        inner_product(2 + j % 2, j).then_inc(*ada_done.step(f"ada{j}"))
                    if j == ADA_TURN - 1:
                        dve.wait_ge(*ada_done(f"ada{ADA_TURN - 1}", i))
                        alone(dve)
                        tt(mods[:, bass.ds(i * ADA_TURN + ADA_FIRST, ADA_TURN)], inner[:, 0:ADA_TURN],
                           vec[:, bass.ds(i * ADA_TURN + (ADA_FIRST + VC["ada_b"][0]), ADA_TURN)], ALU.add).then_inc(
                            *ada_done.step("ada bias"))

                def vectors_input(p):
                    dve.wait_ge(*in_act("a", p, 1))
                    dve.wait_ge(*in_dve("rkr", p, 1))
                    alone(dve)
                    nc.vector.tensor_copy(pv[:, 0:LG], vec[:, bass.ds(p * 7 + VC["pair"][0], LG)]).then_inc(*in_dve.step("pv"))

                def kk_input(p):
                    dve.wait_ge(*in_act("k", p))
                    dve.wait_ge(*in_dve("pv", p))
                    if not isinstance(p, int):
                        dve.wait_ge(*pool_done("y out", p - 1, 1))
                    ts(fl["kk0"], fl["k"], pv[:, KK:KK + 1], None, ALU.mult).then_inc(*in_dve.step("kk0"))

                def decay_input(p):
                    dve.wait_ge(*in_act("sig", p))
                    dve.wait_ge(*in_act("Wt", p, 1))
                    nc.vector.tensor_tensor_scan(fl["cum"], cmask("reset"), fl["sig"], 0.0, ALU.mult, ALU.add).then_inc(*in_dve.step("cum"))
                    dve.wait_ge(*in_dve("cum", p))
                    dve.wait_ge(*in_pe("kk sum", p))
                    tt(cump[:, :], fl["cum"], fl["sig"], ALU.subtract).then_inc(*in_dve.step("cump"))
                    dve.wait_ge(*in_act("a", p))
                    dve.wait_ge(*in_pe("bonus sum", p, 1))
                    ts(fl["rkr"], fl["a"], 1.0, pv[:, KA:KA + 1], ALU.subtract, ALU.mult).then_inc(*in_dve.step("ka"))

                def norm_input(p):
                    dve.wait_ge(*in_act("kk norm", p))
                    ts(fl["nrm"], fl["nrm"], 1e-12, None, ALU.max).then_inc(*in_dve.step("nrm max"))
                    dve.wait_ge(*in_dve("nrm max", p))
                    nc.vector.reciprocal(fl["nrm"], fl["nrm"]).then_inc(*in_dve.step("nrm rec"))

                def kk_and_rate_input(p):
                    dve.wait_ge(*in_dve("nrm rec", p))
                    dve.wait_ge(*in_pool("a1", p, 1))
                    stt(fl["kk"], fl["kk0"], -1.0, fl["nrm"], ALU.mult, ALU.mult).then_inc(*in_dve.step("kk"))
                    dve.wait_ge(*in_dve("kk", p))
                    stt(kka[:, :], fl["kk"], -1.0, fl["a"], ALU.mult, ALU.mult).then_inc(*in_dve.step("kka"))

                def key_input(p):
                    dve.wait_ge(*in_dve("ka", p))
                    stt(fl["k"], fl["rkr"], 1.0, fl["k"], ALU.add, ALU.mult).then_inc(*in_dve.step("k"))

                def k_by_tokens(p):
                    dve.wait_ge(*in_pe("k tok", p))
                    nc.vector.tensor_copy(pairs["k_tok"], two_banks(6)).then_inc(*in_dve.step("k tok"))

                def bonus_input(p):
                    dve.wait_ge(*in_dve("k", p))
                    dve.wait_ge(*in_act("r", p))
                    stt(fl["rkr"], fl["r"], pv[:, RK:RK + 1], fl["k"], ALU.mult, ALU.mult).then_inc(*in_dve.step("rkr"))

                def turn(i, more):
                    dve.wait_ge(*act_done("y gn", i, 1))
                    alone(dve)
                    nc.vector.tensor_copy(pv[:, LG:LB + 1], vec[:, bass.ds(i * 7 + (VC["pair"][0] + LG), 2)]).then_inc(*dve_done.step("pv"))
                    if more:
                        vectors_input(i + 1)
                    dve.wait_ge(*in_pe("bonus sum", i))
                    dve.wait_ge(*in_act("v", i))
                    dve.wait_ge(*pool_done("y bonus", i, 1))
                    tt(fl["bv"], ps[:, 0, :], fl["v"], ALU.mult).then_inc(*dve_done.step("bonus"))
                    for n, b, mask in (("Nab", 6, "strict"), ("Nrb", 2, "incl"), ("Nak", 4, "strict"), ("Nrk", 0, "incl")):
                        dve.wait_ge(*pe_done(n, i))
                        tt(pairs[n][:, :, :], two_banks(b), spread(cmask(mask)), ALU.mult).then_inc(*dve_done.step(n))
                    for k in range(1, 6):
                        if k < 5:
                            dve.wait_ge(*pe_done(f"X{k}", i))
                            if k == 1:
                                dve.wait_ge(*act_done("X0", i))
                            tt(pairs["X"][:, :, :], pairs["X"][:, :, :], two_banks(4), ALU.add).then_inc(*dve_done.step(f"X{k}"))
                        dve.wait_ge(*pe_done(f"XT{k}", i))
                        tt(pairs["XT"][:, :, :], pairs["XT"][:, :, :], two_banks(6), ALU.add).then_inc(*dve_done.step(f"XT{k}"))
                        if k == 1:
                            modulations(i, range(0, 2))
                        if k == 2:
                            modulations(i, range(2, 4))
                        if k == 3:
                            if more:
                                kk_input(i + 1)
                            modulations(i, range(4, 6))
                        if k == 4:
                            modulations(i, range(6, 8))
                            if more:
                                decay_input(i + 1)
                    if more:
                        norm_input(i + 1)

                    def maps(h, which):
                        c = slice(max(1, 4 * h), 4 * h + 4)
                        made = ps[:, 4:8, :].rearrange("p b (c n) -> p (b c) n", n=2 * P)[:, c, :]
                        dve.wait_ge(*pe_done(f"MR{h}", i))
                        if which == "M":
                            tt(M[:, c, :], made[:, :, 0:P], ident.unsqueeze(1).to_broadcast([P, c.stop - c.start, P]),
                               ALU.add).then_inc(*dve_done.step(f"M{h}"))
                        else:
                            tt(R[:, c, :], made[:, :, P:2 * P], R[:, c, :], ALU.add).then_inc(*dve_done.step(f"R{h}"))

                    def state(c):
                        dve.wait_ge(*pe_done(f"S{c}", i))
                        end = c * CH + CH - 1
                        ts(St[:, c % 2, :], bank(2 * (c % 2))[:, c, :], flat["Wt"][:, end:end + 1], None, ALU.mult).then_inc(
                            *dve_done.step(f"S{c}"))
                    maps(0, "M")
                    state(0)
                    maps(0, "R")
                    if more:
                        kk_and_rate_input(i + 1)
                    state(1)
                    maps(1, "M")
                    state(2)
                    maps(1, "R")
                    for c in range(3, NCH - 1):
                        state(c)
                        if more and c == 3:
                            key_input(i + 1)
                        if more and c == 4:
                            bonus_input(i + 1)
                    dve.wait_ge(*pe_done(f"y{NCH - 1}", i))
                    yps = bank(1)
                    nc.vector.tensor_reduce(st[:, MEAN, :], yps, AX.X, ALU.add).then_inc(*dve_done.step("y sum"))
                    dve.wait_ge(*dve_done("y sum", i))
                    ts(st[:, MEAN, :], st[:, MEAN, :], 1.0 / HD, None, ALU.mult).then_inc(*dve_done.step("y mean"))
                    dve.wait_ge(*dve_done("y mean", i))
                    tt(yc, yps, st[:, MEAN, :].unsqueeze(2).to_broadcast([P, NCH, CH]), ALU.subtract).then_inc(*dve_done.step("y cen"))
                    dve.wait_ge(*act_done("y sq", i))
                    nc.vector.tensor_reduce(st[:, SUM, :], ysq, AX.X, ALU.add).then_inc(*dve_done.step("y var"))
                    dve.wait_ge(*act_done("y std", i))
                    nc.vector.reciprocal(st[:, RSTD, :], st[:, STD, :]).then_inc(*dve_done.step("y rstd"))
                    dve.wait_ge(*dve_done("y rstd", i))
                    tt(yn, yc, st[:, RSTD, :].unsqueeze(2).to_broadcast([P, NCH, CH]), ALU.mult).then_inc(*dve_done.step("yn"))
                    if more:
                        k_by_tokens(i + 1)
                    modulations(i, range(8, ADA_TURN))
                for inputs in (vectors_input, kk_input, decay_input, norm_input, kk_and_rate_input, key_input, bonus_input, k_by_tokens):
                    inputs(0)
                with dve.Fori(0, N - 1) as i:
                    turn(i, True)
                turn(N - 1, False)
                dve.wait_ge(*ada_done("ada bias", N - 1))
                for a, b in ((2, 3), (4, 6), (7, 9), (10, 12)):
                    ts(mods[:, a * KT:b * KT], mods[:, a * KT:b * KT], 1.0, None, ALU.add).then_inc(modulated, 1)
                dve.wait_ge(modulated, 5)

            def pe(pe):
                in_pe.enter(pe)
                pe_done.enter(pe)
                def projection(m, b, tiles, first=False):
                    at = "rkv".index(m) * KT
                    for k in tiles:
                        if first:
                            pe.wait_ge(*mix_dve(f"{m}{k}"))
                        last = mm(ps[:, b, :], wtile(0, at + k), xs[m][:, k, :], k == 0, k == KT - 1)
                    if k == KT - 1:
                        last.then_inc(*in_pe.step(m))

                def decay_and_rate(p):
                    pe.wait_ge(*in_act("r", p))
                    mm(ps[:, 1, :], wtile(0, 24, HD), lora["w"][0:HD, :]).then_inc(*in_pe.step("w"))
                    pe.wait_ge(*in_act("k", p))
                    mm(ps[:, 0, :], wtile(0, 25, HD), lora["a"][0:HD, :]).then_inc(*in_pe.step("a"))

                def kk_sum(p):
                    pe.wait_ge(*in_act("kk sq", p))
                    pe.wait_ge(*in_act("sig", p))
                    mm(ps[:, 1, :], blockones, fl["sq"]).then_inc(*in_pe.step("kk sum"))

                def by_tokens(p):
                    pe.wait_ge(*in_pool("b1", p))
                    pe.wait_ge(*dve_done(f"S{NCH - 2}", p, 1))
                    for c in range(NCH):
                        last = nc.tensor.transpose(two_banks(2)[:, c, :], pairs["b"][:, c, :], ident)
                    last.then_inc(*in_pe.step("b tok"))
                    pe.wait_ge(*in_pool("k1", p))
                    for c in range(NCH):
                        last = nc.tensor.transpose(two_banks(6)[:, c, :], pairs["k"][:, c, :], ident)
                    last.then_inc(*in_pe.step("k tok"))
                    pe.wait_ge(*in_dve("rkr", p))
                    mm(ps[:, 0, :], blockones, fl["rkr"]).then_inc(*in_pe.step("bonus sum"))
                    mm(ps[:, 5, :], wtile(0, 26), lora["g0"][:, :], True, False)
                    mm(ps[:, 5, :], wtile(0, 27), lora["g1"][:, :], False, True).then_inc(*in_pe.step("g"))

                def turn(i, more):
                    pe.wait_ge(*in_act("v", i))
                    pe.wait_ge(*dve_done("yn", i, 1))
                    for c in range(NCH):
                        for hh in range(2):
                            last = mm(bank(1)[hh * CH:(hh + 1) * CH, c, :], flat["v"][:, c * CH:(c + 1) * CH],
                                      ident[:, hh * HD:(hh + 1) * HD])
                    last.then_inc(*pe_done.step("v tok"))
                    for n, b, left, right in (("Nab", 6, "b", "a"), ("Nrb", 2, "b", "r"), ("Nak", 4, "k", "a"), ("Nrk", 0, "k", "r")):
                        if n == "Nab":
                            pe.wait_ge(*in_dve("k tok", i))
                        elif n == "Nrb":
                            pe.wait_ge(*in_pool("r1", i))
                            pe.wait_ge(*in_act("b tok", i))
                        elif n == "Nak":
                            pe.wait_ge(*act_done("y gn", i, 1))
                            pe.wait_ge(*act_done("g", i))
                        elif n == "Nrk":
                            pe.wait_ge(*act_done("v tok", i))
                            pe.wait_ge(*dve_done("bonus", i))
                        for c in range(NCH):
                            last = mm(two_banks(b)[:, c, :], pairs[left][:, c, :], pairs[right][:, c, :])
                        last.then_inc(*pe_done.step(n))
                    pe.wait_ge(*pool_done("XT0", i))
                    for c in range(NCH):
                        last = nc.tensor.transpose(two_banks(6)[:, c, :], pairs["XT"][:, c, :], ident)
                    last.then_inc(*pe_done.step("X0"))
                    for k in range(1, 6):
                        pe.wait_ge(*pool_done(f"A{k}", i))
                        if k == 1:
                            pe.wait_ge(*act_done("X0", i))
                            pe.wait_ge(*dve_done("Nrk", i))
                        else:
                            pe.wait_ge(*dve_done(f"XT{k - 1}", i))
                        for c in range(NCH):
                            last = mm(two_banks(2)[:, c, :], join[k % 2][:, c, :], pairs["X"][:, c, :])
                        last.then_inc(*pe_done.step(f"Y{k}"))
                        if k == 1:
                            for c in range(NCH):
                                last = nc.tensor.transpose(two_banks(0)[:, c, :], pairs["a"][:, c, :], ident)
                            last.then_inc(*pe_done.step("a tok"))
                        if k == 2:
                            pe.wait_ge(*act_done("a tok", i))
                            for c in range(NCH):
                                last = mm(bank(0)[:, c, :], pairs["Nak"][:, c, :], v_tok[:, c, :])
                            last.then_inc(*pe_done.step("Nak v"))
                        if more and k == 3:
                            pe.wait_ge(*act_done("Nak v", i))
                            projection("k", 0, range(0, 4))
                        if more and k == 4:
                            decay_and_rate(i + 1)
                        if more and k == 5:
                            projection("v", 4, range(0, 4))
                        pe.wait_ge(*act_done(f"Y{k}", i))
                        for out, b, left, right in (("X", 4, "XT", "Y"), ("XT", 6, "Y", "XT")):
                            if k == 5 and out == "X":
                                continue
                            for c in range(NCH):
                                last = mm(two_banks(b)[:, c, :], pairs[left][:, c, :], pairs[right][:, c, :])
                            last.then_inc(*pe_done.step(f"{out}{k}"))
                        if more and k == 1:
                            pe.wait_ge(*act_done("a tok", i))
                            pe.wait_ge(*loads.arrived(i + 1))
                            projection("r", 1, range(0, 4))
                        if more and k == 2:
                            projection("r", 1, range(4, KT))
                        if more and k == 3:
                            projection("k", 0, range(4, KT))
                        if more and k == 4:
                            kk_sum(i + 1)
                        if more and k == 5:
                            projection("v", 4, range(4, KT))
                    pe.wait_ge(*dve_done("XT5", i))
                    pe.wait_ge(*act_done("Nak v", i))
                    if more:
                        pe.wait_ge(*in_act("kk norm", i + 1))
                    for c in range(NCH):
                        last = mm(two_a_bank(0, P + CH)[:, c // 2, c % 2, :], pairs["XT"][:, c, :], before_X[:, c, :])
                        if c % 4 == 3:
                            last.then_inc(*pe_done.step(f"F{c // 4}"))

                    def maps(h):
                        for c in range(max(1, 4 * h), 4 * h + 4):
                            last = mm(two_a_bank(4, 2 * P)[:, c // 2, c % 2, :], after_X[:, c, 0:P], both[:, c, :])
                        last.then_inc(*pe_done.step(f"MR{h}"))

                    def chunk(c):
                        S0, Sp, yp, q = St[:, (c - 1) % 2, :], bank(2 * (c % 2))[:, c, :], bank(1)[:, c, :], after_X[:, c, P:P + CH]
                        if c < NCH - 1:
                            mm(Sp, pairs["b_tok"][:, c, :], q, True, False)
                            Send = mm(Sp, pairs["k_tok"][:, c, :], v_tok[:, c, :], False, c == 0)
                        mm(yp, pairs["Nrb"][:, c, :], q, True, False)
                        yend = mm(yp, pairs["Nrk"][:, c, :], v_tok[:, c, :], False, c == 0)
                        if c:
                            pe.wait_ge(*dve_done(f"S{c - 1}", i))
                            if c == 4:
                                pe.wait_ge(*dve_done("M1", i))
                            if c < NCH - 1:
                                Send = mm(Sp, M[:, c, :], S0, False, True)
                            if c in (1, 4):
                                pe.wait_ge(*dve_done(f"R{c // 4}", i))
                            yend = mm(yp, R[:, c, :], S0, False, True)
                        if c < NCH - 1:
                            Send.then_inc(*pe_done.step(f"S{c}"))
                        yend.then_inc(*pe_done.step(f"y{c}"))
                    pe.wait_ge(*act_done("F0", i))
                    maps(0)
                    chunk(0)
                    pe.wait_ge(*act_done("F1", i))
                    maps(1)
                    for c in range(1, NCH):
                        chunk(c)
                    if more:
                        by_tokens(i + 1)
                    pe.wait_ge(*dve_done("yn", i))
                    for c in range(NCH):
                        for hh in range(2):
                            last = mm(ps[hh * HD:(hh + 1) * HD, 4, c * CH:(c + 1) * CH], yn[:, c, :],
                                      ident[:, hh * CH:(hh + 1) * CH])
                    last.then_inc(*pe_done.step("y fm"))
                pe.wait_ge(*loads.arrived(0))
                pe.wait_ge(*mix_act("g1"))
                projection("r", 1, range(KT), True)
                projection("k", 0, range(KT), True)
                decay_and_rate(0)
                kk_sum(0)
                projection("v", 4, range(KT), True)
                by_tokens(0)
                with pe.Fori(0, N - 1) as i:
                    turn(i, True)
                turn(N - 1, False)

            phase(sp=sp, act=act, pe=pe, dve=dve, pool=pool)
            return yout, pool_done, "y out", N - 1

        tiles_total = slot[0][:, HT * P + 2 * P:HT * P + 2 * P + T]

        def total_of(factor):
            return squares_total if isinstance(factor, float) else tiles_total

        def total_names(factor):
            squares = isinstance(factor, float)
            return [n for s in range(2) for n in [f"sum{s}"] + [f"square{s}"] * squares + [f"total{s}"]]

        def total_start(dve, dve_done, factor):
            dve_done.enter(dve, 1)
            total_zero(dve_done, factor)

        def total_zero(dve_done, factor):
            nc.vector.memset(total_of(factor), 0.0).then_inc(dve_done.sem, 1)

        def total_add(dve, dve_done, factor, i, s):
            j = i * 2 + s
            dve.wait_ge(*(dve_done("total1", i, 1) if s == 0 else dve_done("total0", i)))
            dve.wait_ge(*dve_done(f"sum{s}", i))
            alone(dve)
            term = tile_of(x, j)
            if isinstance(factor, float):
                nc.vector.tensor_tensor(square[:, :], tile_of(x, j), tile_of(x, j), ALU.mult).then_inc(*dve_done.step(f"square{s}"))
                dve.wait_ge(*dve_done(f"square{s}", i))
                term = square[:, :]
            nc.vector.tensor_tensor(total_of(factor), total_of(factor), term, ALU.add).then_inc(*dve_done.step(f"total{s}"))

        def tiles_done(dve_done):
            return [(dve_done, f"sum{j % 2}", j // 2) for j in range(KT)] + [(dve_done, "total1", KT // 2 - 1)]

        def project(name, stream, sources, ready, factor, x_ready=()):
            n = KT // 2
            pe_done = steps(f"{name}_pe", ["product0", "product1"])
            dve_done = steps(f"{name}_dve", total_names(factor))
            loads = [Loads(s, n, pe_done, f"product{s}") for s in range(2)]

            def sp(sp):
                for s in range(2):
                    sp.wait_ge(*loads[s].vacated())
                with sp.Fori(0, n) as i:
                    for s in range(2):
                        sp.wait_ge(*loads[s].vacated(i))
                        sp.dma_start(loads[s].slot(row(stream, i * 2 + s)), row(stream, i * 2 + s)).then_inc(*loads[s].arrival)

            def pe(pe):
                pe_done.enter(pe)
                for r in ready:
                    pe.wait_ge(*reached(*r))
                with pe.Fori(0, n) as i:
                    for s in range(2):
                        pe.wait_ge(*loads[s].arrived(i))
                        pe.wait_ge(*dve_done(f"sum{s}", i, 1))
                        for k, src in enumerate(sources):
                            last = mm(ps[:, s, :], wtile(s, k), src, k == 0, k == len(sources) - 1)
                        last.then_inc(*pe_done.step(f"product{s}"))

            def dve(dve):
                dve_done.enter(dve, 1)
                for r in x_ready:
                    dve.wait_ge(*reached(*r))
                total_zero(dve_done, factor)
                with dve.Fori(0, n) as i:
                    for s in range(2):
                        dve.wait_ge(*pe_done(f"product{s}", i))
                        f = factor if isinstance(factor, float) else mods[:, bass.ds(i * 2 + (s + factor[0] * 48 + factor[1] * 8), 1)]
                        nc.vector.scalar_tensor_tensor(tile_of(x, i * 2 + s), ps[:, s, :], f,
                                                                  tile_of(x, i * 2 + s), ALU.mult, ALU.add).then_inc(*dve_done.step(f"sum{s}"))
                        total_add(dve, dve_done, factor, i, s)

            phase(sp=sp, pe=pe, dve=dve)
            return tiles_done(dve_done)

        def residual_again(ready):
            act_done = steps("again_act", ["scaled"])

            def act(act):
                act_done.enter(act)
                for r in ready:
                    act.wait_ge(*reached(*r))
                act.dma_start(x[:, :, :], d["x"][:, :, :]).then_inc(x_in, 16)
                act.wait_ge(x_in, 32)
                nc.scalar.activation(x[:, :, :], x[:, :, :], ACT.Copy, scale=ALPHA).then_inc(*act_done.step("scaled"))

            phase(act=act)
            return act_done, "scaled"

        def layer_norm(name, scope, layer, half_layer, ready, following, units=None):
            parts = following and isinstance(following[3], tuple)
            full = keep(f"{name}_in", [P, 2, T], scope) if parts else None
            mean, std, rstd = (keep(f"{name}_{n}", [P, T], scope) for n in ("mean", "std", "rstd"))
            sq = keep(f"{name}_sq", [P, 2, T], scope)
            col = (layer * 2 + half_layer) * KT
            shift = keep(f"{name}_shift", [P, KT], scope)
            pe_done = steps(f"{name}_pe", ["sum"] + [f"sq{j}" for j in range(KT)])
            act_done = steps(f"{name}_act", ["mean", "table"] + [f"sq{j}" for j in range(KT)] + ["std"]
                          + [f"{n}{j}" for j in range(KT) for n in (["in", "hi"] if parts else ["in"] if following else ["shift"])])
            dve_done = steps(f"{name}_dve", ["b scale", "shift"] * bool(following) + [f"centred{j}" for j in range(KT)] + ["rstd"]
                             + [m for j in range(KT + 2) for m in [f"scaled{j}"] * (j < KT) + [f"lo{j - 2}"] * (bool(parts) and j >= 2)])
            pool_done = steps(f"{name}_pool", [f"alpha{j}" for j in range(KT)])

            def pe(pe):
                pe_done.enter(pe)
                pe.wait_ge(*reached(*ready[KT]))
                mm(ps[:, 4, :], ones, tiles_total).then_inc(*pe_done.step("sum"))
                for j in range(KT):
                    pe.wait_ge(*act_done(f"sq{j}"))
                    mm(ps[:, 5, :], ones, sq[:, j % 2, :], j == 0, j == KT - 1).then_inc(*pe_done.step(f"sq{j}"))

            def act(act):
                act_done.enter(act)
                act.wait_ge(*pe_done("sum"))
                nc.scalar.activation(mean[:, :], ps[:, 4, :], ACT.Copy, scale=1.0 / D).then_inc(*act_done.step("mean"))
                nc.scalar.activation(std[:, 0:1], const("ln_eps"), ACT.Sqrt).then_inc(*act_done.step("table"))
                for j in range(KT):
                    act.wait_ge(*dve_done(f"centred{j}"))
                    if j >= 2:
                        act.wait_ge(*pe_done(f"sq{j - 2}"))
                    nc.scalar.activation(sq[:, j % 2, :], x[:, j, :], ACT.Square).then_inc(*act_done.step(f"sq{j}"))
                if units:
                    units.first(act, units.first_hi)
                act.wait_ge(*pe_done(f"sq{KT - 1}"))
                act.wait_ge(*act_done("table"))
                nc.scalar.activation(std[:, :], ps[:, 5, :], ACT.Sqrt, bias=const("ln_eps"), scale=1.0 / D).then_inc(*act_done.step("std"))
                for j in range(KT):
                    act.wait_ge(*dve_done(f"scaled{j}"))
                    if not following:
                        nc.scalar.activation(x[:, j, :], x[:, j, :], ACT.Identity, bias=vcol("ln_b", col + j)).then_inc(*act_done.step(f"shift{j}"))
                    else:
                        l, sh, sc, to = following
                        if parts and j >= 2:
                            act.wait_ge(*dve_done(f"lo{j - 2}"))
                        nc.scalar.activation(full[:, j % 2, :] if parts else to[:, j, :], x[:, j, :], ACT.Identity,
                                             bias=shift[:, j:j + 1], scale=mod(l, sc, j)).then_inc(*act_done.step(f"in{j}"))
                        if parts:
                            act.wait_ge(*act_done(f"in{j}"))
                            nc.scalar.activation(to[0][:, j, :], full[:, j % 2, :], ACT.Copy).then_inc(*act_done.step(f"hi{j}"))

            def dve(dve):
                dve_done.enter(dve)
                if following:
                    l, sh, sc, to = following
                    dve.wait_ge(*reached(*ready[KT - 1]))
                    a, b = l * 48 + sh * KT, l * 48 + sc * KT
                    nc.vector.tensor_tensor(shift[:, :], vec[:, VC["ln_b"][0] + col:VC["ln_b"][0] + col + KT], mods[:, b:b + KT],
                                            ALU.mult).then_inc(*dve_done.step("b scale"))
                    dve.wait_ge(*dve_done("b scale"))
                    nc.vector.tensor_tensor(shift[:, :], shift[:, :], mods[:, a:a + KT], ALU.add).then_inc(*dve_done.step("shift"))
                dve.wait_ge(*act_done("mean"))
                for j in range(KT):
                    nc.vector.tensor_tensor(x[:, j, :], x[:, j, :], mean[:, :], ALU.subtract).then_inc(*dve_done.step(f"centred{j}"))
                if units:
                    units.first(dve, units.first_lo)
                dve.wait_ge(*act_done("std"))
                nc.vector.reciprocal(rstd[:, :], std[:, :]).then_inc(*dve_done.step("rstd"))
                dve.wait_ge(*dve_done("rstd"))
                for j in range(KT + 2):
                    if j < KT:
                        nc.vector.scalar_tensor_tensor(x[:, j, :], x[:, j, :], vcol("ln_g", col + j), rstd[:, :],
                                                                  ALU.mult, ALU.mult).then_inc(*dve_done.step(f"scaled{j}"))
                    if parts and j >= 2:
                        dve.wait_ge(*act_done(f"hi{j - 2}"))
                        hi = following[3][0][:, j - 2, :].bitcast(F32)
                        nc.vector.tensor_tensor(following[3][1][:, j - 2, :], full[:, j % 2, :], hi, ALU.subtract).then_inc(
                            *dve_done.step(f"lo{j - 2}"))

            def pool(pool):
                pool_done.enter(pool)
                for j in range(KT):
                    pool.wait_ge(*act_done(f"in{j}"))
                    nc.gpsimd.tensor_scalar(x[:, j, :], x[:, j, :], vcol("ln_b", col + j), ALPHA, ALU.add, ALU.mult).then_inc(*pool_done.step(f"alpha{j}"))

            if following:
                phase(pe=pe, act=act, dve=dve, pool=pool)
                inputs = [(dve_done, f"lo{j}") if parts else (act_done, f"in{j}") for j in range(KT)]
                return inputs, [(pool_done, f"alpha{KT - 1}")]
            phase(pe=pe, act=act, dve=dve)
            return [(act_done, f"shift{j}") for j in range(KT)], []

        def rms_norm(name, scope, source, ready, gains, out, between=None, units=None, bank=5, later=None):
            n = len(source)
            parts = isinstance(out, tuple)
            full = keep(f"{name}_in", [P, 2, T], scope) if parts else None
            std, rstd = (keep(f"{name}_{m}", [P, T], scope) for m in ("std", "rstd"))
            summed = len(ready) > n
            last = "total" if summed else f"sq{n - 1}"
            sq = None if summed else keep(f"{name}_sq", [P, 2, T], scope)
            pe_done = steps(f"{name}_pe", ["total"] if summed else [f"sq{j}" for j in range(n)])
            act_done = steps(f"{name}_act", ["table"] + [f"sq{j}" for j in range(n) if not summed] + ["std"] + [f"hi{j}" for j in range(n) if parts])
            dve_done = steps(f"{name}_dve", ["rstd"] + [m for j in range(n + 1) for m in
                                                        [f"out{j}"] * (j < n) + [f"lo{j - 1}"] * (parts and j >= 1)])

            def act(act):
                act_done.enter(act)
                act.wait_ge(*reached(*ready[n - 1]))
                nc.scalar.activation(std[:, 0:1], const("rms_eps"), ACT.Sqrt).then_inc(*act_done.step("table"))
                for j in range(0 if summed else n):
                    if j >= 2:
                        act.wait_ge(*pe_done(f"sq{j - 2}"))
                    nc.scalar.activation(sq[:, j % 2, :], source[j], ACT.Square).then_inc(*act_done.step(f"sq{j}"))
                if units:
                    units.first(act, units.first_hi)
                act.wait_ge(*pe_done(last))
                act.wait_ge(*act_done("table"))
                nc.scalar.activation(std[:, :], ps[:, bank, :], ACT.Sqrt, bias=const("rms_eps"), scale=1.0 / (n * P)).then_inc(*act_done.step("std"))

            def act_parts(act):
                if parts:
                    for j in range(n):
                        if between:
                            between(act, j)
                        act.wait_ge(*dve_done(f"out{j}"))
                        nc.scalar.activation(out[0][j], full[:, j % 2, :], ACT.Copy).then_inc(*act_done.step(f"hi{j}"))

            def pe(pe):
                pe_done.enter(pe)
                if summed:
                    pe.wait_ge(*reached(*ready[n]))
                    mm(ps[:, bank, :], ones, squares_total).then_inc(*pe_done.step("total"))
                for j in range(0 if summed else n):
                    pe.wait_ge(*act_done(f"sq{j}"))
                    mm(ps[:, bank, :], ones, sq[:, j % 2, :], j == 0, j == n - 1).then_inc(*pe_done.step(f"sq{j}"))

            def dve(dve):
                dve_done.enter(dve)
                if units:
                    units.first(dve, units.first_lo)
                dve.wait_ge(*act_done("std"))
                nc.vector.reciprocal(rstd[:, :], std[:, :]).then_inc(*dve_done.step("rstd"))
                dve.wait_ge(*dve_done("rstd"))
                for j in range(n + 1):
                    if j < n:
                        nc.vector.scalar_tensor_tensor(full[:, j % 2, :] if parts else out[j], source[j], gains[j], rstd[:, :],
                                                       ALU.mult, ALU.mult).then_inc(*dve_done.step(f"out{j}"))
                    if parts and j >= 1:
                        dve.wait_ge(*act_done(f"hi{j - 1}"))
                        nc.vector.tensor_tensor(out[1][j - 1], full[:, (j - 1) % 2, :], out[0][j - 1].bitcast(F32),
                                                ALU.subtract).then_inc(*dve_done.step(f"lo{j - 1}"))
                        dve.wait_ge(*dve_done(f"lo{j - 1}"))

            phase(pe=pe, act=act, dve=dve)
            if later is None:
                phase(act=act_parts)
            else:
                later.append(act_parts)
            return [(dve_done, f"{'lo' if parts else 'out'}{j}") for j in range(n)]

        class Split:
            def __init__(self, name, scope):
                self.hi = [keep(f"{name}_hi{u}", [P, HT // 2 * P], scope, F32R) for u in range(2)]
                self.lo = [keep(f"{name}_lo{u}", [P, HT // 2 * P], scope, F32R) for u in range(2)]

        def split_hi(sp_, s, u, width):
            return nc.scalar.activation(sp_.hi[u][:, 0:width], slot[s][:, u * width:(u + 1) * width], ACT.Copy)

        def split_lo(sp_, s, u, width):
            return nc.vector.tensor_tensor(sp_.lo[u][:, 0:width], slot[s][:, u * width:(u + 1) * width],
                                           sp_.hi[u][:, 0:width].bitcast(F32), ALU.subtract)

        def three_passes(out, sp_, u, k, source, first, final):
            hi, lo = sp_.hi[u][:, k * P:(k + 1) * P], sp_.lo[u][:, k * P:(k + 1) * P]
            mm(out, hi, source[0], first, False)
            mm(out, hi, source[1], False, False)
            return mm(out, lo, source[0], False, final)

        class Halves:

            def __init__(self, name, split, tiles, turns):
                self.name, self.split, self.width = name, split, tiles // 2 * P
                self.hi_split, self.lo_split = Units(sem(f"{name}_hi_split")), Units(sem(f"{name}_lo_split"))
                self.loads = [Loads(s, turns, self.lo_split, s) for s in range(2)]

            def first(self, eng, part):
                for u in range(2):
                    part(eng, u)

            def first_hi(self, act, u):
                if u == 0:
                    act.wait_ge(*self.loads[0].arrived(0))
                split_hi(self.split, 0, u, self.width).then_inc(*self.hi_split.step())

            def first_lo(self, dve, u):
                dve.wait_ge(*self.hi_split.unit(0, 0, u))
                split_lo(self.split, 0, u, self.width).then_inc(*self.lo_split.step())

        def gated(halves, scope, source, hid, ready, following):
            name, split, loads, width = halves.name, halves.split, halves.loads, halves.width
            hi_split, lo_split = halves.hi_split, halves.lo_split
            n = HT // 2
            sg = keep(f"{name}_silu", [P, 2, T], scope)
            full = keep(f"{name}_full", [P, 2, T], scope)
            pe_done = steps(f"{name}_pe", ["gate0", "up0", "gate1", "up1"])
            act_done = steps(f"{name}_act", ["silu0", "hi0", "silu1", "hi1"])
            dve_done = steps(f"{name}_dve", ["hidden0", "lo0", "hidden1", "lo1"])
            PART = ("gate", "up")

            def sp(sp):
                for s in range(2):
                    sp.wait_ge(*loads[s].vacated())
                    sp.dma_start(loads[s].slot(row(f"{name}_in", s)), row(f"{name}_in", s)).then_inc(*loads[s].arrival)
                with sp.Fori(1, n) as i:
                    for s in range(2):
                        sp.wait_ge(*loads[s].vacated(i))
                        sp.dma_start(loads[s].slot(row(f"{name}_in", i * 2 + s)), row(f"{name}_in", i * 2 + s)).then_inc(*loads[s].arrival)

            def pe(pe):
                pe_done.enter(pe)

                def product(s, u, k):
                    return three_passes(ps[:, 2 * s + u, :], split, u, k, (source[0][:, k, :], source[1][:, k, :]), k == 0, k == KT - 1)

                def turn(i, first):
                    for s in range(2):
                        if not first:
                            pe.wait_ge(*dve_done(f"hidden{s}", i, 1))
                        if first and s == 0:
                            pe.wait_ge(*lo_split.unit(0, 0, 1))
                            for k in range(KT):
                                pe.wait_ge(*reached(*ready[k]))
                                lasts = [product(s, u, k) for u in range(2)]
                            for part, last in zip(PART, lasts):
                                last.then_inc(*pe_done.step(f"{part}{s}"))
                            continue
                        for u, part in enumerate(PART):
                            pe.wait_ge(*lo_split.unit(i, s, u))
                            for k in range(KT):
                                last = product(s, u, k)
                            last.then_inc(*pe_done.step(f"{part}{s}"))
                turn(0, True)
                with pe.Fori(1, n) as i:
                    turn(i, False)

            def act(act):
                act_done.enter(act)

                def hidden(i, s):
                    act.wait_ge(*dve_done(f"hidden{s}", i))
                    act.wait_ge(*pe_done(f"up{s}", i))
                    alone(act)
                    nc.scalar.activation(tile_of(hid[0], i * 2 + s), full[:, s, :], ACT.Copy).then_inc(*act_done.step(f"hi{s}"))

                def turn(i, more):
                    for s in range(2):
                        for u, part in enumerate(PART):
                            if s == 0 or more:
                                if u == 0:
                                    act.wait_ge(*loads[1 - s].arrived(i + s))
                                act.wait_ge(*pe_done(f"{part}{s}", i))
                                split_hi(split, 1 - s, u, width).then_inc(*hi_split.step())
                            else:
                                act.wait_ge(*pe_done(f"{part}{s}", i))
                                following.first_hi(act, u)
                            if u == 0:
                                act.wait_ge(*pe_done(f"gate{s}", i))
                                act.wait_ge(*dve_done(f"hidden{s}", i, 1))
                                nc.scalar.activation(sg[:, s, :], ps[:, 2 * s, :], ACT.Silu).then_inc(*act_done.step(f"silu{s}"))
                            else:
                                hidden(i, s)
                with act.Fori(0, n - 1) as i:
                    turn(i, True)
                turn(n - 1, False)

            def dve(dve):
                dve_done.enter(dve)

                def turn(i, more):
                    for s in range(2):
                        for u in range(2):
                            if s == 0 or more:
                                dve.wait_ge(*hi_split.unit(i + s, 1 - s, u))
                                split_lo(split, 1 - s, u, width).then_inc(*lo_split.step())
                            else:
                                following.first_lo(dve, u)
                            if u == 0:
                                dve.wait_ge(*act_done(f"silu{s}", i))
                                dve.wait_ge(*pe_done(f"up{s}", i))
                                dve.wait_ge(*act_done(f"hi{s}", i, 1))
                                dve.wait_ge(*dve_done(f"lo{s}", i, 1))
                                nc.vector.tensor_tensor(full[:, s, :], sg[:, s, :], ps[:, 2 * s + 1, :], ALU.mult).then_inc(
                                    *dve_done.step(f"hidden{s}"))
                            else:
                                dve.wait_ge(*act_done(f"hi{s}", i))
                                nc.vector.tensor_tensor(tile_of(hid[1], i * 2 + s), full[:, s, :],
                                                        tile_of(hid[0], i * 2 + s).bitcast(F32), ALU.subtract).then_inc(
                                    *dve_done.step(f"lo{s}"))
                with dve.Fori(0, n - 1) as i:
                    turn(i, True)
                turn(n - 1, False)

            phase(sp=sp, pe=pe, act=act, dve=dve)
            return [[(dve_done, f"lo{s}", n - 2) for s in range(2)], [(dve_done, f"lo{s}", n - 1) for s in range(2)]]

        def split_project(halves, stream, source, ready, factor, x_ready, units_free=None):
            name, split, loads = halves.name, halves.split, halves.loads
            hi_split, lo_split = halves.hi_split, halves.lo_split
            n = KT // 2
            half = len(source) // 2
            width = half * P
            pe_done = steps(f"{name}_pe", ["half0", "product0", "half1", "product1"])
            dve_done = steps(f"{name}_dve", total_names(factor))
            PART = ("half", "product")

            def sp(sp):
                for s in range(2):
                    sp.wait_ge(*loads[s].vacated())
                    sp.dma_start(loads[s].slot(row(stream, s)), row(stream, s)).then_inc(*loads[s].arrival)
                with sp.Fori(1, n) as i:
                    for s in range(2):
                        sp.wait_ge(*loads[s].vacated(i))
                        sp.dma_start(loads[s].slot(row(stream, i * 2 + s)), row(stream, i * 2 + s)).then_inc(*loads[s].arrival)

            def pe(pe):
                pe_done.enter(pe)

                def turn(i, first):
                    for s in range(2):
                        if not first:
                            pe.wait_ge(*dve_done(f"sum{s}", i, 1))
                        for u, part in enumerate(PART):
                            pe.wait_ge(*lo_split.unit(i, s, u))
                            if first and s == 0:
                                for r in ready[u]:
                                    pe.wait_ge(*reached(*r))
                            for k in range(half):
                                last = three_passes(ps[:, s, :], split, u, k, source[u * half + k], u == 0 and k == 0,
                                                    u == 1 and k == half - 1)
                            last.then_inc(*pe_done.step(f"{part}{s}"))
                turn(0, True)
                with pe.Fori(1, n) as i:
                    turn(i, False)

            def act(act):
                def turn(i, more):
                    for s in range(2):
                        for u, part in enumerate(PART):
                            if s == 0 or more:
                                if u == 0:
                                    act.wait_ge(*loads[1 - s].arrived(i + s))
                                act.wait_ge(*pe_done(f"{part}{s}", i))
                                split_hi(split, 1 - s, u, width).then_inc(*hi_split.step())
                if units_free:
                    act.wait_ge(*reached(*units_free))
                    for u in range(2):
                        halves.first_hi(act, u)
                with act.Fori(0, n - 1) as i:
                    turn(i, True)
                turn(n - 1, False)

            def dve(dve):
                total_start(dve, dve_done, factor)

                def turn(i, more):
                    for s in range(2):
                        for u in range(2):
                            if s == 0 or more:
                                dve.wait_ge(*hi_split.unit(i + s, 1 - s, u))
                                split_lo(split, 1 - s, u, width).then_inc(*lo_split.step())
                        dve.wait_ge(*pe_done(f"product{s}", i))
                        if isinstance(factor, float):
                            f = factor
                        else:
                            f = mods[:, bass.ds(i * 2 + (s + factor[0] * 48 + factor[1] * 8), 1)]
                        nc.vector.scalar_tensor_tensor(tile_of(x, i * 2 + s), ps[:, s, :], f, tile_of(x, i * 2 + s),
                                                       ALU.mult, ALU.add).then_inc(*dve_done.step(f"sum{s}"))
                        total_add(dve, dve_done, factor, i, s)
                if units_free:
                    for u in range(2):
                        halves.first_lo(dve, u)
                for r in x_ready:
                    dve.wait_ge(*reached(*r))
                with dve.Fori(0, n - 1) as i:
                    turn(i, True)
                turn(n - 1, False)

            phase(sp=sp, pe=pe, act=act, dve=dve)
            return tiles_done(dve_done)

        def parts_of(name, scope, n=KT):
            return tuple(keep(f"{name}_{p}", [P, n, T], scope, F32R) for p in ("hi", "lo"))

        def feed_forward(halves, scope, source, ready, factor, x_ready=()):
            name = halves.name
            hid = parts_of(f"{name}_hidden", scope, HT)
            down = Halves(f"{name}_down", halves.split, HT, KT // 2)
            done = gated(halves, scope, source, hid, ready, down)
            return split_project(down, f"{name}_out", [(hid[0][:, k, :], hid[1][:, k, :]) for k in range(HT)], done, factor, x_ready)

        def split_project_alone(name, split, source, ready, units_free, factor, x_ready=()):
            halves = Halves(name, split, KT, KT // 2)
            return split_project(halves, name, source, ready, factor, x_ready, units_free)

        STEP_TILES = (2, 3, 1, 0)

        def attend(name, scope, turns, work, out, ready, before, zero_first=()):
            N = len(work)
            sx = keep(f"{name}_masked", [P, 4, T], scope)
            probs = keep(f"{name}_probs", [P, 4, T], scope)
            probsT = keep(f"{name}_probsT", [P, 2, T], scope)
            diag = keep(f"{name}_diag", [P, 4, P], scope)
            stat = keep(f"{name}_stat", [P, 3, 4], scope)
            MAX, SUM, INV = range(3)
            L, TR, O = 0, 4, 6
            order = []
            for t in range(N + 4):
                order += [("L", t)] * (t < N) + [("T", t - 3)] * (3 <= t < N + 3) + [("O", t - 4)] * (t >= 4)
            a_order = []
            for t in range(N + 3):
                a_order += [("exp", t)] * (t < N) + [("PT", t - 3)] * (t >= 3)
            d_order = []
            for t in range(N + 1):
                d_order += [("max", t), ("neg", t)] * (t < N) + [("inv", t - 1), ("diag", t - 1)] * (t >= 1)

            def names(eng, seq):
                return before[eng][0] + [f"{a}{n}" for a, n in seq]
            parts = isinstance(out, tuple)
            S = {"pe": steps(f"{name}_pe", names("pe", order)), "act": steps(f"{name}_act", names("act", a_order) + ["out"]),
                 "dve": steps(f"{name}_dve", names("dve", d_order) + ["low out"] * parts)}

            def earlier(what, n, back, turn):
                who = S[{"max": "dve", "T": "pe", "PT": "act", "O": "pe"}[what]]
                return who(f"{what}{n - back}", turn) if n >= back else who(f"{what}{N + n - back}", turn, 1)

            def pe(pe):
                S["pe"].enter(pe)
                for r in ready:
                    pe.wait_ge(*reached(*r))
                with pe.Fori(0, turns) as i:
                    before["pe"][1](pe, i, S)
                    for what, n in order:
                        w = work[n]
                        if what == "L":
                            pe.wait_ge(*earlier("max", n, 4, i))
                            out_l = ps[:, L + n % 4, 0:w["w"]]
                            extra = w.get("extra")
                            keys = tile_of(w["keys_of_turn"], i)[:, 0:w["w"]] if "keys_of_turn" in w else w["keys"]
                            ins = mm(out_l, w["query"], keys, True, not extra)
                            if extra:
                                ins = mm(out_l, *extra, False, True)
                        elif what == "T":
                            pe.wait_ge(*S["dve"](f"diag{n}", i))
                            pe.wait_ge(*earlier("PT", n, 2, i))
                            for b in range(w["w"] // P):
                                ins = mm(ps[:, TR + n % 2, b * P:(b + 1) * P], probs[:, n % 4, b * P:(b + 1) * P], diag[:, n % 4, :])
                        else:
                            pe.wait_ge(*S["act"](f"PT{n}", i))
                            if n == 0:
                                pe.wait_ge(*S["act"]("out", i, 1))
                                if parts:
                                    pe.wait_ge(*S["dve"]("low out", i, 1))
                            hh, q = w["head"], w["tile"]
                            nb = w["w"] // P
                            for b in range(nb):
                                ins = mm(ps[hh * HD:(hh + 1) * HD, O, q * P:(q + 1) * P], w["values"][b],
                                         probsT[:, n % 2, b * P:(b + 1) * P], w["first"] and b == 0, w["last"] and b == nb - 1)
                        ins.then_inc(*S["pe"].step(f"{what}{n}"))

            def act(act):
                S["act"].enter(act)
                with act.Fori(0, turns) as i:
                    before["act"][1](act, i, S)
                    for what, n in a_order:
                        w = work[n]["w"]
                        if what == "exp":
                            act.wait_ge(*S["dve"](f"neg{n}", i))
                            act.wait_ge(*earlier("T", n, 4, i))
                            ins = nc.scalar.activation(probs[:, n % 4, 0:w], sx[:, n % 4, 0:w], ACT.Exp,
                                                       bias=stat[:, MAX, n % 4:n % 4 + 1], accum_out=stat[:, SUM, n % 4:n % 4 + 1])
                        else:
                            act.wait_ge(*S["pe"](f"T{n}", i))
                            act.wait_ge(*earlier("O", n, 2, i))
                            ins = nc.scalar.activation(probsT[:, n % 2, 0:w], ps[:, TR + n % 2, 0:w], ACT.Copy)
                        ins.then_inc(*S["act"].step(f"{what}{n}"))
                    act.wait_ge(*S["pe"](f"O{N - 1}", i))
                    alone(act)
                    nc.scalar.activation(tile_of(out[0] if parts else out, i), ps[:, O, :], ACT.Copy).then_inc(*S["act"].step("out"))

            def dve(dve):
                S["dve"].enter(dve)
                with dve.Fori(0, turns) as i:
                    before["dve"][1](dve, i, S)
                    for what, n in d_order:
                        w = work[n]
                        m = n % 4
                        if what == "max":
                            dve.wait_ge(*S["pe"](f"L{n}", i))
                            alone(dve)
                            ins = nc.vector.tensor_tensor_reduce(
                                out=sx[:, n % 4, 0:w["w"]], in0=ps[:, L + n % 4, 0:w["w"]], in1=w["mask"], scale=1.0,
                                scalar=-3e38, op0=ALU.add, op1=ALU.max, accum_out=stat[:, MAX, m:m + 1])
                        elif what == "neg":
                            dve.wait_ge(*S["dve"](f"max{n}", i))
                            ins = nc.vector.tensor_scalar(stat[:, MAX, m:m + 1], stat[:, MAX, m:m + 1], -1.0, None, ALU.mult)
                        elif what == "inv":
                            dve.wait_ge(*S["act"](f"exp{n}", i))
                            ins = nc.vector.reciprocal(stat[:, INV, m:m + 1], stat[:, SUM, m:m + 1])
                        else:
                            dve.wait_ge(*S["dve"](f"inv{n}", i))
                            dve.wait_ge(*earlier("T", n, 4, i))
                            gate = w.get("gate")
                            ins = nc.vector.tensor_scalar(diag[:, n % 4, :], ident, stat[:, INV, m:m + 1], gate, ALU.mult,
                                                          ALU.mult if gate is not None else ALU.bypass)
                        ins.then_inc(*S["dve"].step(f"{what}{n}"))
                    if parts:
                        dve.wait_ge(*S["act"]("out", i))
                        alone(dve)
                        nc.vector.tensor_tensor(tile_of(out[1], i), ps[:, O, :], tile_of(out[0], i).bitcast(F32),
                                                ALU.subtract).then_inc(*S["dve"].step("low out"))

            phase(pe=pe, act=act, dve=dve)
            return S

        IH = 8
        TOPK = 128

        def sparse_attention(scope, h, branch, out):
            cb = keep("const_attention_1", [P, CB["all"][1]], scope)

            def cc(name):
                return const(name, cb, CB)
            ckv = keep("latent", [P, T], scope)
            kidx = keep("index_keys", [P, T], scope)
            tmp = keep("latent_norm", [P, 2, T], scope)
            qi = keep("index_queries", [P, 2, 2, T], scope)
            wts = keep("index_weights", [P, QT, IH], scope)
            rel = keep("index_relu", [P, 2, T], scope)
            score = keep("index_scores", [P, QT, T], scope)
            best = keep("best", [P, QT, 8], scope)
            relb = keep("rel_bias", [32, 16], scope)
            brow = keep("bias_rows", [16, BIAS_LEN], scope)
            small_in, zeroed, rows_out = sem("rel_bias_in"), sem("index_queries_zeroed"), sem("bias_rows_out")
            scratch = d["bias_scratch"]
            todo = [(m, hh, q) for m in range(IH // 2) for hh in range(2) for q in range(1, QT)]
            NI = len(todo)
            pe_done = steps("idx_pe", ["ckv", "kidx", "widx", "qi0", "qi1", "ckv sq", "bias"]
                         + [n for t, (m, hh, q) in enumerate(todo)
                            for n in (([f"qi{m + 1}"] if hh == 0 and q == 1 and m >= 1 and m < 3 else []) + [f"score{t}"])])
            act_done = steps("idx_act", ["ckv sq", "kidx", "qi0a", "qi0b", "ckv std", "bias"]
                          + [n for t, (m, hh, q) in enumerate(todo)
                             for n in ([f"relu{t}"] + ([f"qi{m + 1}a", f"qi{m + 1}b"] if hh == 0 and q == 3 and m < 3 else []))])
            dve_done = steps("idx_dve", ["widx", "ckv rstd", "ckv"] + [f"add{t}" for t in range(NI)] + [f"causal{q}" for q in range(1, QT)])
            topk_done = steps("top_dve", [f"max{q}" for q in range(1, QT)] + [f"take{q}" for q in range(1, QT)])
            selected = steps("sel_dve", [f"select{q}" for q in range(1, QT)])
            load_a, load_b = Loads(0, 1, pe_done, "widx"), Loads(1, 1, pe_done, "qi1")
            load_c = Loads(0, 1, pe_done, "qi3")

            def sp(sp):
                sp.wait_ge(*load_a.vacated())
                sp.dma_start(load_a.slot(row("dsa_first", 0)), row("dsa_first", 0)).then_inc(*load_a.arrival)
                sp.wait_ge(*load_b.vacated())
                sp.dma_start(load_b.slot(row("dsa_index", 0)), row("dsa_index", 0)).then_inc(*load_b.arrival)
                sp.wait_ge(*reached(*branch[0]))
                sp.dma_start(relb[:, :], d["rel_bias"][:, :]).then_inc(small_in, 16)
                sp.dma_start(cb[:, :], d["const_attention"][:, :]).then_inc(att_in, 16)
                sp.wait_ge(*load_c.vacated())
                sp.dma_start(load_c.slot(row("dsa_index", 1)), row("dsa_index", 1)).then_inc(*load_c.arrival)
                sp.wait_ge(*act_done("bias"))
                sp.dma_start(scratch[:, :], brow[:, :]).then_inc(rows_out, 16)

            def pool(pool):
                pool.wait_ge(*reached(*branch[0]))
                nc.gpsimd.memset(qi[:, :, :, :], 0.0).then_inc(zeroed, 1)

            def pe(pe):
                pe_done.enter(pe)
                pe.wait_ge(*load_a.arrived())
                for n, (name, bank) in enumerate((("ckv", 0), ("kidx", 1))):
                    for k in range(KT):
                        if n == 0:
                            pe.wait_ge(*reached(*branch[k]))
                        last = mm(ps[:, bank, :], wtile(0, n * KT + k), h[:, k, :], k == 0, k == KT - 1)
                    last.then_inc(*pe_done.step(name))
                for q in range(QT):
                    for k in range(KT):
                        last = mm(ps[:, 2, q * IH:(q + 1) * IH], h[:, k, q * P:(q + 1) * P], wtile(0, k, P, IH, 2 * KT * P),
                                  k == 0, k == KT - 1)
                last.then_inc(*pe_done.step("widx"))

                def index_queries(m):
                    load = load_b if m < 2 else load_c
                    if m % 2 == 0:
                        pe.wait_ge(*load.arrived())
                    if m >= 2:
                        pe.wait_ge(*act_done(f"qi{m - 2}b"))
                    for k in range(KT):
                        last = mm(ps[:, 4 + m % 2, :], wtile(load.s, (m % 2) * KT + k), h[:, k, :], k == 0, k == KT - 1)
                    last.then_inc(*pe_done.step(f"qi{m}"))
                index_queries(0)
                index_queries(1)
                pe.wait_ge(*act_done("ckv sq"))
                mm(ps[:, 3, :], ones, tmp[:, 0, :]).then_inc(*pe_done.step("ckv sq"))
                pe.wait_ge(small_in, 16)
                pe.wait_ge(att_in, 16)
                pe.wait_ge(*dve_done("ckv"))
                pe.wait_ge(*act_done("kidx"))
                mm(ps[0:16, 0, :], relb[:, :], cc("onehot")[0:32, 0:T])
                mm(ps[0:16, 1, 0:P], relb[:, :], cc("onehot")[0:32, T:BIAS_LEN]).then_inc(*pe_done.step("bias"))
                for t, (m, hh, q) in enumerate(todo):
                    if hh == 0 and q == 1:
                        if m >= 1 and m < 3:
                            index_queries(m + 1)
                        pe.wait_ge(*act_done(f"qi{m}b"))
                    if t >= 2:
                        pe.wait_ge(*act_done(f"relu{t - 2}"))
                    w = (q + 1) * P
                    mm(ps[:, 6 + t % 2, 0:w], qi[:, m % 2, hh, q * P:(q + 1) * P], kidx[:, 0:w]).then_inc(*pe_done.step(f"score{t}"))

            def act(act):
                act_done.enter(act)
                act.wait_ge(*pe_done("ckv"))
                nc.scalar.activation(tmp[:, 0, :], ps[:, 0, :], ACT.Square).then_inc(*act_done.step("ckv sq"))
                act.wait_ge(*pe_done("kidx"))
                nc.scalar.activation(kidx[:, :], ps[:, 1, :], ACT.Copy).then_inc(*act_done.step("kidx"))
                act.wait_ge(zeroed, 1)

                def index_queries(m):
                    if m >= 2:
                        t = todo.index((m - 2, 1, QT - 1))
                        act.wait_ge(*pe_done(f"score{t}"))
                    act.wait_ge(*pe_done(f"qi{m}"))
                    for hh, ab in ((0, "a"), (1, "b")):
                        r = slice(hh * HD, (hh + 1) * HD)
                        nc.scalar.activation(qi[r, m % 2, hh, :], ps[r, 4 + m % 2, :], ACT.Copy).then_inc(*act_done.step(f"qi{m}{ab}"))
                index_queries(0)
                act.wait_ge(*pe_done("ckv sq"))
                nc.scalar.activation(tmp[:, 1, :], ps[:, 3, :], ACT.Sqrt, bias=const("rms_eps"), scale=1.0 / P).then_inc(*act_done.step("ckv std"))
                act.wait_ge(*pe_done("bias"))
                nc.scalar.activation(brow[:, T:BIAS_LEN], ps[0:16, 1, 0:P], ACT.Copy)
                nc.scalar.activation(brow[:, 0:T], ps[0:16, 0, :], ACT.Copy).then_inc(*act_done.step("bias"))
                for t, (m, hh, q) in enumerate(todo):
                    w = (q + 1) * P
                    act.wait_ge(*pe_done(f"score{t}"))
                    if t >= 2:
                        act.wait_ge(*dve_done(f"add{t - 2}"))
                    nc.scalar.activation(rel[:, t % 2, 0:w], ps[:, 6 + t % 2, 0:w], ACT.Relu).then_inc(*act_done.step(f"relu{t}"))
                    if hh == 0 and q == 3 and m < 3:
                        index_queries(m + 1)

            def dve(dve):
                dve_done.enter(dve)
                topk_done.enter(dve)
                selected.enter(dve)
                dve.wait_ge(*pe_done("widx"))
                nc.vector.tensor_scalar(wts[:, :, :], ps[:, 2, 0:QT * IH].rearrange("p (q h) -> p q h", h=IH),
                                                   IH ** -0.5 * HD ** -0.5, None, ALU.mult).then_inc(*dve_done.step("widx"))
                dve.wait_ge(*act_done("ckv std"))
                nc.vector.reciprocal(tmp[:, 1, :], tmp[:, 1, :]).then_inc(*dve_done.step("ckv rstd"))
                dve.wait_ge(*dve_done("ckv rstd"))
                nc.vector.scalar_tensor_tensor(ckv[:, :], ps[:, 0, :], vcol("kv_norm"), tmp[:, 1, :], ALU.mult, ALU.mult).then_inc(*dve_done.step("ckv"))
                for t, (m, hh, q) in enumerate(todo):
                    w, head = (q + 1) * P, 2 * m + hh
                    dve.wait_ge(*act_done(f"relu{t}"))
                    weight = wts[:, q, head:head + 1]
                    if head == 0:
                        ins = nc.vector.tensor_scalar(score[:, q, 0:w], rel[:, t % 2, 0:w], weight, None, ALU.mult)
                    else:
                        dve.wait_ge(*dve_done(f"add{t - QT + 1}"))
                        ins = nc.vector.scalar_tensor_tensor(score[:, q, 0:w], rel[:, t % 2, 0:w], weight, score[:, q, 0:w],
                                                             ALU.mult, ALU.add)
                    ins.then_inc(*dve_done.step(f"add{t}"))
                dve.wait_ge(att_in, 16)
                dve.wait_ge(*dve_done(f"add{NI - 1}"))
                for q in range(1, QT):
                    own = score[:, q, q * P:(q + 1) * P]
                    nc.vector.tensor_tensor(own, own, cc("causal")[:, T - P:T], ALU.add).then_inc(*dve_done.step(f"causal{q}"))
                dve.wait_ge(*dve_done(f"causal{QT - 1}"))
                with dve.Fori(0, TOPK // 8) as i:
                    for q in range(1, QT):
                        dve.wait_ge(*topk_done(f"take{q}", i, 1))
                        alone(dve)
                        nc.vector.max(best[:, q, :], score[:, q, 0:(q + 1) * P]).then_inc(*topk_done.step(f"max{q}"))
                    for q in range(1, QT):
                        w = (q + 1) * P
                        dve.wait_ge(*topk_done(f"max{q}", i))
                        alone(dve)
                        nc.vector.match_replace(score[:, q, 0:w], best[:, q, :], score[:, q, 0:w], TAKEN).then_inc(*topk_done.step(f"take{q}"))
                dve.wait_ge(*topk_done(f"take{QT - 1}", TOPK // 8 - 1))
                for q in range(1, QT):
                    w = (q + 1) * P
                    nc.vector.tensor_scalar(score[:, q, 0:w], score[:, q, 0:w], TAKEN / 2, NEG, ALU.is_ge, ALU.mult).then_inc(*selected.step(f"select{q}"))

            phase(sp=sp, pool=pool, pe=pe, act=act, dve=dve)

            qs = keep("scaled_queries", [P, KT, T], scope)
            q_pe = steps("dsa_queries_pe", ["query0", "query1"])
            q_act = steps("dsa_queries_act", ["query0", "query1"])
            q_loads = [Loads(s, KT // 2, q_pe, f"query{s}") for s in range(2)]

            def sp_queries(sp):
                for s in range(2):
                    sp.wait_ge(*q_loads[s].vacated())
                with sp.Fori(0, KT // 2) as i:
                    for s in range(2):
                        sp.wait_ge(*q_loads[s].vacated(i))
                        sp.dma_start(q_loads[s].slot(row("dsa_q", i * 2 + s)), row("dsa_q", i * 2 + s)).then_inc(*q_loads[s].arrival)

            def pe_queries(pe):
                q_pe.enter(pe)
                pe.wait_ge(*act_done("bias"))
                with pe.Fori(0, KT // 2) as i:
                    for s in range(2):
                        pe.wait_ge(*q_loads[s].arrived(i))
                        pe.wait_ge(*q_act(f"query{s}", i, 1))
                        for k in range(KT):
                            last = mm(ps[:, s, :], wtile(s, k), h[:, k, :], k == 0, k == KT - 1)
                        last.then_inc(*q_pe.step(f"query{s}"))

            def act_queries(act):
                q_act.enter(act)
                with act.Fori(0, KT // 2) as i:
                    for s in range(2):
                        act.wait_ge(*q_pe(f"query{s}", i))
                        alone(act)
                        nc.scalar.activation(tile_of(qs, i * 2 + s), ps[:, s, :], ACT.Copy, scale=HD ** -0.5).then_inc(
                            *q_act.step(f"query{s}"))

            phase(sp=sp_queries, pe=pe_queries, act=act_queries)
            qz = keep("latent_queries", [P, 2, T], scope)
            vals = keep("dsa_values", [P, QT, P], scope)
            hank = keep("bias_hankel", [P, 2, T], scope)
            hank_in = sem("bias_hankel_in")
            N = KT
            work = []
            for hh in range(2):
                for q in STEP_TILES:
                    w = (q + 1) * P
                    off = T - P - q * P
                    work.append({"head": hh, "tile": q, "w": w, "query": qz[:, hh, q * P:(q + 1) * P], "keys": ckv[:, 0:w],
                                 "mask": cc("causal")[:, T - P:T] if q == 0 else score[:, q, 0:w],
                                 "extra": (cc("flip"), hank[:, hh, off:off + w]),
                                 "values": [vals[:, b, hh * HD:(hh + 1) * HD] for b in range(q + 1)], "first": True, "last": True})
            W = len(work)

            def before_pe(pe, i, S):
                pe.wait_ge(*load.arrived(i))
                pe.wait_ge(*S["act"](f"PT{W - 1}", i, 1))
                mm(ps[:, 4, :], wtile(0, 0), tile_of(qs, i)).then_inc(*S["pe"].step("lat0"))
                mm(ps[:, 5, :], wtile(0, 1), tile_of(qs, i)).then_inc(*S["pe"].step("lat1"))
                pe.wait_ge(*S["dve"]("v", i, 1))
                for b in range(QT):
                    last = mm(ps[:, 7, b * P:(b + 1) * P], ckv[:, b * P:(b + 1) * P], wtile(0, 2))
                last.then_inc(*S["pe"].step("v"))
                pe.wait_ge(*S["act"]("lat1", i))
                pe.wait_ge(hank_in, i * 16 + 16)

            def before_act(act, i, S):
                for hh in range(2):
                    act.wait_ge(*S["pe"](f"lat{hh}", i))
                    nc.scalar.activation(qz[:, hh, :], ps[:, 4 + hh, :], ACT.Copy).then_inc(*S["act"].step(f"lat{hh}"))

            def before_dve(dve, i, S):
                dve.wait_ge(*S["pe"]("v", i))
                nc.vector.tensor_copy(vals[:, :, :], ps[:, 7, :].rearrange("p (b n) -> p b n", n=P)).then_inc(*S["dve"].step("v"))

            S = attend("dsa", scope, N, work, out,
                       [(selected, f"select{QT - 1}"), (act_done, f"relu{NI - 1}"), (dve_done, "ckv"),
                        (q_act, f"query{1}", KT // 2 - 1)],
                       {"pe": (["lat0", "lat1", "v"], before_pe), "act": (["lat0", "lat1"], before_act),
                        "dve": (["v"], before_dve)})
            load = Loads(0, N, S["pe"], "v")

            def sp2(sp):
                sp.wait_ge(*load.vacated())
                sp.wait_ge(rows_out, 16)
                with sp.Fori(0, N) as i:
                    sp.wait_ge(*load.vacated(i))
                    sp.dma_start(load.slot(row("dsa_heads", i)), row("dsa_heads", i)).then_inc(*load.arrival)
                    sp.wait_ge(*S["pe"](f"L{W - 1}", i, 1))
                    sp.dma_start(hank[:, :, :], bass.AP(tensor=scratch.tensor, offset=i * (2 * BIAS_LEN),
                                                              ap=[[1, P], [BIAS_LEN, 2], [1, T]])).then_inc(hank_in, 16)

            phase(sp=sp2)
            return [(S["dve"], "low out", N - 1)]

        def mixer_inputs(scope, h, branch):
            t = {}

            def have(name, shape):
                t[name] = keep(name, shape, scope)
                return t[name]
            cb = have("const_attention_2", [P, CB["all"][1]])

            def cc(name):
                return const(name, cb, CB)
            keys = {n: have(f"keys_{n}", [P, T]) for n in ("slc", "win")}
            vals = have("values", [P, QT, 2 * P])
            gates = have("gates", [P, QT, 24])
            kcmp, vcmp = have("keys_cmp", [P, P]), have("values_cmp", [P, P])
            with ExitStack() as own:
                raw = keep("keys_raw", [P, 3, T], own)
                sq = keep("keys_sq", [P, 2, T], own)
                rstd = keep("keys_rstd", [P, 2, T], own)
                cos = keep("keys_cos", [P, T], own)
                sin = keep("keys_sin", [P, 3, T], own)
                z = keep("forget", [8, 5, T], own)
                c2 = keep("forget_sums", [8, 2, T], own)
                hidden = keep("cmp_hidden", [P, 2, 2, 2 * NCMP], own)
                toks = keep("cmp_tokens", [P, 2, T], own)
                blocks = keep("cmp_blocks", [P, 2, CMP_L // 2, 2 * NCMP], own)
                w2 = keep("cmp_w2", [P, 4 * HD], own)
                csq = keep("cmp_sq", [P, 3, NCMP], own)
            zeroed, sums_out = sem("mixer_zeroed"), sem("forget_sums_out")
            loads_n = 4
            PE = (["kc", "vc", "slc", "gates", "fl", "win", "vals", "kc rot", "slc sum", "win sum", "v twice", "k twice", "slc rot",
                   "win rot"] + [f"cmp{n}" for n in range(loads_n)] + ["k2", "v2", "k2 sum"])
            AC = ["slc sq", "kc", "vc", "gates", "win sq", "slc std", "win std", "abs", "exp", "ln",
                  "hid k0", "hid k1", "hid v0", "hid v1", "k2 sq", "v2", "k2 std"]
            DV = (["z", "vals0", "vals1", "kc cos", "kc sin", "kc"] + [f"{n} {m}" for n in ("slc", "win") for m in ("rstd", "n")]
                  + [f"blocks {u}{g}{r}{n}" for u in "vk" for g in range(2) for r in range(2) for n in range(2)] + [f"{n} {m}" for n in ("slc", "win") for m in ("cos", "sin", "add")]
                  + ["1+e", "min", "logf", "cum", "-cum", "k2 rstd", "k2"])
            pe_done, act_done, dve_done = (steps(f"in2_{n}", q) for n, q in (("pe", PE), ("act", AC), ("dve", DV)))
            load_a, load_b = Loads(0, 1, pe_done, "fl"), Loads(1, 1, pe_done, "vals")
            CMP_BANKS = ((3, 4), (2, 5))
            cmp_loads = [Loads(n % 2, 1, pe_done, f"cmp{n}") for n in range(loads_n)]

            def sp(sp):
                for n, l in enumerate((load_a, load_b)):
                    sp.wait_ge(*l.vacated())
                    sp.dma_start(l.slot(row(f"mix_{n}", 0)), row(f"mix_{n}", 0)).then_inc(*l.arrival)
                sp.wait_ge(*reached(*branch[0]))
                sp.dma_start(cb[:, :], d["const_attention"][:, :]).then_inc(att_in, 16)
                sp.dma_start(w2[:, :], d["cmp_w2"][:, :]).then_inc(att_in, 16)
                for n, l in enumerate(cmp_loads):
                    sp.wait_ge(*l.vacated())
                    sp.dma_start(l.slot(row("cmp_w1", n)), row("cmp_w1", n)).then_inc(*l.arrival)
                sp.wait_ge(*dve_done("-cum"))
                sp.dma_start(d["forget_scratch"].rearrange("s h t -> h s t"), c2[:, :, :]).then_inc(sums_out, 16)

            def pool(pool):
                pool.wait_ge(*reached(*branch[0]))
                for n in (kcmp, vcmp):
                    nc.gpsimd.memset(n[:, :], 0.0).then_inc(zeroed, 1)
                nc.gpsimd.memset(z[:, 4, :], 1.0).then_inc(zeroed, 1)

            def pe(pe):
                pe_done.enter(pe)
                pe.wait_ge(*load_a.arrived())
                for n, (name, bank) in enumerate((("kc", 0), ("vc", 1), ("slc", 2))):
                    for k in range(KT):
                        if n == 0:
                            pe.wait_ge(*reached(*branch[k]))
                        last = mm(ps[:, bank, :], wtile(0, n * KT + k), h[:, k, :], k == 0, k == KT - 1)
                    last.then_inc(*pe_done.step(name))
                at = 3 * KT * P
                for q in range(QT):
                    for k in range(KT):
                        last = mm(ps[:, 3, q * 24:(q + 1) * 24], h[:, k, q * P:(q + 1) * P], wtile(0, k, P, 24, at), k == 0, k == KT - 1)
                last.then_inc(*pe_done.step("gates"))
                for k in range(KT):
                    last = mm(ps[0:8, 4, :], wtile(0, k, P, 8, at + 24 * KT), h[:, k, :], k == 0, k == KT - 1)
                last.then_inc(*pe_done.step("fl"))
                pe.wait_ge(*load_b.arrived())
                for k in range(KT):
                    last = mm(ps[:, 5, :], wtile(1, k), h[:, k, :], k == 0, k == KT - 1)
                last.then_inc(*pe_done.step("win"))
                for q in range(QT):
                    for k in range(KT):
                        last = mm(ps[:, 6 + q // 2, (q % 2) * 256:(q % 2) * 256 + 256], h[:, k, q * P:(q + 1) * P],
                                  wtile(1, k, P, 2 * P, KT * P), k == 0, k == KT - 1)
                last.then_inc(*pe_done.step("vals"))
                pe.wait_ge(att_in, 48)
                pe.wait_ge(*act_done("kc"))
                mm(ps[:, 0, :], cc("rot"), raw[:, 2, :]).then_inc(*pe_done.step("kc rot"))
                for n, (name, bank, free) in enumerate((("slc", 3, (act_done, "gates")), ("win", 4, (dve_done, "z")))):
                    pe.wait_ge(*act_done(f"{name} sq"))
                    pe.wait_ge(*reached(*free))
                    mm(ps[:, bank, :], blockones, sq[:, n, :]).then_inc(*pe_done.step(f"{name} sum"))
                for u, ready, banks in (("v", (act_done, "vc"), (6, 7)), ("k", (dve_done, "kc"), (0, 1))):
                    pe.wait_ge(*reached(*ready))
                    if u == "v":
                        pe.wait_ge(*dve_done("vals1"))
                    for g in range(2):
                        last = mm(ps[:, banks[g], :], cc(f"twice{g}"), toks[:, "kv".index(u), :])
                    last.then_inc(*pe_done.step(f"{u} twice"))
                for n, (name, bank) in enumerate((("slc", 2), ("win", 5))):
                    pe.wait_ge(*dve_done(f"{name} n"))
                    mm(ps[:, bank, :], cc("rot"), raw[:, n, :]).then_inc(*pe_done.step(f"{name} rot"))
                pe.wait_ge(*act_done("win std"))
                for n, l in enumerate(cmp_loads):
                    u, part = n // 2, n % 2
                    pe.wait_ge(*dve_done(f"blocks {'kv'[u]}111"))
                    pe.wait_ge(*dve_done("win sin"))
                    pe.wait_ge(*l.arrived())
                    for e in range(CMP_L // 4):
                        pair = part * (CMP_L // 4) + e
                        for m in range(2):
                            last = mm(ps[:, CMP_BANKS[u][m], 0:2 * NCMP], wtile(n % 2, e * 2 + m), blocks[:, u, pair, :],
                                      pair == 0, pair == CMP_L // 2 - 1)
                    last.then_inc(*pe_done.step(f"cmp{n}"))
                pe.wait_ge(*act_done("hid k1"))
                for g in range(2):
                    for m in range(2):
                        last = mm(ps[g * HD:(g + 1) * HD, 0, 0:NCMP], w2[:, m * HD:(m + 1) * HD],
                                  hidden[:, 0, m, g * NCMP:(g + 1) * NCMP], m == 0, m == 1)
                last.then_inc(*pe_done.step("k2"))
                pe.wait_ge(*act_done("hid v1"))
                for g in range(2):
                    for m in range(2):
                        last = mm(ps[0:NCMP, 6, g * HD:(g + 1) * HD], hidden[:, 1, m, g * NCMP:(g + 1) * NCMP],
                                  w2[:, (2 + m) * HD:(3 + m) * HD], m == 0, m == 1)
                last.then_inc(*pe_done.step("v2"))
                pe.wait_ge(*act_done("k2 sq"))
                mm(ps[:, 1, 0:NCMP], blockones, csq[:, 0, :]).then_inc(*pe_done.step("k2 sum"))

            def act(act):
                act_done.enter(act)
                a = nc.scalar.activation
                act.wait_ge(*pe_done("slc"))
                a(sq[:, 0, :], ps[:, 2, :], ACT.Square).then_inc(*act_done.step("slc sq"))
                a(raw[:, 2, :], ps[:, 0, :], ACT.Copy).then_inc(*act_done.step("kc"))
                a(toks[:, 1, :], ps[:, 1, :], ACT.Copy).then_inc(*act_done.step("vc"))
                act.wait_ge(*pe_done("gates"))
                a(gates[:, :, :], ps[:, 3, 0:QT * 24].rearrange("p (q n) -> p q n", n=24), ACT.Sigmoid).then_inc(*act_done.step("gates"))
                act.wait_ge(*pe_done("win"))
                a(sq[:, 1, :], ps[:, 5, :], ACT.Square).then_inc(*act_done.step("win sq"))
                for n, (name, bank) in enumerate((("slc", 3), ("win", 4))):
                    act.wait_ge(*pe_done(f"{name} sum"))
                    a(rstd[:, n, :], ps[:, bank, :], ACT.Sqrt, bias=const("rms_eps"), scale=1.0 / HD).then_inc(*act_done.step(f"{name} std"))
                act.wait_ge(*dve_done("z"))
                a(z[:, 1, :], z[:, 0, :], ACT.Abs).then_inc(*act_done.step("abs"))
                act.wait_ge(*act_done("abs"))
                a(z[:, 2, :], z[:, 1, :], ACT.Exp, scale=-1.0).then_inc(*act_done.step("exp"))
                act.wait_ge(*dve_done("1+e"))
                a(z[:, 3, :], z[:, 2, :], ACT.Ln).then_inc(*act_done.step("ln"))
                for u in range(2):
                    act.wait_ge(*pe_done(f"cmp{2 * u + 1}"))
                    for m in range(2):
                        a(hidden[:, u, m, :], ps[:, CMP_BANKS[u][m], 0:2 * NCMP], ACT.Silu).then_inc(*act_done.step(f"hid {'kv'[u]}{m}"))
                act.wait_ge(*pe_done("k2"))
                a(csq[:, 0, :], ps[:, 0, 0:NCMP], ACT.Square).then_inc(*act_done.step("k2 sq"))
                act.wait_ge(*pe_done("v2"))
                act.wait_ge(zeroed, 3)
                a(vcmp[0:NCMP, :], ps[0:NCMP, 6, 0:P], ACT.Copy).then_inc(*act_done.step("v2"))
                act.wait_ge(*pe_done("k2 sum"))
                a(csq[:, 1, :], ps[:, 1, 0:NCMP], ACT.Sqrt, bias=const("rms_eps"), scale=1.0 / HD).then_inc(*act_done.step("k2 std"))

            def dve(dve):
                dve_done.enter(dve)
                tt, ts, stt = nc.vector.tensor_tensor, nc.vector.tensor_scalar, nc.vector.scalar_tensor_tensor
                dve.wait_ge(*pe_done("fl"))
                ts(z[:, 0, :], ps[0:8, 4, :], vcol("b_forget")[0:8, :], None, ALU.add).then_inc(*dve_done.step("z"))
                dve.wait_ge(*pe_done("vals"))
                for b in range(2):
                    nc.vector.tensor_copy(vals[:, 2 * b:2 * b + 2, :], ps[:, 6 + b, :].rearrange("p (q n) -> p q n", q=2)).then_inc(*dve_done.step(f"vals{b}"))
                dve.wait_ge(att_in, 48)
                dve.wait_ge(*act_done("kc"))
                tt(cos[:, :], raw[:, 2, :], cc("cos"), ALU.mult).then_inc(*dve_done.step("kc cos"))
                dve.wait_ge(*pe_done("kc rot"))
                tt(sin[:, 2, :], ps[:, 0, :], cc("sin"), ALU.mult).then_inc(*dve_done.step("kc sin"))
                dve.wait_ge(*dve_done("kc sin"))
                tt(toks[:, 0, :], cos[:, :], sin[:, 2, :], ALU.add).then_inc(*dve_done.step("kc"))
                for n, (name, bank) in enumerate((("slc", 2), ("win", 5))):
                    dve.wait_ge(*act_done(f"{name} std"))
                    nc.vector.reciprocal(rstd[:, n, :], rstd[:, n, :]).then_inc(*dve_done.step(f"{name} rstd"))
                    dve.wait_ge(*dve_done(f"{name} rstd"))
                    stt(raw[:, n, :], ps[:, bank, :], vcol(f"k_{name}"), rstd[:, n, :], ALU.mult, ALU.mult).then_inc(*dve_done.step(f"{name} n"))
                for u, banks in (("v", (6, 7)), ("k", (0, 1))):
                    dve.wait_ge(*pe_done(f"{u} twice"))
                    for g in range(2):
                        for r in range(2):
                            for later in range(2):
                                rows, pairs = slice(r * HD, (r + 1) * HD), slice(8 * later, 8 * later + 8)
                                tokens = ps[rows, banks[g], CMP_S * later:CMP_S * (later + NCMP)].rearrange(
                                    "p (n e r) -> p e n r", e=8, r=2)[:, :, :, r]
                                a, _ = VC[f"pos_{u}"]
                                position = vec[rows, a + 8 * later:a + 8 * later + 8].unsqueeze(2).to_broadcast([HD, 8, NCMP])
                                tt(blocks[rows, "kv".index(u), pairs, g * NCMP:(g + 1) * NCMP], tokens, position,
                                   ALU.add).then_inc(*dve_done.step(f"blocks {u}{g}{r}{later}"))
                for n, (name, bank) in enumerate((("slc", 2), ("win", 5))):
                    dve.wait_ge(*dve_done(f"{name} n"))
                    tt(keys[name][:, :], raw[:, n, :], cc("cos"), ALU.mult).then_inc(*dve_done.step(f"{name} cos"))
                    dve.wait_ge(*pe_done(f"{name} rot"))
                    tt(sin[:, n, :], ps[:, bank, :], cc("sin"), ALU.mult).then_inc(*dve_done.step(f"{name} sin"))
                    dve.wait_ge(*dve_done(f"{name} sin"))
                    tt(keys[name][:, :], keys[name][:, :], sin[:, n, :], ALU.add).then_inc(*dve_done.step(f"{name} add"))
                dve.wait_ge(*act_done("exp"))
                ts(z[:, 2, :], z[:, 2, :], 1.0, None, ALU.add).then_inc(*dve_done.step("1+e"))
                ts(z[:, 1, :], z[:, 0, :], 0.0, None, ALU.min).then_inc(*dve_done.step("min"))
                dve.wait_ge(*dve_done("min"))
                dve.wait_ge(*act_done("ln"))
                tt(z[:, 0, :], z[:, 1, :], z[:, 3, :], ALU.subtract).then_inc(*dve_done.step("logf"))
                dve.wait_ge(*dve_done("logf"))
                dve.wait_ge(zeroed, 3)
                nc.vector.tensor_tensor_scan(c2[:, 0, :], z[:, 4, :], z[:, 0, :], 0.0, ALU.mult, ALU.add).then_inc(*dve_done.step("cum"))
                dve.wait_ge(*dve_done("cum"))
                ts(c2[:, 1, :], c2[:, 0, :], -1.0, None, ALU.mult).then_inc(*dve_done.step("-cum"))
                dve.wait_ge(*act_done("k2 std"))
                nc.vector.reciprocal(csq[:, 2, :], csq[:, 1, :]).then_inc(*dve_done.step("k2 rstd"))
                dve.wait_ge(*dve_done("k2 rstd"))
                stt(kcmp[:, 0:NCMP], ps[:, 0, 0:NCMP], vcol("k_cmp"), csq[:, 2, :], ALU.mult, ALU.mult).then_inc(*dve_done.step("k2"))

            phase(sp=sp, pool=pool, pe=pe, act=act, dve=dve)
            return t, cc, [(dve_done, "k2"), (act_done, "v2")], sums_out

        def head_inputs(scope, h, cc, ready):
            N = 4
            out = {n: keep(f"heads_{n}", [P, N, T], scope) for n in ("nsa_q", "fox_q", "fox_k", "fox_v")}
            NQ, FQ, FK, V, NSUM, QSUM, KSUM, ROT = 7, 1, 2, 3, 4, 5, 6, 0
            pe_done = steps("heads_pe", ["nq", "fq", "nq sum", "fk", "fq sum", "v", "rot", "fk sum"])
            act_done = steps("heads_act", ["nq sq", "fq sq", "nq std", "fk sq", "fq std", "v", "fk std"])
            scaled = sem("heads_gains_scaled")
            dve_done = steps("heads_dve", ["nq rstd", "nq n", "nq cos", "fq rstd", "fq", "nq sin", "nq", "fk rstd", "fk"])
            n_load, f_load = Loads(0, N, pe_done, "nq"), Loads(1, N, pe_done, "v")
            with ExitStack() as own:
                sq, std = ({n: keep(f"heads_{n}_{m}", [P, T], own) for n in ("nq", "fq", "fk")} for m in ("sq", "std"))
                qn, qc, qsin = (keep(f"heads_nq_{m}", [P, T], own) for m in ("n", "cos", "sin"))
                gains = keep("heads_query_gains", [P, 2], own)

            def sp(sp):
                sp.wait_ge(*n_load.vacated())
                sp.wait_ge(*f_load.vacated())
                with sp.Fori(0, N) as i:
                    for load, stream in ((n_load, "nsa_q"), (f_load, "fox_qkv")):
                        sp.wait_ge(*load.vacated(i))
                        sp.dma_start(load.slot(row(stream, i)), row(stream, i)).then_inc(*load.arrival)

            def pe(pe):
                pe_done.enter(pe)

                def product(bank, s, at, name):
                    for k in range(KT):
                        last = mm(ps[:, bank, :], wtile(s, at + k), h[:, k, :], k == 0, k == KT - 1)
                    last.then_inc(*pe_done.step(name))

                def turn(i, first):
                    pe.wait_ge(*n_load.arrived(i))
                    pe.wait_ge(*dve_done("nq n", i, 1))
                    product(NQ, 0, 0, "nq")
                    if first:
                        for r in ready:
                            pe.wait_ge(*reached(*r))
                    pe.wait_ge(*f_load.arrived(i))
                    pe.wait_ge(*dve_done("fq", i, 1))
                    product(FQ, 1, 0, "fq")
                    pe.wait_ge(*act_done("nq sq", i))
                    mm(ps[:, NSUM, :], blockones, sq["nq"][:, :]).then_inc(*pe_done.step("nq sum"))
                    pe.wait_ge(*dve_done("fk", i, 1))
                    product(FK, 1, KT, "fk")
                    pe.wait_ge(*act_done("fq sq", i))
                    mm(ps[:, QSUM, :], blockones, sq["fq"][:, :]).then_inc(*pe_done.step("fq sum"))
                    pe.wait_ge(*act_done("v", i, 1))
                    for b in range(QT):
                        for k in range(KT):
                            last = mm(ps[:, V, b * P:(b + 1) * P], h[:, k, b * P:(b + 1) * P], wtile(1, 2 * KT + k), k == 0, k == KT - 1)
                    last.then_inc(*pe_done.step("v"))
                    pe.wait_ge(*dve_done("nq n", i))
                    mm(ps[:, ROT, :], cc("rot"), qn[:, :]).then_inc(*pe_done.step("rot"))
                    pe.wait_ge(*act_done("fk sq", i))
                    mm(ps[:, KSUM, :], blockones, sq["fk"][:, :]).then_inc(*pe_done.step("fk sum"))
                turn(0, True)
                with pe.Fori(1, N) as i:
                    turn(i, False)

            def act(act):
                act_done.enter(act)

                def square(name, bank, i):
                    act.wait_ge(*pe_done(name, i))
                    nc.scalar.activation(sq[name][:, :], ps[:, bank, :], ACT.Square).then_inc(*act_done.step(f"{name} sq"))

                def root(name, bank, read_by, i):
                    act.wait_ge(*pe_done(f"{name} sum", i))
                    act.wait_ge(*dve_done(read_by, i, 1))
                    nc.scalar.activation(std[name][:, :], ps[:, bank, :], ACT.Sqrt, bias=const("rms_eps"), scale=1.0 / HD).then_inc(
                        *act_done.step(f"{name} std"))
                for r in ready:
                    act.wait_ge(*reached(*r))
                with act.Fori(0, N) as i:
                    square("nq", NQ, i)
                    square("fq", FQ, i)
                    root("nq", NSUM, "nq n", i)
                    square("fk", FK, i)
                    root("fq", QSUM, "fq", i)
                    act.wait_ge(*pe_done("v", i))
                    alone(act)
                    nc.scalar.activation(tile_of(out["fox_v"], i), ps[:, V, :], ACT.Copy).then_inc(*act_done.step("v"))
                    root("fk", KSUM, "fk", i)

            def dve(dve):
                dve_done.enter(dve)
                tt, stt = nc.vector.tensor_tensor, nc.vector.scalar_tensor_tensor

                def normed(name, bank, gain, to, step, i):
                    dve.wait_ge(*act_done(f"{name} std", i))
                    nc.vector.reciprocal(std[name][:, :], std[name][:, :]).then_inc(*dve_done.step(f"{name} rstd"))
                    dve.wait_ge(*dve_done(f"{name} rstd", i))
                    alone(dve)
                    stt(to, ps[:, bank, :], gain, std[name][:, :], ALU.mult, ALU.mult).then_inc(*dve_done.step(step))
                for r in ready:
                    dve.wait_ge(*reached(*r))
                for n, name in enumerate(("q_nsa", "q_fox")):
                    nc.vector.tensor_scalar(gains[:, n:n + 1], vcol(name), HD ** -0.5, None, ALU.mult).then_inc(scaled, 1)
                dve.wait_ge(scaled, 2)
                with dve.Fori(0, N) as i:
                    dve.wait_ge(*pe_done("rot", i, 1))
                    normed("nq", NQ, gains[:, 0:1], qn[:, :], "nq n", i)
                    dve.wait_ge(*dve_done("nq n", i))
                    dve.wait_ge(*dve_done("nq", i, 1))
                    tt(qc[:, :], qn[:, :], cc("cos"), ALU.mult).then_inc(*dve_done.step("nq cos"))
                    normed("fq", FQ, gains[:, 1:2], tile_of(out["fox_q"], i), "fq", i)
                    dve.wait_ge(*pe_done("rot", i))
                    tt(qsin[:, :], ps[:, ROT, :], cc("sin"), ALU.mult).then_inc(*dve_done.step("nq sin"))
                    dve.wait_ge(*dve_done("nq sin", i))
                    alone(dve)
                    tt(tile_of(out["nsa_q"], i), qc[:, :], qsin[:, :], ALU.add).then_inc(*dve_done.step("nq"))
                    normed("fk", FK, vcol("k_fox"), tile_of(out["fox_k"], i), "fk", i)

            phase(sp=sp, pe=pe, act=act, dve=dve)
            return out, [(dve_done, "fk", N - 1), (act_done, "fk std", N - 1)]

        def pair_queries(name, scope, source, ready):
            qz = keep(f"{name}_queries", [P, 2, T], scope)
            zeroed = sem(f"{name}_queries_zeroed")

            def pool(pool):
                for r in ready:
                    pool.wait_ge(*reached(*r))
                nc.gpsimd.memset(qz[:, :, :], 0.0).then_inc(zeroed, 1)

            def copies(dve, i, S, last):
                dve.wait_ge(zeroed, 1)
                dve.wait_ge(*S["pe"](last, i, 1))
                alone(dve)
                for hh in range(2):
                    r = slice(hh * HD, (hh + 1) * HD)
                    nc.vector.tensor_copy(qz[r, hh, :], tile_of(source, i)[r, :]).then_inc(*S["dve"].step(f"q{hh}"))
            return qz, pool, copies

        def grouped_attention(scope, queries, t, cc, ready, out):
            gst = keep("pair_gates", [P, QT, 6], scope)
            N = 4
            qz, pool, copy_queries = pair_queries("nsa", scope, queries, ready)
            work = []
            for hh in range(2):
                for q in STEP_TILES:
                    for b, (keys, v0) in enumerate(((t["keys_cmp"], None), (t["keys_slc"], 0), (t["keys_win"], P))):
                        w = P if b == 0 else (q + 1) * P
                        mask = cc("cmp_mask")[:, q * P:(q + 1) * P] if b == 0 else cc("causal")[:, T - w:T]
                        values = ([t["values_cmp"][:, hh * HD:(hh + 1) * HD]] if b == 0 else
                                  [t["values"][:, s, v0 + hh * HD:v0 + (hh + 1) * HD] for s in range(q + 1)])
                        work.append({"head": hh, "tile": q, "w": w, "query": qz[:, hh, q * P:(q + 1) * P], "keys": keys[:, 0:w],
                                     "mask": mask, "values": values, "gate": gst[:, q, hh * 3 + b:hh * 3 + b + 1],
                                     "first": b == 0, "last": b == 2})

            def before_pe(pe, i, S):
                pe.wait_ge(*S["dve"]("q1", i))

            def before_act(act, i, S):
                pass

            def before_dve(dve, i, S):
                copy_queries(dve, i, S, f"L{W - 1}")
                dve.wait_ge(*S["dve"](f"diag{W - 1}", i, 1))
                alone(dve)
                nc.vector.tensor_copy(gst[:, :, :], t["gates"][:, :, bass.ds(i * 6, 6)]).then_inc(*S["dve"].step("gates"))
                dve.wait_ge(*S["dve"]("gates", i))
                if_valid = cc("cmp_valid")[:, 0:1]
                for hh in range(2):
                    nc.vector.tensor_scalar(gst[:, 0, hh * 3:hh * 3 + 1], gst[:, 0, hh * 3:hh * 3 + 1], if_valid, None,
                                                          ALU.mult).then_inc(*S["dve"].step(f"valid{hh}"))

            W = len(work)
            S = attend("nsa", scope, N, work, out, ready,
                       {"pe": ([], before_pe), "act": ([], before_act),
                        "dve": (["q0", "q1", "gates", "valid0", "valid1"], before_dve)})
            phase(pool=pool)
            return [(S["act"], "out", N - 1)], [(S["pe"], f"O{W - 1}", N - 1)]

        def forget_sides(scope, ready):
            left, right = (keep(f"forget_{n}", [P, 2, T], scope) for n in ("left", "right"))
            zeroed = sem("fox_zeroed")

            def pool(pool):
                for r in ready:
                    pool.wait_ge(*reached(*r))
                for n in (left, right):
                    nc.gpsimd.memset(n[:, :, :], 0.0).then_inc(zeroed, 1)
                pool.wait_ge(zeroed, 2)
                nc.gpsimd.memset(left[32:33, :, :], 1.0).then_inc(zeroed, 1)
                nc.gpsimd.memset(right[0:1, :, :], 1.0).then_inc(zeroed, 1)
                pool.wait_ge(zeroed, 4)
            return (left, right, zeroed), pool

        def forgetting_attention(scope, heads, cc, ready, sums_out, sides, out):
            N = 4
            W = 2 * QT
            left, right, zeroed = sides
            qz, pool_queries, copy_queries = pair_queries("fox", scope, heads["fox_q"], ready)
            vals = keep("fox_values", [P, QT, P], scope)
            sums_in = sem("forget_sums_in")
            work = []
            for hh in range(2):
                for q in STEP_TILES:
                    w = (q + 1) * P
                    tok = slice(q * P, (q + 1) * P)
                    work.append({"head": hh, "tile": q, "w": w, "query": qz[:, hh, tok], "keys_of_turn": heads["fox_k"],
                                 "mask": cc("causal")[:, T - w:T], "extra": (left[:, hh, tok], right[:, hh, 0:w]),
                                 "values": [vals[:, s, hh * HD:(hh + 1) * HD] for s in range(q + 1)], "first": True, "last": True})

            def before_pe(pe, i, S):
                pe.wait_ge(sums_in, i * 32 + 32)
                pe.wait_ge(*S["dve"]("values", i))

            def before_act(act, i, S):
                pass

            def before_dve(dve, i, S):
                copy_queries(dve, i, S, f"L{W - 1}")
                dve.wait_ge(*S["pe"](f"O{W - 1}", i, 1))
                alone(dve)
                nc.vector.tensor_copy(vals[:, :, :], tile_of(heads["fox_v"], i).rearrange("p (b n) -> p b n", n=P)).then_inc(
                    *S["dve"].step("values"))

            phase(pool=pool_queries)
            S = attend("fox", scope, N, work, out, ready,
                       {"pe": ([], before_pe), "act": ([], before_act), "dve": (["q0", "q1", "values"], before_dve)})

            def sp(sp):
                sp.wait_ge(sums_out, 16)
                sp.wait_ge(zeroed, 4)
                sums = d["forget_scratch"]
                sp.dma_start(left[0:1, :, :], sums[0:1, 0:2, :]).then_inc(sums_in, 16)
                sp.dma_start(right[32:33, :, :], sums[1:2, 0:2, :]).then_inc(sums_in, 16)
                with sp.Fori(1, N) as i:
                    sp.wait_ge(*S["pe"](f"L{W - 1}", i, 1))
                    sp.dma_start(left[0:1, :, :], sums[0:1, bass.ds(i * 2, 2), :]).then_inc(sums_in, 16)
                    sp.dma_start(right[32:33, :, :], sums[1:2, bass.ds(i * 2, 2), :]).then_inc(sums_in, 16)

            phase(sp=sp)
            return [(S["act"], "out", N - 1)]

        def gated_embedding(scope, source, split, x_ready):
            emb = keep("embedding", [P, 2, T], scope)
            weights = keep("embedding_weights", [P, KT * 2 * P], scope)
            e = keep("projected", [P, KT, T], scope)
            g = keep("embedding_gate", [P, 2, T], scope)
            n = KT // 2
            width = KT * P
            written = sem("result_written")
            e_pe, e_act = (steps(f"embedding_{m}", [f"e{j}" for j in range(KT)]) for m in ("pe", "act"))
            pe_done = steps("ple_pe", ["gate0", "gate1"])
            act_done = steps("ple_act", ["gate0", "gate1"])
            dve_done = steps("ple_dve", ["gated0", "sum0", "gated1", "sum1"])
            hi_split, lo_split = (steps(f"ple_{m}_split", [f"{m}0", f"{m}1"]) for m in ("hi", "lo"))
            loads = [Loads(s, n, lo_split, f"lo{s}") for s in range(2)]

            def unit_hi(s):
                nc.scalar.activation(split.hi[s][:, 0:width], slot[s][:, 0:width], ACT.Copy).then_inc(*hi_split.step(f"hi{s}"))

            def unit_lo(s):
                nc.vector.tensor_tensor(split.lo[s][:, 0:width], slot[s][:, 0:width], split.hi[s][:, 0:width].bitcast(F32),
                                        ALU.subtract).then_inc(*lo_split.step(f"lo{s}"))

            def between(act, j):
                if j == 0:
                    e_act.enter(act)
                    hi_split.enter(act)
                    for s in range(2):
                        act.wait_ge(*loads[s].arrived(0))
                        unit_hi(s)
                act.wait_ge(*e_pe(f"e{j}"))
                nc.scalar.activation(e[:, j, :], ps[:, j % 4, :], ACT.Copy).then_inc(*e_act.step(f"e{j}"))

            branch = rms_norm("rms4", scope, [x[:, j, :] for j in range(KT)], x_ready, [vcol("ple_gate", j) for j in range(KT)],
                              tuple([part[:, j, :] for j in range(KT)] for part in source), between)

            def sp(sp):
                sp.wait_ge(*reached(*x_ready[KT - 1]))
                sp.dma_start(weights[:, :], d["embedding_weights"][:, :]).then_inc(once_in, 16)
                sp.dma_start(emb[:, :, :], d["embedding"][:, :, :]).then_inc(once_in, 16)
                for s in range(2):
                    sp.wait_ge(*loads[s].vacated())
                    sp.dma_start(loads[s].slot(row("ple", s)), row("ple", s)).then_inc(*loads[s].arrival)

            def pe(pe):
                e_pe.enter(pe)
                pe.wait_ge(once_in, 64)
                for j in range(KT):
                    if j >= 4:
                        pe.wait_ge(*e_act(f"e{j - 4}"))
                    for k in range(2):
                        last = mm(ps[:, j % 4, :], weights[:, (2 * j + k) * P:(2 * j + k + 1) * P], emb[:, k, :], k == 0, k == 1)
                    last.then_inc(*e_pe.step(f"e{j}"))
                pe.wait_ge(*reached(*branch[0]))

            def dve(dve):
                lo_split.enter(dve)
                for s in range(2):
                    dve.wait_ge(*hi_split(f"hi{s}"))
                    unit_lo(s)

            phase(sp=sp, pe=pe, dve=dve)
            tiles = [e[:, j, :] for j in range(KT)]
            normed = rms_norm("ple_norm", scope, tiles, [(e_act, f"e{j}") for j in range(KT)], [vcol("ple", j) for j in range(KT)], tiles)

            def sp_gates(sp):
                with sp.Fori(1, n) as i:
                    for s in range(2):
                        sp.wait_ge(*loads[s].vacated(i))
                        sp.dma_start(loads[s].slot(row("ple", i * 2 + s)), row("ple", i * 2 + s)).then_inc(*loads[s].arrival)
                for j in range(KT):
                    sp.wait_ge(*dve_done(f"sum{j % 2}", j // 2))
                    sp.dma_start(d["out"][:, j, :], x[:, j, :]).then_inc(written, 16)
                sp.wait_ge(written, 16 * KT)

            def pe_gates(pe):
                pe_done.enter(pe)

                def turn(i, first):
                    for s in range(2):
                        pe.wait_ge(*lo_split(f"lo{s}", i))
                        pe.wait_ge(*act_done(f"gate{s}", i, 1))
                        for k in range(KT):
                            if first and s == 0:
                                pe.wait_ge(*reached(*branch[k]))
                            last = three_passes(ps[:, 6 + s, :], split, s, k, (source[0][:, k, :], source[1][:, k, :]),
                                                k == 0, k == KT - 1)
                        last.then_inc(*pe_done.step(f"gate{s}"))
                turn(0, True)
                with pe.Fori(1, n) as i:
                    turn(i, False)

            def act_gates(act):
                act_done.enter(act)

                def turn(i, more):
                    for s in range(2):
                        if more:
                            act.wait_ge(*loads[s].arrived(i + 1))
                            act.wait_ge(*pe_done(f"gate{s}", i))
                            unit_hi(s)
                        act.wait_ge(*pe_done(f"gate{s}", i))
                        act.wait_ge(*dve_done(f"gated{s}", i, 1))
                        nc.scalar.activation(g[:, s, :], ps[:, 6 + s, :], ACT.Sigmoid).then_inc(*act_done.step(f"gate{s}"))
                with act.Fori(0, n - 1) as i:
                    turn(i, True)
                turn(n - 1, False)

            def dve_gates(dve):
                dve_done.enter(dve)

                def turn(i, more):
                    for s in range(2):
                        j = i * 2 + s
                        if more:
                            dve.wait_ge(*hi_split(f"hi{s}", i + 1))
                            unit_lo(s)
                        dve.wait_ge(*act_done(f"gate{s}", i))
                        alone(dve)
                        nc.vector.tensor_tensor(tile_of(e, j), tile_of(e, j), g[:, s, :], ALU.mult).then_inc(*dve_done.step(f"gated{s}"))
                        dve.wait_ge(*dve_done(f"gated{s}", i))
                        alone(dve)
                        nc.vector.tensor_tensor(tile_of(x, j), tile_of(x, j), tile_of(e, j), ALU.add).then_inc(*dve_done.step(f"sum{s}"))
                dve.wait_ge(*reached(*normed[KT - 1]))
                with dve.Fori(0, n - 1) as i:
                    turn(i, True)
                turn(n - 1, False)

            phase(sp=sp_gates, pe=pe_gates, act=act_gates, dve=dve_gates)

        ready = modulation()
        with ExitStack() as outer:
            hin = keep("branch_in", [P, KT, T + 1], outer)
            with ExitStack() as scope:
                xs, lora, mix_pe, mix_act, mix_dve = time_mix_inputs(scope, hin, ready)
                yout, rec_done, name, turn = recurrence(scope, hin[:, :, 1:T + 1], xs, lora, mix_pe, mix_act, mix_dve)
            recurred = (rec_done, name, turn)
            scaled = residual_again([recurred])
            summed = project("rwkv_out", "rwkv_out", [yout[:, k, :] for k in range(KT)], [recurred], (0, GT1), [scaled])
        with ExitStack() as outer:
            source = parts_of("ff0_in", outer)
            units = Halves("ff0", Split("ff0_weights", outer), 2 * KT, HT // 2)
            with ExitStack() as scope:
                branch, x_ready = layer_norm("ln00", scope, 0, 0, summed, (0, SH2, SC2, source), units)

            with ExitStack() as scope:
                summed = feed_forward(units, scope, source, branch, (0, GT2), x_ready)
        with ExitStack() as outer:
            h = keep("attention_in", [P, KT, T], outer)
            with ExitStack() as scope:
                branch, x_ready = layer_norm("ln01", scope, 0, 1, summed, (1, SH1, SC1, h))

            with ExitStack() as scope:
                split = Split("dsa_out_weights", scope)
                mixed = parts_of("attended", scope)
                done = sparse_attention(scope, h, branch, mixed)
                summed = split_project_alone("dsa_out", split, [(mixed[0][:, k, :], mixed[1][:, k, :]) for k in range(KT)],
                                             [done, done], branch[KT - 1], (1, GT1), x_ready)
        with ExitStack() as outer:
            source = parts_of("ff1_in", outer)
            units = Halves("ff1", Split("ff1_weights", outer), 2 * KT, HT // 2)
            with ExitStack() as scope:
                branch, x_ready = layer_norm("ln10", scope, 1, 0, summed, (1, SH2, SC2, source), units)

            with ExitStack() as scope:
                summed = feed_forward(units, scope, source, branch, (1, GT2), x_ready)
        tiles_of_x = [x[:, j, :] for j in range(KT)]

        def tiles_of(t):
            return [t[:, j, :] for j in range(KT)]

        def gains(name):
            return [vcol(name, j) for j in range(KT)]
        with ExitStack() as scope:
            normed, _ = layer_norm("ln11", scope, 1, 1, summed, None)
        square, squares_total = keep("tile_square", [P, T]), keep("squares_total", [P, T])[:, :]
        with ExitStack() as outer:
            source = parts_of("ffn1_in", outer)
            units = Halves("ffn1", Split("ffn1_weights", outer), 2 * KT, HT // 2)
            with ExitStack() as scope:
                branch = rms_norm("rms1", scope, tiles_of_x, normed, gains("ffn1"), (tiles_of(source[0]), tiles_of(source[1])), units=units)
            with ExitStack() as scope:
                summed = feed_forward(units, scope, source, branch, 0.5)

        with ExitStack() as outer:
            h = keep("mixer_in", [P, KT, T], outer)
            with ExitStack() as scope:
                branch = rms_norm("rms2", scope, tiles_of_x, summed, gains("mix"), tiles_of(h))
            with ExitStack() as scope:
                mixed = keep("mixed", [P, KT, T], scope)
                with ExitStack() as parts:
                    t, cc, ready, sums_out = mixer_inputs(parts, h, branch)
                    heads, ready = head_inputs(parts, h, cc, ready)
                    sides, zero_sides = forget_sides(parts, ready)
                    with ExitStack() as own:
                        nsa_done, nsa_pe = grouped_attention(own, heads["nsa_q"], t, cc, ready, mixed[:, 0:4, :])
                    phase(pool=zero_sides)
                    with ExitStack() as own:
                        fox_done = forgetting_attention(own, heads, cc, nsa_done + nsa_pe, sums_out, sides, mixed[:, 4:8, :])
                with ExitStack() as own:
                    units = Halves("mix_out", Split("mix_out_weights", own), KT, KT // 2)
                    normed = parts_of("mixed_normed", own)
                    outs, later = [], []
                    for n, part in enumerate(("nsa", "fox")):
                        part_tiles = [mixed[:, 4 * n + j, :] for j in range(4)]
                        outs += rms_norm(f"rms_{part}", own, part_tiles, [fox_done[0]] * 4,
                                         [vcol("out_norm", 4 * n + j) for j in range(4)],
                                         tuple([half[:, 4 * n + j, :] for j in range(4)] for half in normed),
                                         units=units if n == 0 else None, bank=5 - n, later=later)
                    for program in later:
                        phase(act=program)
                    summed = split_project(units, "mix_out", [(normed[0][:, k, :], normed[1][:, k, :]) for k in range(KT)],
                                           [outs[0:4], outs[4:8]], 1.0, ())

        with ExitStack() as outer:
            source = parts_of("ffn2_in", outer)
            units = Halves("ffn2", Split("ffn2_weights", outer), 2 * KT, HT // 2)
            with ExitStack() as scope:
                branch = rms_norm("rms3", scope, tiles_of_x, summed, gains("ffn2"), (tiles_of(source[0]), tiles_of(source[1])), units=units)
            with ExitStack() as scope:
                summed = feed_forward(units, scope, source, branch, 0.5)
        with ExitStack() as scope:
            source = parts_of("embedding_gate_in", scope)
            split = Split("embedding_gate_weights", scope)
            gated_embedding(scope, source, split, summed)

        block = ctx.enter_context(nc.Block())

        @block.sync
        def _(eng):
            for program in programs["sp"]:
                program(eng)

        @block.tensor
        def _(eng):
            for program in programs["pe"]:
                program(eng)

        @block.scalar
        def _(eng):
            for program in programs["act"]:
                program(eng)

        @block.vector
        def _(eng):
            for program in programs["dve"]:
                program(eng)

        @block.gpsimd
        def _(eng):
            for program in programs["pool"]:
                program(eng)


def constant_tables():
    s, t = np.arange(P)[:, None], np.arange(P)[None, :]
    same = (s // CH) == (t // CH)
    ca = np.zeros((P, CA["all"][1]), np.float32)
    cr = np.zeros((P, CR["all"][1]), np.float32)
    cb = np.zeros((P, CB["all"][1]), np.float32)

    def put(table, where, name, values):
        a, n = where[name]
        table[:np.shape(values)[0], a:a + n] = np.reshape(values, (np.shape(values)[0], n))

    put(ca, CA, "ident", s == t)
    put(ca, CA, "blockones", same)
    put(ca, CA, "ones", np.ones((P, P)))
    for name, eps in (("ln_eps", 1e-5), ("gn_eps", HD * 1e-5), ("rms_eps", 1e-6)):
        put(ca, CA, name, np.full((P, 1), eps))
    put(cr, CR, "strict", same & (s < t))
    put(cr, CR, "incl", same & (s <= t))
    for k in range(6):
        put(cr, CR, f"level{k}", ((s >> (k + 1)) == (t >> (k + 1))) & ((s >> k) % 2 == 0) & ((t >> k) % 2 == 1))
    put(cr, CR, "reset", np.tile(np.arange(T) % CH != 0, (P, 1)))
    put(cb, CB, "flip", s + t == P - 1)
    u = np.arange(T)[None, :]
    put(cb, CB, "causal", np.where(u - (T - P) > s, NEG, 0.0))
    half = HD // 8
    inv = np.float32(500000.0) ** (-np.arange(0, 2 * half, 2, dtype=np.float32) / np.float32(2 * half))
    angle = np.arange(T, dtype=np.float32)[None, :] * inv[:, None]
    cos, sin, rot = np.ones((HD, T)), np.zeros((HD, T)), np.zeros((P, P))
    for part in range(2):
        cos[part * half:(part + 1) * half] = np.cos(angle)
        sin[part * half:(part + 1) * half] = np.sin(angle)
    put(cb, CB, "cos", np.tile(cos, (2, 1)))
    put(cb, CB, "sin", np.tile(sin, (2, 1)))
    for g in range(2):
        for e in range(half):
            rot[g * HD + e + half, g * HD + e] = -1.0
            rot[g * HD + e, g * HD + e + half] = 1.0
    put(cb, CB, "rot", rot)
    for g in range(2):
        put(cb, CB, f"twice{g}", s == g * HD + t % HD)
    token = np.arange(P)[:, None, None] + P * np.arange(QT)[None, :, None]
    ends = np.arange(P)[None, None, :] * CMP_S + CMP_L - 1
    put(cb, CB, "cmp_mask", np.where((ends <= token) & (np.arange(P) < NCMP), 0.0, NEG))
    put(cb, CB, "cmp_valid", token[:, :, 0] >= CMP_L - 1)
    n = np.maximum(T - 1 - np.arange(BIAS_LEN), 0)
    large = 16 + (np.log(np.maximum(n, 1).astype(np.float32) / np.float32(16)) / np.float32(math.log(128 / 16))
                  * np.float32(16)).astype(np.int32)
    bucket = np.where(n < 16, n, np.minimum(large, 31))
    put(cb, CB, "onehot", bucket[None, :] == np.arange(32)[:, None])
    return ca, cr, cb


def kernel(**inputs):
    import concourse.bacc as bacc
    from concourse.bass_utils import run_bass_kernel_spmd

    a = {k: np.asarray(v) for k, v in inputs.items()}

    def tiles(w):
        k, m = w.shape
        return w.reshape(k // P, P, m // P, P).transpose(2, 1, 0, 3).reshape(m // P, P, (k // P) * P)

    def rows(w):
        return w.reshape(-1, P, w.shape[1]).transpose(1, 0, 2).reshape(P, -1)

    def col(v):
        return v.reshape(-1, P).T

    def pad(w, n):
        return np.concatenate([w, np.zeros((n - w.shape[0],) + w.shape[1:], np.float32)], 0)

    def feature_major(v):
        return np.ascontiguousarray(v.reshape(T, -1, P).transpose(2, 1, 0))

    ca, cr, cb = constant_tables()
    d = {"const_all": ca, "const_recurrence": cr, "const_attention": cb, "x": feature_major(a["x"][0])}
    pair = np.stack([col(a[n].reshape(-1)) for n in ("rwkv_w0", "rwkv_a0", "rwkv_k_k", "rwkv_k_a", "rwkv_r_k", "rwkv_lnx_g",
                                                     "rwkv_lnx_b")], 2).reshape(P, -1)
    order = np.concatenate([np.arange(g * 256 + j * HD, g * 256 + j * HD + HD) for j in range(4) for g in range(2)])

    def twice(v):
        return np.concatenate([v.reshape(-1)] * 2)[:, None]

    def two_by_two(v):
        return v.reshape(-1, P).T

    vectors = [col(a["ada_b"]), col(a["ln_g"]), col(a["ln_b"]), col(a["rwkv_mu"]), pair, col(a["ffn1_norm_2"]),
               col(a["mix_norm_2"]), col(a["ffn2_norm_2"]), col(a["ple_gate_norm_2"]), col(a["ple_norm_2"]),
               col(np.concatenate([a["out_norm_nsa_2"][0][order], a["out_norm_fox_2"][0]])), col(a["dsa_kv_norm"]),
               twice(a["q_norm_nsa_2"]), twice(a["k_norm_cmp_2"]), twice(a["k_norm_slc_2"]), twice(a["k_norm_win_2"]),
               twice(a["q_norm_fox_2"]), twice(a["k_norm_fox_2"]), pad(a["b_forget_2"].reshape(-1, 1), P),
               two_by_two(a["cmp_pos_k_2"][0]), two_by_two(a["cmp_pos_v_2"][0])]
    d["vectors"] = np.concatenate(vectors, 1)
    d["ada"] = np.concatenate([a["ada_w"][i].T.reshape(6 * KT, P, D) for i in range(2)])
    d["c_rows"] = np.broadcast_to(a["c"].reshape(1, D), (P, D))
    d["lora1"] = rows(np.concatenate([a["rwkv_w1"][0], a["rwkv_a1"][0], a["rwkv_g1"][0]], 1))[None]
    second = [tiles(pad(w, P)) for w in (a["rwkv_w2"][0], a["rwkv_a2"][0], a["rwkv_g2"][0][:P], a["rwkv_g2"][0][P:])]
    d["rwkv"] = np.concatenate([tiles(a["rwkv_w_rkv"][0, m]) for m in range(3)] + second, 2)
    d["rwkv_out"] = tiles(a["rwkv_w_out"][0])

    def feed_forward(name, gate, up, down):
        d[f"{name}_in"] = np.concatenate([tiles(gate), tiles(up)], 2)
        d[f"{name}_out"] = tiles(down)

    for i in range(2):
        feed_forward(f"ff{i}", a["ffn_w_in"][i][:, :HID], a["ffn_w_in"][i][:, HID:], a["ffn_w_out"][i])
    for i in (1, 2):
        feed_forward(f"ffn{i}", a[f"ffn{i}_wg_2"][0], a[f"ffn{i}_wu_2"][0], a[f"ffn{i}_wd_2"][0])
    w = a["dsa_w_in"][0]
    cut = [D, D + P, D + P + 512, D + P + 576]
    wq, wc, wqi, wki, wwi = np.split(w, cut, 1)
    d["dsa_first"] = np.concatenate([tiles(wc)[0], tiles(np.concatenate([wki, wki], 1))[0], rows(wwi)], 1)[None]
    d["dsa_index"] = tiles(wqi).reshape(2, 2, P, D).transpose(0, 2, 1, 3).reshape(2, P, 2 * D)
    uk, uv = a["dsa_w_uk"][0], a["dsa_w_uv"][0]
    none = np.zeros((8, HD, P), np.float32)
    d["dsa_q"] = tiles(wq)
    d["dsa_heads"] = np.concatenate([np.concatenate([uk[0::2], none], 1), np.concatenate([none, uk[1::2]], 1),
                                     np.concatenate([uv[0::2], uv[1::2]], 2)], 2)
    d["dsa_out"] = tiles(a["dsa_w_out"][0])
    d["rel_bias"] = a["rel_bias"]
    sizes = (512, P, P, P, P, P, P, 24, 512, 512, 512, 8)
    qa, kc, vc, ks, vs, kw, vw, ga, qf, kf, vf, fl = np.split(a["w_in_2"][0], np.cumsum(sizes)[:-1], 1)
    ga = ga.reshape(D, 2, 4, 3).transpose(0, 2, 1, 3).reshape(D, 24)
    d["mix_0"] = np.concatenate([tiles(kc)[0], tiles(vc)[0], tiles(ks)[0], rows(ga), rows(fl)], 1)[None]
    d["mix_1"] = np.concatenate([tiles(kw)[0], rows(np.concatenate([vs, vw], 1))], 1)[None]
    d["nsa_q"] = tiles(qa[:, order])
    d["fox_qkv"] = np.concatenate([tiles(qf), tiles(kf), tiles(vf)], 2)

    def first_map(w):
        return w.reshape(2, 8, P, 256).transpose(0, 2, 1, 3).reshape(2, P, 8 * 256)

    d["cmp_w1"] = np.concatenate([first_map(a["cmp_k_w1_2"][0]), first_map(a["cmp_v_w1_2"][0])])
    d["cmp_w2"] = np.concatenate([rows(a["cmp_k_w2_2"][0]), rows(a["cmp_v_w2_2"][0])], 1)
    w = a["w_out_2"][0]
    d["mix_out"] = tiles(np.concatenate([w[:512][order], w[512:]]))
    d["ple"] = tiles(a["ple_w_gate_2"][0])
    d["embedding_weights"] = tiles(a["ple_w_proj_2"][0]).transpose(1, 0, 2).reshape(P, -1)
    d["embedding"] = feature_major(a["p_2"][0, 0])
    d = {k: np.ascontiguousarray(v) for k, v in d.items()}

    nc = bacc.Bacc("TRN2", target_bir_lowering=False, num_devices=1)
    d = {"in_" + k: v for k, v in d.items()}
    t = {k[3:]: nc.dram_tensor(k, v.shape, F32, kind="ExternalInput").ap() for k, v in d.items()}
    t["out"] = nc.dram_tensor("out_features", (P, KT, T), F32, kind="ExternalOutput").ap()
    scratch = nc.dram_tensor("bias_scratch", (16, BIAS_LEN), F32, kind="Internal")
    t["bias_scratch"] = scratch.ap()
    t["forget_scratch"] = nc.dram_tensor("forget_scratch", (2, 8, T), F32, kind="Internal").ap()
    build(nc, t)
    got = run_bass_kernel_spmd(nc, [d], core_ids=[0]).results[0]["out_features"]
    return np.ascontiguousarray(got.transpose(2, 1, 0)).reshape(1, T, D)
```
